# Optimizing a Trainium2 kernel written in Bass

```python
import math
import jax, jax.numpy as jnp
from jax import lax
import numpy as np

D_MODEL = 1024
BATCH = 1
SEQ = 2048
DEPTH = 1
DEC_BATCH = 8
DEC_SEQ = 1
PAST_LEN = 1024
PAGE_SIZE = 128

DN_HEADS = 4
DN_DK = 128
DN_DV = 128
CONV_W = 4
CHUNK = 64
AT_HEADS = 8
AT_HD = 64
DIL_PAIRS = ((128, 1), (512, 4), (2048, 16))
WIN_MAX = max(w for w, _ in DIL_PAIRS)
BAND_BLK = 128
NUM_BUCKETS = 32
MAX_DIST = 2048
FFN_HIDDEN = -(-8 * D_MODEL // (3 * 256)) * 256
PLE_DIM = 256
RMS_EPS = 1e-6
DN_QK = DN_HEADS * DN_DK
DN_V = DN_HEADS * DN_DV
CONV_CH = 2 * DN_QK + DN_V
AT_W = AT_HEADS * AT_HD
MIX_W = DN_V + AT_W
IN_SPLITS = (CONV_CH, CONV_CH + DN_V, CONV_CH + DN_V + DN_HEADS, CONV_CH + DN_V + 2 * DN_HEADS,
             CONV_CH + DN_V + 2 * DN_HEADS + AT_W, CONV_CH + DN_V + 2 * DN_HEADS + 2 * AT_W)
IN_COLS = CONV_CH + DN_V + 2 * DN_HEADS + 3 * AT_W

kernel_name = 'hybrid_gated_delta_dilated_swa_step'

def rmsnorm(x, g):
    xf = x.astype(jnp.float32)
    y = xf * lax.rsqrt(jnp.mean(xf * xf, axis=-1, keepdims=True) + RMS_EPS)
    return (y * g.astype(jnp.float32)).astype(x.dtype)

def l2norm(x):
    xf = x.astype(jnp.float32)
    return xf * lax.rsqrt(jnp.sum(xf * xf, axis=-1, keepdims=True) + 1e-6)

def t5_bucket(n):
    max_exact = NUM_BUCKETS // 2
    n = np.asarray(n)
    large = max_exact + (np.log(np.maximum(n, 1) / max_exact) / math.log(MAX_DIST / max_exact)
                         * (NUM_BUCKETS - max_exact)).astype(np.int32)
    large = np.minimum(large, NUM_BUCKETS - 1)
    return np.where(n < max_exact, n, large).astype(np.int32)

def pair_bias(rel_bias, d, nw):
    return rel_bias[t5_bucket(np.arange(nw) * d)].T.astype(jnp.float32)

def short_conv(u, ctx, w):
    t = u.shape[1]
    ucat = jnp.concatenate([ctx.astype(u.dtype), u], axis=1)
    out = ucat[:, 0:t] * w[0]
    for i in range(1, CONV_W):
        out = out + ucat[:, i:i + t] * w[i]
    return out, ucat[:, -(CONV_W - 1):]

def gated_delta_chunked(q, k, v, beta, g):
    q, k, v = (t.astype(jnp.float32) for t in (q, k, v))
    B, S, H, DK = q.shape
    DV = v.shape[-1]
    N = S // CHUNK

    def chunks(t):
        return jnp.moveaxis(t.reshape(B, N, CHUNK, H, -1), 3, 2)

    qc, kc, vc = chunks(q), chunks(k), chunks(v)
    bc = jnp.moveaxis(beta.reshape(B, N, CHUNK, H), 3, 2)
    gc = jnp.cumsum(jnp.moveaxis(g.reshape(B, N, CHUNK, H), 3, 2), axis=-1)
    incl = np.tril(np.ones((CHUNK, CHUNK), bool))
    strict = np.tril(np.ones((CHUNK, CHUNK), bool), -1)
    decay = jnp.exp(jnp.where(incl, gc[..., :, None] - gc[..., None, :], -jnp.inf))
    kb = kc * bc[..., None]
    lower = jnp.where(strict, jnp.einsum('bnhid,bnhjd->bnhij', kb, kc) * decay, 0.0)
    a_mat = lower + jnp.eye(CHUNK, dtype=jnp.float32)
    u = lax.linalg.triangular_solve(a_mat, vc * bc[..., None], left_side=True, lower=True)
    w = lax.linalg.triangular_solve(a_mat, kb * jnp.exp(gc)[..., None], left_side=True, lower=True)
    intra = jnp.where(incl, jnp.einsum('bnhid,bnhjd->bnhij', qc, kc) * decay, 0.0)
    q_dec = qc * jnp.exp(gc)[..., None]
    k_dec = kc * jnp.exp(gc[..., -1:] - gc)[..., None]
    g_last = jnp.exp(gc[..., -1])

    def step(state, xs):
        u_i, w_i, q_i, k_i, a_i, gl_i = xs
        v_new = u_i - jnp.einsum('bhcd,bhde->bhce', w_i, state)
        o_i = jnp.einsum('bhcd,bhde->bhce', q_i, state) + jnp.einsum('bhij,bhje->bhie', a_i, v_new)
        state = state * gl_i[..., None, None] + jnp.einsum('bhcd,bhce->bhde', k_i, v_new)
        return state, o_i

    xs = tuple(jnp.moveaxis(t, 1, 0) for t in (u, w, q_dec, k_dec, intra, g_last))
    s_fin, o = lax.scan(step, jnp.zeros((B, H, DK, DV), jnp.float32), xs)
    o = jnp.moveaxis(jnp.moveaxis(o, 0, 1), 2, 3).reshape(B, S, H, DV)
    return o, s_fin

def gated_delta_recurrent(q, k, v, beta, g, state):
    xs = tuple(jnp.moveaxis(t.astype(jnp.float32), 1, 0) for t in (q, k, v, beta, g))

    def step(s, x):
        q_t, k_t, v_t, b_t, g_t = x
        s = s * jnp.exp(g_t)[..., None, None]
        kv = jnp.einsum('bhd,bhde->bhe', k_t, s)
        delta = (v_t - kv) * b_t[..., None]
        s = s + k_t[..., :, None] * delta[..., None, :]
        return s, jnp.einsum('bhd,bhde->bhe', q_t, s)

    s_fin, o = lax.scan(step, state.astype(jnp.float32), xs)
    return jnp.moveaxis(o, 0, 1), s_fin

def merge_by_denominator(outs, lses):
    wts = jax.nn.softmax(jnp.stack(lses, 0), axis=0)
    return jnp.sum(wts[..., None] * jnp.stack(outs, 0), axis=0)

def band_attention_strided(q, k, v, bias, d, nw):
    B, S, H, E = q.shape
    M = S // d
    nb = -(-M // BAND_BLK)
    Mp = nb * BAND_BLK

    def to_blocks(t):
        t = t.reshape(B, M, d, H, E).transpose(0, 2, 1, 3, 4)
        t = jnp.pad(t, ((0, 0), (0, 0), (0, Mp - M), (0, 0), (0, 0)))
        return t.reshape(B, d, nb, BAND_BLK, H, E)

    def with_prev(t):
        prev = jnp.pad(t, ((0, 0), (0, 0), (1, 0), (0, 0), (0, 0), (0, 0)))[:, :, :-1]
        return jnp.concatenate([prev, t], axis=3)

    qb = to_blocks(q)
    kk = with_prev(to_blocks(k))
    vv = with_prev(to_blocks(v))
    rel = BAND_BLK + np.arange(BAND_BLK)[:, None] - np.arange(2 * BAND_BLK)[None, :]
    m_key = (np.arange(nb)[:, None, None] - 1) * BAND_BLK + np.arange(2 * BAND_BLK)[None, None, :]
    valid = (rel >= 0) & (rel < nw) & (m_key >= 0)
    b = bias[:, np.clip(rel, 0, nw - 1)]
    s = jnp.einsum('bdnqhe,bdnkhe->bdnhqk', qb, kk, preferred_element_type=jnp.float32) * (E ** -0.5) + b
    s = jnp.where(valid[:, None], s, -jnp.inf)
    m = jnp.max(s, axis=-1, keepdims=True)
    pr = jnp.exp(s - m)
    den = jnp.sum(pr, axis=-1)
    o = jnp.einsum('bdnhqk,bdnkhe->bdnqhe', pr, vv.astype(jnp.float32)) / jnp.moveaxis(den, -1, -2)[..., None]
    lse = m[..., 0] + jnp.log(den)
    o = o.reshape(B, d, Mp, H, E)[:, :, :M].transpose(0, 2, 1, 3, 4).reshape(B, S, H, E)
    lse = jnp.moveaxis(lse, -1, -2).reshape(B, d, Mp, H)[:, :, :M].transpose(0, 2, 1, 3).reshape(B, S, H)
    return o, lse

def dilated_attention_prompt(q, k, v, rel_bias):
    outs, lses = [], []
    for w, d in DIL_PAIRS:
        nw = w // d + 1
        o, l = band_attention_strided(q, k, v, pair_bias(rel_bias, d, nw), d, nw)
        outs.append(o)
        lses.append(l)
    n_keep = min(WIN_MAX, q.shape[1])
    return merge_by_denominator(outs, lses), k[:, -n_keep:], v[:, -n_keep:]

def dilated_attention_sample(q, k, v, win_k, win_v, rel_bias):
    W = win_k.shape[1]
    T = q.shape[1]
    E = q.shape[-1]
    kc = jnp.concatenate([win_k.astype(k.dtype), k], axis=1)
    vc = jnp.concatenate([win_v.astype(v.dtype), v], axis=1)
    outs, lses = [], []
    for w, d in DIL_PAIRS:
        nw = w // d + 1
        idx = W + np.arange(T)[:, None] - d * np.arange(nw)[None, :]
        valid = idx >= 0
        idx = np.maximum(idx, 0)
        kg = kc[:, idx]
        vg = vc[:, idx]
        s = jnp.einsum('bthe,btjhe->bthj', q, kg, preferred_element_type=jnp.float32) * (E ** -0.5) + pair_bias(rel_bias, d, nw)
        s = jnp.where(valid[:, None, :], s, -jnp.inf)
        m = jnp.max(s, axis=-1, keepdims=True)
        pr = jnp.exp(s - m)
        den = jnp.sum(pr, axis=-1)
        outs.append(jnp.einsum('bthj,btjhe->bthe', pr, vg.astype(jnp.float32)) / den[..., None])
        lses.append(m[..., 0] + jnp.log(den))
    return merge_by_denominator(outs, lses), kc[:, -W:], vc[:, -W:]

def decoder_layer(x, p, state, rel_bias, g_pre_mix, w_in, conv_w, a_log, dt_bias, g_dn_out, w_out, g_post_mix,
                  g_pre_ffn, w_gate_up, w_down, g_post_ffn, w_ple_proj, w_ple_gate, g_ple):
    B, S, _ = x.shape
    h = rmsnorm(x, g_pre_mix)
    proj = h @ w_in
    qkv_dn, z_dn, b_dn, a_dn, q_at, k_at, v_at = jnp.split(proj, IN_SPLITS, axis=-1)
    conv_ctx = jnp.zeros((B, CONV_W - 1, CONV_CH), x.dtype) if state is None else state[0]
    qkv_c, new_conv = short_conv(qkv_dn, conv_ctx, conv_w)
    qkv_c = jax.nn.silu(qkv_c)
    q, k, v = jnp.split(qkv_c, [DN_QK, 2 * DN_QK], axis=-1)
    q = l2norm(q.reshape(B, S, DN_HEADS, DN_DK)) * (DN_DK ** -0.5)
    k = l2norm(k.reshape(B, S, DN_HEADS, DN_DK))
    v = v.reshape(B, S, DN_HEADS, DN_DV)
    beta = jax.nn.sigmoid(b_dn.astype(jnp.float32))
    g = -jnp.exp(a_log.astype(jnp.float32)) * jax.nn.softplus(a_dn.astype(jnp.float32) + dt_bias.astype(jnp.float32))
    if state is None:
        o_dn, new_delta = gated_delta_chunked(q, k, v, beta, g)
    else:
        o_dn, new_delta = gated_delta_recurrent(q, k, v, beta, g, state[1])
    o_dn = rmsnorm(o_dn.astype(x.dtype), g_dn_out) * jax.nn.silu(z_dn.reshape(B, S, DN_HEADS, DN_DV))
    q_at = q_at.reshape(B, S, AT_HEADS, AT_HD)
    k_at = k_at.reshape(B, S, AT_HEADS, AT_HD)
    v_at = v_at.reshape(B, S, AT_HEADS, AT_HD)
    if state is None:
        o_at, new_wk, new_wv = dilated_attention_prompt(q_at, k_at, v_at, rel_bias)
    else:
        o_at, new_wk, new_wv = dilated_attention_sample(q_at, k_at, v_at, state[2], state[3], rel_bias)
    mix = jnp.concatenate([o_dn.reshape(B, S, DN_V), o_at.astype(x.dtype).reshape(B, S, AT_W)], axis=-1) @ w_out
    x = x + rmsnorm(mix, g_post_mix)
    gt, up = jnp.split(rmsnorm(x, g_pre_ffn) @ w_gate_up, 2, axis=-1)
    x = x + rmsnorm((jax.nn.silu(gt) * up) @ w_down, g_post_ffn)
    x = x + rmsnorm(jax.nn.sigmoid(x @ w_ple_gate) * (p.astype(x.dtype) @ w_ple_proj), g_ple)
    return x, new_conv, new_delta, new_wk, new_wv

def setup_inputs(seed: int = 0) -> dict:
    key = jax.random.key(seed)
    ks = jax.random.split(key, 24)
    f32 = jnp.float32

    def nrm(k, shape, s=1.0):
        return jax.random.normal(k, shape, f32) * s

    def gain(k, shape):
        return 1.0 + 0.02 * jax.random.normal(k, shape, f32)

    w_buf = min(WIN_MAX, PAST_LEN)
    dt = jnp.exp(jax.random.uniform(ks[13], (DEPTH, DN_HEADS), f32, math.log(1e-3), math.log(1e-1)))
    return {
        'x_prompt': nrm(ks[0], (BATCH, SEQ, D_MODEL)),
        'x_sample': nrm(ks[1], (DEC_BATCH, DEC_SEQ, D_MODEL)),
        'cache_conv': nrm(ks[2], (DEPTH, DEC_BATCH, CONV_W - 1, CONV_CH)),
        'state_delta': nrm(ks[3], (DEPTH, DEC_BATCH, DN_HEADS, DN_DK, DN_DV), DN_DK ** -0.5),
        'cache_win_k': nrm(ks[4], (DEPTH, DEC_BATCH, w_buf, AT_HEADS, AT_HD)),
        'cache_win_v': nrm(ks[5], (DEPTH, DEC_BATCH, w_buf, AT_HEADS, AT_HD)),
        'p_prompt': nrm(ks[6], (DEPTH, BATCH, SEQ, PLE_DIM)),
        'p_sample': nrm(ks[7], (DEPTH, DEC_BATCH, DEC_SEQ, PLE_DIM)),
        'rel_bias': nrm(ks[8], (NUM_BUCKETS, AT_HEADS), 0.5),
        'g_pre_mix': gain(ks[9], (DEPTH, D_MODEL)),
        'w_in': nrm(ks[10], (DEPTH, D_MODEL, IN_COLS), D_MODEL ** -0.5),
        'conv_w': nrm(ks[11], (DEPTH, CONV_W, CONV_CH), CONV_W ** -0.5),
        'a_log': jnp.log(jax.random.uniform(ks[12], (DEPTH, DN_HEADS), f32, 1.0, 16.0)),
        'dt_bias': dt + jnp.log(-jnp.expm1(-dt)),
        'g_dn_out': gain(ks[14], (DEPTH, DN_DV)),
        'w_out': nrm(ks[15], (DEPTH, MIX_W, D_MODEL), MIX_W ** -0.5),
        'g_post_mix': gain(ks[16], (DEPTH, D_MODEL)),
        'g_pre_ffn': gain(ks[17], (DEPTH, D_MODEL)),
        'w_gate_up': nrm(ks[18], (DEPTH, D_MODEL, 2 * FFN_HIDDEN), D_MODEL ** -0.5),
        'w_down': nrm(ks[19], (DEPTH, FFN_HIDDEN, D_MODEL), FFN_HIDDEN ** -0.5),
        'g_post_ffn': gain(ks[20], (DEPTH, D_MODEL)),
        'w_ple_proj': nrm(ks[21], (DEPTH, PLE_DIM, D_MODEL), PLE_DIM ** -0.5),
        'w_ple_gate': nrm(ks[22], (DEPTH, D_MODEL, D_MODEL), D_MODEL ** -0.5),
        'g_ple': gain(ks[23], (DEPTH, D_MODEL)),
    }

def reference(x_prompt, x_sample, cache_conv, state_delta, cache_win_k, cache_win_v, p_prompt, p_sample,
              rel_bias, g_pre_mix, w_in, conv_w, a_log, dt_bias, g_dn_out, w_out, g_post_mix,
              g_pre_ffn, w_gate_up, w_down, g_post_ffn, w_ple_proj, w_ple_gate, g_ple):
    yp, ys = x_prompt, x_sample
    conv_p, delta_p, wk_p, wv_p = [], [], [], []
    conv_s, delta_s, wk_s, wv_s = [], [], [], []
    for i in range(DEPTH):
        lw = (g_pre_mix[i], w_in[i], conv_w[i], a_log[i], dt_bias[i], g_dn_out[i], w_out[i], g_post_mix[i],
              g_pre_ffn[i], w_gate_up[i], w_down[i], g_post_ffn[i], w_ple_proj[i], w_ple_gate[i], g_ple[i])
        yp, c1, d1, k1, v1 = decoder_layer(yp, p_prompt[i], None, rel_bias, *lw)
        ys, c2, d2, k2, v2 = decoder_layer(
            ys, p_sample[i], (cache_conv[i], state_delta[i], cache_win_k[i], cache_win_v[i]), rel_bias, *lw)
        conv_p.append(c1); delta_p.append(d1); wk_p.append(k1); wv_p.append(v1)
        conv_s.append(c2); delta_s.append(d2); wk_s.append(k2); wv_s.append(v2)
    return (yp, ys, jnp.stack(conv_p), jnp.stack(delta_p), jnp.stack(wk_p), jnp.stack(wv_p),
            jnp.stack(conv_s), jnp.stack(delta_s), jnp.stack(wk_s), jnp.stack(wv_s))


_drawn_inputs = setup_inputs


def setup_inputs(seed=0):
    import zlib

    import numpy as np

    out = dict(_drawn_inputs(seed))
    spreads = {}
    factors = {'g_dn_out': 4.009,
     'g_post_mix': 3.834,
     'g_pre_ffn': 3.762,
     'g_post_ffn': 20.204,
     'g_ple': 25.544}
    for name, (base, spread) in spreads.items():
        noise = np.random.default_rng([zlib.crc32(name.encode()), seed]).standard_normal(out[name].shape)
        drawn = base * np.exp(spread * noise) if base else spread * noise
        out[name] = __import__('jax').numpy.asarray(drawn.astype(out[name].dtype))
    for name, factor in factors.items():
        out[name] = (out[name] * factor).astype(out[name].dtype)
    return out
```

```python
from contextlib import ExitStack

import numpy as np

import concourse.bass as bass
from concourse import mybir

F32 = mybir.dt.float32
F32R = mybir.dt.float32r
ALU = mybir.AluOpType
ACT = mybir.ActivationFunctionType
AX_X = mybir.AxisListType.X

P = 128
D = 1024
S = 2048
NSAMP = 8
TB = 412
NB = 5
TOK = NB * TB
KD = D // P
HEADS, DK = 4, 128
AH, HD = 8, 64
FF = 2816
KF = FF // P
PLE = 256
KP = PLE // P
EPS = 1e-6
BIG = 1e30
DILS = (1, 4, 16)
NBIAS = 383
UROW = AH * HD + 2 * AH
PAST = 1024


def allocators(nc, ctx):
    semaphores = []

    def sbuf(name, shape, dtype):
        return ctx.enter_context(nc.sbuf_tensor(name, shape, dtype))

    def psum(name, shape, dtype):
        return ctx.enter_context(nc.psum_tensor(name, shape, dtype))

    def sem(name):
        semaphores.append(nc.alloc_semaphore(name))
        return semaphores[-1]

    def clear():
        nc.clear_and_free_semaphores(semaphores)
        nc.all_engine_barrier()

    ctx.callback(clear)
    return sbuf, psum, sem


def landed(tile, par, per_tile=1):
    return (tile - par) * (8 * per_tile) + 16 * per_tile


def hi_lo_products(pe, out, w_hi, w_lo, a_hi, a_lo, first, last):
    pe.matmul(out, w_hi, a_hi, start=first, stop=False)
    pe.matmul(out, w_lo, a_hi, start=False, stop=False)
    return pe.matmul(out, w_hi, a_lo, start=False, stop=last)


N_DN, N_Z, N_AT = 12, 4, 12
NT = N_DN + N_Z + N_AT
ROW = 2088
SAMP0 = 3 + S


def norm_and_input_projection(nc, t):
    with ExitStack() as ctx:
        sbuf, psum, sem = allocators(nc, ctx)
        h_hi = sbuf("pa_h_hi", [P, KD, TOK], F32R)
        h_lo = sbuf("pa_h_lo", [P, KD, TOK], F32R)
        work = sbuf("pa_work", [P, 6 * ROW], F32)
        w_raw = sbuf("pa_w", [P, 2, KD * P], F32)
        w_hi = sbuf("pa_whi", [P, 2, KD * P], F32R)
        w_lo = sbuf("pa_wlo", [P, 2, KD * P], F32R)
        gain = sbuf("pa_gain", [P, KD], F32)
        eps = sbuf("pa_eps", [P, 1], F32)
        ones_mean = sbuf("pa_ones", [P, P], F32)
        conv_w = sbuf("pa_convw", [P, N_DN * 4], F32)
        mean_ps = psum("pa_mean", [P, 512], F32)
        proj_ps = psum("pa_proj", [P, NB, 512], F32)
        const_loaded = sem("pa_const_loaded")
        consts_set = sem("pa_consts_set")
        x_loaded0 = sem("pa_x_loaded0")
        x_loaded1 = sem("pa_x_loaded1")
        squares_done = sem("pa_squares_done")
        sums_done = sem("pa_sums_done")
        means_done = sem("pa_means_done")
        roots_done = sem("pa_roots_done")
        recips_done = sem("pa_recips_done")
        h_done = sem("pa_h_done")
        h_hi_done = sem("pa_h_hi_done")
        h_lo_done = sem("pa_h_lo_done")
        zeros_set = sem("pa_zeros_set")
        w_loaded0 = sem("pa_w_loaded0")
        w_loaded1 = sem("pa_w_loaded1")
        w_hi_done = sem("pa_w_hi_done")
        w_lo_done = sem("pa_w_lo_done")
        proj_done = sem("pa_proj_done")
        evacuated = sem("pa_evacuated")
        gates_done = sem("pa_gates_done")
        taps_done = sem("pa_taps_done")
        conv_done = sem("pa_conv_done")
        silu_done = sem("pa_silu_done")
        perm4_done = sem("pa_perm4_done")
        perm16_done = sem("pa_perm16_done")
        ctx_loaded0 = sem("pa_ctx_loaded0")
        ctx_loaded1 = sem("pa_ctx_loaded1")
        dn_stored0 = sem("pa_dn_stored0")
        dn_stored1 = sem("pa_dn_stored1")
        z_stored0 = sem("pa_z_stored0")
        z_stored1 = sem("pa_z_stored1")
        at_stored0 = sem("pa_at_stored0")
        at_stored1 = sem("pa_at_stored1")
        block = ctx.enter_context(nc.Block())
        x_loaded = (x_loaded0, x_loaded1)
        w_loaded = (w_loaded0, w_loaded1)
        ctx_loaded = (ctx_loaded0, ctx_loaded1)
        dn_stored = (dn_stored0, dn_stored1)
        z_stored = (z_stored0, z_stored1)
        at_stored = (at_stored0, at_stored1)
        BLK = KD * TB
        xb = [work[:, i * BLK:(i + 1) * BLK].rearrange("p (k t) -> p k t", k=KD) for i in range(2)]
        sq = work[:, 2 * BLK:3 * BLK]
        ssum, std, rstd = (work[:, 3 * BLK + i * TB:3 * BLK + (i + 1) * TB] for i in range(3))
        raw = [work[:, i * ROW:(i + 1) * ROW] for i in range(2)]
        res = [work[:, (2 + i) * ROW:(3 + i) * ROW] for i in range(2)]
        r16 = [work[:, (4 + i) * ROW:(5 + i) * ROW] for i in range(2)]
        A0 = N_DN + N_Z
        CONV_COLS = SAMP0 + 4 * NSAMP - 3

        def samples(row, first, n):
            return row[:, SAMP0:SAMP0 + 4 * NSAMP].rearrange("p (b j) -> p b j", j=4)[:, :, first:first + n]

        @block.sync
        def _(sp):
            sp.dma_start(gain[:, :], t["g_pre_mix"]).then_inc(const_loaded, 16)
            sp.dma_start(conv_w[:, :], t["conv_w"]).then_inc(const_loaded, 16)
            for b in range(NB):
                if b >= 2:
                    sp.wait_ge(h_lo_done, b - 1)
                sp.dma_start(xb[b % 2], t["xT"][b]).then_inc(x_loaded[b % 2], 16)

            def load_w(c, par):
                sp.dma_start(w_raw[:, par, :], t["w_in"][c]).then_inc(w_loaded[par], 16)

            def load_ctx(c, par):
                sp.dma_start(samples(raw[par], 0, 3), t["cache_conv"][c]).then_inc(ctx_loaded[par], 16)

            load_w(0, 0)
            load_w(1, 1)
            sp.wait_ge(h_lo_done, NB)
            load_ctx(0, 0)
            load_ctx(1, 1)

            def conv_tile(c, par, last):
                sp.wait_ge(w_lo_done, c + 1)
                load_w(c + 2, par)
                sp.wait_ge(silu_done, c + 1)
                sp.dma_start(t["dn"][c], res[par][:, 0:S]).then_inc(dn_stored[par], 16)
                sp.dma_start(t["dn_samp"][c], samples(res[par], 0, 1), allow_slow_non_contiguous=True).then_inc(dn_stored[par], 16)
                sp.dma_start(t["conv_tail"][c], raw[par][:, S:S + 3]).then_inc(dn_stored[par], 16)
                sp.dma_start(t["conv_samp"][c], samples(raw[par], 1, 3)).then_inc(dn_stored[par], 16)
                if not last:
                    sp.wait_ge(dn_stored[par], landed(c, par, 4))
                    load_ctx(c + 2, par)

            with sp.Fori(0 // 2, (N_DN - 2) // 2) as j:
                i = 2 * j
                conv_tile(i, 0, False)
                conv_tile(i + 1, 1, False)
            conv_tile(N_DN - 2, 0, True)
            conv_tile(N_DN - 1, 1, True)

            def gate_tile(c, par):
                sp.wait_ge(w_lo_done, c + 1)
                load_w(c + 2, par)
                sp.wait_ge(gates_done, (c - (N_DN - 1)) * NB)
                sp.dma_start(t["z"][c - N_DN], res[par][:, 0:TOK]).then_inc(z_stored[par], 16)

            with sp.Fori(N_DN // 2, A0 // 2) as j:
                i = 2 * j
                gate_tile(i, 0)
                gate_tile(i + 1, 1)

            def attn_tile(c, par, more):
                sp.wait_ge(w_lo_done, c + 1)
                if more:
                    load_w(c + 2, par)
                sp.wait_ge(evacuated, (c - (N_Z - 1)) * NB)
                sp.dma_start(t["at"][c - A0], raw[par][:, 0:TOK]).then_inc(at_stored[par], 16)
                sp.wait_ge(perm4_done, c - (A0 - 1))
                sp.dma_start(t["at4"][c - A0], res[par][:, 0:S]).then_inc(at_stored[par], 16)
                sp.wait_ge(perm16_done, c - (A0 - 1))
                sp.dma_start(t["at16"][c - A0], r16[par][:, 0:S]).then_inc(at_stored[par], 16)

            with sp.Fori(A0 // 2, (NT - 2) // 2) as j:
                i = 2 * j
                attn_tile(i, 0, True)
                attn_tile(i + 1, 1, True)
            attn_tile(NT - 2, 0, True)
            attn_tile(NT - 1, 1, False)
            sp.wait_ge(evacuated, (NT + 1 - N_Z) * NB)
            sp.dma_start(t["ba"], raw[0][0:36, 0:TOK]).then_inc(at_stored[0], 16)
            for par in range(2):
                sp.wait_ge(dn_stored[par], 64 * (N_DN // 2))
                sp.wait_ge(z_stored[par], 16 * (N_Z // 2))
                sp.wait_ge(at_stored[par], 48 * (N_AT // 2) + (0 if par else 16))

        @block.gpsimd
        def _(pool):
            pool.memset(ones_mean[:, :], 1.0 / D).then_inc(consts_set, 1)
            pool.memset(eps[:, :], EPS).then_inc(consts_set, 1)
            for b in range(NB):
                cols = slice(b * TB, (b + 1) * TB)
                pool.wait_ge(h_hi_done, b + 1)
                pool.tensor_tensor(h_lo[:, :, cols], xb[b % 2], h_hi[:, :, cols].bitcast(F32),
                                   ALU.subtract).then_inc(h_lo_done, 1)

            def split_lo(c, par):
                pool.wait_ge(w_hi_done, c + 1)
                pool.tensor_tensor(w_lo[:, par, :], w_raw[:, par, :], w_hi[:, par, :].bitcast(F32),
                                   ALU.subtract).then_inc(w_lo_done, 1)

            with pool.Fori(0, NT // 2) as j:
                i = 2 * j
                split_lo(i, 0)
                split_lo(i + 1, 1)
            split_lo(NT, 0)

        @block.scalar
        def _(act):
            act.wait_ge(consts_set, 2)
            for b in range(NB):
                act.wait_ge(x_loaded[b % 2], 16 * (b // 2 + 1))
                if b:
                    act.wait_ge(sums_done, b)
                act.activation(sq, xb[b % 2].rearrange("p k t -> p (k t)"), ACT.Square).then_inc(squares_done, 1)
                act.wait_ge(means_done, b + 1)
                if b:
                    act.wait_ge(recips_done, b)
                act.activation(std, mean_ps[:, 0:TB], ACT.Sqrt, bias=eps[:, 0:1]).then_inc(roots_done, 1)
                act.wait_ge(h_done, b + 1)
                act.activation(h_hi[:, :, b * TB:(b + 1) * TB], xb[b % 2], ACT.Copy).then_inc(h_hi_done, 1)

            def split_hi(c, par, first):
                act.wait_ge(w_loaded[par], landed(c, par))
                if not first:
                    act.wait_ge(proj_done, (c - 1) * NB)
                act.activation(w_hi[:, par, :], w_raw[:, par, :], ACT.Copy).then_inc(w_hi_done, 1)

            split_hi(0, 0, True)
            split_hi(1, 1, True)

            def conv_tile(c, par):
                split_hi(c + 2, par, False)
                act.wait_ge(conv_done, c + 1)
                act.activation(res[par][:, 0:CONV_COLS], res[par][:, 0:CONV_COLS], ACT.Silu).then_inc(silu_done, 1)

            with act.Fori(0 // 2, N_DN // 2) as j:
                i = 2 * j
                conv_tile(i, 0)
                conv_tile(i + 1, 1)

            def gate_tile(c, par, first):
                if first:
                    act.wait_ge(dn_stored[par], 64 * (N_DN // 2))
                else:
                    act.wait_ge(z_stored[par], landed(c - N_DN - 2, par))
                for b in range(NB):
                    act.wait_ge(proj_done, c * NB + (b + 1))
                    act.activation(res[par][:, b * TB:(b + 1) * TB], proj_ps[:, b, 0:TB],
                                   ACT.Silu).then_inc(gates_done, 1)
                split_hi(c + 2, par, False)

            for c in range(N_DN, A0):
                gate_tile(c, c % 2, c < N_DN + 2)

            def attn_tile(c, par, more, first):
                if more:
                    split_hi(c + 2, par, False)
                act.wait_ge(evacuated, (c - (N_Z - 1)) * NB)
                if not first:
                    act.wait_ge(at_stored[par], landed(c - A0 - 2, par, 3))
                act.activation(r16[par][:, 0:S].rearrange("p (r m) -> p r m", r=16),
                               raw[par][:, 0:S].rearrange("p (m r) -> p r m", r=16),
                               ACT.Copy).then_inc(perm16_done, 1)

            attn_tile(A0, 0, True, True)
            attn_tile(A0 + 1, 1, True, True)
            with act.Fori((A0 + 2) // 2, (NT - 2) // 2) as j:
                i = 2 * j
                attn_tile(i, 0, True, False)
                attn_tile(i + 1, 1, True, False)
            attn_tile(NT - 2, 0, True, False)
            attn_tile(NT - 1, 1, False, False)

        @block.tensor
        def _(pe):
            pe.wait_ge(consts_set, 2)
            for b in range(NB):
                pe.wait_ge(sums_done, b + 1)
                if b:
                    pe.wait_ge(roots_done, b)
                pe.matmul(mean_ps[:, 0:TB], ones_mean[:, :], ssum, start=True, stop=True).then_inc(means_done, 1)
            pe.wait_ge(h_lo_done, NB)

            def project(c, par, read, before):
                pe.wait_ge(w_lo_done, c + 1)
                for b in range(NB):
                    if read is not None:
                        pe.wait_ge(read, (c - (before + 1)) * NB + (b + 1))
                    cols = slice(b * TB, (b + 1) * TB)
                    for k in range(KD):
                        w = slice(k * P, (k + 1) * P)
                        mm = hi_lo_products(pe, proj_ps[:, b, 0:TB], w_hi[:, par, w], w_lo[:, par, w],
                                            h_hi[:, k, cols], h_lo[:, k, cols], k == 0, k == KD - 1)
                    mm.then_inc(proj_done, 1)

            project(0, 0, None, 0)
            project(1, 1, evacuated, 0)
            with pe.Fori(1, N_DN // 2) as j:
                project(2 * j, 0, evacuated, 0)
                project(2 * j + 1, 1, evacuated, 0)
            for c in range(N_DN, A0 + 1):
                if c == N_DN:
                    project(c, c % 2, evacuated, 0)
                else:
                    project(c, c % 2, gates_done, N_DN)
            project(A0 + 1, 1, evacuated, N_Z)
            with pe.Fori((A0 + 2) // 2, NT // 2) as j:
                project(2 * j, 0, evacuated, N_Z)
                project(2 * j + 1, 1, evacuated, N_Z)
            project(NT, 0, evacuated, N_Z)

        @block.vector
        def _(dve):
            dve.wait_ge(const_loaded, 32)
            for b in range(NB):
                dve.wait_ge(squares_done, b + 1)
                if b:
                    dve.wait_ge(means_done, b)
                dve.tensor_reduce(ssum, sq.rearrange("p (k t) -> p t k", k=KD), AX_X, ALU.add).then_inc(sums_done, 1)
                dve.wait_ge(roots_done, b + 1)
                dve.reciprocal(rstd, std).then_inc(recips_done, 1)
                dve.wait_ge(recips_done, b + 1)
                for k in range(KD):
                    m = dve.scalar_tensor_tensor(xb[b % 2][:, k, :], xb[b % 2][:, k, :], gain[:, k:k + 1], rstd,
                                                 ALU.mult, ALU.mult)
                m.then_inc(h_done, 1)
            dve.wait_ge(h_lo_done, NB)
            dve.memset(raw[0][:, 0:3], 0.0).then_inc(zeros_set, 1)
            dve.memset(raw[1][:, 0:3], 0.0).then_inc(zeros_set, 1)
            dve.wait_ge(zeros_set, 2)

            def conv_tile(c, par, first):
                if not first:
                    dve.wait_ge(dn_stored[par], landed(c - 2, par, 4))
                u, out = raw[par], res[par]
                for b in range(NB):
                    dve.wait_ge(proj_done, c * NB + (b + 1))
                    n = min(TB, S - b * TB)
                    m = dve.tensor_copy(u[:, 3 + b * TB:3 + b * TB + n], proj_ps[:, b, 0:n])
                    if n < TB:
                        m = dve.tensor_copy(samples(u, 3, 1), proj_ps[:, b, n:n + NSAMP].rearrange("p (b o) -> p b o", o=1))
                    m.then_inc(evacuated, 1)
                dve.wait_ge(evacuated, (c + 1) * NB)
                dve.wait_ge(ctx_loaded[par], landed(c, par))
                for j in range(4):
                    w = conv_w[:, bass.ds(c * 4 + j, 1)]
                    if j == 0:
                        m = dve.tensor_scalar(out[:, 0:CONV_COLS], u[:, 0:CONV_COLS], w, None, ALU.mult)
                    else:
                        dve.wait_ge(taps_done, c * 3 + j)
                        m = dve.scalar_tensor_tensor(out[:, 0:CONV_COLS], u[:, j:j + CONV_COLS], w,
                                                     out[:, 0:CONV_COLS], ALU.mult, ALU.add)
                    m.then_inc(conv_done if j == 3 else taps_done, 1)

            conv_tile(0, 0, True)
            conv_tile(1, 1, True)
            with dve.Fori(2 // 2, N_DN // 2) as j:
                i = 2 * j
                conv_tile(i, 0, False)
                conv_tile(i + 1, 1, False)

            for par in range(2):
                dve.wait_ge(dn_stored[par], 64 * (N_DN // 2))

            def attn_tile(c, par, first, parts):
                if first:
                    dve.wait_ge(z_stored[par], 16 * (N_Z // 2))
                else:
                    dve.wait_ge(at_stored[par], landed(c - A0 - 2, par, 3))
                for b in range(NB):
                    dve.wait_ge(proj_done, c * NB + (b + 1))
                    dve.tensor_copy(raw[par][0:parts, b * TB:(b + 1) * TB],
                                    proj_ps[0:parts, b, 0:TB]).then_inc(evacuated, 1)
                if parts == P:
                    dve.wait_ge(evacuated, (c - (N_Z - 1)) * NB)
                    dve.tensor_copy(res[par][:, 0:S].rearrange("p (r m) -> p r m", r=4),
                                    raw[par][:, 0:S].rearrange("p (m r) -> p r m", r=4)).then_inc(perm4_done, 1)

            attn_tile(A0, 0, True, P)
            attn_tile(A0 + 1, 1, True, P)
            with dve.Fori((A0 + 2) // 2, NT // 2) as j:
                i = 2 * j
                attn_tile(i, 0, False, P)
                attn_tile(i + 1, 1, False, P)
            attn_tile(NT, 0, False, 36)


CH = P
NC = S // CH
LEVELS = 7
C_IDENT, C_TRIU, C_TRIL, C_LEVEL = 0, 1, 2, 3


def constant_tiles():
    i, j = np.arange(P)[:, None], np.arange(P)[None, :]
    tiles = [i == j, i <= j, i > j]
    for level in range(LEVELS):
        tiles.append((i >> level + 1 == j >> level + 1) & ((i >> level) % 2 == 1) & ((j >> level) % 2 == 0))
    return np.ascontiguousarray(np.stack(tiles, 1).astype(np.float32)).reshape(P, -1)


def heads(tile):
    return tile.rearrange("p (h j) -> p h j", h=HEADS)


def per_head(col):
    return col.rearrange("p (h o) -> p h o", o=1).broadcast_to([P, HEADS, P])


def all_heads(tile):
    return tile.rearrange("p (o j) -> p o j", o=1).broadcast_to([P, HEADS, P])


def delta_prompt(nc, t):
    with ExitStack() as ctx:
        sbuf, psum, sem = allocators(nc, ctx)
        C4 = HEADS * P
        const = sbuf("pb_const", [P, (C_LEVEL + LEVELS) * P], F32)
        logits = sbuf("pb_logits", [36, S], F32)
        lt = sbuf("pb_lt", [P, NC, 36], F32)
        alog = sbuf("pb_alog", [P, HEADS], F32)
        dtb = sbuf("pb_dtb", [P, HEADS], F32)
        beta = sbuf("pb_beta", [P, NC, HEADS], F32)
        g = sbuf("pb_g", [P, NC, HEADS], F32)
        gtmp = sbuf("pb_gtmp", [P, NC, HEADS], F32)
        gc = sbuf("pb_gc", [P, NC, HEADS], F32)
        egc = sbuf("pb_egc", [P, NC, HEADS], F32)
        ekd = sbuf("pb_ekd", [P, NC, HEADS], F32)
        raw = sbuf("pb_raw", [P, 12, P], F32)
        zg = sbuf("pb_z", [P, C4], F32)
        junk = sbuf("pb_junk", [P, 8, P], F32)
        ones = sbuf("pb_one", [P, P], F32)
        ss = sbuf("pb_ss", [P, 8], F32)
        rr = sbuf("pb_rr", [P, 8], F32)
        coef = sbuf("pb_coef", [P, 4, HEADS], F32)
        kn, kbg, kdec, qn, vb, knT, qnT, gbc, gd, E, egr, M, L, X, XT, Z, U, WT, vnew, S_, intra, qdec, osq, orr, o = (
            sbuf("pb_" + n, [P, C4], F32) for n in
            "kn kbg kdec qn vb knT qnT gbc gd E egr M L X XT Z U WT vnew S intra qdec osq orr o".split())
        B = sbuf("pb_B", [P, LEVELS, C4], F32)
        gain = sbuf("pb_gain", [P, 1], F32)
        eps = sbuf("pb_eps", [P, 1], F32)
        ones_mean = sbuf("pb_ones", [P, P], F32)
        ps = psum("pb_ps", [P, 8, C4], F32)
        (const_loaded, consts_set, logits_turned, logits_copied, beta_done, g_steps, gsum_done, gcol_done,
         raw_loaded, z_loaded, stored, raw_turned, gbc_done, rows_done, kq_turned, grams_done, scores_done,
         b0_turned, z_done, xt_done, x_done, u_done, w_done, p1_done, o_done, s_done, msq_done,
         ss_done, roots_done, knT_copied, qnT_copied, abs_done, e_done, egr_done, z_copied, u_copied, w_copied,
         osq_done, oroot_done, coef_steps, k_scaled, q_scaled, v_scaled, g_diff_done, m_done, l_done, mask_done,
         xt_sub, x_sub, i1_done, intra_done, qdec_done, vnew_done, s1_done, s_upd, orr_done, o1_done, out_done) = (
            sem("pb_" + n) for n in
            """const_loaded consts_set logits_turned logits_copied beta_done g_steps gsum_done gcol_done
            raw_loaded z_loaded stored raw_turned gbc_done rows_done kq_turned grams_done scores_done
            b0_turned z_done xt_done x_done u_done w_done p1_done o_done s_done msq_done
            ss_done roots_done knT_copied qnT_copied abs_done e_done egr_done z_copied u_copied w_copied
            osq_done oroot_done coef_steps k_scaled q_scaled v_scaled g_diff_done m_done l_done mask_done
            xt_sub x_sub i1_done intra_done qdec_done vnew_done s1_done s_upd orr_done o1_done out_done""".split())
        block = ctx.enter_context(nc.Block())

        def const_tile(n):
            return const[:, n * P:(n + 1) * P]

        def bank(n):
            return ps[:, n, :]

        def col(tile, h):
            return tile[:, h * P:(h + 1) * P]

        @block.sync
        def _(sp):
            sp.dma_start(const[:, :], t["consts"]).then_inc(const_loaded, 16)
            sp.dma_start(logits[:, :], t["ba"][:, 0:S]).then_inc(const_loaded, 16)
            sp.dma_start(alog[:, :], t["a_log"].partition_broadcast(P)).then_inc(const_loaded, 16)
            sp.dma_start(dtb[:, :], t["dt_bias"].partition_broadcast(P)).then_inc(const_loaded, 16)
            sp.dma_start(gain[:, :], t["g_dn_out"]).then_inc(const_loaded, 16)

            def load_raw(c):
                sp.dma_start(raw[:, :, :], t["dn"].rearrange("n p s -> p n s")[:, :, bass.ds(c * CH, CH)]).then_inc(raw_loaded, 16)

            def load_z(c):
                sp.dma_start(heads(zg[:, :]), t["z"].rearrange("n p s -> p n s")[:, :, bass.ds(c * CH, CH)]).then_inc(z_loaded, 16)

            def store(c):
                sp.wait_ge(out_done, c + 1)
                sp.dma_start(t["mix"].rearrange("n p s -> p n s")[:, 0:HEADS, bass.ds(c * CH, CH)], heads(o[:, :])).then_inc(stored, 16)

            load_raw(0)
            load_z(0)
            with sp.Fori(0, NC - 1) as c:
                sp.wait_ge(raw_turned, c + 1)
                load_raw(c + 1)
                store(c)
                load_z(c + 1)
            store(NC - 1)
            sp.wait_ge(s_upd, NC + 1)
            sp.dma_start(t["delta"].rearrange("h k v -> k h v"), heads(S_[:, :])).then_inc(stored, 16)
            sp.wait_ge(stored, 16 * NC + 16)

        @block.gpsimd
        def _(pool):
            pool.memset(ones_mean[:, :], 1.0 / DK).then_inc(consts_set, 1)
            pool.memset(eps[:, :], EPS).then_inc(consts_set, 1)
            pool.memset(S_[:, :], 0.0).then_inc(consts_set, 1)
            pool.memset(ones[:, :], 1.0).then_inc(consts_set, 1)
            pool.wait_ge(consts_set, 4)
            pool.wait_ge(const_loaded, 80)
            pool.wait_ge(gcol_done, 1)
            with pool.Fori(0, NC) as c:
                pool.wait_ge(rows_done, c)
                gcol = g[:, bass.ds(c, 1), :].rearrange("p o h -> p (o h)")
                pool.tensor_tensor(heads(gbc[:, :]), all_heads(ones[:, :]), per_head(gcol), ALU.mult).then_inc(gbc_done, 1)
                pool.wait_ge(l_done, c + 1)
                for level in range(LEVELS):
                    pool.tensor_tensor(heads(B[:, level, :]), heads(L[:, :]), all_heads(const_tile(C_LEVEL + level)),
                                       ALU.mult).then_inc(mask_done, 1)

        @block.scalar
        def _(act):
            act.wait_ge(const_loaded, 80)
            act.wait_ge(consts_set, 4)
            act.wait_ge(logits_copied, 1)
            act.activation(beta[:, :, :], lt[:, :, 0:HEADS], ACT.Sigmoid).then_inc(beta_done, 1)
            act.wait_ge(g_steps, 1)
            act.activation(gtmp[:, :, :], g[:, :, :], ACT.Abs).then_inc(beta_done, 1)
            act.wait_ge(beta_done, 2)
            act.activation(gtmp[:, :, :], gtmp[:, :, :], ACT.Exp, scale=-1.0).then_inc(beta_done, 1)
            act.activation(alog[:, :], alog[:, :], ACT.Exp).then_inc(beta_done, 1)
            act.wait_ge(beta_done, 4)
            act.activation(gtmp[:, :, :], gtmp[:, :, :], ACT.Ln, bias=1.0).then_inc(beta_done, 1)
            act.wait_ge(gsum_done, 1)
            act.activation(egc[:, :, :], bank(0)[:, 0:NC * HEADS].rearrange("p (c h) -> p c h", c=NC), ACT.Exp).then_inc(gcol_done, 1)
            act.activation(ekd[:, :, :], bank(1)[:, 0:NC * HEADS].rearrange("p (c h) -> p c h", c=NC), ACT.Exp).then_inc(gcol_done, 1)
            with act.Fori(0, NC) as c:
                act.wait_ge(raw_turned, c + 1)
                for h in range(8):
                    m = act.activation(junk[:, h, :], col(bank(h // HEADS), h % HEADS), ACT.Square, accum_out=ss[:, h:h + 1])
                m.then_inc(ss_done, 1)
                act.wait_ge(ss_done, c + 1)
                act.activation(rr[:, :], ss[:, :], ACT.Sqrt, bias=eps[:, 0:1]).then_inc(roots_done, 1)
                act.wait_ge(g_diff_done, c + 1)
                act.activation(gd[:, :], gd[:, :], ACT.Abs).then_inc(abs_done, 1)
                act.activation(egr[:, :], bank(3), ACT.Exp).then_inc(egr_done, 1)
                act.wait_ge(abs_done, c + 1)
                act.activation(E[:, :], gd[:, :], ACT.Exp, scale=-1.0).then_inc(e_done, 1)
                act.wait_ge(kq_turned, c + 1)
                act.activation(knT[:, :], bank(0), ACT.Copy).then_inc(knT_copied, 1)
                act.activation(qnT[:, :], bank(1), ACT.Copy).then_inc(qnT_copied, 1)
                for level in range(1, LEVELS):
                    act.wait_ge(z_done, c * (LEVELS - 1) + level)
                    act.activation(Z[:, :], bank(3), ACT.Copy).then_inc(z_copied, 1)
                act.wait_ge(u_done, c + 1)
                act.activation(U[:, :], bank(5), ACT.Copy).then_inc(u_copied, 1)
                act.wait_ge(w_done, c + 1)
                act.activation(WT[:, :], bank(6), ACT.Copy).then_inc(w_copied, 1)
                act.wait_ge(o_done, c + 1)
                act.activation(osq[:, :], bank(7), ACT.Square).then_inc(osq_done, 1)
                act.wait_ge(msq_done, c + 1)
                act.activation(orr[:, :], bank(2), ACT.Sqrt, bias=eps[:, 0:1]).then_inc(oroot_done, 1)

        @block.tensor
        def _(pe):
            ident = const_tile(C_IDENT)
            triu, tril = const_tile(C_TRIU), const_tile(C_TRIL)
            pe.wait_ge(const_loaded, 80)
            pe.wait_ge(consts_set, 4)
            for c in range(NC):
                m = pe.transpose(ps[:, c // 8, c % 8 * 36:c % 8 * 36 + 36], logits[:, c * CH:(c + 1) * CH], ident[0:36, 0:36])
            m.then_inc(logits_turned, 1)
            pe.wait_ge(g_steps, 4)
            gall = g[:, :, :].rearrange("p c h -> p (c h)")
            pe.matmul(bank(0)[:, 0:NC * HEADS], triu, gall, start=True, stop=True)
            pe.matmul(bank(1)[:, 0:NC * HEADS], tril, gall, start=True, stop=True).then_inc(gsum_done, 1)
            pe.wait_ge(gcol_done, 3)
            with pe.Fori(0, NC) as c:
                pe.wait_ge(raw_loaded, c * 16 + 16)
                pe.wait_ge(oroot_done, c)
                for n, first in ((0, 4), (1, 0), (2, 8)):
                    for h in range(HEADS):
                        m = pe.transpose(col(bank(n), h), raw[:, first + h, :], ident)
                m.then_inc(raw_turned, 1)
                pe.wait_ge(gbc_done, c + 1)
                for h in range(HEADS):
                    m = pe.matmul(col(bank(3), h), col(gbc[:, :], h), triu, start=True, stop=True)
                m.then_inc(rows_done, 1)
                pe.wait_ge(k_scaled, c + 1)
                for h in range(HEADS):
                    pe.transpose(col(bank(0), h), col(kn[:, :], h), ident)
                pe.wait_ge(q_scaled, c + 1)
                for h in range(HEADS):
                    m = pe.transpose(col(bank(1), h), col(qn[:, :], h), ident)
                m.then_inc(kq_turned, 1)
                pe.wait_ge(knT_copied, c + 1)
                for h in range(HEADS):
                    m = pe.matmul(col(bank(4), h), col(knT[:, :], h), col(knT[:, :], h), start=True, stop=True)
                m.then_inc(grams_done, 1)
                pe.wait_ge(qnT_copied, c + 1)
                pe.wait_ge(v_scaled, c + 1)
                for h in range(HEADS):
                    m = pe.matmul(col(bank(2), h), col(knT[:, :], h), col(qnT[:, :], h), start=True, stop=True)
                m.then_inc(scores_done, 1)
                pe.wait_ge(mask_done, c * LEVELS + 1)
                pe.wait_ge(egr_done, c + 1)
                for h in range(HEADS):
                    m = pe.transpose(col(bank(3), h), col(B[:, 0, :], h), ident)
                m.then_inc(b0_turned, 1)
                for level in range(1, LEVELS):
                    pe.wait_ge(mask_done, c * LEVELS + (level + 1))
                    pe.wait_ge(xt_sub, c * LEVELS + level)
                    for h in range(HEADS):
                        m = pe.matmul(col(bank(3), h), col(B[:, level, :], h), col(XT[:, :], h), start=True, stop=True)
                    m.then_inc(z_done, 1)
                    pe.wait_ge(z_copied, c * (LEVELS - 1) + level)
                    pe.wait_ge(x_sub, c * (LEVELS - 1) + level)
                    for h in range(HEADS):
                        m = pe.matmul(col(bank(4), h), col(X[:, :], h), col(Z[:, :], h), start=True, stop=True)
                    m.then_inc(xt_done, 1)
                    if level < LEVELS - 1:
                        for h in range(HEADS):
                            m = pe.matmul(col(bank(5), h), col(Z[:, :], h), col(X[:, :], h), start=True, stop=True)
                        m.then_inc(x_done, 1)
                pe.wait_ge(xt_sub, c * LEVELS + LEVELS)
                for h in range(HEADS):
                    m = pe.matmul(col(bank(5), h), col(XT[:, :], h), col(vb[:, :], h), start=True, stop=True)
                m.then_inc(u_done, 1)
                pe.wait_ge(s_upd, c + 1)
                for h in range(HEADS):
                    m = pe.matmul(col(bank(6), h), col(kbg[:, :], h), col(XT[:, :], h), start=True, stop=True)
                m.then_inc(w_done, 1)
                pe.wait_ge(w_copied, c + 1)
                for h in range(HEADS):
                    m = pe.matmul(col(bank(6), h), col(WT[:, :], h), col(S_[:, :], h), start=True, stop=True)
                m.then_inc(p1_done, 1)
                pe.wait_ge(vnew_done, c + 1)
                pe.wait_ge(intra_done, c + 1)
                pe.wait_ge(qdec_done, c + 1)
                pe.wait_ge(out_done, c)
                for h in range(HEADS):
                    pe.matmul(col(bank(7), h), col(S_[:, :], h), col(qdec[:, :], h), start=True, stop=False)
                    m = pe.matmul(col(bank(7), h), col(vnew[:, :], h), col(intra[:, :], h), start=False, stop=True)
                m.then_inc(o_done, 1)
                for h in range(HEADS):
                    m = pe.matmul(col(bank(6), h), col(kdec[:, :], h), col(vnew[:, :], h), start=True, stop=True)
                m.then_inc(s_done, 1)
                pe.wait_ge(osq_done, c + 1)
                pe.matmul(bank(2), ones_mean[:, :], osq[:, :], start=True, stop=True).then_inc(msq_done, 1)

        @block.vector
        def _(dve):
            dve.wait_ge(const_loaded, 80)
            dve.wait_ge(consts_set, 4)
            dve.wait_ge(logits_turned, 1)
            for n in range(2):
                m = dve.tensor_copy(lt[:, n * 8:(n + 1) * 8, :], ps[:, n, 0:8 * 36].rearrange("p (c h) -> p c h", c=8))
            m.then_inc(logits_copied, 1)
            dve.wait_ge(logits_copied, 1)
            dtb_all = dtb[:, :].rearrange("p (o h) -> p o h", o=1).broadcast_to([P, NC, HEADS])
            dve.tensor_tensor(g[:, :, :], lt[:, :, 32:36], dtb_all, ALU.add).then_inc(g_steps, 1)
            dve.wait_ge(beta_done, 5)
            dve.scalar_tensor_tensor(g[:, :, :], g[:, :, :], 0.0, gtmp[:, :, :], ALU.max, ALU.add).then_inc(g_steps, 1)
            dve.tensor_scalar(alog[:, :], alog[:, :], -1.0, None, ALU.mult).then_inc(g_steps, 1)
            dve.wait_ge(g_steps, 3)
            alog_all = alog[:, :].rearrange("p (o h) -> p o h", o=1).broadcast_to([P, NC, HEADS])
            dve.tensor_tensor(g[:, :, :], g[:, :, :], alog_all, ALU.mult).then_inc(g_steps, 1)
            dve.wait_ge(gcol_done, 2)
            dve.tensor_copy(gc[:, :, :], bank(0)[:, 0:NC * HEADS].rearrange("p (c h) -> p c h", c=NC)).then_inc(gcol_done, 1)
            dve.sem_inc(s_upd, 1)

            with dve.Fori(0, NC) as c:
                def cc(tile):
                    return tile[:, bass.ds(c, 1), :].rearrange("p o h -> p (o h)")

                dve.wait_ge(roots_done, c + 1)
                dve.reciprocal(rr[:, :], rr[:, :]).then_inc(coef_steps, 1)
                dve.wait_ge(coef_steps, c * 4 + 1)
                dve.tensor_tensor(coef[:, 0, :], rr[:, 0:4], cc(beta), ALU.mult).then_inc(coef_steps, 1)
                dve.tensor_tensor(coef[:, 1, :], rr[:, 0:4], cc(ekd), ALU.mult)
                dve.tensor_scalar(coef[:, 2, :], rr[:, 4:8], DK ** -0.5, None, ALU.mult).then_inc(coef_steps, 1)
                dve.tensor_tensor(heads(kn[:, :]), heads(bank(0)), per_head(rr[:, 0:4]), ALU.mult)
                dve.wait_ge(coef_steps, c * 4 + 2)
                dve.tensor_tensor(coef[:, 3, :], coef[:, 0, :], cc(egc), ALU.mult).then_inc(coef_steps, 1)
                dve.wait_ge(coef_steps, c * 4 + 4)
                dve.tensor_tensor(heads(kbg[:, :]), heads(bank(0)), per_head(coef[:, 3, :]), ALU.mult)
                dve.tensor_tensor(heads(kdec[:, :]), heads(bank(0)), per_head(coef[:, 1, :]), ALU.mult).then_inc(k_scaled, 1)
                dve.tensor_tensor(heads(qn[:, :]), heads(bank(1)), per_head(coef[:, 2, :]), ALU.mult).then_inc(q_scaled, 1)
                dve.tensor_tensor(heads(vb[:, :]), heads(bank(2)), per_head(cc(beta)), ALU.mult).then_inc(v_scaled, 1)
                dve.wait_ge(rows_done, c + 1)
                dve.tensor_tensor(heads(gd[:, :]), heads(bank(3)), per_head(cc(gc)), ALU.subtract).then_inc(g_diff_done, 1)
                dve.wait_ge(grams_done, c + 1)
                dve.wait_ge(e_done, c + 1)
                dve.tensor_tensor(M[:, :], bank(4), E[:, :], ALU.mult).then_inc(m_done, 1)
                dve.wait_ge(m_done, c + 1)
                dve.tensor_tensor(heads(L[:, :]), heads(M[:, :]), per_head(cc(beta)), ALU.mult).then_inc(l_done, 1)
                dve.wait_ge(scores_done, c + 1)
                dve.tensor_tensor(intra[:, :], bank(2), E[:, :], ALU.mult).then_inc(i1_done, 1)
                dve.wait_ge(egr_done, c + 1)
                dve.wait_ge(qnT_copied, c + 1)
                dve.tensor_tensor(qdec[:, :], qnT[:, :], egr[:, :], ALU.mult).then_inc(qdec_done, 1)
                dve.wait_ge(i1_done, c + 1)
                dve.tensor_tensor(heads(intra[:, :]), heads(intra[:, :]), all_heads(const_tile(C_TRIU)), ALU.mult).then_inc(intra_done, 1)
                dve.wait_ge(b0_turned, c + 1)
                ident4 = all_heads(const_tile(C_IDENT))
                dve.tensor_tensor(heads(XT[:, :]), ident4, heads(bank(3)), ALU.subtract).then_inc(xt_sub, 1)
                dve.tensor_tensor(heads(X[:, :]), ident4, heads(B[:, 0, :]), ALU.subtract).then_inc(x_sub, 1)
                for level in range(1, LEVELS):
                    dve.wait_ge(xt_done, c * (LEVELS - 1) + level)
                    dve.tensor_tensor(XT[:, :], XT[:, :], bank(4), ALU.subtract).then_inc(xt_sub, 1)
                    if level < LEVELS - 1:
                        dve.wait_ge(x_done, c * (LEVELS - 2) + level)
                        dve.tensor_tensor(X[:, :], X[:, :], bank(5), ALU.subtract).then_inc(x_sub, 1)
                dve.wait_ge(p1_done, c + 1)
                dve.wait_ge(u_copied, c + 1)
                dve.tensor_tensor(vnew[:, :], U[:, :], bank(6), ALU.subtract).then_inc(vnew_done, 1)
                dve.wait_ge(s_done, c + 1)
                last = heads(egr[:, :])[:, :, P - 1:P].broadcast_to([P, HEADS, P])
                dve.tensor_tensor(heads(S_[:, :]), heads(S_[:, :]), last, ALU.mult).then_inc(s1_done, 1)
                dve.wait_ge(s1_done, c + 1)
                dve.tensor_tensor(S_[:, :], S_[:, :], bank(6), ALU.add).then_inc(s_upd, 1)
                dve.wait_ge(oroot_done, c + 1)
                dve.reciprocal(orr[:, :], orr[:, :]).then_inc(orr_done, 1)
                dve.wait_ge(orr_done, c + 1)
                dve.wait_ge(stored, c * 16)
                dve.scalar_tensor_tensor(o[:, :], bank(7), gain[:, 0:1], orr[:, :], ALU.mult, ALU.mult).then_inc(o1_done, 1)
                dve.wait_ge(o1_done, c + 1)
                dve.wait_ge(z_loaded, c * 16 + 16)
                dve.tensor_tensor(o[:, :], o[:, :], zg[:, :], ALU.mult).then_inc(out_done, 1)


QB = S // P
FLAT = P * 384


def bucket_tiles():
    tiles = np.zeros((33, len(DILS), 384), np.float32)
    for v, d in enumerate(DILS):
        for i in range(384):
            rel = 255 - i
            if not 0 <= rel <= P:
                tiles[32, v, i] = -BIG
                continue
            n = rel * d
            large = 16 + int(np.log(max(n, 1) / 16) / np.log(2048 / 16) * 16)
            tiles[n if n < 16 else min(large, 31), v, i] = 1.0
    return tiles.reshape(33, len(DILS) * 384)


def bias_rows(nc, t):
    with ExitStack() as ctx:
        sbuf, psum, sem = allocators(nc, ctx)
        rel = sbuf("pr_rel", [33, AH], F32)
        buckets = sbuf("pr_buckets", [33, len(DILS) * 384], F32)
        rows = sbuf("pr_rows", [AH, len(DILS) * 384], F32)
        ps = psum("pr_ps", [P, len(DILS), 512], F32)
        loaded, ones_set, summed, copied, stored = (sem("pr_" + n) for n in "loaded ones_set summed copied stored".split())
        block = ctx.enter_context(nc.Block())

        @block.sync
        def _(sp):
            sp.dma_start(rel[0:32, :], t["rel_bias"]).then_inc(loaded, 16)
            sp.dma_start(buckets[:, :], t["buckets"]).then_inc(loaded, 16)
            sp.wait_ge(copied, len(DILS))
            for v in range(len(DILS)):
                src = rows[:, v * 384:(v + 1) * 384].rearrange("h (o i) -> h o i", o=1).broadcast_to([AH, P, 384])
                sp.dma_start(t["bias_flat"][v].rearrange("h (q i) -> h q i", i=384), src).then_inc(stored, 16)
            sp.wait_ge(stored, 16 * len(DILS))

        @block.vector
        def _(dve):
            dve.memset(rel[32:33, :], 1.0).then_inc(ones_set, 1)
            dve.wait_ge(summed, 1)
            for v in range(len(DILS)):
                dve.tensor_copy(rows[:, v * 384:(v + 1) * 384], ps[0:AH, v, 0:384]).then_inc(copied, 1)

        @block.tensor
        def _(pe):
            pe.wait_ge(loaded, 32)
            pe.wait_ge(ones_set, 1)
            for v in range(len(DILS)):
                m = pe.matmul(ps[0:AH, v, 0:384], rel[:, :], buckets[:, v * 384:(v + 1) * 384], start=True, stop=True)
            m.then_inc(summed, 1)


def attention_prompt(nc, t):
    with ExitStack() as ctx:
        sbuf, psum, sem = allocators(nc, ctx)
        qkv = sbuf("pg_qkv", [P, 4, 12 * P], F32)
        vtok = sbuf("pg_vtok", [P, 4, AH * HD], F32)
        bias = sbuf("pg_bias", [P, len(DILS), AH * 2 * P], F32)
        ident = sbuf("pg_ident", [P, P], F32)
        s = sbuf("pg_s", [P, 2, 4 * 2 * P], F32)
        e = sbuf("pg_e", [P, 2, 4 * 2 * P], F32)
        eT = sbuf("pg_eT", [P, 2, 4 * 2 * P], F32)
        uo = sbuf("pg_uo", [P, 2, UROW], F32)
        ps = psum("pg_ps", [P, 8, 512], F32)
        loaded = [sem(f"pg_loaded{n}") for n in range(4)]
        stored = [sem(f"pg_stored{n}") for n in range(2)]
        (const_loaded, v_turned, v_copied, scores_done, biased, max_done, e_done, turned, eT_copied, pv_done,
         o_copied) = (sem("pg_" + n) for n in
                      "const_loaded v_turned v_copied scores_done biased max_done e_done turned eT_copied pv_done o_copied".split())
        block = ctx.enter_context(nc.Block())
        SC, TR, OB, VB = 0, 4, 6, 7

        def group_loops(engine, group):
            group(0, 0, "head")
            with engine.Fori(1, 4) as grp:
                group(grp, 0, "full")
            with engine.Fori(4, 8) as grp:
                group(grp, 1, "head")
            with engine.Fori(8, 12) as grp:
                group(grp, 2, "own")

        def own_only(kind, n):
            return kind == "own" or (kind == "head" and n == 0)

        def scores_view(g2, own):
            view = ps[:, SC + 2 * g2:SC + 2 * g2 + 2, :].rearrange("p b (h k) -> p (b h) k", k=2 * P)
            return view[:, :, P:2 * P] if own else view

        def place(h):
            return h % 2 * 2 + h // 2

        def by_place(view):
            return view.rearrange("p (b a) k -> p b a k", b=2)

        def halves(tile, g2, own):
            view = tile[:, g2, :].rearrange("p (h k) -> p h k", k=2 * P)
            return view[:, :, P:2 * P] if own else view

        @block.sync
        def _(sp):
            for v in range(len(DILS)):
                toeplitz = t["bias_flat"][v][:, P - 1:P - 1 + P * (384 - 1)].rearrange("h (q k) -> q h k", k=384 - 1)
                for first in (0, 1, 4, 5):
                    at = first // 4 * 4 + place(first % 4)
                    sp.dma_start(bias[:, v, at * 2 * P:(at + 2) * 2 * P].rearrange("p (h k) -> p h k", h=2),
                                 toeplitz[:, first:first + 3:2, 0:2 * P]).then_inc(const_loaded, 16)
            sp.dma_start(ident[:, :], t["consts"][:, 0:P]).then_inc(const_loaded, 16)

            def group(grp, v, kind):
                src = t[("at", "at4", "at16")[v]].rearrange("n p s -> p n s")
                for n in range(4):
                    u = 4 * grp + n
                    wait_at_least(sp, scores_done, (u - 2) * 2)
                    sp.dma_start(qkv[:, n, :].rearrange("p (n s) -> p n s", n=12),
                                 src[:, :, bass.ds((u - QB * v) * P, P)]).then_inc(loaded[n], 16)

            group_loops(sp, group)

        @block.gpsimd
        def _(pool):
            def group(grp, v, kind):
                for n in range(4):
                    u = 4 * grp + n
                    if v == 0:
                        dst = t["U"][0][bass.ds(u * P, P), :]
                    elif v == 1:
                        dst = t["U"][1].rearrange("(b q r) c -> r b q c", b=4, r=4)[bass.ds(grp - 4, 1), n].rearrange("o q c -> (o q) c")
                    else:
                        dst = t["U"][2].rearrange("(q r) c -> r q c", r=16)[bass.ds(u - 2 * QB, 1)].rearrange("o q c -> (o q) c")
                    pool.wait_ge(o_copied, u + 1)
                    pool.dma_start(dst, uo[:, n % 2, :]).then_inc(stored[n % 2], 16)

            group_loops(pool, group)
            for par in range(2):
                pool.wait_ge(stored[par], 16 * 3 * QB // 2)

        @block.tensor
        def _(pe):
            pe.wait_ge(const_loaded, 16 * (4 * len(DILS) + 1))

            def scores(u, n, g2, own):
                wait_at_least(pe, biased, u * 2 + (g2 - 1))
                view = scores_view(g2, False)
                for h in range(4):
                    tile, row = (g2 * 4 + h) // 2, h % 2 * HD
                    q = qkv[row:row + HD, n, tile * P:(tile + 1) * P]
                    for slot, half in ((n - 1) % 4, 0), (n, 1):
                        if half or not own:
                            k = qkv[row:row + HD, slot, (4 + tile) * P:(5 + tile) * P]
                            m = pe.matmul(view[:, place(h), half * P:(half + 1) * P], q, k, start=True, stop=True)
                m.then_inc(scores_done, 1)

            def transposes(u, n, g2, own):
                pe.wait_ge(e_done, u * 2 + (g2 + 1))
                wait_at_least(pe, eT_copied, u * 2 + g2)
                for h in range(4):
                    for half in range(2):
                        if half or not own:
                            c = (h * 2 + half) * P
                            m = pe.transpose(ps[:, TR + c // 512, c % 512:c % 512 + P], e[:, g2, c:c + P], ident[:, :])
                m.then_inc(turned, 1)

            def values(u, n, g2, own):
                pe.wait_ge(eT_copied, u * 2 + (g2 + 1))
                if g2 == 0:
                    wait_at_least(pe, o_copied, u)
                pe.wait_ge(v_copied, u + 1)
                for h in range(4):
                    for slot, half in ((n - 1) % 4, 0), (n, 1):
                        if half or not own:
                            c = (place(h) * 2 + half) * P
                            hh = (g2 * 4 + h) * HD
                            m = pe.matmul(ps[:, OB, hh:hh + HD], eT[:, g2, c:c + P], vtok[:, slot, hh:hh + HD],
                                          start=own or half == 0, stop=half == 1)
                m.then_inc(pv_done, 1)

            def group(grp, v, kind):
                steps = [(4 * grp + n, n, g2, own_only(kind, n)) for n in range(4) for g2 in range(2)]
                for i in range(len(steps)):
                    u, n, g2, own = steps[i]
                    if g2 == 0:
                        pe.wait_ge(loaded[n], grp * 16 + 16)
                        wait_at_least(pe, v_copied, u)
                        for tile in range(4):
                            m = pe.transpose(ps[:, VB, tile * P:(tile + 1) * P], qkv[:, n, (8 + tile) * P:(9 + tile) * P], ident[:, :])
                        m.then_inc(v_turned, 1)
                    scores(*steps[i])
                    if i >= 2:
                        values(*steps[i - 2])
                    if i >= 1:
                        transposes(*steps[i - 1])
                values(*steps[-2])
                transposes(*steps[-1])
                values(*steps[-1])

            group_loops(pe, group)

        @block.scalar
        def _(act):
            def exponents(u, n, g2, own):
                act.wait_ge(max_done, u * 2 + (g2 + 1))
                wait_at_least(act, turned, u * 2 + (g2 - 1))
                for h in range(4):
                    hh = g2 * 4 + h
                    m = act.activation(halves(e, g2, own)[:, place(h), :], halves(s, g2, own)[:, place(h), :], ACT.Exp,
                                       bias=uo[:, n % 2, AH * HD + hh:AH * HD + hh + 1],
                                       accum_out=uo[:, n % 2, AH * HD + AH + hh:AH * HD + AH + hh + 1])
                m.then_inc(e_done, 1)

            def copy_turned(u, n, g2, own):
                act.wait_ge(turned, u * 2 + (g2 + 1))
                wait_at_least(act, pv_done, u * 2 + (g2 - 1))
                view = ps[:, TR:TR + 2, :].rearrange("p b (h k) -> p (b h) k", k=2 * P)
                act.activation(halves(eT, g2, own), view[:, :, P:2 * P] if own else view, ACT.Copy).then_inc(eT_copied, 1)

            def group(grp, v, kind):
                steps = [(4 * grp + n, n, g2, own_only(kind, n)) for n in range(4) for g2 in range(2)]
                for i in range(len(steps)):
                    u, n, g2, own = steps[i]
                    if g2 == 0:
                        act.wait_ge(v_turned, u + 1)
                        wait_at_least(act, pv_done, (u - 2) * 2)
                        act.activation(vtok[:, n, :], ps[:, VB, :], ACT.Copy).then_inc(v_copied, 1)
                    exponents(*steps[i])
                    if i >= 1:
                        copy_turned(*steps[i - 1])
                copy_turned(*steps[-1])

            group_loops(act, group)

        @block.vector
        def _(dve):
            dve.wait_ge(const_loaded, 16 * (4 * len(DILS) + 1))

            def step(grp, u, n, v, g2, own):
                if g2 == 0 and not (isinstance(grp, int) and n < 2):
                    dve.wait_ge(stored[n % 2], grp * 32 + n // 2 * 16)
                dve.wait_ge(scores_done, u * 2 + (g2 + 1))
                wait_at_least(dve, e_done, u * 2 + (g2 - 1))
                b = bias[:, v, :].rearrange("p (h k) -> p h k", h=AH)[:, g2 * 4:g2 * 4 + 4, :]
                dve.scalar_tensor_tensor(halves(s, g2, own), scores_view(g2, own), HD ** -0.5,
                                         b[:, :, P:2 * P] if own else b, ALU.mult, ALU.add).then_inc(biased, 1)
                dve.wait_ge(biased, u * 2 + (g2 + 1))
                maxima = uo[:, n % 2, AH * HD + g2 * 4:AH * HD + g2 * 4 + 4].rearrange("p (a b) -> p b a", b=2)
                dve.tensor_reduce(maxima, by_place(halves(s, g2, own)), AX_X, ALU.max,
                                  negate=True).then_inc(max_done, 1)

            def copy_out(u, n):
                dve.wait_ge(pv_done, u * 2 + 2)
                dve.wait_ge(e_done, u * 2 + 2)
                dve.tensor_copy(uo[:, n % 2, 0:AH * HD], ps[:, OB, :]).then_inc(o_copied, 1)

            def group(grp, v, kind):
                for n in range(4):
                    for g2 in range(2):
                        u = 4 * grp + n
                        step(grp, u, n, v, g2, own_only(kind, n))
                        if g2 == 1 and n:
                            copy_out(u - 1, n - 1)
                copy_out(4 * grp + 3, 3)

            group_loops(dve, group)


def merge_dilations(nc, t):
    with ExitStack() as ctx:
        sbuf, psum, sem = allocators(nc, ctx)
        NV = len(DILS)
        u = sbuf("pm_u", [P, 2, NV * UROW], F32)
        wt = sbuf("pm_wt", [P, 2, NV * AH], F32)
        negmax = sbuf("pm_negmax", [P, AH], F32)
        total = sbuf("pm_total", [P, 2, AH], F32)
        acc = sbuf("pm_acc", [P, 2, NV, AH * HD], F32)
        out = sbuf("pm_out", [P, 2, AH * HD], F32)
        ident = sbuf("pm_ident", [P, P], F32)
        ps = psum("pm_ps", [P, 2, 512], F32)
        loaded = [sem(f"pm_loaded{n}") for n in range(2)]
        stored = [sem(f"pm_stored{n}") for n in range(2)]
        (const_loaded, max_steps, w_ready, w_exp, weight_steps, scaled, summed, turned, copied) = (sem("pm_" + n) for n in
            "const_loaded max_steps w_ready w_exp weight_steps scaled summed turned copied".split())
        block = ctx.enter_context(nc.Block())

        def field(par, first, n):
            return u[:, par, :].rearrange("p (v c) -> p v c", v=NV)[:, :, first:first + n]

        def by_v(tile, par):
            return tile[:, par, :].rearrange("p (v h) -> p v h", v=NV)

        @block.sync
        def _(sp):
            sp.dma_start(ident[:, :], t["consts"][:, 0:P]).then_inc(const_loaded, 16)

            def load(i, par):
                sp.dma_start(u[:, par, :].rearrange("p (v c) -> p v c", v=NV),
                             t["U"].rearrange("v s c -> s v c")[bass.ds(i * P, P)]).then_inc(loaded[par], 16)

            def step(i, par, more=True):
                if more:
                    sp.wait_ge(scaled, i + 1)
                    load(i + 2, par)
                sp.wait_ge(copied, i + 1)
                sp.dma_start(t["mix"].rearrange("n p s -> p n s")[:, HEADS:2 * HEADS, bass.ds(i * P, P)],
                             out[:, par, :].rearrange("p (n s) -> p n s", n=4)).then_inc(stored[par], 16)

            load(0, 0)
            load(1, 1)
            for_pairs(sp, QB - 2, step)
            step(QB - 2, 0, False)
            step(QB - 1, 1, False)
            for par in range(2):
                sp.wait_ge(stored[par], 16 * QB // 2)

        @block.vector
        def _(dve):
            def step(i, par):
                dve.wait_ge(loaded[par], landed(i, par))
                nm = field(par, AH * HD, AH)
                dve.tensor_tensor(negmax[:, :], nm[:, 0, :], nm[:, 1, :], ALU.min).then_inc(max_steps, 1)
                dve.wait_ge(max_steps, i * 2 + 1)
                dve.tensor_tensor(negmax[:, :], negmax[:, :], nm[:, 2, :], ALU.min).then_inc(max_steps, 1)
                dve.wait_ge(max_steps, i * 2 + 2)
                dve.tensor_tensor(by_v(wt, par), negmax[:, :].rearrange("p (o h) -> p o h", o=1).broadcast_to([P, NV, AH]), nm,
                                  ALU.subtract).then_inc(w_ready, 1)
                dve.wait_ge(w_exp, i + 1)
                tmp = acc[:, par, 0, 0:NV * AH].rearrange("p (v h) -> p v h", v=NV)
                dve.wait_ge(summed, i * 2)
                dve.tensor_tensor(tmp, by_v(wt, par), field(par, AH * HD + AH, AH), ALU.mult).then_inc(weight_steps, 1)
                dve.wait_ge(weight_steps, i * 4 + 1)
                dve.tensor_reduce(total[:, par, :], tmp.rearrange("p v h -> p h v"), AX_X, ALU.add).then_inc(weight_steps, 1)
                dve.wait_ge(weight_steps, i * 4 + 2)
                dve.reciprocal(total[:, par, :], total[:, par, :]).then_inc(weight_steps, 1)
                dve.wait_ge(weight_steps, i * 4 + 3)
                dve.tensor_tensor(by_v(wt, par), by_v(wt, par),
                                  total[:, par, :].rearrange("p (o h) -> p o h", o=1).broadcast_to([P, NV, AH]),
                                  ALU.mult).then_inc(weight_steps, 1)
                dve.wait_ge(weight_steps, i * 4 + 4)
                w = by_v(wt, par)
                for v in range(NV):
                    dve_out = acc[:, par, v, :].rearrange("p (h e) -> p h e", h=AH)
                    rows = field(par, 0, AH * HD)[:, v, :].rearrange("p (h e) -> p h e", h=AH)
                    m = dve.tensor_tensor(dve_out, rows, w[:, v, :].rearrange("p (h o) -> p h o", o=1).broadcast_to([P, AH, HD]), ALU.mult)
                m.then_inc(scaled, 1)

            for_pairs(dve, QB, step)

        @block.gpsimd
        def _(pool):
            def step(i, par):
                pool.wait_ge(scaled, i + 1)
                pool.tensor_tensor(acc[:, par, 1, :], acc[:, par, 1, :], acc[:, par, 2, :], ALU.add).then_inc(summed, 1)
                pool.wait_ge(summed, i * 2 + 1)
                pool.tensor_tensor(acc[:, par, 0, :], acc[:, par, 0, :], acc[:, par, 1, :], ALU.add).then_inc(summed, 1)

            for_pairs(pool, QB, step)

        @block.tensor
        def _(pe):
            pe.wait_ge(const_loaded, 16)

            def step(i, par):
                pe.wait_ge(summed, i * 2 + 2)
                pe.wait_ge(copied, i)
                for n in range(4):
                    m = pe.transpose(ps[:, par, n * P:(n + 1) * P], acc[:, par, 0, n * P:(n + 1) * P], ident[:, :])
                m.then_inc(turned, 1)

            for_pairs(pe, QB, step)

        @block.scalar
        def _(act):
            def step(i, par):
                act.wait_ge(w_ready, i + 1)
                act.activation(wt[:, par, :], wt[:, par, :], ACT.Exp).then_inc(w_exp, 1)
                act.wait_ge(turned, i + 1)
                act.wait_ge(stored[par], i * 8 - par * 8)
                act.activation(out[:, par, :], ps[:, par, :], ACT.Copy).then_inc(copied, 1)

            for_pairs(act, QB, step)


HB = HEADS * NSAMP
NBH = NSAMP * AH
PADS = TOK - S


def head_mask():
    p, n, h = np.meshgrid(np.arange(P), np.arange(4), np.arange(AH), indexing="ij")
    return (2 * n + p // HD == h).astype(np.float32).reshape(P, 4 * AH)


def named(sem, prefix, names):
    return [sem(prefix + n) for n in names.split()]


def delta_samples(nc, t):
    with ExitStack() as ctx:
        sbuf, psum, sem = allocators(nc, ctx)
        state = sbuf("sd_state", [P, HB, P], F32)
        new_state = sbuf("sd_new_state", [P, HB, P], F32)
        diag = sbuf("sd_diag", [P, HB, P], F32)
        ident = sbuf("sd_ident", [P, P], F32)
        ones = sbuf("sd_ones", [P, P], F32)
        eps = sbuf("sd_eps", [P, 1], F32)
        dn = sbuf("sd_dn", [P, 12 * NSAMP], F32)
        z = sbuf("sd_z", [P, HB], F32)
        b_log = sbuf("sd_b", [P, HB], F32)
        a_log_in = sbuf("sd_a", [P, HB], F32)
        alog = sbuf("sd_alog", [P, HEADS], F32)
        dtb = sbuf("sd_dtb", [P, HEADS], F32)
        gain = sbuf("sd_gain", [P, 1], F32)
        sq = sbuf("sd_sq", [P, 2 * HB], F32)
        root = sbuf("sd_root", [P, 2 * HB], F32)
        kq = sbuf("sd_kq", [P, HB, 2], F32)
        kq_prod = sbuf("sd_kqprod", [P, HB], F32)
        soft, soft2, eg, beta, ks, delta, o, osq, oroot = (
            sbuf("sd_" + n, [P, HB], F32) for n in "soft soft2 eg beta ks delta o osq oroot".split())
        out = sbuf("sd_out", [P, HEADS * PADS], F32)
        ps = psum("sd_ps", [P, 8, 512], F32)
        loaded, state_loaded, stored = named(sem, "sd_", "loaded state_loaded stored")
        (consts_set, squares, norms, roots, recips, k_ready, q_ready, products, dots, kqs_done, beta_done, a_ready,
         abs_done, exp_done, ln_done, rate_done, soft_done, g_ready, eg_done, ks_done, v_less, delta_done, diag_done,
         spread, scaled, state_done, o_scaled, o_delta, o_done, o_squares, o_means, o_roots, o_recips, o_gained,
         out_ready, rate_neg) = named(sem, "sd_", """consts_set squares norms roots recips k_ready q_ready products dots kqs_done
         beta_done a_ready abs_done exp_done ln_done rate_done soft_done g_ready eg_done ks_done v_less delta_done
         diag_done spread scaled state_done o_scaled o_delta o_done o_squares o_means o_roots o_recips o_gained
         out_ready rate_neg""")
        block = ctx.enter_context(nc.Block())
        q, k, v = (dn[:, n * HB:(n + 1) * HB] for n in range(3))

        def by_head(tile):
            return tile[:, :].rearrange("p (h b) -> p h b", h=HEADS)

        def per_head_all(col):
            return col[:, :].rearrange("p (h o) -> p h o", o=1).broadcast_to([P, HEADS, NSAMP])

        def along(col, n):
            return col.rearrange("p (c o) -> p c o", o=1).broadcast_to([P, HB, n])

        @block.sync
        def _(sp):
            sp.dma_start(ident[:, :], t["consts"][:, 0:P]).then_inc(loaded, 16)
            sp.dma_start(dn[:, :].rearrange("p (n b) -> p n b", n=12), t["dn_samp"].rearrange("n p b -> p n b")).then_inc(loaded, 16)
            sp.dma_start(by_head(z), t["z"].rearrange("n p s -> p n s")[:, :, S:S + NSAMP]).then_inc(loaded, 16)
            sp.dma_start(by_head(b_log), t["ba"][0:HEADS, S:S + NSAMP].partition_broadcast(P)).then_inc(loaded, 16)
            sp.dma_start(by_head(a_log_in), t["ba"][32:32 + HEADS, S:S + NSAMP].partition_broadcast(P)).then_inc(loaded, 16)
            sp.dma_start(alog[:, :], t["a_log"].partition_broadcast(P)).then_inc(loaded, 16)
            sp.dma_start(dtb[:, :], t["dt_bias"].partition_broadcast(P)).then_inc(loaded, 16)
            sp.dma_start(gain[:, :], t["g_dn_out"]).then_inc(loaded, 16)
            for h in range(HEADS):
                sp.dma_start(state[:, h * NSAMP:(h + 1) * NSAMP, :],
                             t["state"][:, h].rearrange("b k e -> k b e")).then_inc(state_loaded, 16)
            sp.wait_ge(out_ready, 1)
            sp.dma_start(t["mix"].rearrange("n p s -> p n s")[:, 0:HEADS, S:TOK],
                         out[:, :].rearrange("p (h b) -> p h b", h=HEADS)).then_inc(stored, 16)
            sp.wait_ge(state_done, HB)
            for h in range(HEADS):
                sp.dma_start(t["new_state"][:, h].rearrange("b k e -> k b e"),
                             new_state[:, h * NSAMP:(h + 1) * NSAMP, :]).then_inc(stored, 16)
            sp.wait_ge(stored, 16 * (HEADS + 1))

        @block.gpsimd
        def _(pool):
            pool.memset(ones[:, :], 1.0).then_inc(consts_set, 1)
            pool.memset(eps[:, :], EPS).then_inc(consts_set, 1)
            pool.memset(out[:, :], 0.0).then_inc(consts_set, 1)
            pool.wait_ge(delta_done, 1)
            pool.tensor_tensor(diag[:, :, :], ident[:, :].rearrange("p (o j) -> p o j", o=1).broadcast_to([P, HB, P]),
                               along(delta[:, :], P), ALU.mult).then_inc(diag_done, 1)

        @block.scalar
        def _(act):
            act.wait_ge(loaded, 128)
            act.wait_ge(consts_set, 3)
            act.activation(sq[:, :], dn[:, 0:2 * HB], ACT.Square).then_inc(squares, 1)
            act.wait_ge(norms, 1)
            act.activation(root[:, :], ps[:, 0, 0:2 * HB], ACT.Sqrt, bias=eps[:, 0:1]).then_inc(roots, 1)
            act.activation(beta[:, :], b_log[:, :], ACT.Sigmoid).then_inc(beta_done, 1)
            act.wait_ge(a_ready, 1)
            act.activation(soft[:, :], a_log_in[:, :], ACT.Abs).then_inc(abs_done, 1)
            act.wait_ge(abs_done, 1)
            act.activation(soft2[:, :], soft[:, :], ACT.Exp, scale=-1.0).then_inc(exp_done, 1)
            act.activation(alog[:, :], alog[:, :], ACT.Exp).then_inc(rate_done, 1)
            act.wait_ge(exp_done, 1)
            act.activation(soft[:, :], soft2[:, :], ACT.Ln, bias=1.0).then_inc(ln_done, 1)
            act.wait_ge(g_ready, 1)
            act.activation(eg[:, :], a_log_in[:, :], ACT.Exp).then_inc(eg_done, 1)
            act.wait_ge(o_done, 1)
            act.activation(osq[:, :], o[:, :], ACT.Square).then_inc(o_squares, 1)
            act.wait_ge(o_means, 1)
            act.activation(oroot[:, :], ps[:, 3, 0:HB], ACT.Sqrt, bias=eps[:, 0:1], scale=1.0 / DK).then_inc(o_roots, 1)

        @block.tensor
        def _(pe):
            pe.wait_ge(loaded, 128)
            pe.wait_ge(consts_set, 3)
            pe.wait_ge(squares, 1)
            pe.matmul(ps[:, 0, 0:2 * HB], ones[:, :], sq[:, :], start=True, stop=True).then_inc(norms, 1)
            pe.wait_ge(products, 1)
            pe.matmul(ps[:, 1, 0:HB], ones[:, :], kq_prod[:, :], start=True, stop=True).then_inc(dots, 1)
            pe.wait_ge(state_loaded, 16 * HEADS)
            for c in range(HB):
                m = pe.matmul(ps[:, 2, 2 * c:2 * c + 2], state[:, c, :], kq[:, c, :], start=True, stop=True)
            m.then_inc(kqs_done, 1)
            pe.wait_ge(o_squares, 1)
            pe.matmul(ps[:, 3, 0:HB], ones[:, :], osq[:, :], start=True, stop=True).then_inc(o_means, 1)
            pe.wait_ge(diag_done, 1)
            for n in range(8):
                if n >= 4:
                    pe.wait_ge(state_done, 4 * (n - 3))
                pe.matmul(ps[:, 4 + n % 4, :], ones[:, :], diag[:, 4 * n:4 * n + 4, :].rearrange("p c j -> p (c j)"),
                          start=True, stop=True).then_inc(spread, 1)

        @block.vector
        def _(dve):
            dve.wait_ge(loaded, 128)
            dve.wait_ge(consts_set, 3)
            dve.tensor_tensor(by_head(a_log_in), by_head(a_log_in), per_head_all(dtb), ALU.add).then_inc(a_ready, 1)
            dve.wait_ge(roots, 1)
            dve.reciprocal(root[:, :], root[:, :]).then_inc(recips, 1)
            dve.wait_ge(recips, 1)
            dve.tensor_tensor(kq[:, :, 0], k, root[:, HB:2 * HB], ALU.mult).then_inc(k_ready, 1)
            dve.scalar_tensor_tensor(kq[:, :, 1], q, DK ** -0.5, root[:, 0:HB], ALU.mult, ALU.mult).then_inc(q_ready, 1)
            dve.wait_ge(k_ready, 1)
            dve.wait_ge(q_ready, 1)
            dve.tensor_tensor(kq_prod[:, :], kq[:, :, 0], kq[:, :, 1], ALU.mult).then_inc(products, 1)
            dve.wait_ge(rate_done, 1)
            dve.tensor_scalar(alog[:, :], alog[:, :], -1.0, None, ALU.mult).then_inc(rate_neg, 1)
            dve.wait_ge(ln_done, 1)
            dve.scalar_tensor_tensor(soft[:, :], a_log_in[:, :], 0.0, soft[:, :], ALU.max, ALU.add).then_inc(soft_done, 1)
            dve.wait_ge(soft_done, 1)
            dve.wait_ge(rate_neg, 1)
            dve.tensor_tensor(by_head(a_log_in), by_head(soft), per_head_all(alog), ALU.mult).then_inc(g_ready, 1)
            dve.wait_ge(eg_done, 1)
            dve.wait_ge(state_loaded, 16 * HEADS)
            dve.tensor_tensor(new_state[:, :, :], state[:, :, :], along(eg[:, :], P), ALU.mult).then_inc(scaled, 1)
            dve.wait_ge(kqs_done, 1)
            found = ps[:, 2, 0:2 * HB].rearrange("p (c two) -> p c two", two=2)
            dve.tensor_tensor(ks[:, :], found[:, :, 0], eg[:, :], ALU.mult).then_inc(ks_done, 1)
            dve.tensor_tensor(o[:, :], found[:, :, 1], eg[:, :], ALU.mult).then_inc(o_scaled, 1)
            dve.wait_ge(ks_done, 1)
            dve.tensor_tensor(ks[:, :], v, ks[:, :], ALU.subtract).then_inc(v_less, 1)
            dve.wait_ge(v_less, 1)
            dve.wait_ge(beta_done, 1)
            dve.tensor_tensor(delta[:, :], ks[:, :], beta[:, :], ALU.mult).then_inc(delta_done, 1)
            dve.wait_ge(delta_done, 1)
            dve.wait_ge(dots, 1)
            dve.tensor_tensor(osq[:, :], ps[:, 1, 0:HB], delta[:, :], ALU.mult).then_inc(o_delta, 1)
            dve.wait_ge(o_delta, 1)
            dve.wait_ge(o_scaled, 1)
            dve.tensor_tensor(o[:, :], o[:, :], osq[:, :], ALU.add).then_inc(o_done, 1)
            dve.wait_ge(scaled, 1)
            for c in range(HB):
                if c % 4 == 0:
                    dve.wait_ge(spread, c // 4 + 1)
                dve.scalar_tensor_tensor(new_state[:, c, :], ps[:, 4 + c // 4 % 4, c % 4 * P:(c % 4 + 1) * P],
                                         kq[:, c, 0:1], new_state[:, c, :], ALU.mult, ALU.add).then_inc(state_done, 1)
            dve.wait_ge(o_roots, 1)
            dve.reciprocal(oroot[:, :], oroot[:, :]).then_inc(o_recips, 1)
            dve.wait_ge(o_recips, 1)
            dve.scalar_tensor_tensor(o[:, :], o[:, :], gain[:, 0:1], oroot[:, :], ALU.mult, ALU.mult).then_inc(o_gained, 1)
            dve.wait_ge(o_gained, 1)
            dve.tensor_tensor(out[:, :].rearrange("p (h b) -> p h b", h=HEADS)[:, :, 0:NSAMP], by_head(o), by_head(z),
                              ALU.mult).then_inc(out_ready, 1)


def attention_samples(nc, t):
    with ExitStack() as ctx:
        sbuf, psum, sem = allocators(nc, ctx)
        NV = len(DILS)
        KEYS = (P, P, PAST // DILS[2])
        FIRST = (0, P, 2 * P)
        SELF = sum(KEYS)
        KC = NSAMP * AH * HD
        keys = sbuf("sa_keys", [P, NV, KC], F32)
        values = sbuf("sa_values", [P, NV, KC], F32)
        qrow = sbuf("sa_qrow", [P, KC], F32)
        diag = sbuf("sa_diag", [P, KC], F32)
        ident = sbuf("sa_ident", [P, P], F32)
        mask = sbuf("sa_mask", [P, 4 * AH], F32)
        ones = sbuf("sa_ones", [P, P], F32)
        new = sbuf("sa_new", [P, 12, NSAMP], F32)
        q_by_sample = sbuf("sa_qbs", [P, NSAMP, 4], F32)
        prod = sbuf("sa_prod", [P, 4, NSAMP], F32)
        masked = sbuf("sa_masked", [P, 4, NSAMP, AH], F32)
        rows = sbuf("sa_rows", [NSAMP, 2, AH * HD], F32)
        cols = sbuf("sa_cols", [P, NV, NBH], F32)
        bias = sbuf("sa_bias", [NBH, NV, P + 1], F32)
        s = sbuf("sa_s", [NBH, SELF + 1], F32)
        e = sbuf("sa_e", [NBH, SELF + 1], F32)
        negmax = sbuf("sa_negmax", [NBH, 1], F32)
        den = sbuf("sa_den", [NBH, 1], F32)
        w0 = sbuf("sa_w0", [NBH, 1], F32)
        diag0 = sbuf("sa_diag0", [NBH, NBH], F32)
        probs = sbuf("sa_probs", [P, NV, NBH], F32)
        own = sbuf("sa_own", [P, 4, NSAMP], F32)
        out = sbuf("sa_out", [P, 4, PADS], F32)
        ps = psum("sa_ps", [P, 8, 512], F32)
        (loaded, keys_loaded, values_loaded, stored) = named(sem, "sa_", "loaded keys_loaded values_loaded stored")
        (consts_set, q_sorted, diag_done, spread, spread_copied, products, masked_done, rows_turned, rows_copied,
         keys_times_q, cols_done, cols_turned, s_done, self_dots, max_done, e_done, den_done, recip_done, normalised,
         w0_done, diag0_done, probs_turned, probs_copied, w0_spread, pv_done, own_done, out_done) = named(sem, "sa_",
            """consts_set q_sorted diag_done spread spread_copied products masked_done rows_turned rows_copied
            keys_times_q cols_done cols_turned s_done self_dots max_done e_done den_done recip_done normalised
            w0_done diag0_done probs_turned probs_copied w0_spread pv_done own_done out_done""")
        block = ctx.enter_context(nc.Block())

        def gathered(cache, v):
            d = DILS[v]
            tokens = cache.rearrange("b (t d) c -> t d b c", d=d)
            n = PAST // d
            return tokens[n - KEYS[v]:n, 0]

        @block.sync
        def _(sp):
            sp.dma_start(ident[:, :], t["consts"][:, 0:P]).then_inc(loaded, 16)
            sp.dma_start(mask[:, :], t["head_mask"]).then_inc(loaded, 16)
            sp.dma_start(new[:, :, :], t["at"].rearrange("n p s -> p n s")[:, :, S:S + NSAMP]).then_inc(loaded, 16)
            for b in range(NSAMP):
                sp.dma_start(bias[b * AH:(b + 1) * AH, :, :],
                             t["bias_flat"].rearrange("v h i -> h v i")[:, :, P - 1:2 * P]).then_inc(loaded, 16)
            for v in range(NV):
                sp.dma_start(keys[0:KEYS[v], v, :].rearrange("p (b c) -> p b c", b=NSAMP),
                             gathered(t["cache_k"], v)).then_inc(keys_loaded, 16)
            for v in range(NV):
                sp.dma_start(values[0:KEYS[v], v, :].rearrange("p (b c) -> p b c", b=NSAMP),
                             gathered(t["cache_v"], v)).then_inc(values_loaded, 16)
            sp.wait_ge(rows_copied, 1)
            sp.dma_start(t["new_cache_k"][:, PAST - 1], rows[:, 0, :]).then_inc(stored, 16)
            sp.dma_start(t["new_cache_v"][:, PAST - 1], rows[:, 1, :]).then_inc(stored, 16)
            sp.wait_ge(out_done, 2)
            sp.dma_start(t["mix"].rearrange("n p s -> p n s")[:, HEADS:2 * HEADS, S:TOK], out[:, :, :]).then_inc(stored, 16)
            sp.wait_ge(stored, 48)

        @block.gpsimd
        def _(pool):
            pool.memset(ones[:, :], 1.0).then_inc(consts_set, 1)
            pool.memset(out[:, :, :], 0.0).then_inc(consts_set, 1)

        @block.scalar
        def _(act):
            for b in range(NSAMP):
                act.wait_ge(spread, b + 1)
                act.activation(qrow[:, b * 512:(b + 1) * 512], ps[:, b, :], ACT.Copy).then_inc(spread_copied, 1)
            act.wait_ge(rows_turned, 1)
            act.activation(rows[:, :, :], ps[0:NSAMP, 0:2, :], ACT.Copy).then_inc(rows_copied, 1)
            act.wait_ge(max_done, 1)
            act.activation(e[:, :], s[:, :], ACT.Exp, bias=negmax[:, 0:1], accum_out=den[:, 0:1]).then_inc(e_done, 1)
            act.wait_ge(probs_turned, 1)
            for v in range(NV):
                m = act.activation(probs[0:KEYS[v], v, :], ps[0:KEYS[v], 4, v * NBH:(v + 1) * NBH], ACT.Copy)
            m.then_inc(probs_copied, 1)

        @block.tensor
        def _(pe):
            pe.wait_ge(loaded, 176)
            pe.wait_ge(consts_set, 2)
            pe.wait_ge(diag_done, 1)
            for b in range(NSAMP):
                pe.matmul(ps[:, b, :], ones[:, :], diag[:, b * 512:(b + 1) * 512], start=True, stop=True).then_inc(spread, 1)
            pe.wait_ge(spread_copied, 2)
            for n in range(8):
                m = pe.transpose(ps[0:NSAMP, n // 4, n % 4 * P:(n % 4 + 1) * P], new[:, 4 + n, :], ident[:, :])
            m.then_inc(rows_turned, 1)
            pe.wait_ge(spread_copied, 3)
            pe.wait_ge(masked_done, 1)
            for n in range(4):
                m = pe.matmul(ps[0:NBH, 2, 0:2], masked[:, n, :, :].rearrange("p b h -> p (b h)"), ones[:, 0:2],
                              start=n == 0, stop=n == 3)
            m.then_inc(self_dots, 1)
            pe.wait_ge(spread_copied, 4)
            for v in range(NV):
                pe.wait_ge(cols_done, v + 1)
                pe.transpose(ps[0:NBH, 3, FIRST[v]:FIRST[v] + KEYS[v]], cols[0:KEYS[v], v, :],
                             ident[0:KEYS[v], 0:KEYS[v]]).then_inc(cols_turned, 1)
            pe.wait_ge(spread_copied, 5)
            pe.wait_ge(normalised, 1)
            for v in range(NV):
                m = pe.transpose(ps[0:KEYS[v], 4, v * NBH:(v + 1) * NBH], e[:, FIRST[v]:FIRST[v] + KEYS[v]], ident[0:NBH, 0:NBH])
            m.then_inc(probs_turned, 1)
            pe.wait_ge(spread_copied, 6)
            pe.wait_ge(diag0_done, 1)
            pe.matmul(ps[:, 5, 0:NBH], ones[0:NBH, :], diag0[:, :], start=True, stop=True).then_inc(w0_spread, 1)
            pe.wait_ge(spread_copied, 7)
            pe.wait_ge(probs_copied, 1)
            pe.wait_ge(values_loaded, 16 * NV)
            for b in range(NSAMP):
                for n in range(4):
                    for v in range(NV):
                        c = b * 512 + n * P
                        m = pe.matmul(ps[:, 6, b * AH + 2 * n:b * AH + 2 * n + 2], values[0:KEYS[v], v, c:c + P],
                                      probs[0:KEYS[v], v, b * AH + 2 * n:b * AH + 2 * n + 2], start=v == 0, stop=v == NV - 1)
            m.then_inc(pv_done, 1)

        @block.vector
        def _(dve):
            dve.wait_ge(loaded, 176)
            dve.wait_ge(consts_set, 2)
            dve.tensor_copy(q_by_sample[:, :, :], new[:, 0:4, :].rearrange("p n b -> p b n")).then_inc(q_sorted, 1)
            dve.wait_ge(q_sorted, 1)
            qcols = q_by_sample[:, :, :].rearrange("p b n -> p (b n)").rearrange("p (c o) -> p c o", o=1)
            dve.tensor_tensor(diag[:, :].rearrange("p (c j) -> p c j", j=P),
                              ident[:, :].rearrange("p (o j) -> p o j", o=1).broadcast_to([P, 4 * NSAMP, P]),
                              qcols.broadcast_to([P, 4 * NSAMP, P]), ALU.mult).then_inc(diag_done, 1)
            dve.tensor_tensor(prod[:, :, :], new[:, 0:4, :], new[:, 4:8, :], ALU.mult).then_inc(products, 1)
            dve.wait_ge(products, 1)
            for n in range(4):
                m = dve.tensor_tensor(masked[:, n, :, :],
                                      prod[:, n, :].rearrange("p (b o) -> p b o", o=1).broadcast_to([P, NSAMP, AH]),
                                      mask[:, n * AH:(n + 1) * AH].rearrange("p (o h) -> p o h", o=1).broadcast_to([P, NSAMP, AH]),
                                      ALU.mult)
            m.then_inc(masked_done, 1)
            dve.wait_ge(spread_copied, NSAMP)
            dve.wait_ge(keys_loaded, 16 * NV)
            for v in range(NV):
                kv = keys[0:KEYS[v], v, :]
                dve.tensor_tensor(kv, kv, qrow[0:KEYS[v], :], ALU.mult).then_inc(keys_times_q, 1)
                dve.wait_ge(keys_times_q, v + 1)
                dve.tensor_reduce(cols[0:KEYS[v], v, :], kv.rearrange("p (c e) -> p c e", e=HD), AX_X, ALU.add).then_inc(cols_done, 1)
            dve.wait_ge(self_dots, 1)
            dve.wait_ge(cols_turned, NV)
            for v in range(NV):
                dve.scalar_tensor_tensor(s[:, FIRST[v]:FIRST[v] + KEYS[v]], ps[0:NBH, 3, FIRST[v]:FIRST[v] + KEYS[v]],
                                         HD ** -0.5, bias[:, v, P - KEYS[v]:P], ALU.mult, ALU.add).then_inc(s_done, 1)
            dve.scalar_tensor_tensor(s[:, SELF:SELF + 1], ps[0:NBH, 2, 0:1], HD ** -0.5, bias[:, 0, P:P + 1],
                                     ALU.mult, ALU.add).then_inc(s_done, 1)
            dve.wait_ge(s_done, NV + 1)
            dve.tensor_reduce(negmax[:, :], s[:, :], AX_X, ALU.max, negate=True).then_inc(max_done, 1)
            dve.wait_ge(e_done, 1)
            dve.scalar_tensor_tensor(den[:, :], e[:, SELF:SELF + 1], NV - 1.0, den[:, :], ALU.mult, ALU.add).then_inc(den_done, 1)
            dve.wait_ge(den_done, 1)
            dve.reciprocal(den[:, :], den[:, :]).then_inc(recip_done, 1)
            dve.wait_ge(recip_done, 1)
            dve.tensor_scalar(e[:, :], e[:, :], den[:, 0:1], None, ALU.mult).then_inc(normalised, 1)
            dve.wait_ge(normalised, 1)
            dve.tensor_scalar(w0[:, :], e[:, SELF:SELF + 1], float(NV), None, ALU.mult).then_inc(w0_done, 1)
            dve.wait_ge(w0_done, 1)
            dve.tensor_scalar(diag0[:, :], ident[0:NBH, 0:NBH], w0[:, 0:1], None, ALU.mult).then_inc(diag0_done, 1)
            dve.wait_ge(w0_spread, 1)

            def of_head(bank, half):
                return ps[half * HD:(half + 1) * HD, bank, 0:NBH].rearrange("p (b n two) -> p n b two", b=NSAMP, two=2)[:, :, :, half]

            for half in range(2):
                rows_ = slice(half * HD, (half + 1) * HD)
                m = dve.tensor_tensor(own[rows_, :, :], new[rows_, 8:12, :], of_head(5, half), ALU.mult)
            m.then_inc(own_done, 1)
            dve.wait_ge(own_done, 1)
            dve.wait_ge(pv_done, 1)
            for half in range(2):
                rows_ = slice(half * HD, (half + 1) * HD)
                dve.tensor_tensor(out[rows_, :, 0:NSAMP], own[rows_, :, :], of_head(6, half), ALU.add).then_inc(out_done, 1)


def for_pairs(engine, n, step):
    with engine.Fori(0, n // 2) as j:
        step(2 * j, 0)
        step(2 * j + 1, 1)
    if n % 2:
        step(n - 1, 0)


def blocks(engine, step):
    step(0, 0, True)
    with engine.Fori(1, (NB + 1) // 2) as j:
        step(2 * j - 1, 1, False)
        step(2 * j, 0, False)


def output_projection(nc, t):
    with ExitStack() as ctx:
        sbuf, psum, sem = allocators(nc, ctx)
        w_raw = sbuf("pc_w", [P, 2, KD * P], F32)
        w_hi = sbuf("pc_whi", [P, KD, KD * P], F32R)
        w_lo = sbuf("pc_wlo", [P, KD, KD * P], F32R)
        mix = sbuf("pc_mix", [P, KD, TB], F32)
        mix_hi = sbuf("pc_mixhi", [P, 2, KD, TB], F32R)
        mix_lo = sbuf("pc_mixlo", [P, 2, KD, TB], F32R)
        x = sbuf("pc_x", [P, 2, KD, TB], F32)
        out = sbuf("pc_out", [P, 2, KD, TB], F32)
        sq = sbuf("pc_sq", [P, KD, TB], F32)
        ssum = sbuf("pc_ssum", [P, TB], F32)
        rstd = sbuf("pc_rstd", [P, TB], F32)
        gains = sbuf("pc_gains", [P, 2, KD], F32)
        eps = sbuf("pc_eps", [P, 1], F32)
        ones_mean = sbuf("pc_ones", [P, P], F32)
        prod_ps = psum("pc_prod", [P, 7, 512], F32)
        mean_ps = psum("pc_mean", [P, 512], F32)
        gains_loaded = sem("pc_gains_loaded")
        consts_set = sem("pc_consts_set")
        w_loaded = (sem("pc_w_loaded0"), sem("pc_w_loaded1"))
        w_hi_done = sem("pc_w_hi_done")
        w_lo_done = sem("pc_w_lo_done")
        mix_loaded = sem("pc_mix_loaded")
        mix_hi_done = sem("pc_mix_hi_done")
        mix_lo_done = sem("pc_mix_lo_done")
        x_loaded = (sem("pc_x_loaded0"), sem("pc_x_loaded1"))
        prod_done = sem("pc_prod_done")
        bank_read = sem("pc_bank_read")
        squares_done = sem("pc_squares_done")
        sums_done = sem("pc_sums_done")
        means_done = sem("pc_means_done")
        roots_done = sem("pc_roots_done")
        recips_done = sem("pc_recips_done")
        scaled_done = sem("pc_scaled_done")
        x1_done = sem("pc_x1_done")
        h2_done = sem("pc_h2_done")
        stored = (sem("pc_stored0"), sem("pc_stored1"))
        block = ctx.enter_context(nc.Block())

        @block.sync
        def _(sp):
            sp.dma_start(gains[:, 0, :], t["g_post_mix"]).then_inc(gains_loaded, 16)
            sp.dma_start(gains[:, 1, :], t["g_pre_ffn"]).then_inc(gains_loaded, 16)

            def load_w(j, par):
                if not isinstance(j, int):
                    sp.wait_ge(w_lo_done, j - 1)
                sp.dma_start(w_raw[:, par, :], t["w_out"][j]).then_inc(w_loaded[par], 16)

            def load_mix(b):
                sp.wait_ge(mix_lo_done, b)
                sp.dma_start(mix[:, :, :], t["mix"].rearrange("k p t -> p k t")[:, :, bass.ds(b * TB, TB)]
                             ).then_inc(mix_loaded, 16)

            def load_x(b, par):
                sp.dma_start(x[:, par], t["xT"][b]).then_inc(x_loaded[par], 16)

            load_mix(0)
            load_w(0, 0)
            load_w(1, 1)
            with sp.Fori(1, KD // 2) as j:
                load_w(2 * j, 0)
                load_w(2 * j + 1, 1)
            load_x(0, 0)
            load_mix(1)
            load_x(1, 1)

            def finish(b, par):
                sp.wait_ge(x1_done, b + 1)
                sp.dma_start(t["x1"][b], x[:, par]).then_inc(stored[par], 16)
                sp.wait_ge(h2_done, b + 1)
                sp.dma_start(t["h2"][b], out[:, par]).then_inc(stored[par], 16)

            def block_io(b, par):
                load_mix(b + 2)
                finish(b, par)
                sp.wait_ge(stored[par], landed(b, par, 2))
                load_x(b + 2, par)

            for b in range(NB - 2):
                block_io(b, b % 2)
            for b in range(NB - 2, NB):
                finish(b, b % 2)
            for par in range(2):
                sp.wait_ge(stored[par], 32 * ((NB + 1 - par) // 2))

        @block.gpsimd
        def _(pool):
            pool.memset(ones_mean[:, :], 1.0 / D).then_inc(consts_set, 1)
            pool.memset(eps[:, :], EPS).then_inc(consts_set, 1)

            def split_mix(b, par, first):
                pool.wait_ge(mix_hi_done, b + 1)
                pool.tensor_tensor(mix_lo[:, par], mix[:, :, :], mix_hi[:, par].bitcast(F32),
                                   ALU.subtract).then_inc(mix_lo_done, 1)

            def split_w(j, par):
                pool.wait_ge(w_hi_done, j + 1)
                pool.tensor_tensor(w_lo[:, bass.ds(j, 1), :], w_raw[:, par:par + 1, :],
                                   w_hi[:, bass.ds(j, 1), :].bitcast(F32), ALU.subtract).then_inc(w_lo_done, 1)

            split_mix(0, 0, True)
            for_pairs(pool, KD, split_w)
            with pool.Fori(1, (NB + 1) // 2) as j:
                split_mix(2 * j - 1, 1, False)
                split_mix(2 * j, 0, False)

        @block.scalar
        def _(act):
            act.wait_ge(consts_set, 2)

            def split_mix(b, par):
                act.wait_ge(mix_loaded, 16 * b + 16)
                if not isinstance(b, int):
                    act.wait_ge(prod_done, b * KD - KD)
                act.activation(mix_hi[:, par], mix[:, :, :], ACT.Copy).then_inc(mix_hi_done, 1)

            def split_w(j, par):
                act.wait_ge(w_loaded[par], landed(j, par))
                act.activation(w_hi[:, bass.ds(j, 1), :], w_raw[:, par:par + 1, :], ACT.Copy).then_inc(w_hi_done, 1)

            split_mix(0, 0)
            for_pairs(act, KD, split_w)

            def block_work(b, par):
                if not isinstance(b, int):
                    act.wait_ge(stored[par], landed(b, par, 2) - 32)
                for j in range(KD):
                    act.wait_ge(prod_done, b * KD + (j + 1))
                    act.activation(out[:, par, j, :], prod_ps[:, j % 7, 0:TB], ACT.Copy).then_inc(bank_read, 1)
                act.wait_ge(bank_read, b * KD + KD)
                act.activation(sq[:, :, :], out[:, par], ACT.Square).then_inc(squares_done, 1)
                act.wait_ge(means_done, 2 * b + 1)
                act.activation(ssum[:, :], mean_ps[:, 0:TB], ACT.Sqrt, bias=eps[:, 0:1]).then_inc(roots_done, 1)
                act.wait_ge(x1_done, b + 1)
                act.activation(sq[:, :, :], x[:, par], ACT.Square).then_inc(squares_done, 1)
                act.wait_ge(means_done, 2 * b + 2)
                act.activation(ssum[:, :], mean_ps[:, 0:TB], ACT.Sqrt, bias=eps[:, 0:1]).then_inc(roots_done, 1)

            split_mix(1, 1)
            block_work(0, 0)
            with act.Fori(1, NB // 2) as j:
                split_mix(2 * j, 0)
                block_work(2 * j - 1, 1)
                split_mix(2 * j + 1, 1)
                block_work(2 * j, 0)
            split_mix(NB - 1, 0)
            act.wait_ge(stored[1], 32)
            block_work(NB - 2, 1)
            act.wait_ge(stored[0], 64)
            block_work(NB - 1, 0)

        @block.tensor
        def _(pe):
            pe.wait_ge(consts_set, 2)

            def mean(n):
                pe.wait_ge(sums_done, n + 1)
                pe.matmul(mean_ps[:, 0:TB], ones_mean[:, :], ssum[:, :], start=True, stop=True).then_inc(means_done, 1)

            def block_products(b, par, first):
                pe.wait_ge(mix_lo_done, b + 1)
                for j in range(KD):
                    if first:
                        pe.wait_ge(w_lo_done, j + 1)
                    if not first and j == 2:
                        mean(2 * b - 2)
                    if not first and j == 7:
                        mean(2 * b - 1)
                    if j == 7:
                        pe.wait_ge(bank_read, b * KD + 1)
                    elif not first:
                        pe.wait_ge(bank_read, b * KD + (j - 7 if j else 0))
                    for k in range(KD):
                        w = slice(k * P, (k + 1) * P)
                        mm = hi_lo_products(pe, prod_ps[:, j % 7, 0:TB], w_hi[:, j, w], w_lo[:, j, w],
                                            mix_hi[:, par, k, :], mix_lo[:, par, k, :], k == 0, k == KD - 1)
                    mm.then_inc(prod_done, 1)

            blocks(pe, block_products)
            mean(2 * NB - 2)
            mean(2 * NB - 1)

        @block.vector
        def _(dve):
            dve.wait_ge(gains_loaded, 32)

            def rms(n):
                dve.wait_ge(squares_done, n + 1)
                dve.tensor_reduce(ssum[:, :], sq[:, :, :].rearrange("p k t -> p t k"), AX_X, ALU.add).then_inc(sums_done, 1)
                dve.wait_ge(roots_done, n + 1)
                dve.reciprocal(rstd[:, :], ssum[:, :]).then_inc(recips_done, 1)
                dve.wait_ge(recips_done, n + 1)

            def norms(b, par, first):
                rms(2 * b)
                for k in range(KD):
                    m = dve.scalar_tensor_tensor(out[:, par, k, :], out[:, par, k, :], gains[:, 0, k:k + 1],
                                                 rstd[:, :], ALU.mult, ALU.mult)
                m.then_inc(scaled_done, 1)
                dve.wait_ge(x_loaded[par], landed(b, par))
                dve.wait_ge(scaled_done, b + 1)
                dve.tensor_tensor(x[:, par], x[:, par], out[:, par], ALU.add).then_inc(x1_done, 1)
                rms(2 * b + 1)
                for k in range(KD):
                    m = dve.scalar_tensor_tensor(out[:, par, k, :], x[:, par, k, :], gains[:, 1, k:k + 1],
                                                 rstd[:, :], ALU.mult, ALU.mult)
                m.then_inc(h2_done, 1)

            blocks(dve, norms)


def gate_and_up(nc, t):
    with ExitStack() as ctx:
        sbuf, psum, sem = allocators(nc, ctx)
        h_hi = sbuf("pd_h_hi", [P, KD, TOK], F32R)
        h_lo = sbuf("pd_h_lo", [P, KD, TOK], F32R)
        h_raw = sbuf("pd_h", [P, 2, KD, TB], F32)
        w_raw = sbuf("pd_w", [P, 2, KD * P], F32)
        w_hi = sbuf("pd_whi", [P, 2, KD * P], F32R)
        w_lo = sbuf("pd_wlo", [P, 2, KD * P], F32R)
        gate = sbuf("pd_gate", [P, TOK], F32)
        act_row = sbuf("pd_act", [P, TOK], F32)
        prod_ps = psum("pd_prod", [P, NB, 512], F32)
        h_loaded = (sem("pd_h_loaded0"), sem("pd_h_loaded1"))
        h_hi_done = sem("pd_h_hi_done")
        h_lo_done = sem("pd_h_lo_done")
        w_loaded = (sem("pd_w_loaded0"), sem("pd_w_loaded1"))
        w_hi_done = sem("pd_w_hi_done")
        w_lo_done = sem("pd_w_lo_done")
        prod_done = sem("pd_prod_done")
        gates_done = sem("pd_gates_done")
        acts_done = sem("pd_acts_done")
        stored = sem("pd_stored")
        block = ctx.enter_context(nc.Block())

        @block.sync
        def _(sp):
            def load_w(c, par):
                sp.dma_start(w_raw[:, par, :], t["w_gate_up"][c]).then_inc(w_loaded[par], 16)

            load_w(0, 0)
            for b in range(NB):
                if b >= 2:
                    sp.wait_ge(h_lo_done, b - 1)
                sp.dma_start(h_raw[:, b % 2], t["h2"][b]).then_inc(h_loaded[b % 2], 16)
            load_w(1, 1)

            def hidden_tile(j, more):
                if more:
                    sp.wait_ge(w_lo_done, 2 * j + 1)
                    load_w(2 * j + 2, 0)
                    sp.wait_ge(w_lo_done, 2 * j + 2)
                    load_w(2 * j + 3, 1)
                sp.wait_ge(acts_done, j * NB + NB)
                sp.dma_start(t["a"][j], act_row[:, :]).then_inc(stored, 16)

            with sp.Fori(0, KF - 1) as j:
                hidden_tile(j, True)
            hidden_tile(KF - 1, False)
            sp.wait_ge(stored, 16 * KF)

        @block.gpsimd
        def _(pool):
            def split_lo(c, par):
                pool.wait_ge(w_hi_done, c + 1)
                pool.tensor_tensor(w_lo[:, par, :], w_raw[:, par, :], w_hi[:, par, :].bitcast(F32),
                                   ALU.subtract).then_inc(w_lo_done, 1)

            split_lo(0, 0)
            split_lo(1, 1)
            with pool.Fori(1, KF) as j:
                split_lo(2 * j, 0)
                split_lo(2 * j + 1, 1)

        @block.scalar
        def _(act):
            def split_hi(c, par):
                act.wait_ge(w_loaded[par], landed(c, par))
                if not isinstance(c, int):
                    act.wait_ge(prod_done, (c - 1) * NB)
                act.activation(w_hi[:, par, :], w_raw[:, par, :], ACT.Copy).then_inc(w_hi_done, 1)

            split_hi(0, 0)
            for b in range(NB):
                act.wait_ge(h_loaded[b % 2], 16 * (b // 2 + 1))
                act.activation(h_hi[:, :, b * TB:(b + 1) * TB], h_raw[:, b % 2], ACT.Copy).then_inc(h_hi_done, 1)
            split_hi(1, 1)

            def hidden_tile(j, more):
                act.wait_ge(acts_done, j * NB)
                for b in range(NB):
                    act.wait_ge(prod_done, j * (2 * NB) + (b + 1))
                    act.activation(gate[:, b * TB:(b + 1) * TB], prod_ps[:, b, 0:TB], ACT.Silu).then_inc(gates_done, 1)
                if more:
                    split_hi(2 * j + 2, 0)
                    split_hi(2 * j + 3, 1)

            with act.Fori(0, KF - 1) as j:
                hidden_tile(j, True)
            hidden_tile(KF - 1, False)

        @block.tensor
        def _(pe):
            def project(c, par, read, count, waited):
                pe.wait_ge(w_lo_done, c + 1)
                for b in range(NB):
                    if waited:
                        pe.wait_ge(read, count + (b + 1))
                    else:
                        pe.wait_ge(h_lo_done, b + 1)
                    cols = slice(b * TB, (b + 1) * TB)
                    for k in range(KD):
                        w = slice(k * P, (k + 1) * P)
                        mm = hi_lo_products(pe, prod_ps[:, b, 0:TB], w_hi[:, par, w], w_lo[:, par, w],
                                            h_hi[:, k, cols], h_lo[:, k, cols], k == 0, k == KD - 1)
                    mm.then_inc(prod_done, 1)

            project(0, 0, None, 0, False)
            project(1, 1, gates_done, 0, True)
            with pe.Fori(1, KF) as j:
                project(2 * j, 0, acts_done, j * NB - NB, True)
                project(2 * j + 1, 1, gates_done, j * NB, True)

        @block.vector
        def _(dve):
            for b in range(NB):
                cols = slice(b * TB, (b + 1) * TB)
                dve.wait_ge(h_hi_done, b + 1)
                dve.tensor_tensor(h_lo[:, :, cols], h_raw[:, b % 2], h_hi[:, :, cols].bitcast(F32),
                                  ALU.subtract).then_inc(h_lo_done, 1)
            with dve.Fori(0, KF) as j:
                dve.wait_ge(stored, j * 16)
                for b in range(NB):
                    cols = slice(b * TB, (b + 1) * TB)
                    dve.wait_ge(prod_done, j * (2 * NB) + (NB + b + 1))
                    dve.wait_ge(gates_done, j * NB + (b + 1))
                    dve.tensor_tensor(act_row[:, cols], prod_ps[:, b, 0:TB], gate[:, cols],
                                      ALU.mult).then_inc(acts_done, 1)


KH = KF // 2


def wait_at_least(engine, semaphore, value):
    if not isinstance(value, int) or value > 0:
        engine.wait_ge(semaphore, value)


def down_projection(nc, t):
    with ExitStack() as ctx:
        sbuf, psum, sem = allocators(nc, ctx)
        a_raw = sbuf("pe_a", [P, KF, TB], F32)
        a_hi = sbuf("pe_ahi", [P, KF, TB], F32R)
        a_lo = sbuf("pe_alo", [P, KF, TB], F32R)
        w_raw = sbuf("pe_w", [P, 2, KH * P], F32)
        w_hi = sbuf("pe_whi", [P, 4, KH * P], F32R)
        w_lo = sbuf("pe_wlo", [P, 4, KH * P], F32R)
        x = sbuf("pe_x", [P, KD, TB], F32)
        out = sbuf("pe_out", [P, KD, TB], F32)
        sq = sbuf("pe_sq", [P, KD, TB], F32)
        ssum = sbuf("pe_ssum", [P, TB], F32)
        rstd = sbuf("pe_rstd", [P, TB], F32)
        gain = sbuf("pe_gain", [P, KD], F32)
        eps = sbuf("pe_eps", [P, 1], F32)
        ones_mean = sbuf("pe_ones", [P, P], F32)
        prod_ps = psum("pe_prod", [P, 4, 512], F32)
        mean_ps = psum("pe_mean", [P, 512], F32)
        gain_loaded = sem("pe_gain_loaded")
        consts_set = sem("pe_consts_set")
        a_loaded = sem("pe_a_loaded")
        a_hi_done = sem("pe_a_hi_done")
        a_lo_done = sem("pe_a_lo_done")
        a_read = sem("pe_a_read")
        w_loaded = (sem("pe_w_loaded0"), sem("pe_w_loaded1"))
        w_hi_done = sem("pe_w_hi_done")
        w_lo_done = sem("pe_w_lo_done")
        w_half_read = sem("pe_w_half_read")
        x_loaded = sem("pe_x_loaded")
        prod_done = sem("pe_prod_done")
        bank_read = sem("pe_bank_read")
        squares_done = sem("pe_squares_done")
        sums_done = sem("pe_sums_done")
        means_done = sem("pe_means_done")
        roots_done = sem("pe_roots_done")
        recips_done = sem("pe_recips_done")
        scaled_done = sem("pe_scaled_done")
        x2_done = sem("pe_x2_done")
        stored = sem("pe_stored")
        block = ctx.enter_context(nc.Block())

        @block.sync
        def _(sp):
            sp.dma_start(gain[:, :], t["g_post_ffn"]).then_inc(gain_loaded, 16)

            def load_w(n, half, j):
                wait_at_least(sp, w_lo_done, 2 * n + (half - 1))
                sp.dma_start(w_raw[:, half, :], t["w_down"][j][:, half * KH * P:(half + 1) * KH * P]
                             ).then_inc(w_loaded[half], 16)

            def load_a(b):
                wait_at_least(sp, a_lo_done, b * KH)
                sp.dma_start(a_raw[:, :, :], t["a"].rearrange("k p t -> p k t")[:, :, bass.ds(b * TB, TB)]
                             ).then_inc(a_loaded, 16)

            def store_x2(b):
                sp.wait_ge(x2_done, b + 1)
                sp.dma_start(t["x2"][b], x[:, :, :]).then_inc(stored, 16)

            def block_io(b, more):
                for j in range(KD if more else KD - 1):
                    load_w(b * KD + (j + 1), 0, (j + 1) % KD)
                    load_w(b * KD + (j + 1), 1, (j + 1) % KD)
                    if j == 1 and more:
                        load_a(b + 1)
                    if j == 4:
                        if not isinstance(b, int) or b:
                            store_x2(b - 1)
                            sp.wait_ge(stored, b * 16)
                        sp.dma_start(x[:, :, :], t["x1"][b]).then_inc(x_loaded, 16)

            load_w(0, 0, 0)
            load_w(0, 1, 0)
            load_a(0)
            block_io(0, True)
            with sp.Fori(1, NB - 1) as b:
                block_io(b, True)
            block_io(NB - 1, False)
            store_x2(NB - 1)
            sp.wait_ge(stored, 16 * NB)

        @block.gpsimd
        def _(pool):
            pool.memset(ones_mean[:, :], 1.0 / D).then_inc(consts_set, 1)
            pool.memset(eps[:, :], EPS).then_inc(consts_set, 1)
            with pool.Fori(0, KD * NB // 2) as m:
                for q in range(4):
                    pool.wait_ge(w_hi_done, 4 * m + (q + 1))
                    pool.tensor_tensor(w_lo[:, q, :], w_raw[:, q % 2, :], w_hi[:, q, :].bitcast(F32),
                                       ALU.subtract).then_inc(w_lo_done, 1)

        @block.scalar
        def _(act):
            act.wait_ge(consts_set, 2)

            def split_w(n, half, j):
                q = 2 * (j % 2) + half
                act.wait_ge(w_loaded[half], n * 16 + 16)
                wait_at_least(act, prod_done if half else w_half_read, n - 1)
                act.activation(w_hi[:, q, :], w_raw[:, half, :], ACT.Copy).then_inc(w_hi_done, 1)

            def split_a(b):
                act.wait_ge(a_loaded, b * 16 + 16)
                for g in range(KH):
                    if g < KH - 1:
                        wait_at_least(act, a_read, b * (KH - 1) + (g + 2 - KH))
                    else:
                        wait_at_least(act, prod_done, b * KD)
                    act.activation(a_hi[:, 2 * g:2 * g + 2, :], a_raw[:, 2 * g:2 * g + 2, :], ACT.Copy).then_inc(a_hi_done, 1)

            def block_work(b, more):
                for j in range(KD):
                    if more or j < KD - 1:
                        split_w(b * KD + (j + 1), 0, j + 1)
                        split_w(b * KD + (j + 1), 1, j + 1)
                    if more and j == KD - 1:
                        split_a(b + 1)
                    if j == 0:
                        wait_at_least(act, x2_done, b)
                    act.wait_ge(prod_done, b * KD + (j + 1))
                    act.activation(out[:, j, :], prod_ps[:, j % 4, 0:TB], ACT.Copy).then_inc(bank_read, 1)
                act.wait_ge(bank_read, b * KD + KD)
                act.activation(sq[:, :, :], out[:, :, :], ACT.Square).then_inc(squares_done, 1)
                act.wait_ge(means_done, b + 1)
                act.activation(ssum[:, :], mean_ps[:, 0:TB], ACT.Sqrt, bias=eps[:, 0:1]).then_inc(roots_done, 1)

            split_w(0, 0, 0)
            split_w(0, 1, 0)
            split_a(0)
            block_work(0, True)
            with act.Fori(1, NB - 1) as b:
                block_work(b, True)
            block_work(NB - 1, False)

        @block.tensor
        def _(pe):
            pe.wait_ge(consts_set, 2)

            def mean(b):
                pe.wait_ge(sums_done, b + 1)
                pe.matmul(mean_ps[:, 0:TB], ones_mean[:, :], ssum[:, :], start=True, stop=True).then_inc(means_done, 1)

            def block_products(b):
                for j in range(KD):
                    if j == 1 and not isinstance(b, int):
                        mean(b - 1)
                    wait_at_least(pe, bank_read, b * KD + (j - 3))
                    for k in range(KF):
                        if k % KH == 0:
                            pe.wait_ge(w_lo_done, b * (2 * KD) + (2 * j + k // KH + 1))
                        if j == 0 and k % 2 == 0:
                            pe.wait_ge(a_lo_done, b * KH + (k // 2 + 1))
                        q = 2 * (j % 2) + k // KH
                        w = slice(k % KH * P, (k % KH + 1) * P)
                        mm = hi_lo_products(pe, prod_ps[:, j % 4, 0:TB], w_hi[:, q, w], w_lo[:, q, w],
                                            a_hi[:, k, :], a_lo[:, k, :], k == 0, k == KF - 1)
                        if k == KH - 1:
                            mm.then_inc(w_half_read, 1)
                        if j == KD - 1 and k % 2 and k < KF - 1:
                            mm.then_inc(a_read, 1)
                    mm.then_inc(prod_done, 1)

            block_products(0)
            with pe.Fori(1, NB) as b:
                block_products(b)
            mean(NB - 1)

        @block.vector
        def _(dve):
            dve.wait_ge(gain_loaded, 16)

            def split_a(b):
                for g in range(KH):
                    pair = slice(2 * g, 2 * g + 2)
                    dve.wait_ge(a_hi_done, b * KH + (g + 1))
                    dve.tensor_tensor(a_lo[:, pair, :], a_raw[:, pair, :], a_hi[:, pair, :].bitcast(F32),
                                      ALU.subtract).then_inc(a_lo_done, 1)

            def norm(b):
                dve.wait_ge(squares_done, b + 1)
                dve.tensor_reduce(ssum[:, :], sq[:, :, :].rearrange("p k t -> p t k"), AX_X, ALU.add).then_inc(sums_done, 1)
                dve.wait_ge(roots_done, b + 1)
                dve.reciprocal(rstd[:, :], ssum[:, :]).then_inc(recips_done, 1)
                dve.wait_ge(recips_done, b + 1)
                for k in range(KD):
                    m = dve.scalar_tensor_tensor(out[:, k, :], out[:, k, :], gain[:, k:k + 1], rstd[:, :],
                                                 ALU.mult, ALU.mult)
                m.then_inc(scaled_done, 1)
                dve.wait_ge(x_loaded, b * 16 + 16)
                dve.wait_ge(scaled_done, b + 1)
                dve.tensor_tensor(x[:, :, :], x[:, :, :], out[:, :, :], ALU.add).then_inc(x2_done, 1)

            split_a(0)
            with dve.Fori(0, NB - 1) as b:
                split_a(b + 1)
                norm(b)
            norm(NB - 1)


def embedding_gate(nc, t):
    with ExitStack() as ctx:
        sbuf, psum, sem = allocators(nc, ctx)
        w_raw = sbuf("pf_w", [P, 2, KD * P], F32)
        wg_hi = sbuf("pf_wghi", [P, KD, KD * P], F32R)
        wg_lo = sbuf("pf_wglo", [P, KD, KD * P], F32R)
        wp_hi = sbuf("pf_wphi", [P, KD, KP * P], F32R)
        wp_lo = sbuf("pf_wplo", [P, KD, KP * P], F32R)
        x = sbuf("pf_x", [P, 2, KD, TB], F32)
        x_hi = sbuf("pf_xhi", [P, KD, TB], F32R)
        x_lo = sbuf("pf_xlo", [P, KD, TB], F32R)
        p_raw = sbuf("pf_p", [P, KP, TB], F32)
        p_hi = sbuf("pf_phi", [P, KP, TB], F32R)
        p_lo = sbuf("pf_plo", [P, KP, TB], F32R)
        gated = sbuf("pf_gated", [P, 2, KD, TB], F32)
        sq = sbuf("pf_sq", [P, KD, TB], F32)
        ssum = sbuf("pf_ssum", [P, TB], F32)
        rstd = sbuf("pf_rstd", [P, TB], F32)
        gain = sbuf("pf_gain", [P, KD], F32)
        eps = sbuf("pf_eps", [P, 1], F32)
        ones_mean = sbuf("pf_ones", [P, P], F32)
        proj_ps = psum("pf_proj", [P, 4, 512], F32)
        gate_ps = psum("pf_gate", [P, 2, 512], F32)
        mean_ps = psum("pf_mean", [P, 512], F32)
        gain_loaded = sem("pf_gain_loaded")
        consts_set = sem("pf_consts_set")
        w_loaded = (sem("pf_w_loaded0"), sem("pf_w_loaded1"))
        w_hi_done = sem("pf_w_hi_done")
        w_lo_done = sem("pf_w_lo_done")
        x_loaded = (sem("pf_x_loaded0"), sem("pf_x_loaded1"))
        x_hi_done = sem("pf_x_hi_done")
        x_lo_done = sem("pf_x_lo_done")
        x_read = sem("pf_x_read")
        p_loaded = sem("pf_p_loaded")
        p_hi_done = sem("pf_p_hi_done")
        p_lo_done = sem("pf_p_lo_done")
        proj_done = sem("pf_proj_done")
        gate_done = sem("pf_gate_done")
        sigmoids_done = sem("pf_sigmoids_done")
        gated_done = sem("pf_gated_done")
        squares_done = sem("pf_squares_done")
        sums_done = sem("pf_sums_done")
        means_done = sem("pf_means_done")
        roots_done = sem("pf_roots_done")
        recips_done = sem("pf_recips_done")
        scaled_done = sem("pf_scaled_done")
        y_done = sem("pf_y_done")
        stored = (sem("pf_stored0"), sem("pf_stored1"))
        block = ctx.enter_context(nc.Block())
        WIDTHS = (KP * P, KD * P)

        @block.sync
        def _(sp):
            sp.dma_start(gain[:, :], t["g_ple"]).then_inc(gain_loaded, 16)

            def load_w(j, kind):
                wait_at_least(sp, w_lo_done, 2 * j + (kind - 1))
                src = t["w_ple_gate" if kind else "w_ple_proj"]
                sp.dma_start(w_raw[:, kind, 0:WIDTHS[kind]], src[j]).then_inc(w_loaded[kind], 16)

            def load_p(b):
                wait_at_least(sp, p_lo_done, b)
                sp.dma_start(p_raw[:, :, :], t["pT"][b]).then_inc(p_loaded, 16)

            def load_x(b, par):
                sp.dma_start(x[:, par], t["x2"][b]).then_inc(x_loaded[par], 16)

            load_p(0)
            load_x(0, 0)
            load_w(0, 0)
            load_w(0, 1)
            with sp.Fori(1, KD) as j:
                load_w(j, 0)
                load_w(j, 1)
            load_p(1)
            load_x(1, 1)
            for b in range(NB):
                par = b % 2
                if b < NB - 2:
                    load_p(b + 2)
                sp.wait_ge(y_done, b + 1)
                sp.dma_start(t["y"][b], x[:, par]).then_inc(stored[par], 16)
                if b < NB - 2:
                    sp.wait_ge(stored[par], landed(b, par))
                    load_x(b + 2, par)
            for par in range(2):
                sp.wait_ge(stored[par], 16 * ((NB + 1 - par) // 2))

        @block.gpsimd
        def _(pool):
            pool.memset(ones_mean[:, :], 1.0 / D).then_inc(consts_set, 1)
            pool.memset(eps[:, :], EPS).then_inc(consts_set, 1)

            def split_block(b, par, first):
                pool.wait_ge(p_hi_done, b + 1)
                pool.tensor_tensor(p_lo[:, :, :], p_raw[:, :, :], p_hi[:, :, :].bitcast(F32), ALU.subtract).then_inc(p_lo_done, 1)
                for k in range(KD):
                    pool.wait_ge(x_hi_done, b * KD + (k + 1))
                    pool.tensor_tensor(x_lo[:, k, :], x[:, par, k, :], x_hi[:, k, :].bitcast(F32),
                                       ALU.subtract).then_inc(x_lo_done, 1)

            split_block(0, 0, True)
            with pool.Fori(0, KD) as j:
                for kind, (hi, lo) in enumerate(((wp_hi, wp_lo), (wg_hi, wg_lo))):
                    pool.wait_ge(w_hi_done, 2 * j + (kind + 1))
                    pool.tensor_tensor(lo[:, bass.ds(j, 1), :], w_raw[:, kind:kind + 1, 0:WIDTHS[kind]],
                                       hi[:, bass.ds(j, 1), :].bitcast(F32), ALU.subtract).then_inc(w_lo_done, 1)
            with pool.Fori(1, (NB + 1) // 2) as j:
                split_block(2 * j - 1, 1, False)
                split_block(2 * j, 0, False)

        @block.scalar
        def _(act):
            act.wait_ge(consts_set, 2)

            def split_block(b, par):
                act.wait_ge(p_loaded, b * 16 + 16)
                wait_at_least(act, proj_done, b * KD)
                act.activation(p_hi[:, :, :], p_raw[:, :, :], ACT.Copy).then_inc(p_hi_done, 1)
                act.wait_ge(x_loaded[par], landed(b, par))
                for k in range(KD):
                    if k < KD - 1:
                        wait_at_least(act, x_read, b * (KD - 1) + (k + 2 - KD))
                    else:
                        wait_at_least(act, gate_done, b * KD)
                    act.activation(x_hi[:, k, :], x[:, par, k, :], ACT.Copy).then_inc(x_hi_done, 1)

            def block_work(b, par, more):
                if not isinstance(b, int) or b >= 2:
                    act.wait_ge(y_done, b - 1)
                for j in range(KD):
                    if j == KD - 1 and more:
                        split_block(b + 1, 1 - par)
                    act.wait_ge(gate_done, b * KD + (j + 1))
                    act.activation(gated[:, par, j, :], gate_ps[:, j % 2, 0:TB], ACT.Sigmoid).then_inc(sigmoids_done, 1)
                act.wait_ge(gated_done, b * KD + KD)
                act.activation(sq[:, :, :], gated[:, par], ACT.Square).then_inc(squares_done, 1)
                act.wait_ge(means_done, b + 1)
                act.activation(ssum[:, :], mean_ps[:, 0:TB], ACT.Sqrt, bias=eps[:, 0:1]).then_inc(roots_done, 1)

            split_block(0, 0)
            with act.Fori(0, KD) as j:
                for kind, hi in enumerate((wp_hi, wg_hi)):
                    act.wait_ge(w_loaded[kind], j * 16 + 16)
                    act.activation(hi[:, bass.ds(j, 1), :], w_raw[:, kind:kind + 1, 0:WIDTHS[kind]], ACT.Copy).then_inc(w_hi_done, 1)
            block_work(0, 0, True)
            with act.Fori(1, NB // 2) as j:
                block_work(2 * j - 1, 1, True)
                block_work(2 * j, 0, True)
            block_work(NB - 2, 1, True)
            block_work(NB - 1, 0, False)

        @block.tensor
        def _(pe):
            pe.wait_ge(consts_set, 2)
            LEAD = 2

            def mean(b):
                pe.wait_ge(sums_done, b + 1)
                pe.matmul(mean_ps[:, 0:TB], ones_mean[:, :], ssum[:, :], start=True, stop=True).then_inc(means_done, 1)

            def project(b, j, first):
                if first:
                    pe.wait_ge(w_lo_done, 2 * j + 1)
                wait_at_least(pe, gated_done, b * KD + (j - 3))
                for k in range(KP):
                    w = slice(k * P, (k + 1) * P)
                    mm = hi_lo_products(pe, proj_ps[:, j % 4, 0:TB], wp_hi[:, j, w], wp_lo[:, j, w],
                                        p_hi[:, k, :], p_lo[:, k, :], k == 0, k == KP - 1)
                mm.then_inc(proj_done, 1)

            def block_products(b, par, first):
                pe.wait_ge(p_lo_done, b + 1)
                for j in range(LEAD):
                    project(b, j, first)
                for j in range(KD):
                    if j == 2 and not first:
                        mean(b - 1)
                    if j + LEAD < KD:
                        project(b, j + LEAD, first)
                    if first:
                        pe.wait_ge(w_lo_done, 2 * j + 2)
                    wait_at_least(pe, sigmoids_done, b * KD + (j - 1))
                    for k in range(KD):
                        if j == 0:
                            pe.wait_ge(x_lo_done, b * KD + (k + 1))
                        w = slice(k * P, (k + 1) * P)
                        mm = hi_lo_products(pe, gate_ps[:, j % 2, 0:TB], wg_hi[:, j, w], wg_lo[:, j, w],
                                            x_hi[:, k, :], x_lo[:, k, :], k == 0, k == KD - 1)
                        if j == KD - 1 and k < KD - 1:
                            mm.then_inc(x_read, 1)
                    mm.then_inc(gate_done, 1)

            blocks(pe, block_products)
            mean(NB - 1)

        @block.vector
        def _(dve):
            dve.wait_ge(gain_loaded, 16)

            def block_work(b, par, first):
                for j in range(KD):
                    dve.wait_ge(proj_done, b * KD + (j + 1))
                    dve.wait_ge(sigmoids_done, b * KD + (j + 1))
                    dve.tensor_tensor(gated[:, par, j, :], proj_ps[:, j % 4, 0:TB], gated[:, par, j, :],
                                      ALU.mult).then_inc(gated_done, 1)
                dve.wait_ge(squares_done, b + 1)
                dve.tensor_reduce(ssum[:, :], sq[:, :, :].rearrange("p k t -> p t k"), AX_X, ALU.add).then_inc(sums_done, 1)
                dve.wait_ge(roots_done, b + 1)
                dve.reciprocal(rstd[:, :], ssum[:, :]).then_inc(recips_done, 1)
                dve.wait_ge(recips_done, b + 1)
                for k in range(KD):
                    m = dve.scalar_tensor_tensor(gated[:, par, k, :], gated[:, par, k, :], gain[:, k:k + 1],
                                                 rstd[:, :], ALU.mult, ALU.mult)
                m.then_inc(scaled_done, 1)
                dve.wait_ge(scaled_done, b + 1)
                dve.wait_ge(x_lo_done, b * KD + KD)
                dve.tensor_tensor(x[:, par], x[:, par], gated[:, par], ALU.add).then_inc(y_done, 1)

            blocks(dve, block_work)


def shift_caches(nc, t, shifted):
    with nc.Block() as block:

        @block.scalar
        def _(act):
            for b in range(NSAMP):
                for new, old in (("new_cache_k", "cache_k"), ("new_cache_v", "cache_v")):
                    act.dma_start(t[new][b, 0:PAST - 1], t[old][b, 1:PAST]).then_inc(shifted, 16)


def wait_for_caches(nc, shifted):
    with nc.Block() as block:

        @block.sync
        def _(sp):
            sp.wait_ge(shifted, 16 * 2 * NSAMP)


SCRATCH = {"dn": (12, P, S), "dn_samp": (12, P, NSAMP), "z": (4, P, TOK), "at4": (12, P, S), "at16": (12, P, S),
           "ba": (36, TOK), "bias_flat": (len(DILS), AH, FLAT), "U": (len(DILS), S, UROW), "mix": (KD, P, TOK),
           "x1": (NB, P, KD, TB), "h2": (NB, P, KD, TB), "a": (KF, P, TOK), "x2": (NB, P, KD, TB)}

RESULTS = {"y": (NB, P, KD, TB), "at": (12, P, TOK), "conv_tail": (12, P, 3), "conv_samp": (12, P, NSAMP, 3),
           "delta": (HEADS, P, P), "new_state": (NSAMP, HEADS, P, P),
           "new_cache_k": (NSAMP, PAST, AH * HD), "new_cache_v": (NSAMP, PAST, AH * HD)}


def build(nc, t):
    for name, shape in SCRATCH.items():
        t[name] = nc.dram_tensor("scratch_" + name, list(shape), F32, kind="Internal").ap()
    with nc.semaphore("caches_shifted") as shifted:
        bias_rows(nc, t)
        norm_and_input_projection(nc, t)
        delta_prompt(nc, t)
        delta_samples(nc, t)
        attention_prompt(nc, t)
        merge_dilations(nc, t)
        attention_samples(nc, t)
        output_projection(nc, t)
        shift_caches(nc, t, shifted)
        gate_and_up(nc, t)
        down_projection(nc, t)
        embedding_gate(nc, t)
        wait_for_caches(nc, shifted)


def tiles_of(w, k, n):
    return np.ascontiguousarray(w.reshape(k, P, n, P).transpose(2, 1, 0, 3)).reshape(n, P, k * P)


def columns_of(g, k):
    return np.ascontiguousarray(g.reshape(k, P).T)


def blocks_of(prompt, sample, k):
    x = np.zeros((TOK, k * P), np.float32)
    x[:S] = prompt
    x[S:S + NSAMP] = sample
    return np.ascontiguousarray(x.reshape(NB, TB, k, P).transpose(0, 3, 2, 1)).reshape(NB, P, k, TB)


def layouts(i):
    dn_cols = (N_DN + N_Z) * P
    w_in = np.zeros((D, (NT + 1) * P), np.float32)
    w_in[:, :dn_cols] = i["w_in"][0][:, :dn_cols]
    w_in[:, dn_cols:NT * P] = i["w_in"][0][:, dn_cols + 2 * HEADS:]
    w_in[:, NT * P:NT * P + HEADS] = i["w_in"][0][:, dn_cols:dn_cols + HEADS]
    w_in[:, NT * P + 32:NT * P + 32 + HEADS] = i["w_in"][0][:, dn_cols + HEADS:dn_cols + 2 * HEADS]
    gate_up = i["w_gate_up"][0].reshape(D, 2, KF, P).transpose(0, 2, 1, 3).reshape(D, 2 * FF)
    return {
        "xT": blocks_of(i["x_prompt"][0], i["x_sample"][:, 0], KD),
        "pT": blocks_of(i["p_prompt"][0, 0], i["p_sample"][0, :, 0], KP),
        "w_in": tiles_of(w_in, KD, NT + 1),
        "conv_w": np.ascontiguousarray(i["conv_w"][0].reshape(4, N_DN, P).transpose(2, 1, 0)).reshape(P, 4 * N_DN),
        "cache_conv": np.ascontiguousarray(i["cache_conv"][0].reshape(NSAMP, 3, N_DN, P).transpose(2, 3, 0, 1)),
        "w_out": tiles_of(i["w_out"][0], KD, KD),
        "w_gate_up": tiles_of(gate_up, KD, 2 * KF),
        "w_down": tiles_of(i["w_down"][0], KF, KD),
        "w_ple_gate": tiles_of(i["w_ple_gate"][0], KD, KD),
        "w_ple_proj": tiles_of(i["w_ple_proj"][0], KP, KD),
        "g_pre_mix": columns_of(i["g_pre_mix"][0], KD),
        "g_post_mix": columns_of(i["g_post_mix"][0], KD),
        "g_pre_ffn": columns_of(i["g_pre_ffn"][0], KD),
        "g_post_ffn": columns_of(i["g_post_ffn"][0], KD),
        "g_ple": columns_of(i["g_ple"][0], KD),
        "g_dn_out": i["g_dn_out"][0].reshape(P, 1),
        "a_log": i["a_log"][0],
        "dt_bias": i["dt_bias"][0],
        "rel_bias": i["rel_bias"],
        "state": i["state_delta"][0],
        "cache_k": i["cache_win_k"][0].reshape(NSAMP, PAST, AH * HD),
        "cache_v": i["cache_win_v"][0].reshape(NSAMP, PAST, AH * HD),
        "consts": constant_tiles(),
        "buckets": bucket_tiles(),
        "head_mask": head_mask(),
    }


def kernel(**inputs):
    import concourse.bacc as bacc
    from concourse.bass_utils import run_bass_kernel_spmd

    nc = bacc.Bacc("TRN2", target_bir_lowering=False, num_devices=1)
    arrays, t = {}, {}
    for name, a in layouts({n: np.asarray(a) for n, a in inputs.items()}).items():
        arrays["in_" + name] = np.ascontiguousarray(a)
        t[name] = nc.dram_tensor("in_" + name, list(a.shape), F32, kind="ExternalInput").ap()
    for name, shape in RESULTS.items():
        t[name] = nc.dram_tensor("out_" + name, list(shape), F32, kind="ExternalOutput").ap()
    build(nc, t)
    result = run_bass_kernel_spmd(nc, [arrays], core_ids=[0]).results[0]
    r = {name: np.asarray(result["out_" + name]).reshape(shape) for name, shape in RESULTS.items()}

    y = r["y"].transpose(0, 3, 2, 1).reshape(TOK, D)
    k_prompt, v_prompt = (r["at"][4 * n:4 * n + 4, :, 0:S].reshape(AH * HD, S).T.reshape(1, 1, S, AH, HD) for n in (1, 2))
    channels = N_DN * P
    return (y[:S].reshape(1, S, D), y[S:S + NSAMP].reshape(NSAMP, 1, D),
            r["conv_tail"].reshape(channels, 3).T.reshape(1, 1, 3, channels),
            r["delta"].reshape(1, 1, HEADS, DK, DK), k_prompt, v_prompt,
            r["conv_samp"].transpose(2, 3, 0, 1).reshape(1, NSAMP, 3, channels),
            r["new_state"].reshape(1, NSAMP, HEADS, DK, DK),
            r["new_cache_k"].reshape(1, NSAMP, PAST, AH, HD), r["new_cache_v"].reshape(1, NSAMP, PAST, AH, HD))
```

```python
from contextlib import ExitStack

import numpy as np

import concourse.bass as bass
from concourse import mybir

F32 = mybir.dt.float32
F32R = mybir.dt.float32r
ALU = mybir.AluOpType
ACT = mybir.ActivationFunctionType
AX_X = mybir.AxisListType.X

P = 128
D = 1024
S = 2048
NSAMP = 8
TB = 412
NB = 5
TOK = NB * TB
KD = D // P
HEADS, DK = 4, 128
AH, HD = 8, 64
FF = 2816
KF = FF // P
PLE = 256
KP = PLE // P
EPS = 1e-6
BIG = 1e30
DILS = (1, 4, 16)
NBIAS = 383
UROW = AH * HD + 2 * AH
PAST = 1024


def allocators(nc, ctx):
    semaphores = []

    def sbuf(name, shape, dtype):
        return ctx.enter_context(nc.sbuf_tensor(name, shape, dtype))

    def psum(name, shape, dtype):
        return ctx.enter_context(nc.psum_tensor(name, shape, dtype))

    def sem(name):
        semaphores.append(nc.alloc_semaphore(name))
        return semaphores[-1]

    def clear():
        nc.clear_and_free_semaphores(semaphores)
        nc.all_engine_barrier()

    ctx.callback(clear)
    return sbuf, psum, sem


def landed(tile, par, per_tile=1):
    return (tile - par) * (8 * per_tile) + 16 * per_tile


def hi_lo_products(pe, out, w_hi, w_lo, a_hi, a_lo, first, last):
    pe.matmul(out, w_hi, a_hi, start=first, stop=False)
    pe.matmul(out, w_lo, a_hi, start=False, stop=False)
    return pe.matmul(out, w_hi, a_lo, start=False, stop=last)


N_DN, N_Z, N_AT = 12, 4, 12
NT = N_DN + N_Z + N_AT
ROW = 2088
SAMP0 = 3 + S


def norm_and_input_projection(nc, t):
    with ExitStack() as ctx:
        sbuf, psum, sem = allocators(nc, ctx)
        h_hi = sbuf("pa_h_hi", [P, KD, TOK], F32R)
        h_lo = sbuf("pa_h_lo", [P, KD, TOK], F32R)
        work = sbuf("pa_work", [P, 6 * ROW], F32)
        w_raw = sbuf("pa_w", [P, 2, KD * P], F32)
        w_hi = sbuf("pa_whi", [P, 2, KD * P], F32R)
        w_lo = sbuf("pa_wlo", [P, 2, KD * P], F32R)
        gain = sbuf("pa_gain", [P, KD], F32)
        eps = sbuf("pa_eps", [P, 1], F32)
        ones_mean = sbuf("pa_ones", [P, P], F32)
        conv_w = sbuf("pa_convw", [P, N_DN * 4], F32)
        mean_ps = psum("pa_mean", [P, 512], F32)
        proj_ps = psum("pa_proj", [P, NB, 512], F32)
        const_loaded = sem("pa_const_loaded")
        consts_set = sem("pa_consts_set")
        x_loaded0 = sem("pa_x_loaded0")
        x_loaded1 = sem("pa_x_loaded1")
        squares_done = sem("pa_squares_done")
        sums_done = sem("pa_sums_done")
        means_done = sem("pa_means_done")
        roots_done = sem("pa_roots_done")
        recips_done = sem("pa_recips_done")
        h_done = sem("pa_h_done")
        h_hi_done = sem("pa_h_hi_done")
        h_lo_done = sem("pa_h_lo_done")
        zeros_set = sem("pa_zeros_set")
        w_loaded0 = sem("pa_w_loaded0")
        w_loaded1 = sem("pa_w_loaded1")
        w_hi_done = sem("pa_w_hi_done")
        w_lo_done = sem("pa_w_lo_done")
        proj_done = sem("pa_proj_done")
        evacuated = sem("pa_evacuated")
        gates_done = sem("pa_gates_done")
        taps_done = sem("pa_taps_done")
        conv_done = sem("pa_conv_done")
        silu_done = sem("pa_silu_done")
        perm4_done = sem("pa_perm4_done")
        perm16_done = sem("pa_perm16_done")
        ctx_loaded0 = sem("pa_ctx_loaded0")
        ctx_loaded1 = sem("pa_ctx_loaded1")
        dn_stored0 = sem("pa_dn_stored0")
        dn_stored1 = sem("pa_dn_stored1")
        z_stored0 = sem("pa_z_stored0")
        z_stored1 = sem("pa_z_stored1")
        at_stored0 = sem("pa_at_stored0")
        at_stored1 = sem("pa_at_stored1")
        block = ctx.enter_context(nc.Block())
        x_loaded = (x_loaded0, x_loaded1)
        w_loaded = (w_loaded0, w_loaded1)
        ctx_loaded = (ctx_loaded0, ctx_loaded1)
        dn_stored = (dn_stored0, dn_stored1)
        z_stored = (z_stored0, z_stored1)
        at_stored = (at_stored0, at_stored1)
        BLK = KD * TB
        xb = [work[:, i * BLK:(i + 1) * BLK].rearrange("p (k t) -> p k t", k=KD) for i in range(2)]
        sq = work[:, 2 * BLK:3 * BLK]
        ssum, std, rstd = (work[:, 3 * BLK + i * TB:3 * BLK + (i + 1) * TB] for i in range(3))
        raw = [work[:, i * ROW:(i + 1) * ROW] for i in range(2)]
        res = [work[:, (2 + i) * ROW:(3 + i) * ROW] for i in range(2)]
        r16 = [work[:, (4 + i) * ROW:(5 + i) * ROW] for i in range(2)]
        A0 = N_DN + N_Z
        CONV_COLS = SAMP0 + 4 * NSAMP - 3

        def samples(row, first, n):
            return row[:, SAMP0:SAMP0 + 4 * NSAMP].rearrange("p (b j) -> p b j", j=4)[:, :, first:first + n]

        @block.sync
        def _(sp):
            sp.dma_start(gain[:, :], t["g_pre_mix"]).then_inc(const_loaded, 16)
            sp.dma_start(conv_w[:, :], t["conv_w"]).then_inc(const_loaded, 16)
            for b in range(NB):
                if b >= 2:
                    sp.wait_ge(h_lo_done, b - 1)
                sp.dma_start(xb[b % 2], t["xT"][b]).then_inc(x_loaded[b % 2], 16)

            def load_w(c, par):
                sp.dma_start(w_raw[:, par, :], t["w_in"][c]).then_inc(w_loaded[par], 16)

            def load_ctx(c, par):
                sp.dma_start(samples(raw[par], 0, 3), t["cache_conv"][c]).then_inc(ctx_loaded[par], 16)

            load_w(0, 0)
            load_w(1, 1)
            sp.wait_ge(h_lo_done, NB)
            load_ctx(0, 0)
            load_ctx(1, 1)

            def conv_tile(c, par, last):
                sp.wait_ge(w_lo_done, c + 1)
                load_w(c + 2, par)
                sp.wait_ge(silu_done, c + 1)
                sp.dma_start(t["dn"][c], res[par][:, 0:S]).then_inc(dn_stored[par], 16)
                sp.dma_start(t["dn_samp"][c], samples(res[par], 0, 1), allow_slow_non_contiguous=True).then_inc(dn_stored[par], 16)
                sp.dma_start(t["conv_tail"][c], raw[par][:, S:S + 3]).then_inc(dn_stored[par], 16)
                sp.dma_start(t["conv_samp"][c], samples(raw[par], 1, 3)).then_inc(dn_stored[par], 16)
                if not last:
                    sp.wait_ge(dn_stored[par], landed(c, par, 4))
                    load_ctx(c + 2, par)

            with sp.Fori(0 // 2, (N_DN - 2) // 2) as j:
                i = 2 * j
                conv_tile(i, 0, False)
                conv_tile(i + 1, 1, False)
            conv_tile(N_DN - 2, 0, True)
            conv_tile(N_DN - 1, 1, True)

            def gate_tile(c, par):
                sp.wait_ge(w_lo_done, c + 1)
                load_w(c + 2, par)
                sp.wait_ge(gates_done, (c - (N_DN - 1)) * NB)
                sp.dma_start(t["z"][c - N_DN], res[par][:, 0:TOK]).then_inc(z_stored[par], 16)

            with sp.Fori(N_DN // 2, A0 // 2) as j:
                i = 2 * j
                gate_tile(i, 0)
                gate_tile(i + 1, 1)

            def attn_tile(c, par, more):
                sp.wait_ge(w_lo_done, c + 1)
                if more:
                    load_w(c + 2, par)
                sp.wait_ge(evacuated, (c - (N_Z - 1)) * NB)
                sp.dma_start(t["at"][c - A0], raw[par][:, 0:TOK]).then_inc(at_stored[par], 16)
                sp.wait_ge(perm4_done, c - (A0 - 1))
                sp.dma_start(t["at4"][c - A0], res[par][:, 0:S]).then_inc(at_stored[par], 16)
                sp.wait_ge(perm16_done, c - (A0 - 1))
                sp.dma_start(t["at16"][c - A0], r16[par][:, 0:S]).then_inc(at_stored[par], 16)

            with sp.Fori(A0 // 2, (NT - 2) // 2) as j:
                i = 2 * j
                attn_tile(i, 0, True)
                attn_tile(i + 1, 1, True)
            attn_tile(NT - 2, 0, True)
            attn_tile(NT - 1, 1, False)
            sp.wait_ge(evacuated, (NT + 1 - N_Z) * NB)
            sp.dma_start(t["ba"], raw[0][0:36, 0:TOK]).then_inc(at_stored[0], 16)
            for par in range(2):
                sp.wait_ge(dn_stored[par], 64 * (N_DN // 2))
                sp.wait_ge(z_stored[par], 16 * (N_Z // 2))
                sp.wait_ge(at_stored[par], 48 * (N_AT // 2) + (0 if par else 16))

        @block.gpsimd
        def _(pool):
            pool.memset(ones_mean[:, :], 1.0 / D).then_inc(consts_set, 1)
            pool.memset(eps[:, :], EPS).then_inc(consts_set, 1)
            for b in range(NB):
                cols = slice(b * TB, (b + 1) * TB)
                pool.wait_ge(h_hi_done, b + 1)
                pool.tensor_tensor(h_lo[:, :, cols], xb[b % 2], h_hi[:, :, cols].bitcast(F32),
                                   ALU.subtract).then_inc(h_lo_done, 1)

            def split_lo(c, par):
                pool.wait_ge(w_hi_done, c + 1)
                pool.tensor_tensor(w_lo[:, par, :], w_raw[:, par, :], w_hi[:, par, :].bitcast(F32),
                                   ALU.subtract).then_inc(w_lo_done, 1)

            with pool.Fori(0, NT // 2) as j:
                i = 2 * j
                split_lo(i, 0)
                split_lo(i + 1, 1)
            split_lo(NT, 0)

        @block.scalar
        def _(act):
            act.wait_ge(consts_set, 2)
            for b in range(NB):
                act.wait_ge(x_loaded[b % 2], 16 * (b // 2 + 1))
                if b:
                    act.wait_ge(sums_done, b)
                act.activation(sq, xb[b % 2].rearrange("p k t -> p (k t)"), ACT.Square).then_inc(squares_done, 1)
                act.wait_ge(means_done, b + 1)
                if b:
                    act.wait_ge(recips_done, b)
                act.activation(std, mean_ps[:, 0:TB], ACT.Sqrt, bias=eps[:, 0:1]).then_inc(roots_done, 1)
                act.wait_ge(h_done, b + 1)
                act.activation(h_hi[:, :, b * TB:(b + 1) * TB], xb[b % 2], ACT.Copy).then_inc(h_hi_done, 1)

            def split_hi(c, par, first):
                act.wait_ge(w_loaded[par], landed(c, par))
                if not first:
                    act.wait_ge(proj_done, (c - 1) * NB)
                act.activation(w_hi[:, par, :], w_raw[:, par, :], ACT.Copy).then_inc(w_hi_done, 1)

            split_hi(0, 0, True)
            split_hi(1, 1, True)

            def conv_tile(c, par):
                split_hi(c + 2, par, False)
                act.wait_ge(conv_done, c + 1)
                act.activation(res[par][:, 0:CONV_COLS], res[par][:, 0:CONV_COLS], ACT.Silu).then_inc(silu_done, 1)

            with act.Fori(0 // 2, N_DN // 2) as j:
                i = 2 * j
                conv_tile(i, 0)
                conv_tile(i + 1, 1)

            def gate_tile(c, par, first):
                if first:
                    act.wait_ge(dn_stored[par], 64 * (N_DN // 2))
                else:
                    act.wait_ge(z_stored[par], landed(c - N_DN - 2, par))
                for b in range(NB):
                    act.wait_ge(proj_done, c * NB + (b + 1))
                    act.activation(res[par][:, b * TB:(b + 1) * TB], proj_ps[:, b, 0:TB],
                                   ACT.Silu).then_inc(gates_done, 1)
                split_hi(c + 2, par, False)

            for c in range(N_DN, A0):
                gate_tile(c, c % 2, c < N_DN + 2)

            def attn_tile(c, par, more, first):
                if more:
                    split_hi(c + 2, par, False)
                act.wait_ge(evacuated, (c - (N_Z - 1)) * NB)
                if not first:
                    act.wait_ge(at_stored[par], landed(c - A0 - 2, par, 3))
                act.activation(r16[par][:, 0:S].rearrange("p (r m) -> p r m", r=16),
                               raw[par][:, 0:S].rearrange("p (m r) -> p r m", r=16),
                               ACT.Copy).then_inc(perm16_done, 1)

            attn_tile(A0, 0, True, True)
            attn_tile(A0 + 1, 1, True, True)
            with act.Fori((A0 + 2) // 2, (NT - 2) // 2) as j:
                i = 2 * j
                attn_tile(i, 0, True, False)
                attn_tile(i + 1, 1, True, False)
            attn_tile(NT - 2, 0, True, False)
            attn_tile(NT - 1, 1, False, False)

        @block.tensor
        def _(pe):
            pe.wait_ge(consts_set, 2)
            for b in range(NB):
                pe.wait_ge(sums_done, b + 1)
                if b:
                    pe.wait_ge(roots_done, b)
                pe.matmul(mean_ps[:, 0:TB], ones_mean[:, :], ssum, start=True, stop=True).then_inc(means_done, 1)
            pe.wait_ge(h_lo_done, NB)

            def project(c, par, read, before):
                pe.wait_ge(w_lo_done, c + 1)
                for b in range(NB):
                    if read is not None:
                        pe.wait_ge(read, (c - (before + 1)) * NB + (b + 1))
                    cols = slice(b * TB, (b + 1) * TB)
                    for k in range(KD):
                        w = slice(k * P, (k + 1) * P)
                        mm = hi_lo_products(pe, proj_ps[:, b, 0:TB], w_hi[:, par, w], w_lo[:, par, w],
                                            h_hi[:, k, cols], h_lo[:, k, cols], k == 0, k == KD - 1)
                    mm.then_inc(proj_done, 1)

            project(0, 0, None, 0)
            project(1, 1, evacuated, 0)
            with pe.Fori(1, N_DN // 2) as j:
                project(2 * j, 0, evacuated, 0)
                project(2 * j + 1, 1, evacuated, 0)
            for c in range(N_DN, A0 + 1):
                if c == N_DN:
                    project(c, c % 2, evacuated, 0)
                else:
                    project(c, c % 2, gates_done, N_DN)
            project(A0 + 1, 1, evacuated, N_Z)
            with pe.Fori((A0 + 2) // 2, NT // 2) as j:
                project(2 * j, 0, evacuated, N_Z)
                project(2 * j + 1, 1, evacuated, N_Z)
            project(NT, 0, evacuated, N_Z)

        @block.vector
        def _(dve):
            dve.wait_ge(const_loaded, 32)
            for b in range(NB):
                dve.wait_ge(squares_done, b + 1)
                if b:
                    dve.wait_ge(means_done, b)
                dve.tensor_reduce(ssum, sq.rearrange("p (k t) -> p t k", k=KD), AX_X, ALU.add).then_inc(sums_done, 1)
                dve.wait_ge(roots_done, b + 1)
                dve.reciprocal(rstd, std).then_inc(recips_done, 1)
                dve.wait_ge(recips_done, b + 1)
                for k in range(KD):
                    m = dve.scalar_tensor_tensor(xb[b % 2][:, k, :], xb[b % 2][:, k, :], gain[:, k:k + 1], rstd,
                                                 ALU.mult, ALU.mult)
                m.then_inc(h_done, 1)
            dve.wait_ge(h_lo_done, NB)
            dve.memset(raw[0][:, 0:3], 0.0).then_inc(zeros_set, 1)
            dve.memset(raw[1][:, 0:3], 0.0).then_inc(zeros_set, 1)
            dve.wait_ge(zeros_set, 2)

            def conv_tile(c, par, first):
                if not first:
                    dve.wait_ge(dn_stored[par], landed(c - 2, par, 4))
                u, out = raw[par], res[par]
                for b in range(NB):
                    dve.wait_ge(proj_done, c * NB + (b + 1))
                    n = min(TB, S - b * TB)
                    m = dve.tensor_copy(u[:, 3 + b * TB:3 + b * TB + n], proj_ps[:, b, 0:n])
                    if n < TB:
                        m = dve.tensor_copy(samples(u, 3, 1), proj_ps[:, b, n:n + NSAMP].rearrange("p (b o) -> p b o", o=1))
                    m.then_inc(evacuated, 1)
                dve.wait_ge(evacuated, (c + 1) * NB)
                dve.wait_ge(ctx_loaded[par], landed(c, par))
                for j in range(4):
                    w = conv_w[:, bass.ds(c * 4 + j, 1)]
                    if j == 0:
                        m = dve.tensor_scalar(out[:, 0:CONV_COLS], u[:, 0:CONV_COLS], w, None, ALU.mult)
                    else:
                        dve.wait_ge(taps_done, c * 3 + j)
                        m = dve.scalar_tensor_tensor(out[:, 0:CONV_COLS], u[:, j:j + CONV_COLS], w,
                                                     out[:, 0:CONV_COLS], ALU.mult, ALU.add)
                    m.then_inc(conv_done if j == 3 else taps_done, 1)

            conv_tile(0, 0, True)
            conv_tile(1, 1, True)
            with dve.Fori(2 // 2, N_DN // 2) as j:
                i = 2 * j
                conv_tile(i, 0, False)
                conv_tile(i + 1, 1, False)

            for par in range(2):
                dve.wait_ge(dn_stored[par], 64 * (N_DN // 2))

            def attn_tile(c, par, first, parts):
                if first:
                    dve.wait_ge(z_stored[par], 16 * (N_Z // 2))
                else:
                    dve.wait_ge(at_stored[par], landed(c - A0 - 2, par, 3))
                for b in range(NB):
                    dve.wait_ge(proj_done, c * NB + (b + 1))
                    dve.tensor_copy(raw[par][0:parts, b * TB:(b + 1) * TB],
                                    proj_ps[0:parts, b, 0:TB]).then_inc(evacuated, 1)
                if parts == P:
                    dve.wait_ge(evacuated, (c - (N_Z - 1)) * NB)
                    dve.tensor_copy(res[par][:, 0:S].rearrange("p (r m) -> p r m", r=4),
                                    raw[par][:, 0:S].rearrange("p (m r) -> p r m", r=4)).then_inc(perm4_done, 1)

            attn_tile(A0, 0, True, P)
            attn_tile(A0 + 1, 1, True, P)
            with dve.Fori((A0 + 2) // 2, NT // 2) as j:
                i = 2 * j
                attn_tile(i, 0, False, P)
                attn_tile(i + 1, 1, False, P)
            attn_tile(NT, 0, False, 36)


CH = P
NC = S // CH
LEVELS = 7
C_IDENT, C_TRIU, C_TRIL, C_LEVEL = 0, 1, 2, 3


def for_pairs(engine, n, step):
    with engine.Fori(0, n // 2) as j:
        step(2 * j, 0)
        step(2 * j + 1, 1)
    if n % 2:
        step(n - 1, 0)


def named(sem, prefix, names):
    return [sem(prefix + n) for n in names.split()]


def constant_tiles():
    i, j = np.arange(P)[:, None], np.arange(P)[None, :]
    tiles = [i == j, i <= j, i > j]
    for level in range(LEVELS):
        tiles.append((i >> level + 1 == j >> level + 1) & ((i >> level) % 2 == 1) & ((j >> level) % 2 == 0))
    return np.ascontiguousarray(np.stack(tiles, 1).astype(np.float32)).reshape(P, -1)


def heads(tile):
    return tile.rearrange("p (h j) -> p h j", h=HEADS)


def per_head(col):
    return col.rearrange("p (h o) -> p h o", o=1).broadcast_to([P, HEADS, P])


def all_heads(tile):
    return tile.rearrange("p (o j) -> p o j", o=1).broadcast_to([P, HEADS, P])


def delta_and_attention(nc, t):
    with ExitStack() as ctx:
        sbuf, psum, sem = allocators(nc, ctx)
        C4 = HEADS * P
        const = sbuf("pb_const", [P, (C_LEVEL + LEVELS) * P], F32)
        logits = sbuf("pb_logits", [36, S], F32)
        lt = sbuf("pb_lt", [P, NC, 36], F32)
        alog = sbuf("pb_alog", [P, HEADS], F32)
        dtb = sbuf("pb_dtb", [P, HEADS], F32)
        beta = sbuf("pb_beta", [P, NC, HEADS], F32)
        g = sbuf("pb_g", [P, NC, HEADS], F32)
        gtmp = sbuf("pb_gtmp", [P, NC, HEADS], F32)
        gc = sbuf("pb_gc", [P, NC, HEADS], F32)
        egc = sbuf("pb_egc", [P, NC, HEADS], F32)
        ekd = sbuf("pb_ekd", [P, NC, HEADS], F32)
        raw = sbuf("pb_raw", [P, 12, P], F32)
        zg = sbuf("pb_z", [P, C4], F32)
        junk = sbuf("pb_junk", [P, 8, P], F32)
        ones = sbuf("pb_one", [P, P], F32)
        ss = sbuf("pb_ss", [P, 8], F32)
        rr = sbuf("pb_rr", [P, 8], F32)
        coef = sbuf("pb_coef", [P, 4, HEADS], F32)
        kn, kbg, kdec, qn, vb, knT, qnT, gbc, gd, E, egr, M, L, X, XT, Z, U, WT, vnew, S_, intra, qdec, osq, orr, o = (
            sbuf("pb_" + n, [P, C4], F32) for n in
            "kn kbg kdec qn vb knT qnT gbc gd E egr M L X XT Z U WT vnew S intra qdec osq orr o".split())
        B = sbuf("pb_B", [P, LEVELS, C4], F32)
        gain = sbuf("pb_gain", [P, 1], F32)
        eps = sbuf("pb_eps", [P, 1], F32)
        ones_mean = sbuf("pb_ones", [P, P], F32)
        qkv = [sbuf(f"pb_qkv{v}", [P, 2, 12 * P], F32) for v in range(len(DILS))]
        vtok = [sbuf(f"pb_vtok{v}", [P, 2, AH * HD], F32) for v in range(len(DILS))]
        bias = [sbuf(f"pb_bias{v}", [P, 2, AH * 2 * P], F32) for v in range(2)]
        bias_own = sbuf("pb_bias_own", [P, AH * P], F32)
        s = sbuf("pb_s", [P, 2, 4 * P], F32)
        e = sbuf("pb_e", [P, 2, 4 * P], F32)
        eT = sbuf("pb_eT", [P, 2, 4 * P], F32)
        uo = [sbuf(f"pb_uo{v}", [P, UROW], F32) for v in range(len(DILS))]
        ps = psum("pb_ps", [P, 8, C4], F32)
        qkv_loaded = [[sem(f"pb_qkv_loaded{v}{par}") for par in range(2)] for v in range(len(DILS))]
        uo_stored = [sem(f"pb_uo_stored{v}") for v in range(len(DILS))]
        (bias_loaded, v_turned, v_copied, step_scored, biased, max_done, exp_done, turned, eT_copied, pv_done,
         o_copied, uo_free, o_free, chunk_ended) = named(sem, "pb_", """bias_loaded v_turned v_copied step_scored biased max_done
            exp_done turned eT_copied pv_done o_copied uo_free o_free chunk_ended""")
        (const_loaded, consts_set, logits_turned, logits_copied, beta_done, g_steps, gsum_done, gcol_done,
         raw_loaded, z_loaded, stored, raw_turned, gbc_done, rows_done, kq_turned, grams_done, scores_done,
         b0_turned, z_done, xt_done, x_done, u_done, w_done, p1_done, o_done, s_done, msq_done,
         ss_done, roots_done, knT_copied, qnT_copied, abs_done, e_done, egr_done, z_copied, u_copied, w_copied,
         osq_done, oroot_done, coef_steps, k_scaled, q_scaled, v_scaled, g_diff_done, m_done, l_done, mask_done,
         xt_sub, x_sub, i1_done, intra_done, qdec_done, vnew_done, s1_done, s_upd, orr_done, o1_done, out_done) = (
            sem("pb_" + n) for n in
            """const_loaded consts_set logits_turned logits_copied beta_done g_steps gsum_done gcol_done
            raw_loaded z_loaded stored raw_turned gbc_done rows_done kq_turned grams_done scores_done
            b0_turned z_done xt_done x_done u_done w_done p1_done o_done s_done msq_done
            ss_done roots_done knT_copied qnT_copied abs_done e_done egr_done z_copied u_copied w_copied
            osq_done oroot_done coef_steps k_scaled q_scaled v_scaled g_diff_done m_done l_done mask_done
            xt_sub x_sub i1_done intra_done qdec_done vnew_done s1_done s_upd orr_done o1_done out_done""".split())
        block = ctx.enter_context(nc.Block())

        def const_tile(n):
            return const[:, n * P:(n + 1) * P]

        def bank(n):
            return ps[:, n, :]

        SCORES, TURNS, OUTPUT = 4, 6, 7
        UNITS = len(DILS)
        STEPS = 4 * UNITS
        SLOTS = STEPS + 2

        def step_heads(j):
            first = j % 4 // 2 * 4 + j % 2
            return j // 4, (first, first + 2)

        def keys_seen(tile, j):
            view = tile.rearrange("p (h k) -> p h k", h=2)
            return view[:, :, P:2 * P] if j // 4 == 2 else view

        def col(tile, h):
            return tile[:, h * P:(h + 1) * P]

        @block.sync
        def _(sp):
            sp.dma_start(const[:, :], t["consts"]).then_inc(const_loaded, 16)
            sp.dma_start(logits[:, :], t["ba"][:, 0:S]).then_inc(const_loaded, 16)
            sp.dma_start(alog[:, :], t["a_log"].partition_broadcast(P)).then_inc(const_loaded, 16)
            sp.dma_start(dtb[:, :], t["dt_bias"].partition_broadcast(P)).then_inc(const_loaded, 16)
            sp.dma_start(gain[:, :], t["g_dn_out"]).then_inc(const_loaded, 16)

            def load_raw(c):
                sp.dma_start(raw[:, :, :], t["dn"].rearrange("n p s -> p n s")[:, :, bass.ds(c * CH, CH)]).then_inc(raw_loaded, 16)

            def load_z(c):
                sp.dma_start(heads(zg[:, :]), t["z"].rearrange("n p s -> p n s")[:, :, bass.ds(c * CH, CH)]).then_inc(z_loaded, 16)

            def load_unit(v, c, par):
                src = t[("at", "at4", "at16")[v]].rearrange("n p s -> p n s")[:, :, bass.ds(c * P, P)]
                sp.dma_start(qkv[v][:, par, :].rearrange("p (n s) -> p n s", n=12), src).then_inc(qkv_loaded[v][par], 16)

            load_raw(0)
            for v in range(UNITS):
                load_unit(v, 0, 0)
            load_z(0)
            for v in range(UNITS):
                toeplitz = t["bias_flat"][v][:, P - 1:P - 1 + P * (384 - 1)].rearrange("h (q k) -> q h k", k=384 - 1)
                if v < 2:
                    for first in range(2):
                        lo = P if first == 0 else 0
                        sp.dma_start(bias[v][:, first, :].rearrange("p (h k) -> p h k", h=AH)[:, :, lo:2 * P],
                                     toeplitz[:, :, lo:2 * P]).then_inc(bias_loaded, 16)
                else:
                    sp.dma_start(bias_own[:, :].rearrange("p (h k) -> p h k", h=AH), toeplitz[:, :, P:2 * P]).then_inc(bias_loaded, 16)
            sp.sem_inc(uo_free, UNITS)
            sp.sem_inc(o_free, 1)

            def chunk(c, par, more):
                if more:
                    sp.wait_ge(raw_turned, c + 1)
                    load_raw(c + 1)
                for v in range(UNITS):
                    if more:
                        sp.wait_ge(step_scored, c * STEPS + (4 * v + 4))
                        load_unit(v, c + 1, 1 - par)
                    sp.wait_ge(o_copied, c * UNITS + (v + 2))
                    sp.dma_start(t["U"][v][bass.ds(c * P, P), :], uo[v][:, :]).then_inc(uo_stored[v], 16)
                    if v:
                        sp.wait_ge(uo_stored[v - 1], c * 16 + 16)
                        sp.sem_inc(uo_free, 1)
                sp.wait_ge(out_done, c + 2)
                sp.sem_inc(chunk_ended, 1)
                sp.dma_start(t["mix"].rearrange("n p s -> p n s")[:, 0:HEADS, bass.ds(c * CH, CH)], heads(o[:, :])).then_inc(stored, 16)
                if more:
                    load_z(c + 1)
                sp.wait_ge(uo_stored[UNITS - 1], c * 16 + 16)
                sp.sem_inc(uo_free, 1)
                sp.wait_ge(stored, c * 16 + 16)
                sp.sem_inc(o_free, 1)

            with sp.Fori(0, NC // 2 - 1) as j:
                chunk(2 * j, 0, True)
                chunk(2 * j + 1, 1, True)
            chunk(NC - 2, 0, True)
            chunk(NC - 1, 1, False)
            sp.wait_ge(s_upd, NC + 1)
            sp.dma_start(t["delta"].rearrange("h k v -> k h v"), heads(S_[:, :])).then_inc(stored, 16)
            sp.wait_ge(stored, 16 * NC + 16)

        @block.gpsimd
        def _(pool):
            pool.memset(ones_mean[:, :], 1.0 / DK).then_inc(consts_set, 1)
            pool.memset(eps[:, :], EPS).then_inc(consts_set, 1)
            pool.memset(S_[:, :], 0.0).then_inc(consts_set, 1)
            pool.memset(ones[:, :], 1.0).then_inc(consts_set, 1)
            for v in range(2):
                pool.memset(qkv[v][:, 1, 4 * P:8 * P], 0.0).then_inc(consts_set, 1)
                pool.memset(vtok[v][:, 1, :], 0.0).then_inc(consts_set, 1)
                pool.memset(bias[v][:, 0, :].rearrange("p (h k) -> p h k", h=AH)[:, :, 0:P], -BIG).then_inc(consts_set, 1)
            pool.wait_ge(consts_set, 10)
            pool.wait_ge(const_loaded, 80)
            pool.wait_ge(gcol_done, 1)
            with pool.Fori(0, NC) as c:
                gcol = g[:, bass.ds(c, 1), :].rearrange("p o h -> p (o h)")
                pool.tensor_tensor(heads(gbc[:, :]), all_heads(ones[:, :]), per_head(gcol), ALU.mult).then_inc(gbc_done, 1)
                pool.wait_ge(l_done, c + 1)
                for level in range(LEVELS):
                    pool.tensor_tensor(heads(B[:, level, :]), heads(L[:, :]), all_heads(const_tile(C_LEVEL + level)),
                                       ALU.mult).then_inc(mask_done, 1)

        @block.scalar
        def _(act):
            act.wait_ge(const_loaded, 80)
            act.wait_ge(consts_set, 10)
            act.wait_ge(logits_copied, 1)
            act.activation(beta[:, :, :], lt[:, :, 0:HEADS], ACT.Sigmoid).then_inc(beta_done, 1)
            act.wait_ge(g_steps, 1)
            act.activation(gtmp[:, :, :], g[:, :, :], ACT.Abs).then_inc(beta_done, 1)
            act.wait_ge(beta_done, 2)
            act.activation(gtmp[:, :, :], gtmp[:, :, :], ACT.Exp, scale=-1.0).then_inc(beta_done, 1)
            act.activation(alog[:, :], alog[:, :], ACT.Exp).then_inc(beta_done, 1)
            act.wait_ge(beta_done, 4)
            act.activation(gtmp[:, :, :], gtmp[:, :, :], ACT.Ln, bias=1.0).then_inc(beta_done, 1)
            act.wait_ge(gsum_done, 1)
            act.activation(egc[:, :, :], bank(0)[:, 0:NC * HEADS].rearrange("p (c h) -> p c h", c=NC), ACT.Exp).then_inc(gcol_done, 1)
            act.activation(ekd[:, :, :], bank(1)[:, 0:NC * HEADS].rearrange("p (c h) -> p c h", c=NC), ACT.Exp).then_inc(gcol_done, 1)

            def slot(c, par, j):
                if j % 4 == 0 and j < STEPS:
                    v = j // 4
                    act.wait_ge(v_turned, c * UNITS + (v + 1))
                    act.activation(vtok[v][:, par, :], bank(TURNS), ACT.Copy).then_inc(v_copied, 1)
                if 1 <= j <= STEPS:
                    i = j - 1
                    act.wait_ge(turned, c * STEPS + j)
                    if i >= 2:
                        act.wait_ge(pv_done, c * STEPS + (i - 1))
                    act.activation(keys_seen(eT[:, i % 2, :], i), keys_seen(bank(TURNS), i), ACT.Copy).then_inc(eT_copied, 1)
                if j < STEPS:
                    v, hs = step_heads(j)
                    act.wait_ge(max_done, c * STEPS + (j + 1))
                    if j >= 2:
                        act.wait_ge(turned, c * STEPS + (j - 1))
                    for n, h in enumerate(hs):
                        nm, dn = AH * HD + h, AH * HD + AH + h
                        m = act.activation(keys_seen(e[:, j % 2, :], j)[:, n, :], keys_seen(s[:, j % 2, :], j)[:, n, :], ACT.Exp,
                                           bias=uo[v][:, nm:nm + 1], accum_out=uo[v][:, dn:dn + 1])
                    m.then_inc(exp_done, 1)

            def chunk(c, par):
                act.wait_ge(raw_turned, c + 1)
                for h in range(8):
                    m = act.activation(junk[:, h, :], col(bank(h // HEADS), h % HEADS), ACT.Square, accum_out=ss[:, h:h + 1])
                m.then_inc(ss_done, 1)
                act.wait_ge(ss_done, c + 1)
                act.activation(rr[:, :], ss[:, :], ACT.Sqrt, bias=eps[:, 0:1]).then_inc(roots_done, 1)
                act.wait_ge(g_diff_done, c + 1)
                act.activation(gd[:, :], gd[:, :], ACT.Abs).then_inc(abs_done, 1)
                act.activation(egr[:, :], bank(3), ACT.Exp).then_inc(egr_done, 1)
                act.wait_ge(abs_done, c + 1)
                act.activation(E[:, :], gd[:, :], ACT.Exp, scale=-1.0).then_inc(e_done, 1)
                slot(c, par, 0)
                act.wait_ge(kq_turned, c + 1)
                act.activation(knT[:, :], bank(0), ACT.Copy).then_inc(knT_copied, 1)
                act.activation(qnT[:, :], bank(1), ACT.Copy).then_inc(qnT_copied, 1)
                slot(c, par, 1)
                slot(c, par, 2)
                for level in range(1, LEVELS):
                    act.wait_ge(z_done, c * (LEVELS - 1) + level)
                    act.activation(Z[:, :], bank(0), ACT.Copy).then_inc(z_copied, 1)
                    slot(c, par, level + 2)
                act.wait_ge(u_done, c + 1)
                act.activation(U[:, :], bank(2), ACT.Copy).then_inc(u_copied, 1)
                act.wait_ge(w_done, c + 1)
                act.activation(WT[:, :], bank(1), ACT.Copy).then_inc(w_copied, 1)
                slot(c, par, 9)
                slot(c, par, 10)
                act.wait_ge(o_done, c + 1)
                act.activation(osq[:, :], bank(2), ACT.Square).then_inc(osq_done, 1)
                slot(c, par, 11)
                act.wait_ge(msq_done, c + 1)
                act.activation(orr[:, :], bank(1), ACT.Sqrt, bias=eps[:, 0:1]).then_inc(oroot_done, 1)
                slot(c, par, 12)
                slot(c, par, 13)

            for_pairs(act, NC, chunk)

        @block.tensor
        def _(pe):
            ident = const_tile(C_IDENT)
            triu, tril = const_tile(C_TRIU), const_tile(C_TRIL)
            pe.wait_ge(const_loaded, 80)
            pe.wait_ge(consts_set, 10)
            for c in range(NC):
                m = pe.transpose(ps[:, c // 8, c % 8 * 36:c % 8 * 36 + 36], logits[:, c * CH:(c + 1) * CH], ident[0:36, 0:36])
            m.then_inc(logits_turned, 1)
            pe.wait_ge(g_steps, 4)
            gall = g[:, :, :].rearrange("p c h -> p (c h)")
            pe.matmul(bank(0)[:, 0:NC * HEADS], triu, gall, start=True, stop=True)
            pe.matmul(bank(1)[:, 0:NC * HEADS], tril, gall, start=True, stop=True).then_inc(gsum_done, 1)
            pe.wait_ge(gcol_done, 3)

            pe.wait_ge(bias_loaded, 16 * 5)

            def halves(par, j):
                return ((par, 1),) if j // 4 == 2 else ((1 - par, 0), (par, 1))

            def unit_start(c, par, v):
                pe.wait_ge(qkv_loaded[v][par], (c - par) * 8 + 16)
                if v:
                    pe.wait_ge(eT_copied, c * STEPS + (4 * v - 1))
                for n in range(4):
                    m = pe.transpose(col(bank(TURNS), n), qkv[v][:, par, (8 + n) * P:(9 + n) * P], ident)
                m.then_inc(v_turned, 1)

            def score(c, par, j):
                v, hs = step_heads(j)
                if j >= 2:
                    pe.wait_ge(biased, c * STEPS + (j - 1))
                for n, h in enumerate(hs):
                    tile, rows = h // 2, slice(h % 2 * HD, h % 2 * HD + HD)
                    for unit, half in halves(par, j):
                        m = pe.matmul(col(bank(SCORES + j % 2), 2 * n + half), qkv[v][rows, par, tile * P:(tile + 1) * P],
                                      qkv[v][rows, unit, (4 + tile) * P:(5 + tile) * P], start=True, stop=True)
                m.then_inc(step_scored, 1)

            def turn(c, par, j):
                pe.wait_ge(exp_done, c * STEPS + (j + 1))
                if j == 0:
                    pe.wait_ge(v_copied, c * UNITS + 1)
                elif j % 4 == 3 and j < STEPS - 1:
                    pe.wait_ge(v_copied, c * UNITS + (j // 4 + 2))
                else:
                    pe.wait_ge(eT_copied, c * STEPS + j)
                for n in range(2):
                    for unit, half in halves(par, j):
                        m = pe.transpose(col(bank(TURNS), 2 * n + half), col(e[:, j % 2, :], 2 * n + half), ident)
                m.then_inc(turned, 1)

            def values(c, par, j):
                v, hs = step_heads(j)
                pe.wait_ge(eT_copied, c * STEPS + (j + 1))
                if j % 4 == 0:
                    pe.wait_ge(o_copied, c * UNITS + (v + 1))
                for n, h in enumerate(hs):
                    hh = slice(h * HD, (h + 1) * HD)
                    for unit, half in halves(par, j):
                        m = pe.matmul(bank(OUTPUT)[:, hh], col(eT[:, j % 2, :], 2 * n + half), vtok[v][:, unit, hh],
                                      start=j // 4 == 2 or half == 0, stop=half == 1)
                m.then_inc(pv_done, 1)

            def slot(c, par, j):
                if j % 4 == 0 and j < STEPS:
                    unit_start(c, par, j // 4)
                if j < STEPS:
                    score(c, par, j)
                if j >= 2:
                    values(c, par, j - 2)
                if 1 <= j <= STEPS:
                    turn(c, par, j - 1)

            def chunk(c, par):
                pe.wait_ge(raw_loaded, c * 16 + 16)
                for h in range(HEADS):
                    pe.transpose(col(bank(0), h), raw[:, 4 + h, :], ident)
                pe.wait_ge(s_upd, c + 1)
                pe.wait_ge(gbc_done, c + 1)
                for h in range(HEADS):
                    m = pe.matmul(col(bank(3), h), col(gbc[:, :], h), triu, start=True, stop=True)
                m.then_inc(rows_done, 1)
                pe.wait_ge(out_done, c + 1)
                for n, first in ((1, 0), (2, 8)):
                    for h in range(HEADS):
                        m = pe.transpose(col(bank(n), h), raw[:, first + h, :], ident)
                m.then_inc(raw_turned, 1)
                slot(c, par, 0)
                pe.wait_ge(k_scaled, c + 1)
                for h in range(HEADS):
                    pe.transpose(col(bank(0), h), col(kn[:, :], h), ident)
                pe.wait_ge(q_scaled, c + 1)
                for h in range(HEADS):
                    m = pe.transpose(col(bank(1), h), col(qn[:, :], h), ident)
                m.then_inc(kq_turned, 1)
                slot(c, par, 1)
                pe.wait_ge(knT_copied, c + 1)
                pe.wait_ge(egr_done, c + 1)
                pe.wait_ge(g_diff_done, c + 1)
                for h in range(HEADS):
                    m = pe.matmul(col(bank(3), h), col(knT[:, :], h), col(knT[:, :], h), start=True, stop=True)
                m.then_inc(grams_done, 1)
                pe.wait_ge(qnT_copied, c + 1)
                pe.wait_ge(v_scaled, c + 1)
                for h in range(HEADS):
                    m = pe.matmul(col(bank(2), h), col(knT[:, :], h), col(qnT[:, :], h), start=True, stop=True)
                m.then_inc(scores_done, 1)
                slot(c, par, 2)
                pe.wait_ge(mask_done, c * LEVELS + 1)
                for h in range(HEADS):
                    m = pe.transpose(col(bank(0), h), col(B[:, 0, :], h), ident)
                m.then_inc(b0_turned, 1)
                for level in range(1, LEVELS):
                    pe.wait_ge(mask_done, c * LEVELS + (level + 1))
                    pe.wait_ge(xt_sub, c * LEVELS + level)
                    for h in range(HEADS):
                        m = pe.matmul(col(bank(0), h), col(B[:, level, :], h), col(XT[:, :], h), start=True, stop=True)
                    m.then_inc(z_done, 1)
                    slot(c, par, level + 2)
                    pe.wait_ge(z_copied, c * (LEVELS - 1) + level)
                    pe.wait_ge(x_sub, c * (LEVELS - 1) + level)
                    for h in range(HEADS):
                        m = pe.matmul(col(bank(1), h), col(X[:, :], h), col(Z[:, :], h), start=True, stop=True)
                    m.then_inc(xt_done, 1)
                    if level < LEVELS - 1:
                        if level == 1:
                            pe.wait_ge(i1_done, c + 1)
                        for h in range(HEADS):
                            m = pe.matmul(col(bank(2), h), col(Z[:, :], h), col(X[:, :], h), start=True, stop=True)
                        m.then_inc(x_done, 1)
                pe.wait_ge(xt_sub, c * LEVELS + LEVELS)
                for h in range(HEADS):
                    m = pe.matmul(col(bank(1), h), col(kbg[:, :], h), col(XT[:, :], h), start=True, stop=True)
                m.then_inc(w_done, 1)
                for h in range(HEADS):
                    m = pe.matmul(col(bank(2), h), col(XT[:, :], h), col(vb[:, :], h), start=True, stop=True)
                m.then_inc(u_done, 1)
                slot(c, par, 9)
                pe.wait_ge(w_copied, c + 1)
                for h in range(HEADS):
                    m = pe.matmul(col(bank(3), h), col(WT[:, :], h), col(S_[:, :], h), start=True, stop=True)
                m.then_inc(p1_done, 1)
                slot(c, par, 10)
                pe.wait_ge(vnew_done, c + 1)
                pe.wait_ge(intra_done, c + 1)
                pe.wait_ge(qdec_done, c + 1)
                for h in range(HEADS):
                    pe.matmul(col(bank(2), h), col(S_[:, :], h), col(qdec[:, :], h), start=True, stop=False)
                    m = pe.matmul(col(bank(2), h), col(vnew[:, :], h), col(intra[:, :], h), start=False, stop=True)
                m.then_inc(o_done, 1)
                for h in range(HEADS):
                    m = pe.matmul(col(bank(3), h), col(kdec[:, :], h), col(vnew[:, :], h), start=True, stop=True)
                m.then_inc(s_done, 1)
                slot(c, par, 11)
                pe.wait_ge(osq_done, c + 1)
                pe.matmul(bank(1), ones_mean[:, :], osq[:, :], start=True, stop=True).then_inc(msq_done, 1)
                slot(c, par, 12)
                slot(c, par, 13)

            for_pairs(pe, NC, chunk)

        @block.vector
        def _(dve):
            dve.wait_ge(const_loaded, 80)
            dve.wait_ge(consts_set, 10)
            dve.wait_ge(logits_turned, 1)
            for n in range(2):
                m = dve.tensor_copy(lt[:, n * 8:(n + 1) * 8, :], ps[:, n, 0:8 * 36].rearrange("p (c h) -> p c h", c=8))
            m.then_inc(logits_copied, 1)
            dve.wait_ge(logits_copied, 1)
            dtb_all = dtb[:, :].rearrange("p (o h) -> p o h", o=1).broadcast_to([P, NC, HEADS])
            dve.tensor_tensor(g[:, :, :], lt[:, :, 32:36], dtb_all, ALU.add).then_inc(g_steps, 1)
            dve.wait_ge(beta_done, 5)
            dve.scalar_tensor_tensor(g[:, :, :], g[:, :, :], 0.0, gtmp[:, :, :], ALU.max, ALU.add).then_inc(g_steps, 1)
            dve.tensor_scalar(alog[:, :], alog[:, :], -1.0, None, ALU.mult).then_inc(g_steps, 1)
            dve.wait_ge(g_steps, 3)
            alog_all = alog[:, :].rearrange("p (o h) -> p o h", o=1).broadcast_to([P, NC, HEADS])
            dve.tensor_tensor(g[:, :, :], g[:, :, :], alog_all, ALU.mult).then_inc(g_steps, 1)
            dve.wait_ge(gcol_done, 2)
            dve.tensor_copy(gc[:, :, :], bank(0)[:, 0:NC * HEADS].rearrange("p (c h) -> p c h", c=NC)).then_inc(gcol_done, 1)
            dve.sem_inc(s_upd, 1)
            dve.sem_inc(out_done, 1)
            dve.sem_inc(o_copied, 1)
            dve.wait_ge(bias_loaded, 16 * 5)

            def slot(c, par, jj, j):
                if j < STEPS:
                    v, hs = step_heads(j)
                    if j % 4 == 0:
                        dve.wait_ge(uo_free, c * UNITS + (v + 1))
                    dve.wait_ge(step_scored, c * STEPS + (j + 1))
                    if j >= 2:
                        dve.wait_ge(exp_done, c * STEPS + (j - 1))
                    if v == 2:
                        table = bias_own[:, :].rearrange("p (h k) -> p h k", h=AH)
                    else:
                        both = 1 if par else ((jj + 7) // 8 if v == 0 else jj % 2)
                        table = bias[v][:, bass.ds(both, 1), :].rearrange("p o (h k) -> p (o h) k", h=AH)
                    dve.scalar_tensor_tensor(keys_seen(s[:, j % 2, :], j), keys_seen(bank(SCORES + j % 2), j), HD ** -0.5,
                                             table[:, hs[0]:hs[0] + 3:2, :], ALU.mult, ALU.add).then_inc(biased, 1)
                    dve.wait_ge(biased, c * STEPS + (j + 1))
                    nm = AH * HD + hs[0]
                    dve.tensor_reduce(uo[v][:, nm:nm + 3:2], keys_seen(s[:, j % 2, :], j), AX_X, ALU.max,
                                      negate=True).then_inc(max_done, 1)
                if j >= 5 and j % 4 == 1:
                    v = (j - 5) // 4
                    dve.wait_ge(pv_done, c * STEPS + (j - 1))
                    dve.wait_ge(exp_done, c * STEPS + (j - 1))
                    dve.tensor_copy(uo[v][:, 0:AH * HD], bank(OUTPUT)).then_inc(o_copied, 1)

            def chunk(c, par, jj):
                def cc(tile):
                    return tile[:, bass.ds(c, 1), :].rearrange("p o h -> p (o h)")

                dve.wait_ge(roots_done, c + 1)
                dve.reciprocal(rr[:, :], rr[:, :]).then_inc(coef_steps, 1)
                dve.wait_ge(coef_steps, c * 4 + 1)
                dve.tensor_tensor(coef[:, 0, :], rr[:, 0:4], cc(beta), ALU.mult).then_inc(coef_steps, 1)
                dve.tensor_tensor(coef[:, 1, :], rr[:, 0:4], cc(ekd), ALU.mult)
                dve.tensor_scalar(coef[:, 2, :], rr[:, 4:8], DK ** -0.5, None, ALU.mult).then_inc(coef_steps, 1)
                dve.tensor_tensor(heads(kn[:, :]), heads(bank(0)), per_head(rr[:, 0:4]), ALU.mult)
                dve.wait_ge(coef_steps, c * 4 + 2)
                dve.tensor_tensor(coef[:, 3, :], coef[:, 0, :], cc(egc), ALU.mult).then_inc(coef_steps, 1)
                dve.wait_ge(coef_steps, c * 4 + 4)
                dve.tensor_tensor(heads(kbg[:, :]), heads(bank(0)), per_head(coef[:, 3, :]), ALU.mult)
                dve.tensor_tensor(heads(kdec[:, :]), heads(bank(0)), per_head(coef[:, 1, :]), ALU.mult).then_inc(k_scaled, 1)
                dve.tensor_tensor(heads(qn[:, :]), heads(bank(1)), per_head(coef[:, 2, :]), ALU.mult).then_inc(q_scaled, 1)
                dve.tensor_tensor(heads(vb[:, :]), heads(bank(2)), per_head(cc(beta)), ALU.mult).then_inc(v_scaled, 1)
                dve.wait_ge(rows_done, c + 1)
                dve.tensor_tensor(heads(gd[:, :]), heads(bank(3)), per_head(cc(gc)), ALU.subtract).then_inc(g_diff_done, 1)
                slot(c, par, jj, 0)
                slot(c, par, jj, 1)
                dve.wait_ge(grams_done, c + 1)
                dve.wait_ge(e_done, c + 1)
                dve.tensor_tensor(M[:, :], bank(3), E[:, :], ALU.mult).then_inc(m_done, 1)
                dve.wait_ge(m_done, c + 1)
                dve.tensor_tensor(heads(L[:, :]), heads(M[:, :]), per_head(cc(beta)), ALU.mult).then_inc(l_done, 1)
                dve.wait_ge(scores_done, c + 1)
                dve.tensor_tensor(intra[:, :], bank(2), E[:, :], ALU.mult).then_inc(i1_done, 1)
                dve.wait_ge(egr_done, c + 1)
                dve.wait_ge(qnT_copied, c + 1)
                dve.tensor_tensor(qdec[:, :], qnT[:, :], egr[:, :], ALU.mult).then_inc(qdec_done, 1)
                dve.wait_ge(i1_done, c + 1)
                dve.tensor_tensor(heads(intra[:, :]), heads(intra[:, :]), all_heads(const_tile(C_TRIU)), ALU.mult).then_inc(intra_done, 1)
                slot(c, par, jj, 2)
                dve.wait_ge(b0_turned, c + 1)
                ident4 = all_heads(const_tile(C_IDENT))
                dve.tensor_tensor(heads(XT[:, :]), ident4, heads(bank(0)), ALU.subtract).then_inc(xt_sub, 1)
                dve.tensor_tensor(heads(X[:, :]), ident4, heads(B[:, 0, :]), ALU.subtract).then_inc(x_sub, 1)
                for level in range(1, LEVELS):
                    slot(c, par, jj, level + 2)
                    dve.wait_ge(xt_done, c * (LEVELS - 1) + level)
                    dve.tensor_tensor(XT[:, :], XT[:, :], bank(1), ALU.subtract).then_inc(xt_sub, 1)
                    if level < LEVELS - 1:
                        dve.wait_ge(x_done, c * (LEVELS - 2) + level)
                        dve.tensor_tensor(X[:, :], X[:, :], bank(2), ALU.subtract).then_inc(x_sub, 1)
                slot(c, par, jj, 9)
                dve.wait_ge(p1_done, c + 1)
                dve.wait_ge(u_copied, c + 1)
                dve.tensor_tensor(vnew[:, :], U[:, :], bank(3), ALU.subtract).then_inc(vnew_done, 1)
                slot(c, par, jj, 10)
                dve.wait_ge(s_done, c + 1)
                last = heads(egr[:, :])[:, :, P - 1:P].broadcast_to([P, HEADS, P])
                dve.tensor_tensor(heads(S_[:, :]), heads(S_[:, :]), last, ALU.mult).then_inc(s1_done, 1)
                dve.wait_ge(s1_done, c + 1)
                dve.tensor_tensor(S_[:, :], S_[:, :], bank(3), ALU.add).then_inc(s_upd, 1)
                slot(c, par, jj, 11)
                dve.wait_ge(oroot_done, c + 1)
                dve.reciprocal(orr[:, :], orr[:, :]).then_inc(orr_done, 1)
                dve.wait_ge(orr_done, c + 1)
                dve.wait_ge(o_free, c + 1)
                dve.scalar_tensor_tensor(o[:, :], bank(2), gain[:, 0:1], orr[:, :], ALU.mult, ALU.mult).then_inc(o1_done, 1)
                dve.wait_ge(o1_done, c + 1)
                dve.wait_ge(z_loaded, c * 16 + 16)
                dve.tensor_tensor(o[:, :], o[:, :], zg[:, :], ALU.mult).then_inc(out_done, 1)
                slot(c, par, jj, 12)
                slot(c, par, jj, 13)

            with dve.Fori(0, NC // 2) as jj:
                chunk(2 * jj, 0, jj)
                chunk(2 * jj + 1, 1, jj)


QB = S // P
FLAT = P * 384


def bucket_tiles():
    tiles = np.zeros((33, len(DILS), 384), np.float32)
    for v, d in enumerate(DILS):
        for i in range(384):
            rel = 255 - i
            if not 0 <= rel <= P:
                tiles[32, v, i] = -BIG
                continue
            n = rel * d
            large = 16 + int(np.log(max(n, 1) / 16) / np.log(2048 / 16) * 16)
            tiles[n if n < 16 else min(large, 31), v, i] = 1.0
    return tiles.reshape(33, len(DILS) * 384)


def bias_rows(nc, t):
    with ExitStack() as ctx:
        sbuf, psum, sem = allocators(nc, ctx)
        rel = sbuf("pr_rel", [33, AH], F32)
        buckets = sbuf("pr_buckets", [33, len(DILS) * 384], F32)
        rows = sbuf("pr_rows", [AH, len(DILS) * 384], F32)
        ps = psum("pr_ps", [P, len(DILS), 512], F32)
        loaded, ones_set, summed, copied, stored = (sem("pr_" + n) for n in "loaded ones_set summed copied stored".split())
        block = ctx.enter_context(nc.Block())

        @block.sync
        def _(sp):
            sp.dma_start(rel[0:32, :], t["rel_bias"]).then_inc(loaded, 16)
            sp.dma_start(buckets[:, :], t["buckets"]).then_inc(loaded, 16)
            sp.wait_ge(copied, len(DILS))
            for v in range(len(DILS)):
                src = rows[:, v * 384:(v + 1) * 384].rearrange("h (o i) -> h o i", o=1).broadcast_to([AH, P, 384])
                sp.dma_start(t["bias_flat"][v].rearrange("h (q i) -> h q i", i=384), src).then_inc(stored, 16)
            sp.wait_ge(stored, 16 * len(DILS))

        @block.vector
        def _(dve):
            dve.memset(rel[32:33, :], 1.0).then_inc(ones_set, 1)
            dve.wait_ge(summed, 1)
            for v in range(len(DILS)):
                dve.tensor_copy(rows[:, v * 384:(v + 1) * 384], ps[0:AH, v, 0:384]).then_inc(copied, 1)

        @block.tensor
        def _(pe):
            pe.wait_ge(loaded, 32)
            pe.wait_ge(ones_set, 1)
            for v in range(len(DILS)):
                m = pe.matmul(ps[0:AH, v, 0:384], rel[:, :], buckets[:, v * 384:(v + 1) * 384], start=True, stop=True)
            m.then_inc(summed, 1)


def merge_dilations(nc, t):
    with ExitStack() as ctx:
        sbuf, psum, sem = allocators(nc, ctx)
        NV = len(DILS)
        u = sbuf("pm_u", [P, 2, NV * UROW], F32)
        wt = sbuf("pm_wt", [P, 2, NV * AH], F32)
        negmax = sbuf("pm_negmax", [P, AH], F32)
        total = sbuf("pm_total", [P, 2, AH], F32)
        acc = sbuf("pm_acc", [P, 2, NV, AH * HD], F32)
        out = sbuf("pm_out", [P, 2, AH * HD], F32)
        ident = sbuf("pm_ident", [P, P], F32)
        ps = psum("pm_ps", [P, 2, 512], F32)
        loaded = [sem(f"pm_loaded{n}") for n in range(2)]
        stored = [sem(f"pm_stored{n}") for n in range(2)]
        (const_loaded, max_steps, w_ready, w_exp, weight_steps, scaled, summed, turned, copied) = (sem("pm_" + n) for n in
            "const_loaded max_steps w_ready w_exp weight_steps scaled summed turned copied".split())
        block = ctx.enter_context(nc.Block())

        def field(par, first, n):
            return u[:, par, :].rearrange("p (v c) -> p v c", v=NV)[:, :, first:first + n]

        def by_v(tile, par):
            return tile[:, par, :].rearrange("p (v h) -> p v h", v=NV)

        @block.sync
        def _(sp):
            sp.dma_start(ident[:, :], t["consts"][:, 0:P]).then_inc(const_loaded, 16)

            def load(i, par):
                for v, d in enumerate(DILS):
                    rows = u[:, par, v * UROW:(v + 1) * UROW]
                    if d == 1:
                        sp.dma_start(rows, t["U"][v][bass.ds(i * P, P)]).then_inc(loaded[par], 16)
                    else:
                        src = t["U"][v].rearrange("(r m) c -> m r c", r=d)[bass.ds(i * (P // d), P // d)]
                        sp.dma_start(rows, src).then_inc(loaded[par], 16)

            def step(i, par, more=True):
                if more:
                    sp.wait_ge(scaled, i + 1)
                    load(i + 2, par)
                sp.wait_ge(copied, i + 1)
                sp.dma_start(t["mix"].rearrange("n p s -> p n s")[:, HEADS:2 * HEADS, bass.ds(i * P, P)],
                             out[:, par, :].rearrange("p (n s) -> p n s", n=4)).then_inc(stored[par], 16)

            load(0, 0)
            load(1, 1)
            for_pairs(sp, QB - 2, step)
            step(QB - 2, 0, False)
            step(QB - 1, 1, False)
            for par in range(2):
                sp.wait_ge(stored[par], 16 * QB // 2)

        @block.vector
        def _(dve):
            def step(i, par):
                dve.wait_ge(loaded[par], landed(i, par, NV))
                nm = field(par, AH * HD, AH)
                dve.tensor_tensor(negmax[:, :], nm[:, 0, :], nm[:, 1, :], ALU.min).then_inc(max_steps, 1)
                dve.wait_ge(max_steps, i * 2 + 1)
                dve.tensor_tensor(negmax[:, :], negmax[:, :], nm[:, 2, :], ALU.min).then_inc(max_steps, 1)
                dve.wait_ge(max_steps, i * 2 + 2)
                dve.tensor_tensor(by_v(wt, par), negmax[:, :].rearrange("p (o h) -> p o h", o=1).broadcast_to([P, NV, AH]), nm,
                                  ALU.subtract).then_inc(w_ready, 1)
                dve.wait_ge(w_exp, i + 1)
                tmp = acc[:, par, 0, 0:NV * AH].rearrange("p (v h) -> p v h", v=NV)
                dve.wait_ge(summed, i * 2)
                dve.tensor_tensor(tmp, by_v(wt, par), field(par, AH * HD + AH, AH), ALU.mult).then_inc(weight_steps, 1)
                dve.wait_ge(weight_steps, i * 4 + 1)
                dve.tensor_reduce(total[:, par, :], tmp.rearrange("p v h -> p h v"), AX_X, ALU.add).then_inc(weight_steps, 1)
                dve.wait_ge(weight_steps, i * 4 + 2)
                dve.reciprocal(total[:, par, :], total[:, par, :]).then_inc(weight_steps, 1)
                dve.wait_ge(weight_steps, i * 4 + 3)
                dve.tensor_tensor(by_v(wt, par), by_v(wt, par),
                                  total[:, par, :].rearrange("p (o h) -> p o h", o=1).broadcast_to([P, NV, AH]),
                                  ALU.mult).then_inc(weight_steps, 1)
                dve.wait_ge(weight_steps, i * 4 + 4)
                w = by_v(wt, par)
                for v in range(NV):
                    dve_out = acc[:, par, v, :].rearrange("p (h e) -> p h e", h=AH)
                    rows = field(par, 0, AH * HD)[:, v, :].rearrange("p (h e) -> p h e", h=AH)
                    m = dve.tensor_tensor(dve_out, rows, w[:, v, :].rearrange("p (h o) -> p h o", o=1).broadcast_to([P, AH, HD]), ALU.mult)
                m.then_inc(scaled, 1)

            for_pairs(dve, QB, step)

        @block.gpsimd
        def _(pool):
            def step(i, par):
                pool.wait_ge(scaled, i + 1)
                pool.tensor_tensor(acc[:, par, 1, :], acc[:, par, 1, :], acc[:, par, 2, :], ALU.add).then_inc(summed, 1)
                pool.wait_ge(summed, i * 2 + 1)
                pool.tensor_tensor(acc[:, par, 0, :], acc[:, par, 0, :], acc[:, par, 1, :], ALU.add).then_inc(summed, 1)

            for_pairs(pool, QB, step)

        @block.tensor
        def _(pe):
            pe.wait_ge(const_loaded, 16)

            def step(i, par):
                pe.wait_ge(summed, i * 2 + 2)
                pe.wait_ge(copied, i)
                for n in range(4):
                    m = pe.transpose(ps[:, par, n * P:(n + 1) * P], acc[:, par, 0, n * P:(n + 1) * P], ident[:, :])
                m.then_inc(turned, 1)

            for_pairs(pe, QB, step)

        @block.scalar
        def _(act):
            def step(i, par):
                act.wait_ge(w_ready, i + 1)
                act.activation(wt[:, par, :], wt[:, par, :], ACT.Exp).then_inc(w_exp, 1)
                act.wait_ge(turned, i + 1)
                act.wait_ge(stored[par], i * 8 - par * 8)
                act.activation(out[:, par, :], ps[:, par, :], ACT.Copy).then_inc(copied, 1)

            for_pairs(act, QB, step)


HB = HEADS * NSAMP
NBH = NSAMP * AH
PADS = TOK - S


def head_mask():
    p, n, h = np.meshgrid(np.arange(P), np.arange(4), np.arange(AH), indexing="ij")
    return (2 * n + p // HD == h).astype(np.float32).reshape(P, 4 * AH)


def delta_samples(nc, t):
    with ExitStack() as ctx:
        sbuf, psum, sem = allocators(nc, ctx)
        state = sbuf("sd_state", [P, HB, P], F32)
        new_state = sbuf("sd_new_state", [P, HB, P], F32)
        diag = sbuf("sd_diag", [P, HB, P], F32)
        ident = sbuf("sd_ident", [P, P], F32)
        ones = sbuf("sd_ones", [P, P], F32)
        eps = sbuf("sd_eps", [P, 1], F32)
        dn = sbuf("sd_dn", [P, 12 * NSAMP], F32)
        z = sbuf("sd_z", [P, HB], F32)
        b_log = sbuf("sd_b", [P, HB], F32)
        a_log_in = sbuf("sd_a", [P, HB], F32)
        alog = sbuf("sd_alog", [P, HEADS], F32)
        dtb = sbuf("sd_dtb", [P, HEADS], F32)
        gain = sbuf("sd_gain", [P, 1], F32)
        sq = sbuf("sd_sq", [P, 2 * HB], F32)
        root = sbuf("sd_root", [P, 2 * HB], F32)
        kq = sbuf("sd_kq", [P, HB, 2], F32)
        kq_prod = sbuf("sd_kqprod", [P, HB], F32)
        soft, soft2, eg, beta, ks, delta, o, osq, oroot = (
            sbuf("sd_" + n, [P, HB], F32) for n in "soft soft2 eg beta ks delta o osq oroot".split())
        out = sbuf("sd_out", [P, HEADS * PADS], F32)
        ps = psum("sd_ps", [P, 8, 512], F32)
        loaded, state_loaded, stored = named(sem, "sd_", "loaded state_loaded stored")
        (consts_set, squares, norms, roots, recips, k_ready, q_ready, products, dots, kqs_done, beta_done, a_ready,
         abs_done, exp_done, ln_done, rate_done, soft_done, g_ready, eg_done, ks_done, v_less, delta_done, diag_done,
         spread, scaled, state_done, o_scaled, o_delta, o_done, o_squares, o_means, o_roots, o_recips, o_gained,
         out_ready, rate_neg) = named(sem, "sd_", """consts_set squares norms roots recips k_ready q_ready products dots kqs_done
         beta_done a_ready abs_done exp_done ln_done rate_done soft_done g_ready eg_done ks_done v_less delta_done
         diag_done spread scaled state_done o_scaled o_delta o_done o_squares o_means o_roots o_recips o_gained
         out_ready rate_neg""")
        block = ctx.enter_context(nc.Block())
        q, k, v = (dn[:, n * HB:(n + 1) * HB] for n in range(3))

        def by_head(tile):
            return tile[:, :].rearrange("p (h b) -> p h b", h=HEADS)

        def per_head_all(col):
            return col[:, :].rearrange("p (h o) -> p h o", o=1).broadcast_to([P, HEADS, NSAMP])

        def along(col, n):
            return col.rearrange("p (c o) -> p c o", o=1).broadcast_to([P, HB, n])

        @block.sync
        def _(sp):
            sp.dma_start(ident[:, :], t["consts"][:, 0:P]).then_inc(loaded, 16)
            sp.dma_start(dn[:, :].rearrange("p (n b) -> p n b", n=12), t["dn_samp"].rearrange("n p b -> p n b")).then_inc(loaded, 16)
            sp.dma_start(by_head(z), t["z"].rearrange("n p s -> p n s")[:, :, S:S + NSAMP]).then_inc(loaded, 16)
            sp.dma_start(by_head(b_log), t["ba"][0:HEADS, S:S + NSAMP].partition_broadcast(P)).then_inc(loaded, 16)
            sp.dma_start(by_head(a_log_in), t["ba"][32:32 + HEADS, S:S + NSAMP].partition_broadcast(P)).then_inc(loaded, 16)
            sp.dma_start(alog[:, :], t["a_log"].partition_broadcast(P)).then_inc(loaded, 16)
            sp.dma_start(dtb[:, :], t["dt_bias"].partition_broadcast(P)).then_inc(loaded, 16)
            sp.dma_start(gain[:, :], t["g_dn_out"]).then_inc(loaded, 16)
            for h in range(HEADS):
                sp.dma_start(state[:, h * NSAMP:(h + 1) * NSAMP, :],
                             t["state"][:, h].rearrange("b k e -> k b e")).then_inc(state_loaded, 16)
            sp.wait_ge(out_ready, 1)
            sp.dma_start(t["mix"].rearrange("n p s -> p n s")[:, 0:HEADS, S:TOK],
                         out[:, :].rearrange("p (h b) -> p h b", h=HEADS)).then_inc(stored, 16)
            sp.wait_ge(state_done, HB)
            for h in range(HEADS):
                sp.dma_start(t["new_state"][:, h].rearrange("b k e -> k b e"),
                             new_state[:, h * NSAMP:(h + 1) * NSAMP, :]).then_inc(stored, 16)
            sp.wait_ge(stored, 16 * (HEADS + 1))

        @block.gpsimd
        def _(pool):
            pool.memset(ones[:, :], 1.0).then_inc(consts_set, 1)
            pool.memset(eps[:, :], EPS).then_inc(consts_set, 1)
            pool.memset(out[:, :], 0.0).then_inc(consts_set, 1)
            pool.wait_ge(delta_done, 1)
            pool.tensor_tensor(diag[:, :, :], ident[:, :].rearrange("p (o j) -> p o j", o=1).broadcast_to([P, HB, P]),
                               along(delta[:, :], P), ALU.mult).then_inc(diag_done, 1)

        @block.scalar
        def _(act):
            act.wait_ge(loaded, 128)
            act.wait_ge(consts_set, 3)
            act.activation(sq[:, :], dn[:, 0:2 * HB], ACT.Square).then_inc(squares, 1)
            act.wait_ge(norms, 1)
            act.activation(root[:, :], ps[:, 0, 0:2 * HB], ACT.Sqrt, bias=eps[:, 0:1]).then_inc(roots, 1)
            act.activation(beta[:, :], b_log[:, :], ACT.Sigmoid).then_inc(beta_done, 1)
            act.wait_ge(a_ready, 1)
            act.activation(soft[:, :], a_log_in[:, :], ACT.Abs).then_inc(abs_done, 1)
            act.wait_ge(abs_done, 1)
            act.activation(soft2[:, :], soft[:, :], ACT.Exp, scale=-1.0).then_inc(exp_done, 1)
            act.activation(alog[:, :], alog[:, :], ACT.Exp).then_inc(rate_done, 1)
            act.wait_ge(exp_done, 1)
            act.activation(soft[:, :], soft2[:, :], ACT.Ln, bias=1.0).then_inc(ln_done, 1)
            act.wait_ge(g_ready, 1)
            act.activation(eg[:, :], a_log_in[:, :], ACT.Exp).then_inc(eg_done, 1)
            act.wait_ge(o_done, 1)
            act.activation(osq[:, :], o[:, :], ACT.Square).then_inc(o_squares, 1)
            act.wait_ge(o_means, 1)
            act.activation(oroot[:, :], ps[:, 3, 0:HB], ACT.Sqrt, bias=eps[:, 0:1], scale=1.0 / DK).then_inc(o_roots, 1)

        @block.tensor
        def _(pe):
            pe.wait_ge(loaded, 128)
            pe.wait_ge(consts_set, 3)
            pe.wait_ge(squares, 1)
            pe.matmul(ps[:, 0, 0:2 * HB], ones[:, :], sq[:, :], start=True, stop=True).then_inc(norms, 1)
            pe.wait_ge(products, 1)
            pe.matmul(ps[:, 1, 0:HB], ones[:, :], kq_prod[:, :], start=True, stop=True).then_inc(dots, 1)
            pe.wait_ge(state_loaded, 16 * HEADS)
            for c in range(HB):
                m = pe.matmul(ps[:, 2, 2 * c:2 * c + 2], state[:, c, :], kq[:, c, :], start=True, stop=True)
            m.then_inc(kqs_done, 1)
            pe.wait_ge(o_squares, 1)
            pe.matmul(ps[:, 3, 0:HB], ones[:, :], osq[:, :], start=True, stop=True).then_inc(o_means, 1)
            pe.wait_ge(diag_done, 1)
            for n in range(8):
                if n >= 4:
                    pe.wait_ge(state_done, 4 * (n - 3))
                pe.matmul(ps[:, 4 + n % 4, :], ones[:, :], diag[:, 4 * n:4 * n + 4, :].rearrange("p c j -> p (c j)"),
                          start=True, stop=True).then_inc(spread, 1)

        @block.vector
        def _(dve):
            dve.wait_ge(loaded, 128)
            dve.wait_ge(consts_set, 3)
            dve.tensor_tensor(by_head(a_log_in), by_head(a_log_in), per_head_all(dtb), ALU.add).then_inc(a_ready, 1)
            dve.wait_ge(roots, 1)
            dve.reciprocal(root[:, :], root[:, :]).then_inc(recips, 1)
            dve.wait_ge(recips, 1)
            dve.tensor_tensor(kq[:, :, 0], k, root[:, HB:2 * HB], ALU.mult).then_inc(k_ready, 1)
            dve.scalar_tensor_tensor(kq[:, :, 1], q, DK ** -0.5, root[:, 0:HB], ALU.mult, ALU.mult).then_inc(q_ready, 1)
            dve.wait_ge(k_ready, 1)
            dve.wait_ge(q_ready, 1)
            dve.tensor_tensor(kq_prod[:, :], kq[:, :, 0], kq[:, :, 1], ALU.mult).then_inc(products, 1)
            dve.wait_ge(rate_done, 1)
            dve.tensor_scalar(alog[:, :], alog[:, :], -1.0, None, ALU.mult).then_inc(rate_neg, 1)
            dve.wait_ge(ln_done, 1)
            dve.scalar_tensor_tensor(soft[:, :], a_log_in[:, :], 0.0, soft[:, :], ALU.max, ALU.add).then_inc(soft_done, 1)
            dve.wait_ge(soft_done, 1)
            dve.wait_ge(rate_neg, 1)
            dve.tensor_tensor(by_head(a_log_in), by_head(soft), per_head_all(alog), ALU.mult).then_inc(g_ready, 1)
            dve.wait_ge(eg_done, 1)
            dve.wait_ge(state_loaded, 16 * HEADS)
            dve.tensor_tensor(new_state[:, :, :], state[:, :, :], along(eg[:, :], P), ALU.mult).then_inc(scaled, 1)
            dve.wait_ge(kqs_done, 1)
            found = ps[:, 2, 0:2 * HB].rearrange("p (c two) -> p c two", two=2)
            dve.tensor_tensor(ks[:, :], found[:, :, 0], eg[:, :], ALU.mult).then_inc(ks_done, 1)
            dve.tensor_tensor(o[:, :], found[:, :, 1], eg[:, :], ALU.mult).then_inc(o_scaled, 1)
            dve.wait_ge(ks_done, 1)
            dve.tensor_tensor(ks[:, :], v, ks[:, :], ALU.subtract).then_inc(v_less, 1)
            dve.wait_ge(v_less, 1)
            dve.wait_ge(beta_done, 1)
            dve.tensor_tensor(delta[:, :], ks[:, :], beta[:, :], ALU.mult).then_inc(delta_done, 1)
            dve.wait_ge(delta_done, 1)
            dve.wait_ge(dots, 1)
            dve.tensor_tensor(osq[:, :], ps[:, 1, 0:HB], delta[:, :], ALU.mult).then_inc(o_delta, 1)
            dve.wait_ge(o_delta, 1)
            dve.wait_ge(o_scaled, 1)
            dve.tensor_tensor(o[:, :], o[:, :], osq[:, :], ALU.add).then_inc(o_done, 1)
            dve.wait_ge(scaled, 1)
            for c in range(HB):
                if c % 4 == 0:
                    dve.wait_ge(spread, c // 4 + 1)
                dve.scalar_tensor_tensor(new_state[:, c, :], ps[:, 4 + c // 4 % 4, c % 4 * P:(c % 4 + 1) * P],
                                         kq[:, c, 0:1], new_state[:, c, :], ALU.mult, ALU.add).then_inc(state_done, 1)
            dve.wait_ge(o_roots, 1)
            dve.reciprocal(oroot[:, :], oroot[:, :]).then_inc(o_recips, 1)
            dve.wait_ge(o_recips, 1)
            dve.scalar_tensor_tensor(o[:, :], o[:, :], gain[:, 0:1], oroot[:, :], ALU.mult, ALU.mult).then_inc(o_gained, 1)
            dve.wait_ge(o_gained, 1)
            dve.tensor_tensor(out[:, :].rearrange("p (h b) -> p h b", h=HEADS)[:, :, 0:NSAMP], by_head(o), by_head(z),
                              ALU.mult).then_inc(out_ready, 1)


def attention_samples(nc, t):
    with ExitStack() as ctx:
        sbuf, psum, sem = allocators(nc, ctx)
        NV = len(DILS)
        KEYS = (P, P, PAST // DILS[2])
        FIRST = (0, P, 2 * P)
        SELF = sum(KEYS)
        KC = NSAMP * AH * HD
        keys = sbuf("sa_keys", [P, NV, KC], F32)
        values = sbuf("sa_values", [P, NV, KC], F32)
        qrow = sbuf("sa_qrow", [P, KC], F32)
        diag = sbuf("sa_diag", [P, KC], F32)
        ident = sbuf("sa_ident", [P, P], F32)
        mask = sbuf("sa_mask", [P, 4 * AH], F32)
        ones = sbuf("sa_ones", [P, P], F32)
        new = sbuf("sa_new", [P, 12, NSAMP], F32)
        q_by_sample = sbuf("sa_qbs", [P, NSAMP, 4], F32)
        prod = sbuf("sa_prod", [P, 4, NSAMP], F32)
        masked = sbuf("sa_masked", [P, 4, NSAMP, AH], F32)
        rows = sbuf("sa_rows", [NSAMP, 2, AH * HD], F32)
        cols = sbuf("sa_cols", [P, NV, NBH], F32)
        bias = sbuf("sa_bias", [NBH, NV, P + 1], F32)
        s = sbuf("sa_s", [NBH, SELF + 1], F32)
        e = sbuf("sa_e", [NBH, SELF + 1], F32)
        negmax = sbuf("sa_negmax", [NBH, 1], F32)
        den = sbuf("sa_den", [NBH, 1], F32)
        w0 = sbuf("sa_w0", [NBH, 1], F32)
        diag0 = sbuf("sa_diag0", [NBH, NBH], F32)
        probs = sbuf("sa_probs", [P, NV, NBH], F32)
        own = sbuf("sa_own", [P, 4, NSAMP], F32)
        out = sbuf("sa_out", [P, 4, PADS], F32)
        ps = psum("sa_ps", [P, 8, 512], F32)
        (loaded, keys_loaded, values_loaded, stored) = named(sem, "sa_", "loaded keys_loaded values_loaded stored")
        (consts_set, q_sorted, diag_done, spread, spread_copied, products, masked_done, rows_turned, rows_copied,
         keys_times_q, cols_done, cols_turned, s_done, self_dots, max_done, e_done, den_done, recip_done, normalised,
         w0_done, diag0_done, probs_turned, probs_copied, w0_spread, pv_done, own_done, out_done) = named(sem, "sa_",
            """consts_set q_sorted diag_done spread spread_copied products masked_done rows_turned rows_copied
            keys_times_q cols_done cols_turned s_done self_dots max_done e_done den_done recip_done normalised
            w0_done diag0_done probs_turned probs_copied w0_spread pv_done own_done out_done""")
        block = ctx.enter_context(nc.Block())

        def gathered(cache, v):
            d = DILS[v]
            tokens = cache.rearrange("b (t d) c -> t d b c", d=d)
            n = PAST // d
            return tokens[n - KEYS[v]:n, 0]

        @block.sync
        def _(sp):
            sp.dma_start(ident[:, :], t["consts"][:, 0:P]).then_inc(loaded, 16)
            sp.dma_start(mask[:, :], t["head_mask"]).then_inc(loaded, 16)
            sp.dma_start(new[:, :, :], t["at"].rearrange("n p s -> p n s")[:, :, S:S + NSAMP]).then_inc(loaded, 16)
            for b in range(NSAMP):
                sp.dma_start(bias[b * AH:(b + 1) * AH, :, :],
                             t["bias_flat"].rearrange("v h i -> h v i")[:, :, P - 1:2 * P]).then_inc(loaded, 16)
            for v in range(NV):
                sp.dma_start(keys[0:KEYS[v], v, :].rearrange("p (b c) -> p b c", b=NSAMP),
                             gathered(t["cache_k"], v)).then_inc(keys_loaded, 16)
            for v in range(NV):
                sp.dma_start(values[0:KEYS[v], v, :].rearrange("p (b c) -> p b c", b=NSAMP),
                             gathered(t["cache_v"], v)).then_inc(values_loaded, 16)
            sp.wait_ge(rows_copied, 1)
            sp.dma_start(t["new_cache_k"][:, PAST - 1], rows[:, 0, :]).then_inc(stored, 16)
            sp.dma_start(t["new_cache_v"][:, PAST - 1], rows[:, 1, :]).then_inc(stored, 16)
            sp.wait_ge(out_done, 2)
            sp.dma_start(t["mix"].rearrange("n p s -> p n s")[:, HEADS:2 * HEADS, S:TOK], out[:, :, :]).then_inc(stored, 16)
            sp.wait_ge(stored, 48)

        @block.gpsimd
        def _(pool):
            pool.memset(ones[:, :], 1.0).then_inc(consts_set, 1)
            pool.memset(out[:, :, :], 0.0).then_inc(consts_set, 1)

        @block.scalar
        def _(act):
            for b in range(NSAMP):
                act.wait_ge(spread, b + 1)
                act.activation(qrow[:, b * 512:(b + 1) * 512], ps[:, b, :], ACT.Copy).then_inc(spread_copied, 1)
            act.wait_ge(rows_turned, 1)
            act.activation(rows[:, :, :], ps[0:NSAMP, 0:2, :], ACT.Copy).then_inc(rows_copied, 1)
            act.wait_ge(max_done, 1)
            act.activation(e[:, :], s[:, :], ACT.Exp, bias=negmax[:, 0:1], accum_out=den[:, 0:1]).then_inc(e_done, 1)
            act.wait_ge(probs_turned, 1)
            for v in range(NV):
                m = act.activation(probs[0:KEYS[v], v, :], ps[0:KEYS[v], 4, v * NBH:(v + 1) * NBH], ACT.Copy)
            m.then_inc(probs_copied, 1)

        @block.tensor
        def _(pe):
            pe.wait_ge(loaded, 176)
            pe.wait_ge(consts_set, 2)
            pe.wait_ge(diag_done, 1)
            for b in range(NSAMP):
                pe.matmul(ps[:, b, :], ones[:, :], diag[:, b * 512:(b + 1) * 512], start=True, stop=True).then_inc(spread, 1)
            pe.wait_ge(spread_copied, 2)
            for n in range(8):
                m = pe.transpose(ps[0:NSAMP, n // 4, n % 4 * P:(n % 4 + 1) * P], new[:, 4 + n, :], ident[:, :])
            m.then_inc(rows_turned, 1)
            pe.wait_ge(spread_copied, 3)
            pe.wait_ge(masked_done, 1)
            for n in range(4):
                m = pe.matmul(ps[0:NBH, 2, 0:2], masked[:, n, :, :].rearrange("p b h -> p (b h)"), ones[:, 0:2],
                              start=n == 0, stop=n == 3)
            m.then_inc(self_dots, 1)
            pe.wait_ge(spread_copied, 4)
            for v in range(NV):
                pe.wait_ge(cols_done, v + 1)
                pe.transpose(ps[0:NBH, 3, FIRST[v]:FIRST[v] + KEYS[v]], cols[0:KEYS[v], v, :],
                             ident[0:KEYS[v], 0:KEYS[v]]).then_inc(cols_turned, 1)
            pe.wait_ge(spread_copied, 5)
            pe.wait_ge(normalised, 1)
            for v in range(NV):
                m = pe.transpose(ps[0:KEYS[v], 4, v * NBH:(v + 1) * NBH], e[:, FIRST[v]:FIRST[v] + KEYS[v]], ident[0:NBH, 0:NBH])
            m.then_inc(probs_turned, 1)
            pe.wait_ge(spread_copied, 6)
            pe.wait_ge(diag0_done, 1)
            pe.matmul(ps[:, 5, 0:NBH], ones[0:NBH, :], diag0[:, :], start=True, stop=True).then_inc(w0_spread, 1)
            pe.wait_ge(spread_copied, 7)
            pe.wait_ge(probs_copied, 1)
            pe.wait_ge(values_loaded, 16 * NV)
            for b in range(NSAMP):
                for n in range(4):
                    for v in range(NV):
                        c = b * 512 + n * P
                        m = pe.matmul(ps[:, 6, b * AH + 2 * n:b * AH + 2 * n + 2], values[0:KEYS[v], v, c:c + P],
                                      probs[0:KEYS[v], v, b * AH + 2 * n:b * AH + 2 * n + 2], start=v == 0, stop=v == NV - 1)
            m.then_inc(pv_done, 1)

        @block.vector
        def _(dve):
            dve.wait_ge(loaded, 176)
            dve.wait_ge(consts_set, 2)
            dve.tensor_copy(q_by_sample[:, :, :], new[:, 0:4, :].rearrange("p n b -> p b n")).then_inc(q_sorted, 1)
            dve.wait_ge(q_sorted, 1)
            qcols = q_by_sample[:, :, :].rearrange("p b n -> p (b n)").rearrange("p (c o) -> p c o", o=1)
            dve.tensor_tensor(diag[:, :].rearrange("p (c j) -> p c j", j=P),
                              ident[:, :].rearrange("p (o j) -> p o j", o=1).broadcast_to([P, 4 * NSAMP, P]),
                              qcols.broadcast_to([P, 4 * NSAMP, P]), ALU.mult).then_inc(diag_done, 1)
            dve.tensor_tensor(prod[:, :, :], new[:, 0:4, :], new[:, 4:8, :], ALU.mult).then_inc(products, 1)
            dve.wait_ge(products, 1)
            for n in range(4):
                m = dve.tensor_tensor(masked[:, n, :, :],
                                      prod[:, n, :].rearrange("p (b o) -> p b o", o=1).broadcast_to([P, NSAMP, AH]),
                                      mask[:, n * AH:(n + 1) * AH].rearrange("p (o h) -> p o h", o=1).broadcast_to([P, NSAMP, AH]),
                                      ALU.mult)
            m.then_inc(masked_done, 1)
            dve.wait_ge(spread_copied, NSAMP)
            dve.wait_ge(keys_loaded, 16 * NV)
            for v in range(NV):
                kv = keys[0:KEYS[v], v, :]
                dve.tensor_tensor(kv, kv, qrow[0:KEYS[v], :], ALU.mult).then_inc(keys_times_q, 1)
                dve.wait_ge(keys_times_q, v + 1)
                dve.tensor_reduce(cols[0:KEYS[v], v, :], kv.rearrange("p (c e) -> p c e", e=HD), AX_X, ALU.add).then_inc(cols_done, 1)
            dve.wait_ge(self_dots, 1)
            dve.wait_ge(cols_turned, NV)
            for v in range(NV):
                dve.scalar_tensor_tensor(s[:, FIRST[v]:FIRST[v] + KEYS[v]], ps[0:NBH, 3, FIRST[v]:FIRST[v] + KEYS[v]],
                                         HD ** -0.5, bias[:, v, P - KEYS[v]:P], ALU.mult, ALU.add).then_inc(s_done, 1)
            dve.scalar_tensor_tensor(s[:, SELF:SELF + 1], ps[0:NBH, 2, 0:1], HD ** -0.5, bias[:, 0, P:P + 1],
                                     ALU.mult, ALU.add).then_inc(s_done, 1)
            dve.wait_ge(s_done, NV + 1)
            dve.tensor_reduce(negmax[:, :], s[:, :], AX_X, ALU.max, negate=True).then_inc(max_done, 1)
            dve.wait_ge(e_done, 1)
            dve.scalar_tensor_tensor(den[:, :], e[:, SELF:SELF + 1], NV - 1.0, den[:, :], ALU.mult, ALU.add).then_inc(den_done, 1)
            dve.wait_ge(den_done, 1)
            dve.reciprocal(den[:, :], den[:, :]).then_inc(recip_done, 1)
            dve.wait_ge(recip_done, 1)
            dve.tensor_scalar(e[:, :], e[:, :], den[:, 0:1], None, ALU.mult).then_inc(normalised, 1)
            dve.wait_ge(normalised, 1)
            dve.tensor_scalar(w0[:, :], e[:, SELF:SELF + 1], float(NV), None, ALU.mult).then_inc(w0_done, 1)
            dve.wait_ge(w0_done, 1)
            dve.tensor_scalar(diag0[:, :], ident[0:NBH, 0:NBH], w0[:, 0:1], None, ALU.mult).then_inc(diag0_done, 1)
            dve.wait_ge(w0_spread, 1)

            def of_head(bank, half):
                return ps[half * HD:(half + 1) * HD, bank, 0:NBH].rearrange("p (b n two) -> p n b two", b=NSAMP, two=2)[:, :, :, half]

            for half in range(2):
                rows_ = slice(half * HD, (half + 1) * HD)
                m = dve.tensor_tensor(own[rows_, :, :], new[rows_, 8:12, :], of_head(5, half), ALU.mult)
            m.then_inc(own_done, 1)
            dve.wait_ge(own_done, 1)
            dve.wait_ge(pv_done, 1)
            for half in range(2):
                rows_ = slice(half * HD, (half + 1) * HD)
                dve.tensor_tensor(out[rows_, :, 0:NSAMP], own[rows_, :, :], of_head(6, half), ALU.add).then_inc(out_done, 1)


def blocks(engine, step):
    step(0, 0, True)
    with engine.Fori(1, (NB + 1) // 2) as j:
        step(2 * j - 1, 1, False)
        step(2 * j, 0, False)


def output_projection(nc, t):
    with ExitStack() as ctx:
        sbuf, psum, sem = allocators(nc, ctx)
        w_raw = sbuf("pc_w", [P, 2, KD * P], F32)
        w_hi = sbuf("pc_whi", [P, KD, KD * P], F32R)
        w_lo = sbuf("pc_wlo", [P, KD, KD * P], F32R)
        mix = sbuf("pc_mix", [P, KD, TB], F32)
        mix_hi = sbuf("pc_mixhi", [P, 2, KD, TB], F32R)
        mix_lo = sbuf("pc_mixlo", [P, 2, KD, TB], F32R)
        x = sbuf("pc_x", [P, 2, KD, TB], F32)
        out = sbuf("pc_out", [P, 2, KD, TB], F32)
        sq = sbuf("pc_sq", [P, KD, TB], F32)
        ssum = sbuf("pc_ssum", [P, TB], F32)
        rstd = sbuf("pc_rstd", [P, TB], F32)
        gains = sbuf("pc_gains", [P, 2, KD], F32)
        eps = sbuf("pc_eps", [P, 1], F32)
        ones_mean = sbuf("pc_ones", [P, P], F32)
        prod_ps = psum("pc_prod", [P, 7, 512], F32)
        mean_ps = psum("pc_mean", [P, 512], F32)
        gains_loaded = sem("pc_gains_loaded")
        consts_set = sem("pc_consts_set")
        w_loaded = (sem("pc_w_loaded0"), sem("pc_w_loaded1"))
        w_hi_done = sem("pc_w_hi_done")
        w_lo_done = sem("pc_w_lo_done")
        mix_loaded = sem("pc_mix_loaded")
        mix_hi_done = sem("pc_mix_hi_done")
        mix_lo_done = sem("pc_mix_lo_done")
        x_loaded = (sem("pc_x_loaded0"), sem("pc_x_loaded1"))
        prod_done = sem("pc_prod_done")
        bank_read = sem("pc_bank_read")
        squares_done = sem("pc_squares_done")
        sums_done = sem("pc_sums_done")
        means_done = sem("pc_means_done")
        roots_done = sem("pc_roots_done")
        recips_done = sem("pc_recips_done")
        scaled_done = sem("pc_scaled_done")
        x1_done = sem("pc_x1_done")
        h2_done = sem("pc_h2_done")
        stored = (sem("pc_stored0"), sem("pc_stored1"))
        block = ctx.enter_context(nc.Block())

        @block.sync
        def _(sp):
            sp.dma_start(gains[:, 0, :], t["g_post_mix"]).then_inc(gains_loaded, 16)
            sp.dma_start(gains[:, 1, :], t["g_pre_ffn"]).then_inc(gains_loaded, 16)

            def load_w(j, par):
                if not isinstance(j, int):
                    sp.wait_ge(w_lo_done, j - 1)
                sp.dma_start(w_raw[:, par, :], t["w_out"][j]).then_inc(w_loaded[par], 16)

            def load_mix(b):
                sp.wait_ge(mix_lo_done, b)
                sp.dma_start(mix[:, :, :], t["mix"].rearrange("k p t -> p k t")[:, :, bass.ds(b * TB, TB)]
                             ).then_inc(mix_loaded, 16)

            def load_x(b, par):
                sp.dma_start(x[:, par], t["xT"][b]).then_inc(x_loaded[par], 16)

            load_mix(0)
            load_w(0, 0)
            load_w(1, 1)
            with sp.Fori(1, KD // 2) as j:
                load_w(2 * j, 0)
                load_w(2 * j + 1, 1)
            load_x(0, 0)
            load_mix(1)
            load_x(1, 1)

            def finish(b, par):
                sp.wait_ge(x1_done, b + 1)
                sp.dma_start(t["x1"][b], x[:, par]).then_inc(stored[par], 16)
                sp.wait_ge(h2_done, b + 1)
                sp.dma_start(t["h2"][b], out[:, par]).then_inc(stored[par], 16)

            def block_io(b, par):
                load_mix(b + 2)
                finish(b, par)
                sp.wait_ge(stored[par], landed(b, par, 2))
                load_x(b + 2, par)

            for b in range(NB - 2):
                block_io(b, b % 2)
            for b in range(NB - 2, NB):
                finish(b, b % 2)
            for par in range(2):
                sp.wait_ge(stored[par], 32 * ((NB + 1 - par) // 2))

        @block.gpsimd
        def _(pool):
            pool.memset(ones_mean[:, :], 1.0 / D).then_inc(consts_set, 1)
            pool.memset(eps[:, :], EPS).then_inc(consts_set, 1)

            def split_mix(b, par, first):
                pool.wait_ge(mix_hi_done, b + 1)
                pool.tensor_tensor(mix_lo[:, par], mix[:, :, :], mix_hi[:, par].bitcast(F32),
                                   ALU.subtract).then_inc(mix_lo_done, 1)

            def split_w(j, par):
                pool.wait_ge(w_hi_done, j + 1)
                pool.tensor_tensor(w_lo[:, bass.ds(j, 1), :], w_raw[:, par:par + 1, :],
                                   w_hi[:, bass.ds(j, 1), :].bitcast(F32), ALU.subtract).then_inc(w_lo_done, 1)

            split_mix(0, 0, True)
            for_pairs(pool, KD, split_w)
            with pool.Fori(1, (NB + 1) // 2) as j:
                split_mix(2 * j - 1, 1, False)
                split_mix(2 * j, 0, False)

        @block.scalar
        def _(act):
            act.wait_ge(consts_set, 2)

            def split_mix(b, par):
                act.wait_ge(mix_loaded, 16 * b + 16)
                if not isinstance(b, int):
                    act.wait_ge(prod_done, b * KD - KD)
                act.activation(mix_hi[:, par], mix[:, :, :], ACT.Copy).then_inc(mix_hi_done, 1)

            def split_w(j, par):
                act.wait_ge(w_loaded[par], landed(j, par))
                act.activation(w_hi[:, bass.ds(j, 1), :], w_raw[:, par:par + 1, :], ACT.Copy).then_inc(w_hi_done, 1)

            split_mix(0, 0)
            for_pairs(act, KD, split_w)

            def block_work(b, par):
                if not isinstance(b, int):
                    act.wait_ge(stored[par], landed(b, par, 2) - 32)
                for j in range(KD):
                    act.wait_ge(prod_done, b * KD + (j + 1))
                    act.activation(out[:, par, j, :], prod_ps[:, j % 7, 0:TB], ACT.Copy).then_inc(bank_read, 1)
                act.wait_ge(bank_read, b * KD + KD)
                act.activation(sq[:, :, :], out[:, par], ACT.Square).then_inc(squares_done, 1)
                act.wait_ge(means_done, 2 * b + 1)
                act.activation(ssum[:, :], mean_ps[:, 0:TB], ACT.Sqrt, bias=eps[:, 0:1]).then_inc(roots_done, 1)
                act.wait_ge(x1_done, b + 1)
                act.activation(sq[:, :, :], x[:, par], ACT.Square).then_inc(squares_done, 1)
                act.wait_ge(means_done, 2 * b + 2)
                act.activation(ssum[:, :], mean_ps[:, 0:TB], ACT.Sqrt, bias=eps[:, 0:1]).then_inc(roots_done, 1)

            split_mix(1, 1)
            block_work(0, 0)
            with act.Fori(1, NB // 2) as j:
                split_mix(2 * j, 0)
                block_work(2 * j - 1, 1)
                split_mix(2 * j + 1, 1)
                block_work(2 * j, 0)
            split_mix(NB - 1, 0)
            act.wait_ge(stored[1], 32)
            block_work(NB - 2, 1)
            act.wait_ge(stored[0], 64)
            block_work(NB - 1, 0)

        @block.tensor
        def _(pe):
            pe.wait_ge(consts_set, 2)

            def mean(n):
                pe.wait_ge(sums_done, n + 1)
                pe.matmul(mean_ps[:, 0:TB], ones_mean[:, :], ssum[:, :], start=True, stop=True).then_inc(means_done, 1)

            def block_products(b, par, first):
                pe.wait_ge(mix_lo_done, b + 1)
                for j in range(KD):
                    if first:
                        pe.wait_ge(w_lo_done, j + 1)
                    if not first and j == 2:
                        mean(2 * b - 2)
                    if not first and j == 7:
                        mean(2 * b - 1)
                    if j == 7:
                        pe.wait_ge(bank_read, b * KD + 1)
                    elif not first:
                        pe.wait_ge(bank_read, b * KD + (j - 7 if j else 0))
                    for k in range(KD):
                        w = slice(k * P, (k + 1) * P)
                        mm = hi_lo_products(pe, prod_ps[:, j % 7, 0:TB], w_hi[:, j, w], w_lo[:, j, w],
                                            mix_hi[:, par, k, :], mix_lo[:, par, k, :], k == 0, k == KD - 1)
                    mm.then_inc(prod_done, 1)

            blocks(pe, block_products)
            mean(2 * NB - 2)
            mean(2 * NB - 1)

        @block.vector
        def _(dve):
            dve.wait_ge(gains_loaded, 32)

            def rms(n):
                dve.wait_ge(squares_done, n + 1)
                dve.tensor_reduce(ssum[:, :], sq[:, :, :].rearrange("p k t -> p t k"), AX_X, ALU.add).then_inc(sums_done, 1)
                dve.wait_ge(roots_done, n + 1)
                dve.reciprocal(rstd[:, :], ssum[:, :]).then_inc(recips_done, 1)
                dve.wait_ge(recips_done, n + 1)

            def norms(b, par, first):
                rms(2 * b)
                for k in range(KD):
                    m = dve.scalar_tensor_tensor(out[:, par, k, :], out[:, par, k, :], gains[:, 0, k:k + 1],
                                                 rstd[:, :], ALU.mult, ALU.mult)
                m.then_inc(scaled_done, 1)
                dve.wait_ge(x_loaded[par], landed(b, par))
                dve.wait_ge(scaled_done, b + 1)
                dve.tensor_tensor(x[:, par], x[:, par], out[:, par], ALU.add).then_inc(x1_done, 1)
                rms(2 * b + 1)
                for k in range(KD):
                    m = dve.scalar_tensor_tensor(out[:, par, k, :], x[:, par, k, :], gains[:, 1, k:k + 1],
                                                 rstd[:, :], ALU.mult, ALU.mult)
                m.then_inc(h2_done, 1)

            blocks(dve, norms)


def gate_and_up(nc, t):
    with ExitStack() as ctx:
        sbuf, psum, sem = allocators(nc, ctx)
        h_hi = sbuf("pd_h_hi", [P, KD, TOK], F32R)
        h_lo = sbuf("pd_h_lo", [P, KD, TOK], F32R)
        h_raw = sbuf("pd_h", [P, 2, KD, TB], F32)
        w_raw = sbuf("pd_w", [P, 2, KD * P], F32)
        w_hi = sbuf("pd_whi", [P, 2, KD * P], F32R)
        w_lo = sbuf("pd_wlo", [P, 2, KD * P], F32R)
        gate = sbuf("pd_gate", [P, TOK], F32)
        act_row = sbuf("pd_act", [P, TOK], F32)
        prod_ps = psum("pd_prod", [P, NB, 512], F32)
        h_loaded = (sem("pd_h_loaded0"), sem("pd_h_loaded1"))
        h_hi_done = sem("pd_h_hi_done")
        h_lo_done = sem("pd_h_lo_done")
        w_loaded = (sem("pd_w_loaded0"), sem("pd_w_loaded1"))
        w_hi_done = sem("pd_w_hi_done")
        w_lo_done = sem("pd_w_lo_done")
        prod_done = sem("pd_prod_done")
        gates_done = sem("pd_gates_done")
        acts_done = sem("pd_acts_done")
        stored = sem("pd_stored")
        block = ctx.enter_context(nc.Block())

        @block.sync
        def _(sp):
            def load_w(c, par):
                sp.dma_start(w_raw[:, par, :], t["w_gate_up"][c]).then_inc(w_loaded[par], 16)

            load_w(0, 0)
            for b in range(NB):
                if b >= 2:
                    sp.wait_ge(h_lo_done, b - 1)
                sp.dma_start(h_raw[:, b % 2], t["h2"][b]).then_inc(h_loaded[b % 2], 16)
            load_w(1, 1)

            def hidden_tile(j, more):
                if more:
                    sp.wait_ge(w_lo_done, 2 * j + 1)
                    load_w(2 * j + 2, 0)
                    sp.wait_ge(w_lo_done, 2 * j + 2)
                    load_w(2 * j + 3, 1)
                sp.wait_ge(acts_done, j * NB + NB)
                sp.dma_start(t["a"][j], act_row[:, :]).then_inc(stored, 16)

            with sp.Fori(0, KF - 1) as j:
                hidden_tile(j, True)
            hidden_tile(KF - 1, False)
            sp.wait_ge(stored, 16 * KF)

        @block.gpsimd
        def _(pool):
            def split_lo(c, par):
                pool.wait_ge(w_hi_done, c + 1)
                pool.tensor_tensor(w_lo[:, par, :], w_raw[:, par, :], w_hi[:, par, :].bitcast(F32),
                                   ALU.subtract).then_inc(w_lo_done, 1)

            split_lo(0, 0)
            split_lo(1, 1)
            with pool.Fori(1, KF) as j:
                split_lo(2 * j, 0)
                split_lo(2 * j + 1, 1)

        @block.scalar
        def _(act):
            def split_hi(c, par):
                act.wait_ge(w_loaded[par], landed(c, par))
                if not isinstance(c, int):
                    act.wait_ge(prod_done, (c - 1) * NB)
                act.activation(w_hi[:, par, :], w_raw[:, par, :], ACT.Copy).then_inc(w_hi_done, 1)

            split_hi(0, 0)
            for b in range(NB):
                act.wait_ge(h_loaded[b % 2], 16 * (b // 2 + 1))
                act.activation(h_hi[:, :, b * TB:(b + 1) * TB], h_raw[:, b % 2], ACT.Copy).then_inc(h_hi_done, 1)
            split_hi(1, 1)

            def hidden_tile(j, more):
                act.wait_ge(acts_done, j * NB)
                for b in range(NB):
                    act.wait_ge(prod_done, j * (2 * NB) + (b + 1))
                    act.activation(gate[:, b * TB:(b + 1) * TB], prod_ps[:, b, 0:TB], ACT.Silu).then_inc(gates_done, 1)
                if more:
                    split_hi(2 * j + 2, 0)
                    split_hi(2 * j + 3, 1)

            with act.Fori(0, KF - 1) as j:
                hidden_tile(j, True)
            hidden_tile(KF - 1, False)

        @block.tensor
        def _(pe):
            def project(c, par, read, count, waited):
                pe.wait_ge(w_lo_done, c + 1)
                for b in range(NB):
                    if waited:
                        pe.wait_ge(read, count + (b + 1))
                    else:
                        pe.wait_ge(h_lo_done, b + 1)
                    cols = slice(b * TB, (b + 1) * TB)
                    for k in range(KD):
                        w = slice(k * P, (k + 1) * P)
                        mm = hi_lo_products(pe, prod_ps[:, b, 0:TB], w_hi[:, par, w], w_lo[:, par, w],
                                            h_hi[:, k, cols], h_lo[:, k, cols], k == 0, k == KD - 1)
                    mm.then_inc(prod_done, 1)

            project(0, 0, None, 0, False)
            project(1, 1, gates_done, 0, True)
            with pe.Fori(1, KF) as j:
                project(2 * j, 0, acts_done, j * NB - NB, True)
                project(2 * j + 1, 1, gates_done, j * NB, True)

        @block.vector
        def _(dve):
            for b in range(NB):
                cols = slice(b * TB, (b + 1) * TB)
                dve.wait_ge(h_hi_done, b + 1)
                dve.tensor_tensor(h_lo[:, :, cols], h_raw[:, b % 2], h_hi[:, :, cols].bitcast(F32),
                                  ALU.subtract).then_inc(h_lo_done, 1)
            with dve.Fori(0, KF) as j:
                dve.wait_ge(stored, j * 16)
                for b in range(NB):
                    cols = slice(b * TB, (b + 1) * TB)
                    dve.wait_ge(prod_done, j * (2 * NB) + (NB + b + 1))
                    dve.wait_ge(gates_done, j * NB + (b + 1))
                    dve.tensor_tensor(act_row[:, cols], prod_ps[:, b, 0:TB], gate[:, cols],
                                      ALU.mult).then_inc(acts_done, 1)


KH = KF // 2


def wait_at_least(engine, semaphore, value):
    if not isinstance(value, int) or value > 0:
        engine.wait_ge(semaphore, value)


def down_projection(nc, t):
    with ExitStack() as ctx:
        sbuf, psum, sem = allocators(nc, ctx)
        a_raw = sbuf("pe_a", [P, KF, TB], F32)
        a_hi = sbuf("pe_ahi", [P, KF, TB], F32R)
        a_lo = sbuf("pe_alo", [P, KF, TB], F32R)
        w_raw = sbuf("pe_w", [P, 2, KH * P], F32)
        w_hi = sbuf("pe_whi", [P, 4, KH * P], F32R)
        w_lo = sbuf("pe_wlo", [P, 4, KH * P], F32R)
        x = sbuf("pe_x", [P, KD, TB], F32)
        out = sbuf("pe_out", [P, KD, TB], F32)
        sq = sbuf("pe_sq", [P, KD, TB], F32)
        ssum = sbuf("pe_ssum", [P, TB], F32)
        rstd = sbuf("pe_rstd", [P, TB], F32)
        gain = sbuf("pe_gain", [P, KD], F32)
        eps = sbuf("pe_eps", [P, 1], F32)
        ones_mean = sbuf("pe_ones", [P, P], F32)
        prod_ps = psum("pe_prod", [P, 4, 512], F32)
        mean_ps = psum("pe_mean", [P, 512], F32)
        gain_loaded = sem("pe_gain_loaded")
        consts_set = sem("pe_consts_set")
        a_loaded = sem("pe_a_loaded")
        a_hi_done = sem("pe_a_hi_done")
        a_lo_done = sem("pe_a_lo_done")
        a_read = sem("pe_a_read")
        w_loaded = (sem("pe_w_loaded0"), sem("pe_w_loaded1"))
        w_hi_done = sem("pe_w_hi_done")
        w_lo_done = sem("pe_w_lo_done")
        w_half_read = sem("pe_w_half_read")
        x_loaded = sem("pe_x_loaded")
        prod_done = sem("pe_prod_done")
        bank_read = sem("pe_bank_read")
        squares_done = sem("pe_squares_done")
        sums_done = sem("pe_sums_done")
        means_done = sem("pe_means_done")
        roots_done = sem("pe_roots_done")
        recips_done = sem("pe_recips_done")
        scaled_done = sem("pe_scaled_done")
        x2_done = sem("pe_x2_done")
        stored = sem("pe_stored")
        block = ctx.enter_context(nc.Block())

        @block.sync
        def _(sp):
            sp.dma_start(gain[:, :], t["g_post_ffn"]).then_inc(gain_loaded, 16)

            def load_w(n, half, j):
                wait_at_least(sp, w_lo_done, 2 * n + (half - 1))
                sp.dma_start(w_raw[:, half, :], t["w_down"][j][:, half * KH * P:(half + 1) * KH * P]
                             ).then_inc(w_loaded[half], 16)

            def load_a(b):
                wait_at_least(sp, a_lo_done, b * KH)
                sp.dma_start(a_raw[:, :, :], t["a"].rearrange("k p t -> p k t")[:, :, bass.ds(b * TB, TB)]
                             ).then_inc(a_loaded, 16)

            def store_x2(b):
                sp.wait_ge(x2_done, b + 1)
                sp.dma_start(t["x2"][b], x[:, :, :]).then_inc(stored, 16)

            def block_io(b, more):
                for j in range(KD if more else KD - 1):
                    load_w(b * KD + (j + 1), 0, (j + 1) % KD)
                    load_w(b * KD + (j + 1), 1, (j + 1) % KD)
                    if j == 1 and more:
                        load_a(b + 1)
                    if j == 4:
                        if not isinstance(b, int) or b:
                            store_x2(b - 1)
                            sp.wait_ge(stored, b * 16)
                        sp.dma_start(x[:, :, :], t["x1"][b]).then_inc(x_loaded, 16)

            load_w(0, 0, 0)
            load_w(0, 1, 0)
            load_a(0)
            block_io(0, True)
            with sp.Fori(1, NB - 1) as b:
                block_io(b, True)
            block_io(NB - 1, False)
            store_x2(NB - 1)
            sp.wait_ge(stored, 16 * NB)

        @block.gpsimd
        def _(pool):
            pool.memset(ones_mean[:, :], 1.0 / D).then_inc(consts_set, 1)
            pool.memset(eps[:, :], EPS).then_inc(consts_set, 1)
            with pool.Fori(0, KD * NB // 2) as m:
                for q in range(4):
                    pool.wait_ge(w_hi_done, 4 * m + (q + 1))
                    pool.tensor_tensor(w_lo[:, q, :], w_raw[:, q % 2, :], w_hi[:, q, :].bitcast(F32),
                                       ALU.subtract).then_inc(w_lo_done, 1)

        @block.scalar
        def _(act):
            act.wait_ge(consts_set, 2)

            def split_w(n, half, j):
                q = 2 * (j % 2) + half
                act.wait_ge(w_loaded[half], n * 16 + 16)
                wait_at_least(act, prod_done if half else w_half_read, n - 1)
                act.activation(w_hi[:, q, :], w_raw[:, half, :], ACT.Copy).then_inc(w_hi_done, 1)

            def split_a(b):
                act.wait_ge(a_loaded, b * 16 + 16)
                for g in range(KH):
                    if g < KH - 1:
                        wait_at_least(act, a_read, b * (KH - 1) + (g + 2 - KH))
                    else:
                        wait_at_least(act, prod_done, b * KD)
                    act.activation(a_hi[:, 2 * g:2 * g + 2, :], a_raw[:, 2 * g:2 * g + 2, :], ACT.Copy).then_inc(a_hi_done, 1)

            def block_work(b, more):
                for j in range(KD):
                    if more or j < KD - 1:
                        split_w(b * KD + (j + 1), 0, j + 1)
                        split_w(b * KD + (j + 1), 1, j + 1)
                    if more and j == KD - 1:
                        split_a(b + 1)
                    if j == 0:
                        wait_at_least(act, x2_done, b)
                    act.wait_ge(prod_done, b * KD + (j + 1))
                    act.activation(out[:, j, :], prod_ps[:, j % 4, 0:TB], ACT.Copy).then_inc(bank_read, 1)
                act.wait_ge(bank_read, b * KD + KD)
                act.activation(sq[:, :, :], out[:, :, :], ACT.Square).then_inc(squares_done, 1)
                act.wait_ge(means_done, b + 1)
                act.activation(ssum[:, :], mean_ps[:, 0:TB], ACT.Sqrt, bias=eps[:, 0:1]).then_inc(roots_done, 1)

            split_w(0, 0, 0)
            split_w(0, 1, 0)
            split_a(0)
            block_work(0, True)
            with act.Fori(1, NB - 1) as b:
                block_work(b, True)
            block_work(NB - 1, False)

        @block.tensor
        def _(pe):
            pe.wait_ge(consts_set, 2)

            def mean(b):
                pe.wait_ge(sums_done, b + 1)
                pe.matmul(mean_ps[:, 0:TB], ones_mean[:, :], ssum[:, :], start=True, stop=True).then_inc(means_done, 1)

            def block_products(b):
                for j in range(KD):
                    if j == 1 and not isinstance(b, int):
                        mean(b - 1)
                    wait_at_least(pe, bank_read, b * KD + (j - 3))
                    for k in range(KF):
                        if k % KH == 0:
                            pe.wait_ge(w_lo_done, b * (2 * KD) + (2 * j + k // KH + 1))
                        if j == 0 and k % 2 == 0:
                            pe.wait_ge(a_lo_done, b * KH + (k // 2 + 1))
                        q = 2 * (j % 2) + k // KH
                        w = slice(k % KH * P, (k % KH + 1) * P)
                        mm = hi_lo_products(pe, prod_ps[:, j % 4, 0:TB], w_hi[:, q, w], w_lo[:, q, w],
                                            a_hi[:, k, :], a_lo[:, k, :], k == 0, k == KF - 1)
                        if k == KH - 1:
                            mm.then_inc(w_half_read, 1)
                        if j == KD - 1 and k % 2 and k < KF - 1:
                            mm.then_inc(a_read, 1)
                    mm.then_inc(prod_done, 1)

            block_products(0)
            with pe.Fori(1, NB) as b:
                block_products(b)
            mean(NB - 1)

        @block.vector
        def _(dve):
            dve.wait_ge(gain_loaded, 16)

            def split_a(b):
                for g in range(KH):
                    pair = slice(2 * g, 2 * g + 2)
                    dve.wait_ge(a_hi_done, b * KH + (g + 1))
                    dve.tensor_tensor(a_lo[:, pair, :], a_raw[:, pair, :], a_hi[:, pair, :].bitcast(F32),
                                      ALU.subtract).then_inc(a_lo_done, 1)

            def norm(b):
                dve.wait_ge(squares_done, b + 1)
                dve.tensor_reduce(ssum[:, :], sq[:, :, :].rearrange("p k t -> p t k"), AX_X, ALU.add).then_inc(sums_done, 1)
                dve.wait_ge(roots_done, b + 1)
                dve.reciprocal(rstd[:, :], ssum[:, :]).then_inc(recips_done, 1)
                dve.wait_ge(recips_done, b + 1)
                for k in range(KD):
                    m = dve.scalar_tensor_tensor(out[:, k, :], out[:, k, :], gain[:, k:k + 1], rstd[:, :],
                                                 ALU.mult, ALU.mult)
                m.then_inc(scaled_done, 1)
                dve.wait_ge(x_loaded, b * 16 + 16)
                dve.wait_ge(scaled_done, b + 1)
                dve.tensor_tensor(x[:, :, :], x[:, :, :], out[:, :, :], ALU.add).then_inc(x2_done, 1)

            split_a(0)
            with dve.Fori(0, NB - 1) as b:
                split_a(b + 1)
                norm(b)
            norm(NB - 1)


def embedding_gate(nc, t):
    with ExitStack() as ctx:
        sbuf, psum, sem = allocators(nc, ctx)
        w_raw = sbuf("pf_w", [P, 2, KD * P], F32)
        wg_hi = sbuf("pf_wghi", [P, KD, KD * P], F32R)
        wg_lo = sbuf("pf_wglo", [P, KD, KD * P], F32R)
        wp_hi = sbuf("pf_wphi", [P, KD, KP * P], F32R)
        wp_lo = sbuf("pf_wplo", [P, KD, KP * P], F32R)
        x = sbuf("pf_x", [P, 2, KD, TB], F32)
        x_hi = sbuf("pf_xhi", [P, KD, TB], F32R)
        x_lo = sbuf("pf_xlo", [P, KD, TB], F32R)
        p_raw = sbuf("pf_p", [P, KP, TB], F32)
        p_hi = sbuf("pf_phi", [P, KP, TB], F32R)
        p_lo = sbuf("pf_plo", [P, KP, TB], F32R)
        gated = sbuf("pf_gated", [P, 2, KD, TB], F32)
        sq = sbuf("pf_sq", [P, KD, TB], F32)
        ssum = sbuf("pf_ssum", [P, TB], F32)
        rstd = sbuf("pf_rstd", [P, TB], F32)
        gain = sbuf("pf_gain", [P, KD], F32)
        eps = sbuf("pf_eps", [P, 1], F32)
        ones_mean = sbuf("pf_ones", [P, P], F32)
        proj_ps = psum("pf_proj", [P, 4, 512], F32)
        gate_ps = psum("pf_gate", [P, 2, 512], F32)
        mean_ps = psum("pf_mean", [P, 512], F32)
        gain_loaded = sem("pf_gain_loaded")
        consts_set = sem("pf_consts_set")
        w_loaded = (sem("pf_w_loaded0"), sem("pf_w_loaded1"))
        w_hi_done = sem("pf_w_hi_done")
        w_lo_done = sem("pf_w_lo_done")
        x_loaded = (sem("pf_x_loaded0"), sem("pf_x_loaded1"))
        x_hi_done = sem("pf_x_hi_done")
        x_lo_done = sem("pf_x_lo_done")
        x_read = sem("pf_x_read")
        p_loaded = sem("pf_p_loaded")
        p_hi_done = sem("pf_p_hi_done")
        p_lo_done = sem("pf_p_lo_done")
        proj_done = sem("pf_proj_done")
        gate_done = sem("pf_gate_done")
        sigmoids_done = sem("pf_sigmoids_done")
        gated_done = sem("pf_gated_done")
        squares_done = sem("pf_squares_done")
        sums_done = sem("pf_sums_done")
        means_done = sem("pf_means_done")
        roots_done = sem("pf_roots_done")
        recips_done = sem("pf_recips_done")
        scaled_done = sem("pf_scaled_done")
        y_done = sem("pf_y_done")
        stored = (sem("pf_stored0"), sem("pf_stored1"))
        block = ctx.enter_context(nc.Block())
        WIDTHS = (KP * P, KD * P)

        @block.sync
        def _(sp):
            sp.dma_start(gain[:, :], t["g_ple"]).then_inc(gain_loaded, 16)

            def load_w(j, kind):
                wait_at_least(sp, w_lo_done, 2 * j + (kind - 1))
                src = t["w_ple_gate" if kind else "w_ple_proj"]
                sp.dma_start(w_raw[:, kind, 0:WIDTHS[kind]], src[j]).then_inc(w_loaded[kind], 16)

            def load_p(b):
                wait_at_least(sp, p_lo_done, b)
                sp.dma_start(p_raw[:, :, :], t["pT"][b]).then_inc(p_loaded, 16)

            def load_x(b, par):
                sp.dma_start(x[:, par], t["x2"][b]).then_inc(x_loaded[par], 16)

            load_p(0)
            load_x(0, 0)
            load_w(0, 0)
            load_w(0, 1)
            with sp.Fori(1, KD) as j:
                load_w(j, 0)
                load_w(j, 1)
            load_p(1)
            load_x(1, 1)
            for b in range(NB):
                par = b % 2
                if b < NB - 2:
                    load_p(b + 2)
                sp.wait_ge(y_done, b + 1)
                sp.dma_start(t["y"][b], x[:, par]).then_inc(stored[par], 16)
                if b < NB - 2:
                    sp.wait_ge(stored[par], landed(b, par))
                    load_x(b + 2, par)
            for par in range(2):
                sp.wait_ge(stored[par], 16 * ((NB + 1 - par) // 2))

        @block.gpsimd
        def _(pool):
            pool.memset(ones_mean[:, :], 1.0 / D).then_inc(consts_set, 1)
            pool.memset(eps[:, :], EPS).then_inc(consts_set, 1)

            def split_block(b, par, first):
                pool.wait_ge(p_hi_done, b + 1)
                pool.tensor_tensor(p_lo[:, :, :], p_raw[:, :, :], p_hi[:, :, :].bitcast(F32), ALU.subtract).then_inc(p_lo_done, 1)
                for k in range(KD):
                    pool.wait_ge(x_hi_done, b * KD + (k + 1))
                    pool.tensor_tensor(x_lo[:, k, :], x[:, par, k, :], x_hi[:, k, :].bitcast(F32),
                                       ALU.subtract).then_inc(x_lo_done, 1)

            split_block(0, 0, True)
            with pool.Fori(0, KD) as j:
                for kind, (hi, lo) in enumerate(((wp_hi, wp_lo), (wg_hi, wg_lo))):
                    pool.wait_ge(w_hi_done, 2 * j + (kind + 1))
                    pool.tensor_tensor(lo[:, bass.ds(j, 1), :], w_raw[:, kind:kind + 1, 0:WIDTHS[kind]],
                                       hi[:, bass.ds(j, 1), :].bitcast(F32), ALU.subtract).then_inc(w_lo_done, 1)
            with pool.Fori(1, (NB + 1) // 2) as j:
                split_block(2 * j - 1, 1, False)
                split_block(2 * j, 0, False)

        @block.scalar
        def _(act):
            act.wait_ge(consts_set, 2)

            def split_block(b, par):
                act.wait_ge(p_loaded, b * 16 + 16)
                wait_at_least(act, proj_done, b * KD)
                act.activation(p_hi[:, :, :], p_raw[:, :, :], ACT.Copy).then_inc(p_hi_done, 1)
                act.wait_ge(x_loaded[par], landed(b, par))
                for k in range(KD):
                    if k < KD - 1:
                        wait_at_least(act, x_read, b * (KD - 1) + (k + 2 - KD))
                    else:
                        wait_at_least(act, gate_done, b * KD)
                    act.activation(x_hi[:, k, :], x[:, par, k, :], ACT.Copy).then_inc(x_hi_done, 1)

            def block_work(b, par, more):
                if not isinstance(b, int) or b >= 2:
                    act.wait_ge(y_done, b - 1)
                for j in range(KD):
                    if j == KD - 1 and more:
                        split_block(b + 1, 1 - par)
                    act.wait_ge(gate_done, b * KD + (j + 1))
                    act.activation(gated[:, par, j, :], gate_ps[:, j % 2, 0:TB], ACT.Sigmoid).then_inc(sigmoids_done, 1)
                act.wait_ge(gated_done, b * KD + KD)
                act.activation(sq[:, :, :], gated[:, par], ACT.Square).then_inc(squares_done, 1)
                act.wait_ge(means_done, b + 1)
                act.activation(ssum[:, :], mean_ps[:, 0:TB], ACT.Sqrt, bias=eps[:, 0:1]).then_inc(roots_done, 1)

            split_block(0, 0)
            with act.Fori(0, KD) as j:
                for kind, hi in enumerate((wp_hi, wg_hi)):
                    act.wait_ge(w_loaded[kind], j * 16 + 16)
                    act.activation(hi[:, bass.ds(j, 1), :], w_raw[:, kind:kind + 1, 0:WIDTHS[kind]], ACT.Copy).then_inc(w_hi_done, 1)
            block_work(0, 0, True)
            with act.Fori(1, NB // 2) as j:
                block_work(2 * j - 1, 1, True)
                block_work(2 * j, 0, True)
            block_work(NB - 2, 1, True)
            block_work(NB - 1, 0, False)

        @block.tensor
        def _(pe):
            pe.wait_ge(consts_set, 2)
            LEAD = 2

            def mean(b):
                pe.wait_ge(sums_done, b + 1)
                pe.matmul(mean_ps[:, 0:TB], ones_mean[:, :], ssum[:, :], start=True, stop=True).then_inc(means_done, 1)

            def project(b, j, first):
                if first:
                    pe.wait_ge(w_lo_done, 2 * j + 1)
                wait_at_least(pe, gated_done, b * KD + (j - 3))
                for k in range(KP):
                    w = slice(k * P, (k + 1) * P)
                    mm = hi_lo_products(pe, proj_ps[:, j % 4, 0:TB], wp_hi[:, j, w], wp_lo[:, j, w],
                                        p_hi[:, k, :], p_lo[:, k, :], k == 0, k == KP - 1)
                mm.then_inc(proj_done, 1)

            def block_products(b, par, first):
                pe.wait_ge(p_lo_done, b + 1)
                for j in range(LEAD):
                    project(b, j, first)
                for j in range(KD):
                    if j == 2 and not first:
                        mean(b - 1)
                    if j + LEAD < KD:
                        project(b, j + LEAD, first)
                    if first:
                        pe.wait_ge(w_lo_done, 2 * j + 2)
                    wait_at_least(pe, sigmoids_done, b * KD + (j - 1))
                    for k in range(KD):
                        if j == 0:
                            pe.wait_ge(x_lo_done, b * KD + (k + 1))
                        w = slice(k * P, (k + 1) * P)
                        mm = hi_lo_products(pe, gate_ps[:, j % 2, 0:TB], wg_hi[:, j, w], wg_lo[:, j, w],
                                            x_hi[:, k, :], x_lo[:, k, :], k == 0, k == KD - 1)
                        if j == KD - 1 and k < KD - 1:
                            mm.then_inc(x_read, 1)
                    mm.then_inc(gate_done, 1)

            blocks(pe, block_products)
            mean(NB - 1)

        @block.vector
        def _(dve):
            dve.wait_ge(gain_loaded, 16)

            def block_work(b, par, first):
                for j in range(KD):
                    dve.wait_ge(proj_done, b * KD + (j + 1))
                    dve.wait_ge(sigmoids_done, b * KD + (j + 1))
                    dve.tensor_tensor(gated[:, par, j, :], proj_ps[:, j % 4, 0:TB], gated[:, par, j, :],
                                      ALU.mult).then_inc(gated_done, 1)
                dve.wait_ge(squares_done, b + 1)
                dve.tensor_reduce(ssum[:, :], sq[:, :, :].rearrange("p k t -> p t k"), AX_X, ALU.add).then_inc(sums_done, 1)
                dve.wait_ge(roots_done, b + 1)
                dve.reciprocal(rstd[:, :], ssum[:, :]).then_inc(recips_done, 1)
                dve.wait_ge(recips_done, b + 1)
                for k in range(KD):
                    m = dve.scalar_tensor_tensor(gated[:, par, k, :], gated[:, par, k, :], gain[:, k:k + 1],
                                                 rstd[:, :], ALU.mult, ALU.mult)
                m.then_inc(scaled_done, 1)
                dve.wait_ge(scaled_done, b + 1)
                dve.wait_ge(x_lo_done, b * KD + KD)
                dve.tensor_tensor(x[:, par], x[:, par], gated[:, par], ALU.add).then_inc(y_done, 1)

            blocks(dve, block_work)


def shift_caches(nc, t, shifted):
    with nc.Block() as block:

        @block.scalar
        def _(act):
            for b in range(NSAMP):
                for new, old in (("new_cache_k", "cache_k"), ("new_cache_v", "cache_v")):
                    act.dma_start(t[new][b, 0:PAST - 1], t[old][b, 1:PAST]).then_inc(shifted, 16)


def wait_for_caches(nc, shifted):
    with nc.Block() as block:

        @block.sync
        def _(sp):
            sp.wait_ge(shifted, 16 * 2 * NSAMP)


SCRATCH = {"dn": (12, P, S), "dn_samp": (12, P, NSAMP), "z": (4, P, TOK), "at4": (12, P, S), "at16": (12, P, S),
           "ba": (36, TOK), "bias_flat": (len(DILS), AH, FLAT), "U": (len(DILS), S, UROW), "mix": (KD, P, TOK),
           "x1": (NB, P, KD, TB), "h2": (NB, P, KD, TB), "a": (KF, P, TOK), "x2": (NB, P, KD, TB)}

RESULTS = {"y": (NB, P, KD, TB), "at": (12, P, TOK), "conv_tail": (12, P, 3), "conv_samp": (12, P, NSAMP, 3),
           "delta": (HEADS, P, P), "new_state": (NSAMP, HEADS, P, P),
           "new_cache_k": (NSAMP, PAST, AH * HD), "new_cache_v": (NSAMP, PAST, AH * HD)}


def build(nc, t):
    for name, shape in SCRATCH.items():
        t[name] = nc.dram_tensor("scratch_" + name, list(shape), F32, kind="Internal").ap()
    with nc.semaphore("caches_shifted") as shifted:
        bias_rows(nc, t)
        norm_and_input_projection(nc, t)
        delta_and_attention(nc, t)
        delta_samples(nc, t)
        merge_dilations(nc, t)
        attention_samples(nc, t)
        output_projection(nc, t)
        shift_caches(nc, t, shifted)
        gate_and_up(nc, t)
        down_projection(nc, t)
        embedding_gate(nc, t)
        wait_for_caches(nc, shifted)


def tiles_of(w, k, n):
    return np.ascontiguousarray(w.reshape(k, P, n, P).transpose(2, 1, 0, 3)).reshape(n, P, k * P)


def columns_of(g, k):
    return np.ascontiguousarray(g.reshape(k, P).T)


def blocks_of(prompt, sample, k):
    x = np.zeros((TOK, k * P), np.float32)
    x[:S] = prompt
    x[S:S + NSAMP] = sample
    return np.ascontiguousarray(x.reshape(NB, TB, k, P).transpose(0, 3, 2, 1)).reshape(NB, P, k, TB)


def layouts(i):
    dn_cols = (N_DN + N_Z) * P
    w_in = np.zeros((D, (NT + 1) * P), np.float32)
    w_in[:, :dn_cols] = i["w_in"][0][:, :dn_cols]
    w_in[:, dn_cols:NT * P] = i["w_in"][0][:, dn_cols + 2 * HEADS:]
    w_in[:, NT * P:NT * P + HEADS] = i["w_in"][0][:, dn_cols:dn_cols + HEADS]
    w_in[:, NT * P + 32:NT * P + 32 + HEADS] = i["w_in"][0][:, dn_cols + HEADS:dn_cols + 2 * HEADS]
    gate_up = i["w_gate_up"][0].reshape(D, 2, KF, P).transpose(0, 2, 1, 3).reshape(D, 2 * FF)
    return {
        "xT": blocks_of(i["x_prompt"][0], i["x_sample"][:, 0], KD),
        "pT": blocks_of(i["p_prompt"][0, 0], i["p_sample"][0, :, 0], KP),
        "w_in": tiles_of(w_in, KD, NT + 1),
        "conv_w": np.ascontiguousarray(i["conv_w"][0].reshape(4, N_DN, P).transpose(2, 1, 0)).reshape(P, 4 * N_DN),
        "cache_conv": np.ascontiguousarray(i["cache_conv"][0].reshape(NSAMP, 3, N_DN, P).transpose(2, 3, 0, 1)),
        "w_out": tiles_of(i["w_out"][0], KD, KD),
        "w_gate_up": tiles_of(gate_up, KD, 2 * KF),
        "w_down": tiles_of(i["w_down"][0], KF, KD),
        "w_ple_gate": tiles_of(i["w_ple_gate"][0], KD, KD),
        "w_ple_proj": tiles_of(i["w_ple_proj"][0], KP, KD),
        "g_pre_mix": columns_of(i["g_pre_mix"][0], KD),
        "g_post_mix": columns_of(i["g_post_mix"][0], KD),
        "g_pre_ffn": columns_of(i["g_pre_ffn"][0], KD),
        "g_post_ffn": columns_of(i["g_post_ffn"][0], KD),
        "g_ple": columns_of(i["g_ple"][0], KD),
        "g_dn_out": i["g_dn_out"][0].reshape(P, 1),
        "a_log": i["a_log"][0],
        "dt_bias": i["dt_bias"][0],
        "rel_bias": i["rel_bias"],
        "state": i["state_delta"][0],
        "cache_k": i["cache_win_k"][0].reshape(NSAMP, PAST, AH * HD),
        "cache_v": i["cache_win_v"][0].reshape(NSAMP, PAST, AH * HD),
        "consts": constant_tiles(),
        "buckets": bucket_tiles(),
        "head_mask": head_mask(),
    }


def kernel(**inputs):
    import concourse.bacc as bacc
    from concourse.bass_utils import run_bass_kernel_spmd

    nc = bacc.Bacc("TRN2", target_bir_lowering=False, num_devices=1)
    arrays, t = {}, {}
    for name, a in layouts({n: np.asarray(a) for n, a in inputs.items()}).items():
        arrays["in_" + name] = np.ascontiguousarray(a)
        t[name] = nc.dram_tensor("in_" + name, list(a.shape), F32, kind="ExternalInput").ap()
    for name, shape in RESULTS.items():
        t[name] = nc.dram_tensor("out_" + name, list(shape), F32, kind="ExternalOutput").ap()
    build(nc, t)
    result = run_bass_kernel_spmd(nc, [arrays], core_ids=[0]).results[0]
    r = {name: np.asarray(result["out_" + name]).reshape(shape) for name, shape in RESULTS.items()}

    y = r["y"].transpose(0, 3, 2, 1).reshape(TOK, D)
    k_prompt, v_prompt = (r["at"][4 * n:4 * n + 4, :, 0:S].reshape(AH * HD, S).T.reshape(1, 1, S, AH, HD) for n in (1, 2))
    channels = N_DN * P
    return (y[:S].reshape(1, S, D), y[S:S + NSAMP].reshape(NSAMP, 1, D),
            r["conv_tail"].reshape(channels, 3).T.reshape(1, 1, 3, channels),
            r["delta"].reshape(1, 1, HEADS, DK, DK), k_prompt, v_prompt,
            r["conv_samp"].transpose(2, 3, 0, 1).reshape(1, NSAMP, 3, channels),
            r["new_state"].reshape(1, NSAMP, HEADS, DK, DK),
            r["new_cache_k"].reshape(1, NSAMP, PAST, AH, HD), r["new_cache_v"].reshape(1, NSAMP, PAST, AH, HD))
```

```python
from contextlib import ExitStack

import numpy as np

import concourse.bass as bass
from concourse import mybir

F32 = mybir.dt.float32
F32R = mybir.dt.float32r
ALU = mybir.AluOpType
ACT = mybir.ActivationFunctionType
AX_X = mybir.AxisListType.X

P = 128
D = 1024
S = 2048
NSAMP = 8
TB = 412
NB = 5
TOK = NB * TB
KD = D // P
HEADS, DK = 4, 128
AH, HD = 8, 64
FF = 2816
KF = FF // P
PLE = 256
KP = PLE // P
EPS = 1e-6
BIG = 1e30
DILS = (1, 4, 16)
UROW = AH * HD + 2 * AH
PAST = 1024


def allocators(nc, ctx):
    semaphores = []

    def sbuf(name, shape, dtype):
        return ctx.enter_context(nc.sbuf_tensor(name, shape, dtype))

    def psum(name, shape, dtype):
        return ctx.enter_context(nc.psum_tensor(name, shape, dtype))

    def sem(name):
        semaphores.append(nc.alloc_semaphore(name))
        return semaphores[-1]

    def clear():
        nc.clear_and_free_semaphores(semaphores)
        nc.all_engine_barrier()

    ctx.callback(clear)
    return sbuf, psum, sem


def landed(tile, par, per_tile=1):
    return (tile - par) * (8 * per_tile) + 16 * per_tile


def hi_lo_products(pe, out, w_hi, w_lo, a_hi, a_lo, first, last):
    pe.matmul(out, w_hi, a_hi, start=first, stop=False)
    pe.matmul(out, w_lo, a_hi, start=False, stop=False)
    return pe.matmul(out, w_hi, a_lo, start=False, stop=last)


N_DN, N_Z, N_AT = 12, 4, 12
NT = N_DN + N_Z + N_AT
ROW = 2088
SAMP0 = 3 + S


def norm_and_input_projection(nc, t):
    with ExitStack() as ctx:
        sbuf, psum, sem = allocators(nc, ctx)
        h_hi = sbuf("pa_h_hi", [P, KD, TOK], F32R)
        h_lo = sbuf("pa_h_lo", [P, KD, TOK], F32R)
        work = sbuf("pa_work", [P, 6 * ROW], F32)
        w_raw = sbuf("pa_w", [P, 2, KD * P], F32)
        w_hi = sbuf("pa_whi", [P, 2, KD * P], F32R)
        w_lo = sbuf("pa_wlo", [P, 2, KD * P], F32R)
        gain = sbuf("pa_gain", [P, KD], F32)
        eps = sbuf("pa_eps", [P, 1], F32)
        ones_mean = sbuf("pa_ones", [P, P], F32)
        conv_w = sbuf("pa_convw", [P, N_DN * 4], F32)
        mean_ps = psum("pa_mean", [P, 512], F32)
        proj_ps = psum("pa_proj", [P, NB, 512], F32)
        const_loaded = sem("pa_const_loaded")
        consts_set = sem("pa_consts_set")
        x_loaded0 = sem("pa_x_loaded0")
        x_loaded1 = sem("pa_x_loaded1")
        squares_done = sem("pa_squares_done")
        sums_done = sem("pa_sums_done")
        means_done = sem("pa_means_done")
        roots_done = sem("pa_roots_done")
        recips_done = sem("pa_recips_done")
        h_done = sem("pa_h_done")
        h_hi_done = sem("pa_h_hi_done")
        h_lo_done = sem("pa_h_lo_done")
        zeros_set = sem("pa_zeros_set")
        w_loaded0 = sem("pa_w_loaded0")
        w_loaded1 = sem("pa_w_loaded1")
        w_hi_done = sem("pa_w_hi_done")
        w_lo_done = sem("pa_w_lo_done")
        proj_done = sem("pa_proj_done")
        evacuated = sem("pa_evacuated")
        gates_done = sem("pa_gates_done")
        taps_done = sem("pa_taps_done")
        conv_done = sem("pa_conv_done")
        silu_done = sem("pa_silu_done")
        perm4_done = sem("pa_perm4_done")
        perm16_done = sem("pa_perm16_done")
        ctx_loaded0 = sem("pa_ctx_loaded0")
        ctx_loaded1 = sem("pa_ctx_loaded1")
        dn_stored0 = sem("pa_dn_stored0")
        dn_stored1 = sem("pa_dn_stored1")
        z_stored0 = sem("pa_z_stored0")
        z_stored1 = sem("pa_z_stored1")
        at_stored0 = sem("pa_at_stored0")
        at_stored1 = sem("pa_at_stored1")
        block = ctx.enter_context(nc.Block())
        x_loaded = (x_loaded0, x_loaded1)
        w_loaded = (w_loaded0, w_loaded1)
        ctx_loaded = (ctx_loaded0, ctx_loaded1)
        dn_stored = (dn_stored0, dn_stored1)
        z_stored = (z_stored0, z_stored1)
        at_stored = (at_stored0, at_stored1)
        BLK = KD * TB
        xb = [work[:, i * BLK:(i + 1) * BLK].rearrange("p (k t) -> p k t", k=KD) for i in range(2)]
        sq = work[:, 2 * BLK:3 * BLK]
        ssum, std, rstd = (work[:, 3 * BLK + i * TB:3 * BLK + (i + 1) * TB] for i in range(3))
        raw = [work[:, i * ROW:(i + 1) * ROW] for i in range(2)]
        res = [work[:, (2 + i) * ROW:(3 + i) * ROW] for i in range(2)]
        r16 = [work[:, (4 + i) * ROW:(5 + i) * ROW] for i in range(2)]
        A0 = N_DN + N_Z
        CONV_COLS = SAMP0 + 4 * NSAMP - 3

        def samples(row, first, n):
            return row[:, SAMP0:SAMP0 + 4 * NSAMP].rearrange("p (b j) -> p b j", j=4)[:, :, first:first + n]

        @block.sync
        def _(sp):
            sp.dma_start(gain[:, :], t["g_pre_mix"]).then_inc(const_loaded, 16)
            sp.dma_start(conv_w[:, :], t["conv_w"]).then_inc(const_loaded, 16)

            def load_w(c, par):
                sp.dma_start(w_raw[:, par, :], t["w_in"][c]).then_inc(w_loaded[par], 16)

            for b in range(NB):
                if b >= 2:
                    sp.wait_ge(h_lo_done, b - 1)
                sp.dma_start(xb[b % 2], t["xT"][b]).then_inc(x_loaded[b % 2], 16)
                if b == 0:
                    load_w(0, 0)

            def load_ctx(c, par):
                sp.dma_start(samples(raw[par], 0, 3), t["cache_conv"][c]).then_inc(ctx_loaded[par], 16)

            load_w(1, 1)
            sp.wait_ge(h_lo_done, NB)
            load_ctx(0, 0)
            load_ctx(1, 1)

            def conv_tile(c, par, last):
                sp.wait_ge(w_lo_done, c + 1)
                load_w(c + 2, par)
                sp.wait_ge(silu_done, c + 1)
                sp.dma_start(t["dn"][c], res[par][:, 0:S]).then_inc(dn_stored[par], 16)
                sp.dma_start(t["dn_samp"][c], samples(res[par], 0, 1), allow_slow_non_contiguous=True).then_inc(dn_stored[par], 16)
                sp.dma_start(t["conv_tail"][c], raw[par][:, S:S + 3]).then_inc(dn_stored[par], 16)
                sp.dma_start(t["conv_samp"][c], samples(raw[par], 1, 3)).then_inc(dn_stored[par], 16)
                if not last:
                    sp.wait_ge(dn_stored[par], landed(c, par, 4))
                    load_ctx(c + 2, par)

            with sp.Fori(0 // 2, (N_DN - 2) // 2) as j:
                i = 2 * j
                conv_tile(i, 0, False)
                conv_tile(i + 1, 1, False)
            conv_tile(N_DN - 2, 0, True)
            conv_tile(N_DN - 1, 1, True)

            def gate_tile(c, par):
                sp.wait_ge(w_lo_done, c + 1)
                load_w(c + 2, par)
                sp.wait_ge(gates_done, (c - (N_DN - 1)) * NB)
                sp.dma_start(t["z"][c - N_DN], res[par][:, 0:TOK]).then_inc(z_stored[par], 16)

            with sp.Fori(N_DN // 2, A0 // 2) as j:
                i = 2 * j
                gate_tile(i, 0)
                gate_tile(i + 1, 1)

            def attn_tile(c, par, more):
                sp.wait_ge(w_lo_done, c + 1)
                if more:
                    load_w(c + 2, par)
                sp.wait_ge(evacuated, (c - (N_Z - 1)) * NB)
                sp.dma_start(t["at"][c - A0], raw[par][:, 0:TOK]).then_inc(at_stored[par], 16)
                sp.wait_ge(perm4_done, c - (A0 - 1))
                sp.dma_start(t["at4"][c - A0], res[par][:, 0:S]).then_inc(at_stored[par], 16)
                sp.wait_ge(perm16_done, c - (A0 - 1))
                sp.dma_start(t["at16"][c - A0], r16[par][:, 0:S]).then_inc(at_stored[par], 16)

            with sp.Fori(A0 // 2, (NT - 2) // 2) as j:
                i = 2 * j
                attn_tile(i, 0, True)
                attn_tile(i + 1, 1, True)
            attn_tile(NT - 2, 0, True)
            attn_tile(NT - 1, 1, False)
            sp.wait_ge(evacuated, (NT + 1 - N_Z) * NB)
            sp.dma_start(t["ba"], raw[0][0:36, 0:TOK]).then_inc(at_stored[0], 16)
            for par in range(2):
                sp.wait_ge(dn_stored[par], 64 * (N_DN // 2))
                sp.wait_ge(z_stored[par], 16 * (N_Z // 2))
                sp.wait_ge(at_stored[par], 48 * (N_AT // 2) + (0 if par else 16))

        @block.gpsimd
        def _(pool):
            pool.memset(ones_mean[:, :], 1.0 / D).then_inc(consts_set, 1)
            pool.memset(eps[:, :], EPS).then_inc(consts_set, 1)

            def split_lo(c, par):
                pool.wait_ge(w_hi_done, c + 1)
                pool.tensor_tensor(w_lo[:, par, :], w_raw[:, par, :], w_hi[:, par, :].bitcast(F32),
                                   ALU.subtract).then_inc(w_lo_done, 1)

            split_lo(0, 0)
            for b in range(NB):
                cols = slice(b * TB, (b + 1) * TB)
                pool.wait_ge(h_hi_done, b + 1)
                pool.tensor_tensor(h_lo[:, :, cols], xb[b % 2], h_hi[:, :, cols].bitcast(F32),
                                   ALU.subtract).then_inc(h_lo_done, 1)

            split_lo(1, 1)
            with pool.Fori(1, NT // 2) as j:
                i = 2 * j
                split_lo(i, 0)
                split_lo(i + 1, 1)
            split_lo(NT, 0)

        @block.scalar
        def _(act):
            act.wait_ge(consts_set, 2)

            def split_hi(c, par, first):
                act.wait_ge(w_loaded[par], landed(c, par))
                if not first:
                    act.wait_ge(proj_done, (c - 1) * NB)
                act.activation(w_hi[:, par, :], w_raw[:, par, :], ACT.Copy).then_inc(w_hi_done, 1)

            split_hi(0, 0, True)

            def square(b):
                act.wait_ge(x_loaded[b % 2], 16 * (b // 2 + 1))
                if b:
                    act.wait_ge(sums_done, b)
                act.activation(sq, xb[b % 2].rearrange("p k t -> p (k t)"), ACT.Square).then_inc(squares_done, 1)

            square(0)
            for b in range(NB):
                act.wait_ge(means_done, b + 1)
                if b:
                    act.wait_ge(recips_done, b)
                act.activation(std, mean_ps[:, 0:TB], ACT.Sqrt, bias=eps[:, 0:1]).then_inc(roots_done, 1)
                if b + 1 < NB:
                    square(b + 1)
                act.wait_ge(h_done, b + 1)
                act.activation(h_hi[:, :, b * TB:(b + 1) * TB], xb[b % 2], ACT.Copy).then_inc(h_hi_done, 1)

            split_hi(1, 1, True)

            def conv_tile(c, par):
                split_hi(c + 2, par, False)
                act.wait_ge(conv_done, c + 1)
                act.activation(res[par][:, 0:CONV_COLS], res[par][:, 0:CONV_COLS], ACT.Silu).then_inc(silu_done, 1)

            with act.Fori(0 // 2, N_DN // 2) as j:
                i = 2 * j
                conv_tile(i, 0)
                conv_tile(i + 1, 1)

            def gate_tile(c, par, first):
                if first:
                    act.wait_ge(dn_stored[par], 64 * (N_DN // 2))
                else:
                    act.wait_ge(z_stored[par], landed(c - N_DN - 2, par))
                for b in range(NB):
                    act.wait_ge(proj_done, c * NB + (b + 1))
                    act.activation(res[par][:, b * TB:(b + 1) * TB], proj_ps[:, b, 0:TB],
                                   ACT.Silu).then_inc(gates_done, 1)
                split_hi(c + 2, par, False)

            for c in range(N_DN, A0):
                gate_tile(c, c % 2, c < N_DN + 2)

            def attn_tile(c, par, more, first):
                if more:
                    split_hi(c + 2, par, False)
                act.wait_ge(evacuated, (c - (N_Z - 1)) * NB)
                if not first:
                    act.wait_ge(at_stored[par], landed(c - A0 - 2, par, 3))
                act.activation(r16[par][:, 0:S].rearrange("p (r m) -> p r m", r=16),
                               raw[par][:, 0:S].rearrange("p (m r) -> p r m", r=16),
                               ACT.Copy).then_inc(perm16_done, 1)

            attn_tile(A0, 0, True, True)
            attn_tile(A0 + 1, 1, True, True)
            with act.Fori((A0 + 2) // 2, (NT - 2) // 2) as j:
                i = 2 * j
                attn_tile(i, 0, True, False)
                attn_tile(i + 1, 1, True, False)
            attn_tile(NT - 2, 0, True, False)
            attn_tile(NT - 1, 1, False, False)

        @block.tensor
        def _(pe):
            pe.wait_ge(consts_set, 2)

            def mean(b):
                pe.wait_ge(sums_done, b + 1)
                if b:
                    pe.wait_ge(roots_done, b)
                pe.matmul(mean_ps[:, 0:TB], ones_mean[:, :], ssum, start=True, stop=True).then_inc(means_done, 1)

            def project(c, par, read, before):
                pe.wait_ge(w_lo_done, c + 1)
                for b in range(NB):
                    if read is None:
                        if b + 2 < NB:
                            mean(b + 2)
                        pe.wait_ge(h_lo_done, b + 1)
                    if read is not None:
                        pe.wait_ge(read, (c - (before + 1)) * NB + (b + 1))
                    cols = slice(b * TB, (b + 1) * TB)
                    for k in range(KD):
                        w = slice(k * P, (k + 1) * P)
                        mm = hi_lo_products(pe, proj_ps[:, b, 0:TB], w_hi[:, par, w], w_lo[:, par, w],
                                            h_hi[:, k, cols], h_lo[:, k, cols], k == 0, k == KD - 1)
                    mm.then_inc(proj_done, 1)

            mean(0)
            mean(1)
            project(0, 0, None, 0)
            project(1, 1, evacuated, 0)
            with pe.Fori(1, N_DN // 2) as j:
                project(2 * j, 0, evacuated, 0)
                project(2 * j + 1, 1, evacuated, 0)
            for c in range(N_DN, A0 + 1):
                if c == N_DN:
                    project(c, c % 2, evacuated, 0)
                else:
                    project(c, c % 2, gates_done, N_DN)
            project(A0 + 1, 1, evacuated, N_Z)
            with pe.Fori((A0 + 2) // 2, NT // 2) as j:
                project(2 * j, 0, evacuated, N_Z)
                project(2 * j + 1, 1, evacuated, N_Z)
            project(NT, 0, evacuated, N_Z)

        @block.vector
        def _(dve):
            dve.wait_ge(const_loaded, 32)

            def add_squares(b):
                dve.wait_ge(squares_done, b + 1)
                if b:
                    dve.wait_ge(means_done, b)
                dve.tensor_reduce(ssum, sq.rearrange("p (k t) -> p t k", k=KD), AX_X, ALU.add).then_inc(sums_done, 1)

            add_squares(0)
            for b in range(NB):
                dve.wait_ge(roots_done, b + 1)
                dve.reciprocal(rstd, std).then_inc(recips_done, 1)
                dve.wait_ge(recips_done, b + 1)
                for k in range(KD):
                    m = dve.scalar_tensor_tensor(xb[b % 2][:, k, :], xb[b % 2][:, k, :], gain[:, k:k + 1], rstd,
                                                 ALU.mult, ALU.mult)
                m.then_inc(h_done, 1)
                if b + 1 < NB:
                    add_squares(b + 1)
            dve.wait_ge(h_lo_done, NB)
            dve.memset(raw[0][:, 0:3], 0.0).then_inc(zeros_set, 1)
            dve.memset(raw[1][:, 0:3], 0.0).then_inc(zeros_set, 1)
            dve.wait_ge(zeros_set, 2)

            def conv_tile(c, par, first):
                if not first:
                    dve.wait_ge(dn_stored[par], landed(c - 2, par, 4))
                u, out = raw[par], res[par]
                for b in range(NB):
                    dve.wait_ge(proj_done, c * NB + (b + 1))
                    n = min(TB, S - b * TB)
                    m = dve.tensor_copy(u[:, 3 + b * TB:3 + b * TB + n], proj_ps[:, b, 0:n])
                    if n < TB:
                        m = dve.tensor_copy(samples(u, 3, 1), proj_ps[:, b, n:n + NSAMP].rearrange("p (b o) -> p b o", o=1))
                    m.then_inc(evacuated, 1)
                dve.wait_ge(evacuated, (c + 1) * NB)
                dve.wait_ge(ctx_loaded[par], landed(c, par))
                for j in range(4):
                    w = conv_w[:, bass.ds(c * 4 + j, 1)]
                    if j == 0:
                        m = dve.tensor_scalar(out[:, 0:CONV_COLS], u[:, 0:CONV_COLS], w, None, ALU.mult)
                    else:
                        dve.wait_ge(taps_done, c * 3 + j)
                        m = dve.scalar_tensor_tensor(out[:, 0:CONV_COLS], u[:, j:j + CONV_COLS], w,
                                                     out[:, 0:CONV_COLS], ALU.mult, ALU.add)
                    m.then_inc(conv_done if j == 3 else taps_done, 1)

            conv_tile(0, 0, True)
            conv_tile(1, 1, True)
            with dve.Fori(2 // 2, N_DN // 2) as j:
                i = 2 * j
                conv_tile(i, 0, False)
                conv_tile(i + 1, 1, False)

            for par in range(2):
                dve.wait_ge(dn_stored[par], 64 * (N_DN // 2))

            def attn_tile(c, par, first, parts):
                if first:
                    dve.wait_ge(z_stored[par], 16 * (N_Z // 2))
                else:
                    dve.wait_ge(at_stored[par], landed(c - A0 - 2, par, 3))
                for b in range(NB):
                    dve.wait_ge(proj_done, c * NB + (b + 1))
                    dve.tensor_copy(raw[par][0:parts, b * TB:(b + 1) * TB],
                                    proj_ps[0:parts, b, 0:TB]).then_inc(evacuated, 1)
                if parts == P:
                    dve.wait_ge(evacuated, (c - (N_Z - 1)) * NB)
                    dve.tensor_copy(res[par][:, 0:S].rearrange("p (r m) -> p r m", r=4),
                                    raw[par][:, 0:S].rearrange("p (m r) -> p r m", r=4)).then_inc(perm4_done, 1)

            attn_tile(A0, 0, True, P)
            attn_tile(A0 + 1, 1, True, P)
            with dve.Fori((A0 + 2) // 2, NT // 2) as j:
                i = 2 * j
                attn_tile(i, 0, False, P)
                attn_tile(i + 1, 1, False, P)
            attn_tile(NT, 0, False, 36)


CH = P
NC = S // CH
LEVELS = 7
C_IDENT, C_TRIU, C_TRIL, C_LEVEL = 0, 1, 2, 3


def for_pairs(engine, n, step):
    with engine.Fori(0, n // 2) as j:
        step(2 * j, 0)
        step(2 * j + 1, 1)
    if n % 2:
        step(n - 1, 0)


def named(sem, prefix, names):
    return [sem(prefix + n) for n in names.split()]


def constant_tiles():
    i, j = np.arange(P)[:, None], np.arange(P)[None, :]
    tiles = [i == j, i <= j, i > j]
    for level in range(LEVELS):
        tiles.append((i >> level + 1 == j >> level + 1) & ((i >> level) % 2 == 1) & ((j >> level) % 2 == 0))
    return np.ascontiguousarray(np.stack(tiles, 1).astype(np.float32)).reshape(P, -1)


def heads(tile):
    return tile.rearrange("p (h j) -> p h j", h=HEADS)


def per_head(col):
    return col.rearrange("p (h o) -> p h o", o=1).broadcast_to([P, HEADS, P])


def all_heads(tile):
    return tile.rearrange("p (o j) -> p o j", o=1).broadcast_to([P, HEADS, P])


def delta_and_attention(nc, t):
    with ExitStack() as ctx:
        sbuf, psum, sem = allocators(nc, ctx)
        C4 = HEADS * P
        const = sbuf("pb_const", [P, (C_LEVEL + LEVELS) * P], F32)
        logits = sbuf("pb_logits", [36, S], F32)
        lt = sbuf("pb_lt", [P, NC, 36], F32)
        alog = sbuf("pb_alog", [P, HEADS], F32)
        dtb = sbuf("pb_dtb", [P, HEADS], F32)
        beta = sbuf("pb_beta", [P, NC, HEADS], F32)
        g = sbuf("pb_g", [P, NC, HEADS], F32)
        gtmp = sbuf("pb_gtmp", [P, NC, HEADS], F32)
        gc = sbuf("pb_gc", [P, NC, HEADS], F32)
        egc = sbuf("pb_egc", [P, NC, HEADS], F32)
        ekd = sbuf("pb_ekd", [P, NC, HEADS], F32)
        raw = sbuf("pb_raw", [P, 12, P], F32)
        zg = sbuf("pb_z", [P, C4], F32)
        squares = sbuf("pb_squares", [P, 8, P], F32)
        ones = sbuf("pb_one", [P, P], F32)
        ss = sbuf("pb_ss", [P, 8], F32)
        rr = sbuf("pb_rr", [P, 8], F32)
        coef = sbuf("pb_coef", [P, HEADS], F32)
        betag = sbuf("pb_betag", [P, NC, HEADS], F32)
        kn, kbg, kdec, qn, vb, knT, qnT, gbc, gd, E, egr, M, L, X, XT, Z, U, WT, vnew, S_, intra, qdec, osq, orr, o, o_raw = (
            sbuf("pb_" + n, [P, C4], F32) for n in
            "kn kbg kdec qn vb knT qnT gbc gd E egr M L X XT Z U WT vnew S intra qdec osq orr o o_raw".split())
        B = sbuf("pb_B", [P, LEVELS, C4], F32)
        gain = sbuf("pb_gain", [P, 1], F32)
        eps = sbuf("pb_eps", [P, 1], F32)
        ones_mean = sbuf("pb_ones", [P, P], F32)
        qkv = [sbuf(f"pb_qkv{v}", [P, 2, 12 * P], F32) for v in range(len(DILS))]
        vtok = [sbuf(f"pb_vtok{v}", [P, 2, AH * HD], F32) for v in range(len(DILS))]
        bias = [sbuf(f"pb_bias{v}", [P, 2, AH * 2 * P], F32) for v in range(2)]
        bias_own = sbuf("pb_bias_own", [P, AH * P], F32)
        s = sbuf("pb_s", [P, 2, 4 * P], F32)
        e = sbuf("pb_e", [P, 2, 4 * P], F32)
        eT = sbuf("pb_eT", [P, 2, 4 * P], F32)
        uo = [sbuf(f"pb_uo{v}", [P, UROW], F32) for v in range(len(DILS))]
        ps = psum("pb_ps", [P, 8, C4], F32)
        qkv_loaded = [[sem(f"pb_qkv_loaded{v}{par}") for par in range(2)] for v in range(len(DILS))]
        uo_stored = [sem(f"pb_uo_stored{v}") for v in range(len(DILS))]
        (bias_loaded, v_turned, v_copied, step_scored, biased, max_done, exp_done, turned, eT_copied, pv_done,
         o_copied, uo_free, o_free, chunk_ended) = named(sem, "pb_", """bias_loaded v_turned v_copied step_scored biased max_done
            exp_done turned eT_copied pv_done o_copied uo_free o_free chunk_ended""")
        (const_loaded, consts_set, logits_turned, logits_copied, beta_done, g_steps, gsum_done, gcol_done,
         raw_loaded, z_loaded, stored, raw_turned, gbc_done, rows_done, kq_turned, grams_done, scores_done,
         b0_turned, z_done, xt_done, x_done, u_done, w_done, p1_done, o_done, s_done, msq_done,
         squared, norms_done, ss_kept, roots_done, knT_copied, qnT_copied, abs_done, e_done, egr_done, z_copied, u_copied, w_copied,
         osq_done, o_kept, kq_raw_turned, betag_done, k_side_done, oroot_done, coef_steps, k_scaled, q_scaled, v_scaled, g_diff_done, m_done, l_done, mask_done,
         xt_sub, x_sub, i1_done, intra_done, qdec_done, vnew_done, s1_done, s_upd, orr_done, o1_done, out_done) = (
            sem("pb_" + n) for n in
            """const_loaded consts_set logits_turned logits_copied beta_done g_steps gsum_done gcol_done
            raw_loaded z_loaded stored raw_turned gbc_done rows_done kq_turned grams_done scores_done
            b0_turned z_done xt_done x_done u_done w_done p1_done o_done s_done msq_done
            squared norms_done ss_kept roots_done knT_copied qnT_copied abs_done e_done egr_done z_copied u_copied w_copied
            osq_done o_kept kq_raw_turned betag_done k_side_done oroot_done coef_steps k_scaled q_scaled v_scaled g_diff_done m_done l_done mask_done
            xt_sub x_sub i1_done intra_done qdec_done vnew_done s1_done s_upd orr_done o1_done out_done""".split())
        block = ctx.enter_context(nc.Block())

        def const_tile(n):
            return const[:, n * P:(n + 1) * P]

        def bank(n):
            return ps[:, n, :]

        SCORES, TURNS, OUTPUT = 4, 6, 7
        UNITS = len(DILS)
        STEPS = 4 * UNITS

        def step_heads(j):
            first = j % 4 // 2 * 4 + j % 2
            return j // 4, (first, first + 2)

        def keys_seen(tile, j):
            view = tile.rearrange("p (h k) -> p h k", h=2)
            return view[:, :, P:2 * P] if j // 4 == 2 else view

        def col(tile, h):
            return tile[:, h * P:(h + 1) * P]

        @block.sync
        def _(sp):
            sp.dma_start(const[:, :], t["consts"]).then_inc(const_loaded, 16)
            sp.dma_start(logits[:, :], t["ba"][:, 0:S]).then_inc(const_loaded, 16)
            sp.dma_start(alog[:, :], t["a_log"].partition_broadcast(P)).then_inc(const_loaded, 16)
            sp.dma_start(dtb[:, :], t["dt_bias"].partition_broadcast(P)).then_inc(const_loaded, 16)
            sp.dma_start(gain[:, :], t["g_dn_out"]).then_inc(const_loaded, 16)

            def load_raw(c):
                sp.dma_start(raw[:, :, :], t["dn"].rearrange("n p s -> p n s")[:, :, bass.ds(c * CH, CH)]).then_inc(raw_loaded, 16)

            def load_z(c):
                sp.dma_start(heads(zg[:, :]), t["z"].rearrange("n p s -> p n s")[:, :, bass.ds(c * CH, CH)]).then_inc(z_loaded, 16)

            def load_unit(v, c, par):
                src = t[("at", "at4", "at16")[v]].rearrange("n p s -> p n s")[:, :, bass.ds(c * P, P)]
                sp.dma_start(qkv[v][:, par, :].rearrange("p (n s) -> p n s", n=12), src).then_inc(qkv_loaded[v][par], 16)

            load_raw(0)
            for v in range(UNITS):
                load_unit(v, 0, 0)
            load_z(0)
            for v in range(UNITS):
                toeplitz = t["bias_flat"][v][:, P - 1:P - 1 + P * (384 - 1)].rearrange("h (q k) -> q h k", k=384 - 1)
                if v < 2:
                    for first in range(2):
                        lo = P if first == 0 else 0
                        sp.dma_start(bias[v][:, first, :].rearrange("p (h k) -> p h k", h=AH)[:, :, lo:2 * P],
                                     toeplitz[:, :, lo:2 * P]).then_inc(bias_loaded, 16)
                else:
                    sp.dma_start(bias_own[:, :].rearrange("p (h k) -> p h k", h=AH), toeplitz[:, :, P:2 * P]).then_inc(bias_loaded, 16)
            sp.sem_inc(uo_free, UNITS)
            sp.sem_inc(o_free, 1)

            def store(c):
                sp.wait_ge(out_done, c + 1)
                sp.sem_inc(chunk_ended, 1)
                sp.dma_start(t["mix"].rearrange("n p s -> p n s")[:, 0:HEADS, bass.ds(c * CH, CH)], heads(o[:, :])).then_inc(stored, 16)

            def chunk(c, par, more, first=False):
                if more:
                    sp.wait_ge(raw_turned, c + 1)
                    load_raw(c + 1)
                if not first:
                    store(c - 1)
                    load_z(c)
                for v in range(UNITS):
                    if more:
                        sp.wait_ge(step_scored, c * STEPS + (4 * v + 4))
                        load_unit(v, c + 1, 1 - par)
                    sp.wait_ge(o_copied, c * UNITS + (v + 2))
                    sp.dma_start(t["U"][v][bass.ds(c * P, P), :], uo[v][:, :]).then_inc(uo_stored[v], 16)
                    if v:
                        sp.wait_ge(uo_stored[v - 1], c * 16 + 16)
                        sp.sem_inc(uo_free, 1)
                sp.wait_ge(uo_stored[UNITS - 1], c * 16 + 16)
                sp.sem_inc(uo_free, 1)
                if not first:
                    sp.wait_ge(stored, c * 16)
                    sp.sem_inc(o_free, 1)

            chunk(0, 0, True, True)
            chunk(1, 1, True)
            with sp.Fori(1, NC // 2 - 1) as j:
                chunk(2 * j, 0, True)
                chunk(2 * j + 1, 1, True)
            chunk(NC - 2, 0, True)
            chunk(NC - 1, 1, False)
            store(NC - 1)
            sp.wait_ge(s_upd, NC + 1)
            sp.dma_start(t["delta"].rearrange("h k v -> k h v"), heads(S_[:, :])).then_inc(stored, 16)
            sp.wait_ge(stored, 16 * NC + 16)

        @block.gpsimd
        def _(pool):
            pool.memset(ones_mean[:, :], 1.0 / DK).then_inc(consts_set, 1)
            pool.memset(eps[:, :], EPS).then_inc(consts_set, 1)
            pool.memset(S_[:, :], 0.0).then_inc(consts_set, 1)
            pool.memset(ones[:, :], 1.0).then_inc(consts_set, 1)
            for v in range(2):
                pool.memset(qkv[v][:, 1, 4 * P:8 * P], 0.0).then_inc(consts_set, 1)
                pool.memset(vtok[v][:, 1, :], 0.0).then_inc(consts_set, 1)
                pool.memset(bias[v][:, 0, :].rearrange("p (h k) -> p h k", h=AH)[:, :, 0:P], -BIG).then_inc(consts_set, 1)
            pool.wait_ge(consts_set, 10)
            pool.wait_ge(const_loaded, 80)
            pool.wait_ge(gcol_done, 1)
            def cc(tile, c):
                return tile[:, bass.ds(c, 1), :].rearrange("p o h -> p (o h)")

            def finish(c):
                pool.wait_ge(o1_done, c + 1)
                pool.wait_ge(z_loaded, c * 16 + 16)
                pool.tensor_tensor(o[:, :], o[:, :], zg[:, :], ALU.mult).then_inc(out_done, 1)

            def chunk(c, first=False):
                pool.tensor_tensor(heads(gbc[:, :]), all_heads(ones[:, :]), per_head(cc(g, c)), ALU.mult).then_inc(gbc_done, 1)
                pool.wait_ge(k_scaled, c + 1)
                pool.wait_ge(s_upd, c + 1)
                pool.tensor_tensor(heads(kbg[:, :]), heads(kn[:, :]), per_head(cc(betag, c)), ALU.mult)
                pool.tensor_tensor(heads(kdec[:, :]), heads(kn[:, :]), per_head(cc(ekd, c)), ALU.mult).then_inc(k_side_done, 1)
                pool.wait_ge(l_done, c + 1)
                for level in range(LEVELS):
                    pool.tensor_tensor(heads(B[:, level, :]), heads(L[:, :]), all_heads(const_tile(C_LEVEL + level)),
                                       ALU.mult).then_inc(mask_done, 1)
                if not first:
                    finish(c - 1)

            pool.wait_ge(gcol_done, 3)
            pool.wait_ge(betag_done, 1)
            chunk(0, True)
            with pool.Fori(1, NC) as c:
                chunk(c)
            finish(NC - 1)

        @block.scalar
        def _(act):
            act.wait_ge(const_loaded, 80)
            act.wait_ge(consts_set, 10)
            act.wait_ge(logits_copied, 1)
            act.activation(beta[:, :, :], lt[:, :, 0:HEADS], ACT.Sigmoid).then_inc(beta_done, 1)
            act.wait_ge(g_steps, 1)
            act.activation(gtmp[:, :, :], g[:, :, :], ACT.Abs).then_inc(beta_done, 1)
            act.wait_ge(beta_done, 2)
            act.activation(gtmp[:, :, :], gtmp[:, :, :], ACT.Exp, scale=-1.0).then_inc(beta_done, 1)
            act.activation(alog[:, :], alog[:, :], ACT.Exp).then_inc(beta_done, 1)
            act.wait_ge(beta_done, 4)
            act.activation(gtmp[:, :, :], gtmp[:, :, :], ACT.Ln, bias=1.0).then_inc(beta_done, 1)
            act.wait_ge(gsum_done, 1)
            act.activation(egc[:, :, :], bank(0)[:, 0:NC * HEADS].rearrange("p (c h) -> p c h", c=NC), ACT.Exp).then_inc(gcol_done, 1)
            act.activation(ekd[:, :, :], bank(1)[:, 0:NC * HEADS].rearrange("p (c h) -> p c h", c=NC), ACT.Exp).then_inc(gcol_done, 1)

            def square(c):
                act.wait_ge(raw_loaded, c * 16 + 16)
                act.activation(squares[:, :, :], raw[:, 0:8, :], ACT.Square).then_inc(squared, 1)

            def keep_norms(c):
                act.wait_ge(norms_done, c + 1)
                act.activation(ss[:, :], bank(3)[:, 0:16].rearrange("p (h two) -> p h two", two=2)[:, :, 0], ACT.Copy).then_inc(ss_kept, 1)

            def roots(c):
                act.wait_ge(ss_kept, c + 1)
                act.activation(rr[:, :], ss[:, :], ACT.Sqrt, bias=eps[:, 0:1]).then_inc(roots_done, 1)

            act.sem_inc(oroot_done, 1)
            act.sem_inc(o_kept, 1)

            def slot(c, par, j):
                if j % 4 == 0 and j < STEPS:
                    v = j // 4
                    act.wait_ge(v_turned, c * UNITS + (v + 1))
                    act.activation(vtok[v][:, par, :], bank(TURNS), ACT.Copy).then_inc(v_copied, 1)
                if 1 <= j <= STEPS:
                    i = j - 1
                    act.wait_ge(turned, c * STEPS + j)
                    if i >= 2:
                        act.wait_ge(pv_done, c * STEPS + (i - 1))
                    act.activation(keys_seen(eT[:, i % 2, :], i), keys_seen(bank(TURNS), i), ACT.Copy).then_inc(eT_copied, 1)
                if j < STEPS:
                    v, hs = step_heads(j)
                    act.wait_ge(max_done, c * STEPS + (j + 1))
                    if j >= 2:
                        act.wait_ge(turned, c * STEPS + (j - 1))
                    for n, h in enumerate(hs):
                        nm, dn = AH * HD + h, AH * HD + AH + h
                        m = act.activation(keys_seen(e[:, j % 2, :], j)[:, n, :], keys_seen(s[:, j % 2, :], j)[:, n, :], ACT.Exp,
                                           bias=uo[v][:, nm:nm + 1], accum_out=uo[v][:, dn:dn + 1])
                    m.then_inc(exp_done, 1)

            def chunk(c, par, first=False, more=True):
                slot(c, par, 0)
                act.wait_ge(g_diff_done, c + 1)
                act.activation(gd[:, :], gd[:, :], ACT.Abs).then_inc(abs_done, 1)
                act.activation(egr[:, :], bank(3), ACT.Exp).then_inc(egr_done, 1)
                act.wait_ge(abs_done, c + 1)
                act.activation(E[:, :], gd[:, :], ACT.Exp, scale=-1.0).then_inc(e_done, 1)
                slot(c, par, 1)
                act.wait_ge(kq_turned, c + 1)
                act.activation(knT[:, :], bank(0), ACT.Copy).then_inc(knT_copied, 1)
                act.activation(qnT[:, :], bank(1), ACT.Copy).then_inc(qnT_copied, 1)
                slot(c, par, 2)
                slot(c, par, 3)
                for level in range(1, LEVELS):
                    act.wait_ge(z_done, c * (LEVELS - 1) + level)
                    act.activation(Z[:, :], bank(0), ACT.Copy).then_inc(z_copied, 1)
                    if more and level == 2:
                        square(c + 1)
                    if more and level == 4:
                        keep_norms(c + 1)
                    slot(c, par, level + 3)
                act.wait_ge(u_done, c + 1)
                act.activation(U[:, :], bank(2), ACT.Copy).then_inc(u_copied, 1)
                act.wait_ge(w_done, c + 1)
                act.activation(WT[:, :], bank(1), ACT.Copy).then_inc(w_copied, 1)
                slot(c, par, 10)
                slot(c, par, 11)
                act.wait_ge(o_done, c + 1)
                act.activation(osq[:, :], bank(2), ACT.Square).then_inc(osq_done, 1)
                if not first:
                    act.wait_ge(o1_done, c)
                act.activation(o_raw[:, :], bank(2), ACT.Copy).then_inc(o_kept, 1)
                slot(c, par, 12)
                if more:
                    roots(c + 1)
                act.wait_ge(msq_done, c + 1)
                act.activation(orr[:, :], bank(3), ACT.Sqrt, bias=eps[:, 0:1]).then_inc(oroot_done, 1)
                slot(c, par, 13)

            square(0)
            keep_norms(0)
            roots(0)
            chunk(0, 0, True)
            chunk(1, 1)
            with act.Fori(1, NC // 2 - 1) as j:
                chunk(2 * j, 0)
                chunk(2 * j + 1, 1)
            chunk(NC - 2, 0)
            chunk(NC - 1, 1, more=False)

        @block.tensor
        def _(pe):
            ident = const_tile(C_IDENT)
            triu, tril = const_tile(C_TRIU), const_tile(C_TRIL)
            pe.wait_ge(const_loaded, 80)
            pe.wait_ge(consts_set, 10)
            for c in range(NC):
                m = pe.transpose(ps[:, c // 8, c % 8 * 36:c % 8 * 36 + 36], logits[:, c * CH:(c + 1) * CH], ident[0:36, 0:36])
            m.then_inc(logits_turned, 1)
            pe.wait_ge(g_steps, 4)
            gall = g[:, :, :].rearrange("p c h -> p (c h)")
            pe.matmul(bank(0)[:, 0:NC * HEADS], triu, gall, start=True, stop=True)
            pe.matmul(bank(1)[:, 0:NC * HEADS], tril, gall, start=True, stop=True).then_inc(gsum_done, 1)
            pe.wait_ge(gcol_done, 3)

            pe.wait_ge(bias_loaded, 16 * 5)

            def halves(par, j):
                return ((par, 1),) if j // 4 == 2 else ((1 - par, 0), (par, 1))

            def unit_start(c, par, v):
                pe.wait_ge(qkv_loaded[v][par], (c - par) * 8 + 16)
                if v:
                    pe.wait_ge(eT_copied, c * STEPS + (4 * v - 1))
                for n in range(4):
                    m = pe.transpose(col(bank(TURNS), n), qkv[v][:, par, (8 + n) * P:(9 + n) * P], ident)
                m.then_inc(v_turned, 1)

            def score(c, par, j):
                v, hs = step_heads(j)
                if j >= 2:
                    pe.wait_ge(biased, c * STEPS + (j - 1))
                for n, h in enumerate(hs):
                    tile, rows = h // 2, slice(h % 2 * HD, h % 2 * HD + HD)
                    for unit, half in halves(par, j):
                        m = pe.matmul(col(bank(SCORES + j % 2), 2 * n + half), qkv[v][rows, par, tile * P:(tile + 1) * P],
                                      qkv[v][rows, unit, (4 + tile) * P:(5 + tile) * P], start=True, stop=True)
                m.then_inc(step_scored, 1)

            def turn(c, par, j):
                pe.wait_ge(exp_done, c * STEPS + (j + 1))
                if j == 0:
                    pe.wait_ge(v_copied, c * UNITS + 1)
                elif j % 4 == 3 and j < STEPS - 1:
                    pe.wait_ge(v_copied, c * UNITS + (j // 4 + 2))
                else:
                    pe.wait_ge(eT_copied, c * STEPS + j)
                for n in range(2):
                    for unit, half in halves(par, j):
                        m = pe.transpose(col(bank(TURNS), 2 * n + half), col(e[:, j % 2, :], 2 * n + half), ident)
                m.then_inc(turned, 1)

            def values(c, par, j):
                v, hs = step_heads(j)
                pe.wait_ge(eT_copied, c * STEPS + (j + 1))
                if j % 4 == 0:
                    pe.wait_ge(o_copied, c * UNITS + (v + 1))
                for n, h in enumerate(hs):
                    hh = slice(h * HD, (h + 1) * HD)
                    for unit, half in halves(par, j):
                        m = pe.matmul(bank(OUTPUT)[:, hh], col(eT[:, j % 2, :], 2 * n + half), vtok[v][:, unit, hh],
                                      start=j // 4 == 2 or half == 0, stop=half == 1)
                m.then_inc(pv_done, 1)

            def slot(c, par, j):
                if j % 4 == 0 and j < STEPS:
                    unit_start(c, par, j // 4)
                if j < STEPS:
                    score(c, par, j)
                if j >= 2:
                    values(c, par, j - 2)
                if 1 <= j <= STEPS:
                    turn(c, par, j - 1)

            def norms(c):
                pe.wait_ge(squared, c + 1)
                for i in range(8):
                    m = pe.matmul(bank(3)[:, 2 * i:2 * i + 2], squares[:, (4 + i) % 8, :], ones[:, 0:2], start=True, stop=True)
                m.then_inc(norms_done, 1)

            def chunk(c, par, more=True):
                pe.wait_ge(raw_loaded, c * 16 + 16)
                for n, first in ((0, 4), (1, 0)):
                    for h in range(HEADS):
                        m = pe.transpose(col(bank(n), h), raw[:, first + h, :], ident)
                m.then_inc(kq_raw_turned, 1)
                slot(c, par, 0)
                pe.wait_ge(oroot_done, c + 1)
                pe.wait_ge(gbc_done, c + 1)
                for h in range(HEADS):
                    m = pe.matmul(col(bank(3), h), col(gbc[:, :], h), triu, start=True, stop=True)
                m.then_inc(rows_done, 1)
                pe.wait_ge(o_kept, c + 1)
                for h in range(HEADS):
                    m = pe.transpose(col(bank(2), h), raw[:, 8 + h, :], ident)
                m.then_inc(raw_turned, 1)
                slot(c, par, 1)
                pe.wait_ge(k_scaled, c + 1)
                for h in range(HEADS):
                    pe.transpose(col(bank(0), h), col(kn[:, :], h), ident)
                pe.wait_ge(q_scaled, c + 1)
                for h in range(HEADS):
                    m = pe.transpose(col(bank(1), h), col(qn[:, :], h), ident)
                m.then_inc(kq_turned, 1)
                slot(c, par, 2)
                pe.wait_ge(knT_copied, c + 1)
                pe.wait_ge(egr_done, c + 1)
                pe.wait_ge(g_diff_done, c + 1)
                for h in range(HEADS):
                    m = pe.matmul(col(bank(3), h), col(knT[:, :], h), col(knT[:, :], h), start=True, stop=True)
                m.then_inc(grams_done, 1)
                pe.wait_ge(qnT_copied, c + 1)
                pe.wait_ge(v_scaled, c + 1)
                for h in range(HEADS):
                    m = pe.matmul(col(bank(2), h), col(knT[:, :], h), col(qnT[:, :], h), start=True, stop=True)
                m.then_inc(scores_done, 1)
                slot(c, par, 3)
                pe.wait_ge(mask_done, c * LEVELS + 1)
                for h in range(HEADS):
                    m = pe.transpose(col(bank(0), h), col(B[:, 0, :], h), ident)
                m.then_inc(b0_turned, 1)
                for level in range(1, LEVELS):
                    pe.wait_ge(mask_done, c * LEVELS + (level + 1))
                    pe.wait_ge(xt_sub, c * LEVELS + level)
                    for h in range(HEADS):
                        m = pe.matmul(col(bank(0), h), col(B[:, level, :], h), col(XT[:, :], h), start=True, stop=True)
                    m.then_inc(z_done, 1)
                    if more and level == 3:
                        pe.wait_ge(m_done, c + 1)
                        norms(c + 1)
                    slot(c, par, level + 3)
                    pe.wait_ge(z_copied, c * (LEVELS - 1) + level)
                    pe.wait_ge(x_sub, c * (LEVELS - 1) + level)
                    for h in range(HEADS):
                        m = pe.matmul(col(bank(1), h), col(X[:, :], h), col(Z[:, :], h), start=True, stop=True)
                    m.then_inc(xt_done, 1)
                    if level < LEVELS - 1:
                        if level == 1:
                            pe.wait_ge(i1_done, c + 1)
                        for h in range(HEADS):
                            m = pe.matmul(col(bank(2), h), col(Z[:, :], h), col(X[:, :], h), start=True, stop=True)
                        m.then_inc(x_done, 1)
                pe.wait_ge(xt_sub, c * LEVELS + LEVELS)
                pe.wait_ge(k_side_done, c + 1)
                for h in range(HEADS):
                    m = pe.matmul(col(bank(1), h), col(kbg[:, :], h), col(XT[:, :], h), start=True, stop=True)
                m.then_inc(w_done, 1)
                for h in range(HEADS):
                    m = pe.matmul(col(bank(2), h), col(XT[:, :], h), col(vb[:, :], h), start=True, stop=True)
                m.then_inc(u_done, 1)
                slot(c, par, 10)
                if more:
                    pe.wait_ge(ss_kept, c + 2)
                pe.wait_ge(w_copied, c + 1)
                for h in range(HEADS):
                    m = pe.matmul(col(bank(3), h), col(WT[:, :], h), col(S_[:, :], h), start=True, stop=True)
                m.then_inc(p1_done, 1)
                slot(c, par, 11)
                pe.wait_ge(vnew_done, c + 1)
                pe.wait_ge(intra_done, c + 1)
                pe.wait_ge(qdec_done, c + 1)
                for h in range(HEADS):
                    pe.matmul(col(bank(2), h), col(S_[:, :], h), col(qdec[:, :], h), start=True, stop=False)
                    m = pe.matmul(col(bank(2), h), col(vnew[:, :], h), col(intra[:, :], h), start=False, stop=True)
                m.then_inc(o_done, 1)
                for h in range(HEADS):
                    m = pe.matmul(col(bank(3), h), col(kdec[:, :], h), col(vnew[:, :], h), start=True, stop=True)
                m.then_inc(s_done, 1)
                slot(c, par, 12)
                pe.wait_ge(osq_done, c + 1)
                pe.wait_ge(s_upd, c + 2)
                pe.matmul(bank(3), ones_mean[:, :], osq[:, :], start=True, stop=True).then_inc(msq_done, 1)
                slot(c, par, 13)

            norms(0)
            pe.wait_ge(ss_kept, 1)
            with pe.Fori(0, NC // 2 - 1) as j:
                chunk(2 * j, 0)
                chunk(2 * j + 1, 1)
            chunk(NC - 2, 0)
            chunk(NC - 1, 1, False)

        @block.vector
        def _(dve):
            dve.wait_ge(const_loaded, 80)
            dve.wait_ge(consts_set, 10)
            dve.wait_ge(logits_turned, 1)
            for n in range(2):
                m = dve.tensor_copy(lt[:, n * 8:(n + 1) * 8, :], ps[:, n, 0:8 * 36].rearrange("p (c h) -> p c h", c=8))
            m.then_inc(logits_copied, 1)
            dve.wait_ge(logits_copied, 1)
            dtb_all = dtb[:, :].rearrange("p (o h) -> p o h", o=1).broadcast_to([P, NC, HEADS])
            dve.tensor_tensor(g[:, :, :], lt[:, :, 32:36], dtb_all, ALU.add).then_inc(g_steps, 1)
            dve.wait_ge(beta_done, 5)
            dve.scalar_tensor_tensor(g[:, :, :], g[:, :, :], 0.0, gtmp[:, :, :], ALU.max, ALU.add).then_inc(g_steps, 1)
            dve.tensor_scalar(alog[:, :], alog[:, :], -1.0, None, ALU.mult).then_inc(g_steps, 1)
            dve.wait_ge(g_steps, 3)
            alog_all = alog[:, :].rearrange("p (o h) -> p o h", o=1).broadcast_to([P, NC, HEADS])
            dve.tensor_tensor(g[:, :, :], g[:, :, :], alog_all, ALU.mult).then_inc(g_steps, 1)
            dve.wait_ge(gcol_done, 2)
            dve.tensor_copy(gc[:, :, :], bank(0)[:, 0:NC * HEADS].rearrange("p (c h) -> p c h", c=NC)).then_inc(gcol_done, 1)
            dve.sem_inc(s_upd, 1)
            dve.sem_inc(o_copied, 1)
            dve.tensor_tensor(betag[:, :, :], beta[:, :, :], egc[:, :, :], ALU.mult).then_inc(betag_done, 1)
            dve.wait_ge(bias_loaded, 16 * 5)

            def slot(c, par, jj, j):
                if j < STEPS:
                    v, hs = step_heads(j)
                    if j % 4 == 0:
                        dve.wait_ge(uo_free, c * UNITS + (v + 1))
                    dve.wait_ge(step_scored, c * STEPS + (j + 1))
                    if j >= 2:
                        dve.wait_ge(exp_done, c * STEPS + (j - 1))
                    if v == 2:
                        table = bias_own[:, :].rearrange("p (h k) -> p h k", h=AH)
                    else:
                        both = 1 if par else ((jj + 7) // 8 if v == 0 else jj % 2)
                        table = bias[v][:, bass.ds(both, 1), :].rearrange("p o (h k) -> p (o h) k", h=AH)
                    dve.scalar_tensor_tensor(keys_seen(s[:, j % 2, :], j), keys_seen(bank(SCORES + j % 2), j), HD ** -0.5,
                                             table[:, hs[0]:hs[0] + 3:2, :], ALU.mult, ALU.add).then_inc(biased, 1)
                    dve.wait_ge(biased, c * STEPS + (j + 1))
                    nm = AH * HD + hs[0]
                    dve.tensor_reduce(uo[v][:, nm:nm + 3:2], keys_seen(s[:, j % 2, :], j), AX_X, ALU.max,
                                      negate=True).then_inc(max_done, 1)
                if j >= 5 and j % 4 == 1:
                    v = (j - 5) // 4
                    dve.wait_ge(pv_done, c * STEPS + (j - 1))
                    dve.wait_ge(exp_done, c * STEPS + (j - 1))
                    dve.tensor_copy(uo[v][:, 0:AH * HD], bank(OUTPUT)).then_inc(o_copied, 1)

            def finish(c):
                dve.wait_ge(oroot_done, c + 2)
                dve.reciprocal(orr[:, :], orr[:, :]).then_inc(orr_done, 1)
                dve.wait_ge(orr_done, c + 1)
                dve.wait_ge(o_kept, c + 2)
                dve.wait_ge(o_free, c + 1)
                dve.scalar_tensor_tensor(o[:, :], o_raw[:, :], gain[:, 0:1], orr[:, :], ALU.mult, ALU.mult).then_inc(o1_done, 1)

            def chunk(c, par, jj, first=False):
                def cc(tile):
                    return tile[:, bass.ds(c, 1), :].rearrange("p o h -> p (o h)")

                dve.wait_ge(roots_done, c + 1)
                dve.reciprocal(rr[:, :], rr[:, :]).then_inc(coef_steps, 1)
                dve.wait_ge(coef_steps, c * 2 + 1)
                dve.tensor_scalar(coef[:, :], rr[:, 4:8], DK ** -0.5, None, ALU.mult).then_inc(coef_steps, 1)
                dve.wait_ge(kq_raw_turned, c + 1)
                dve.tensor_tensor(heads(kn[:, :]), heads(bank(0)), per_head(rr[:, 0:4]), ALU.mult).then_inc(k_scaled, 1)
                dve.wait_ge(coef_steps, c * 2 + 2)
                dve.tensor_tensor(heads(qn[:, :]), heads(bank(1)), per_head(coef[:, :]), ALU.mult).then_inc(q_scaled, 1)
                slot(c, par, jj, 0)
                dve.wait_ge(rows_done, c + 1)
                dve.tensor_tensor(heads(gd[:, :]), heads(bank(3)), per_head(cc(gc)), ALU.subtract).then_inc(g_diff_done, 1)
                dve.wait_ge(raw_turned, c + 1)
                dve.tensor_tensor(heads(vb[:, :]), heads(bank(2)), per_head(cc(beta)), ALU.mult).then_inc(v_scaled, 1)
                slot(c, par, jj, 1)
                slot(c, par, jj, 2)
                dve.wait_ge(grams_done, c + 1)
                dve.wait_ge(e_done, c + 1)
                dve.tensor_tensor(M[:, :], bank(3), E[:, :], ALU.mult).then_inc(m_done, 1)
                dve.wait_ge(m_done, c + 1)
                dve.tensor_tensor(heads(L[:, :]), heads(M[:, :]), per_head(cc(beta)), ALU.mult).then_inc(l_done, 1)
                dve.wait_ge(scores_done, c + 1)
                dve.tensor_tensor(intra[:, :], bank(2), E[:, :], ALU.mult).then_inc(i1_done, 1)
                dve.wait_ge(egr_done, c + 1)
                dve.wait_ge(qnT_copied, c + 1)
                dve.tensor_tensor(qdec[:, :], qnT[:, :], egr[:, :], ALU.mult).then_inc(qdec_done, 1)
                dve.wait_ge(i1_done, c + 1)
                dve.tensor_tensor(heads(intra[:, :]), heads(intra[:, :]), all_heads(const_tile(C_TRIU)), ALU.mult).then_inc(intra_done, 1)
                slot(c, par, jj, 3)
                dve.wait_ge(b0_turned, c + 1)
                ident4 = all_heads(const_tile(C_IDENT))
                dve.tensor_tensor(heads(XT[:, :]), ident4, heads(bank(0)), ALU.subtract).then_inc(xt_sub, 1)
                dve.tensor_tensor(heads(X[:, :]), ident4, heads(B[:, 0, :]), ALU.subtract).then_inc(x_sub, 1)
                for level in range(1, LEVELS):
                    slot(c, par, jj, level + 3)
                    dve.wait_ge(xt_done, c * (LEVELS - 1) + level)
                    dve.tensor_tensor(XT[:, :], XT[:, :], bank(1), ALU.subtract).then_inc(xt_sub, 1)
                    if level == 3 and not first:
                        finish(c - 1)
                    if level < LEVELS - 1:
                        dve.wait_ge(x_done, c * (LEVELS - 2) + level)
                        dve.tensor_tensor(X[:, :], X[:, :], bank(2), ALU.subtract).then_inc(x_sub, 1)
                slot(c, par, jj, 10)
                dve.wait_ge(p1_done, c + 1)
                dve.wait_ge(u_copied, c + 1)
                dve.tensor_tensor(vnew[:, :], U[:, :], bank(3), ALU.subtract).then_inc(vnew_done, 1)
                slot(c, par, jj, 11)
                dve.wait_ge(s_done, c + 1)
                last = heads(egr[:, :])[:, :, P - 1:P].broadcast_to([P, HEADS, P])
                dve.tensor_tensor(heads(S_[:, :]), heads(S_[:, :]), last, ALU.mult).then_inc(s1_done, 1)
                dve.wait_ge(s1_done, c + 1)
                dve.tensor_tensor(S_[:, :], S_[:, :], bank(3), ALU.add).then_inc(s_upd, 1)
                slot(c, par, jj, 12)
                slot(c, par, jj, 13)

            chunk(0, 0, 0, True)
            chunk(1, 1, 0)
            with dve.Fori(1, NC // 2) as jj:
                chunk(2 * jj, 0, jj)
                chunk(2 * jj + 1, 1, jj)
            finish(NC - 1)


QB = S // P
FLAT = P * 384


def bucket_tiles():
    tiles = np.zeros((33, len(DILS), 384), np.float32)
    for v, d in enumerate(DILS):
        for i in range(384):
            rel = 255 - i
            if not 0 <= rel <= P:
                tiles[32, v, i] = -BIG
                continue
            n = rel * d
            large = 16 + int(np.log(max(n, 1) / 16) / np.log(2048 / 16) * 16)
            tiles[n if n < 16 else min(large, 31), v, i] = 1.0
    return tiles.reshape(33, len(DILS) * 384)


def bias_rows(t, sbuf, ps, sem):
    rel = sbuf("pr_rel", [33, AH], F32)
    buckets = sbuf("pr_buckets", [33, len(DILS) * 384], F32)
    rows = sbuf("pr_rows", [AH, len(DILS) * 384], F32)
    loaded, ones_set, summed, copied, stored = named(sem, "pr_", "loaded ones_set summed copied stored")

    def load(sp):
        sp.dma_start(rel[0:32, :], t["rel_bias"]).then_inc(loaded, 16)
        sp.dma_start(buckets[:, :], t["buckets"]).then_inc(loaded, 16)

    def store(sp):
        sp.wait_ge(copied, len(DILS))
        for v in range(len(DILS)):
            src = rows[:, v * 384:(v + 1) * 384].rearrange("h (o i) -> h o i", o=1).broadcast_to([AH, P, 384])
            sp.dma_start(t["bias_flat"][v].rearrange("h (q i) -> h q i", i=384), src).then_inc(stored, 16)

    def finish(sp):
        sp.wait_ge(stored, 16 * len(DILS))

    def set_ones(dve):
        dve.memset(rel[32:33, :], 1.0).then_inc(ones_set, 1)

    def copy_rows(dve):
        dve.wait_ge(summed, 1)
        for v in range(len(DILS)):
            dve.tensor_copy(rows[:, v * 384:(v + 1) * 384], ps[0:AH, 4 + v, 0:384]).then_inc(copied, 1)

    def sum_rows(pe):
        pe.wait_ge(loaded, 32)
        pe.wait_ge(ones_set, 1)
        for v in range(len(DILS)):
            m = pe.matmul(ps[0:AH, 4 + v, 0:384], rel[:, :], buckets[:, v * 384:(v + 1) * 384], start=True, stop=True)
        m.then_inc(summed, 1)

    return load, store, finish, set_ones, copy_rows, sum_rows


HB = HEADS * NSAMP
NBH = NSAMP * AH
PADS = TOK - S


def head_mask():
    p, n, h = np.meshgrid(np.arange(P), np.arange(4), np.arange(AH), indexing="ij")
    return (2 * n + p // HD == h).astype(np.float32).reshape(P, 4 * AH)


def bias_and_delta_samples(nc, t):
    with ExitStack() as ctx:
        sbuf, psum, sem = allocators(nc, ctx)
        state = sbuf("sd_state", [P, HB, P], F32)
        new_state = sbuf("sd_new_state", [P, HB, P], F32)
        diag = sbuf("sd_diag", [P, HB, P], F32)
        ident = sbuf("sd_ident", [P, P], F32)
        ones = sbuf("sd_ones", [P, P], F32)
        eps = sbuf("sd_eps", [P, 1], F32)
        dn = sbuf("sd_dn", [P, 12 * NSAMP], F32)
        z = sbuf("sd_z", [P, HB], F32)
        b_log = sbuf("sd_b", [P, HB], F32)
        a_log_in = sbuf("sd_a", [P, HB], F32)
        alog = sbuf("sd_alog", [P, HEADS], F32)
        dtb = sbuf("sd_dtb", [P, HEADS], F32)
        gain = sbuf("sd_gain", [P, 1], F32)
        sq = sbuf("sd_sq", [P, 2 * HB], F32)
        root = sbuf("sd_root", [P, 2 * HB], F32)
        kq = sbuf("sd_kq", [P, HB, 2], F32)
        kq_prod = sbuf("sd_kqprod", [P, HB], F32)
        soft, soft2, eg, beta, ks, delta, o, osq, oroot = (
            sbuf("sd_" + n, [P, HB], F32) for n in "soft soft2 eg beta ks delta o osq oroot".split())
        out = sbuf("sd_out", [P, HEADS * PADS], F32)
        ps = psum("sd_ps", [P, 8, 512], F32)
        loaded, state_loaded, stored = named(sem, "sd_", "loaded state_loaded stored")
        (consts_set, squares, norms, roots, recips, k_ready, q_ready, products, dots, kqs_done, beta_done, a_ready,
         abs_done, exp_done, ln_done, rate_done, soft_done, g_ready, eg_done, ks_done, v_less, delta_done, diag_done,
         spread, scaled, state_done, o_scaled, o_delta, o_done, o_squares, o_means, o_roots, o_recips, o_gained,
         out_ready, rate_neg) = named(sem, "sd_", """consts_set squares norms roots recips k_ready q_ready products dots kqs_done
         beta_done a_ready abs_done exp_done ln_done rate_done soft_done g_ready eg_done ks_done v_less delta_done
         diag_done spread scaled state_done o_scaled o_delta o_done o_squares o_means o_roots o_recips o_gained
         out_ready rate_neg""")
        load_bias, store_bias, finish_bias, set_bias_ones, copy_bias_rows, sum_bias_rows = bias_rows(t, sbuf, ps, sem)
        block = ctx.enter_context(nc.Block())
        q, k, v = (dn[:, n * HB:(n + 1) * HB] for n in range(3))

        def by_head(tile):
            return tile[:, :].rearrange("p (h b) -> p h b", h=HEADS)

        def per_head_all(col):
            return col[:, :].rearrange("p (h o) -> p h o", o=1).broadcast_to([P, HEADS, NSAMP])

        def along(col, n):
            return col.rearrange("p (c o) -> p c o", o=1).broadcast_to([P, HB, n])

        @block.sync
        def _(sp):
            load_bias(sp)
            sp.dma_start(ident[:, :], t["consts"][:, 0:P]).then_inc(loaded, 16)
            sp.dma_start(dn[:, :].rearrange("p (n b) -> p n b", n=12), t["dn_samp"].rearrange("n p b -> p n b")).then_inc(loaded, 16)
            sp.dma_start(by_head(z), t["z"].rearrange("n p s -> p n s")[:, :, S:S + NSAMP]).then_inc(loaded, 16)
            sp.dma_start(by_head(b_log), t["ba"][0:HEADS, S:S + NSAMP].partition_broadcast(P)).then_inc(loaded, 16)
            sp.dma_start(by_head(a_log_in), t["ba"][32:32 + HEADS, S:S + NSAMP].partition_broadcast(P)).then_inc(loaded, 16)
            sp.dma_start(alog[:, :], t["a_log"].partition_broadcast(P)).then_inc(loaded, 16)
            sp.dma_start(dtb[:, :], t["dt_bias"].partition_broadcast(P)).then_inc(loaded, 16)
            sp.dma_start(gain[:, :], t["g_dn_out"]).then_inc(loaded, 16)
            for h in range(HEADS):
                sp.dma_start(state[:, h * NSAMP:(h + 1) * NSAMP, :],
                             t["state"][:, h].rearrange("b k e -> k b e")).then_inc(state_loaded, 16)
            store_bias(sp)
            sp.wait_ge(out_ready, 1)
            sp.dma_start(t["mix"].rearrange("n p s -> p n s")[:, 0:HEADS, S:TOK],
                         out[:, :].rearrange("p (h b) -> p h b", h=HEADS)).then_inc(stored, 16)
            sp.wait_ge(state_done, HB)
            for h in range(HEADS):
                sp.dma_start(t["new_state"][:, h].rearrange("b k e -> k b e"),
                             new_state[:, h * NSAMP:(h + 1) * NSAMP, :]).then_inc(stored, 16)
            sp.wait_ge(stored, 16 * (HEADS + 1))
            finish_bias(sp)

        @block.gpsimd
        def _(pool):
            pool.memset(ones[:, :], 1.0).then_inc(consts_set, 1)
            pool.memset(eps[:, :], EPS).then_inc(consts_set, 1)
            pool.memset(out[:, :], 0.0).then_inc(consts_set, 1)
            pool.wait_ge(delta_done, 1)
            pool.tensor_tensor(diag[:, :, :], ident[:, :].rearrange("p (o j) -> p o j", o=1).broadcast_to([P, HB, P]),
                               along(delta[:, :], P), ALU.mult).then_inc(diag_done, 1)

        @block.scalar
        def _(act):
            act.wait_ge(loaded, 128)
            act.wait_ge(consts_set, 3)
            act.activation(sq[:, :], dn[:, 0:2 * HB], ACT.Square).then_inc(squares, 1)
            act.wait_ge(norms, 1)
            act.activation(root[:, :], ps[:, 0, 0:2 * HB], ACT.Sqrt, bias=eps[:, 0:1]).then_inc(roots, 1)
            act.activation(beta[:, :], b_log[:, :], ACT.Sigmoid).then_inc(beta_done, 1)
            act.wait_ge(a_ready, 1)
            act.activation(soft[:, :], a_log_in[:, :], ACT.Abs).then_inc(abs_done, 1)
            act.wait_ge(abs_done, 1)
            act.activation(soft2[:, :], soft[:, :], ACT.Exp, scale=-1.0).then_inc(exp_done, 1)
            act.activation(alog[:, :], alog[:, :], ACT.Exp).then_inc(rate_done, 1)
            act.wait_ge(exp_done, 1)
            act.activation(soft[:, :], soft2[:, :], ACT.Ln, bias=1.0).then_inc(ln_done, 1)
            act.wait_ge(g_ready, 1)
            act.activation(eg[:, :], a_log_in[:, :], ACT.Exp).then_inc(eg_done, 1)
            act.wait_ge(o_done, 1)
            act.activation(osq[:, :], o[:, :], ACT.Square).then_inc(o_squares, 1)
            act.wait_ge(o_means, 1)
            act.activation(oroot[:, :], ps[:, 3, 0:HB], ACT.Sqrt, bias=eps[:, 0:1], scale=1.0 / DK).then_inc(o_roots, 1)

        @block.tensor
        def _(pe):
            sum_bias_rows(pe)
            pe.wait_ge(loaded, 128)
            pe.wait_ge(consts_set, 3)
            pe.wait_ge(squares, 1)
            pe.matmul(ps[:, 0, 0:2 * HB], ones[:, :], sq[:, :], start=True, stop=True).then_inc(norms, 1)
            pe.wait_ge(products, 1)
            pe.matmul(ps[:, 1, 0:HB], ones[:, :], kq_prod[:, :], start=True, stop=True).then_inc(dots, 1)
            pe.wait_ge(state_loaded, 16 * HEADS)
            for c in range(HB):
                m = pe.matmul(ps[:, 2, 2 * c:2 * c + 2], state[:, c, :], kq[:, c, :], start=True, stop=True)
            m.then_inc(kqs_done, 1)
            pe.wait_ge(o_squares, 1)
            pe.matmul(ps[:, 3, 0:HB], ones[:, :], osq[:, :], start=True, stop=True).then_inc(o_means, 1)
            pe.wait_ge(diag_done, 1)
            for n in range(8):
                if n >= 4:
                    pe.wait_ge(state_done, 4 * (n - 3))
                pe.matmul(ps[:, 4 + n % 4, :], ones[:, :], diag[:, 4 * n:4 * n + 4, :].rearrange("p c j -> p (c j)"),
                          start=True, stop=True).then_inc(spread, 1)

        @block.vector
        def _(dve):
            set_bias_ones(dve)
            dve.wait_ge(loaded, 128)
            dve.wait_ge(consts_set, 3)
            dve.tensor_tensor(by_head(a_log_in), by_head(a_log_in), per_head_all(dtb), ALU.add).then_inc(a_ready, 1)
            copy_bias_rows(dve)
            dve.wait_ge(roots, 1)
            dve.reciprocal(root[:, :], root[:, :]).then_inc(recips, 1)
            dve.wait_ge(recips, 1)
            dve.tensor_tensor(kq[:, :, 0], k, root[:, HB:2 * HB], ALU.mult).then_inc(k_ready, 1)
            dve.scalar_tensor_tensor(kq[:, :, 1], q, DK ** -0.5, root[:, 0:HB], ALU.mult, ALU.mult).then_inc(q_ready, 1)
            dve.wait_ge(k_ready, 1)
            dve.wait_ge(q_ready, 1)
            dve.tensor_tensor(kq_prod[:, :], kq[:, :, 0], kq[:, :, 1], ALU.mult).then_inc(products, 1)
            dve.wait_ge(rate_done, 1)
            dve.tensor_scalar(alog[:, :], alog[:, :], -1.0, None, ALU.mult).then_inc(rate_neg, 1)
            dve.wait_ge(ln_done, 1)
            dve.scalar_tensor_tensor(soft[:, :], a_log_in[:, :], 0.0, soft[:, :], ALU.max, ALU.add).then_inc(soft_done, 1)
            dve.wait_ge(soft_done, 1)
            dve.wait_ge(rate_neg, 1)
            dve.tensor_tensor(by_head(a_log_in), by_head(soft), per_head_all(alog), ALU.mult).then_inc(g_ready, 1)
            dve.wait_ge(eg_done, 1)
            dve.wait_ge(state_loaded, 16 * HEADS)
            dve.tensor_tensor(new_state[:, :, :], state[:, :, :], along(eg[:, :], P), ALU.mult).then_inc(scaled, 1)
            dve.wait_ge(kqs_done, 1)
            found = ps[:, 2, 0:2 * HB].rearrange("p (c two) -> p c two", two=2)
            dve.tensor_tensor(ks[:, :], found[:, :, 0], eg[:, :], ALU.mult).then_inc(ks_done, 1)
            dve.tensor_tensor(o[:, :], found[:, :, 1], eg[:, :], ALU.mult).then_inc(o_scaled, 1)
            dve.wait_ge(ks_done, 1)
            dve.tensor_tensor(ks[:, :], v, ks[:, :], ALU.subtract).then_inc(v_less, 1)
            dve.wait_ge(v_less, 1)
            dve.wait_ge(beta_done, 1)
            dve.tensor_tensor(delta[:, :], ks[:, :], beta[:, :], ALU.mult).then_inc(delta_done, 1)
            dve.wait_ge(delta_done, 1)
            dve.wait_ge(dots, 1)
            dve.tensor_tensor(osq[:, :], ps[:, 1, 0:HB], delta[:, :], ALU.mult).then_inc(o_delta, 1)
            dve.wait_ge(o_delta, 1)
            dve.wait_ge(o_scaled, 1)
            dve.tensor_tensor(o[:, :], o[:, :], osq[:, :], ALU.add).then_inc(o_done, 1)
            dve.wait_ge(scaled, 1)
            for c in range(HB):
                if c % 4 == 0:
                    dve.wait_ge(spread, c // 4 + 1)
                dve.scalar_tensor_tensor(new_state[:, c, :], ps[:, 4 + c // 4 % 4, c % 4 * P:(c % 4 + 1) * P],
                                         kq[:, c, 0:1], new_state[:, c, :], ALU.mult, ALU.add).then_inc(state_done, 1)
            dve.wait_ge(o_roots, 1)
            dve.reciprocal(oroot[:, :], oroot[:, :]).then_inc(o_recips, 1)
            dve.wait_ge(o_recips, 1)
            dve.scalar_tensor_tensor(o[:, :], o[:, :], gain[:, 0:1], oroot[:, :], ALU.mult, ALU.mult).then_inc(o_gained, 1)
            dve.wait_ge(o_gained, 1)
            dve.tensor_tensor(out[:, :].rearrange("p (h b) -> p h b", h=HEADS)[:, :, 0:NSAMP], by_head(o), by_head(z),
                              ALU.mult).then_inc(out_ready, 1)


def attention_samples(t, sbuf, ps, sem):
    NV = len(DILS)
    KEYS = (P, P, PAST // DILS[2])
    FIRST = (0, P, 2 * P)
    SELF = sum(KEYS)
    KC = NSAMP * AH * HD
    keys = sbuf("sa_keys", [P, NV, KC], F32)
    values = sbuf("sa_values", [P, NV, KC], F32)
    qrow = sbuf("sa_qrow", [P, KC], F32)
    diag = sbuf("sa_diag", [P, KC], F32)
    ident = sbuf("sa_ident", [P, P], F32)
    mask = sbuf("sa_mask", [P, 4 * AH], F32)
    ones = sbuf("sa_ones", [P, P], F32)
    new = sbuf("sa_new", [P, 12, NSAMP], F32)
    q_by_sample = sbuf("sa_qbs", [P, NSAMP, 4], F32)
    prod = sbuf("sa_prod", [P, 4, NSAMP], F32)
    masked = sbuf("sa_masked", [P, 4, NSAMP, AH], F32)
    rows = sbuf("sa_rows", [NSAMP, 2, AH * HD], F32)
    cols = sbuf("sa_cols", [P, NV, NBH], F32)
    bias = sbuf("sa_bias", [NBH, NV, P + 1], F32)
    s = sbuf("sa_s", [NBH, SELF + 1], F32)
    e = sbuf("sa_e", [NBH, SELF + 1], F32)
    negmax = sbuf("sa_negmax", [NBH, 1], F32)
    den = sbuf("sa_den", [NBH, 1], F32)
    w0 = sbuf("sa_w0", [NBH, 1], F32)
    diag0 = sbuf("sa_diag0", [NBH, NBH], F32)
    probs = sbuf("sa_probs", [P, NV, NBH], F32)
    own = sbuf("sa_own", [P, 4, NSAMP], F32)
    out = sbuf("sa_out", [P, 4, PADS], F32)
    (loaded, keys_loaded, values_loaded, stored) = named(sem, "sa_", "loaded keys_loaded values_loaded stored")
    (consts_set, q_sorted, diag_done, spread, spread_copied, products, masked_done, rows_turned, rows_copied,
     keys_times_q, first_times_q, cols_done, cols_turned, s_done, self_dots, max_done, e_done, den_done, recip_done, normalised,
     w0_done, diag0_done, probs_turned, probs_copied, w0_spread, pv_done, own_done, out_done) = named(sem, "sa_",
        """consts_set q_sorted diag_done spread spread_copied products masked_done rows_turned rows_copied
        keys_times_q first_times_q cols_done cols_turned s_done self_dots max_done e_done den_done recip_done normalised
        w0_done diag0_done probs_turned probs_copied w0_spread pv_done own_done out_done""")

    def gathered(cache, v):
        d = DILS[v]
        tokens = cache.rearrange("b (t d) c -> t d b c", d=d)
        n = PAST // d
        return tokens[n - KEYS[v]:n, 0]

    def load_program(sp):
        sp.dma_start(ident[:, :], t["consts"][:, 0:P]).then_inc(loaded, 16)
        sp.dma_start(mask[:, :], t["head_mask"]).then_inc(loaded, 16)
        sp.dma_start(new[:, :, :], t["at"].rearrange("n p s -> p n s")[:, :, S:S + NSAMP]).then_inc(loaded, 16)
        for b in range(NSAMP):
            sp.dma_start(bias[b * AH:(b + 1) * AH, :, :],
                         t["bias_flat"].rearrange("v h i -> h v i")[:, :, P - 1:2 * P]).then_inc(loaded, 16)

    def load_keys(sp):
        for v in range(NV):
            sp.dma_start(keys[0:KEYS[v], v, :].rearrange("p (b c) -> p b c", b=NSAMP),
                         gathered(t["cache_k"], v)).then_inc(keys_loaded, 16)

    def load_values(sp):
        for v in range(NV):
            sp.dma_start(values[0:KEYS[v], v, :].rearrange("p (b c) -> p b c", b=NSAMP),
                         gathered(t["cache_v"], v)).then_inc(values_loaded, 16)

    def store_program(sp):
        sp.wait_ge(rows_copied, 1)
        sp.dma_start(t["new_cache_k"][:, PAST - 1], rows[:, 0, :]).then_inc(stored, 16)
        sp.dma_start(t["new_cache_v"][:, PAST - 1], rows[:, 1, :]).then_inc(stored, 16)
        sp.wait_ge(out_done, 2)
        sp.dma_start(t["mix"].rearrange("n p s -> p n s")[:, HEADS:2 * HEADS, S:TOK], out[:, :, :]).then_inc(stored, 16)
        sp.wait_ge(stored, 48)

    def gpsimd_start(pool):
        pool.memset(ones[:, :], 1.0).then_inc(consts_set, 1)
        pool.memset(out[:, :, :], 0.0).then_inc(consts_set, 1)

    def scalar_start(act):
        for b in range(NSAMP):
            act.wait_ge(spread, b + 1)
            act.activation(qrow[:, b * 512:(b + 1) * 512], ps[:, b, :], ACT.Copy).then_inc(spread_copied, 1)

    def scalar_program(act):
        act.wait_ge(rows_turned, 1)
        act.activation(rows[:, :, :], ps[0:NSAMP, 0:2, :], ACT.Copy).then_inc(rows_copied, 1)
        act.wait_ge(max_done, 1)
        act.activation(e[:, :], s[:, :], ACT.Exp, bias=negmax[:, 0:1], accum_out=den[:, 0:1]).then_inc(e_done, 1)
        act.wait_ge(probs_turned, 1)
        for v in range(NV):
            m = act.activation(probs[0:KEYS[v], v, :], ps[0:KEYS[v], 4, v * NBH:(v + 1) * NBH], ACT.Copy)
        m.then_inc(probs_copied, 1)

    def tensor_start(pe):
        pe.wait_ge(loaded, 176)
        pe.wait_ge(consts_set, 2)
        pe.wait_ge(diag_done, 1)
        for b in range(NSAMP):
            pe.matmul(ps[:, b, :], ones[:, :], diag[:, b * 512:(b + 1) * 512], start=True, stop=True).then_inc(spread, 1)
        pe.wait_ge(spread_copied, NSAMP)

    def tensor_program(pe):
        for n in range(8):
            m = pe.transpose(ps[0:NSAMP, n // 4, n % 4 * P:(n % 4 + 1) * P], new[:, 4 + n, :], ident[:, :])
        m.then_inc(rows_turned, 1)
        pe.wait_ge(masked_done, 1)
        for n in range(4):
            m = pe.matmul(ps[0:NBH, 2, 0:2], masked[:, n, :, :].rearrange("p b h -> p (b h)"), ones[:, 0:2],
                          start=n == 0, stop=n == 3)
        m.then_inc(self_dots, 1)
        for n, v in enumerate((1, 2, 0)):
            pe.wait_ge(cols_done, n + 1)
            pe.transpose(ps[0:NBH, 3, FIRST[v]:FIRST[v] + KEYS[v]], cols[0:KEYS[v], v, :],
                         ident[0:KEYS[v], 0:KEYS[v]]).then_inc(cols_turned, 1)
        pe.wait_ge(normalised, 1)
        for v in range(NV):
            m = pe.transpose(ps[0:KEYS[v], 4, v * NBH:(v + 1) * NBH], e[:, FIRST[v]:FIRST[v] + KEYS[v]], ident[0:NBH, 0:NBH])
        m.then_inc(probs_turned, 1)
        pe.wait_ge(diag0_done, 1)
        pe.matmul(ps[:, 5, 0:NBH], ones[0:NBH, :], diag0[:, :], start=True, stop=True).then_inc(w0_spread, 1)
        pe.wait_ge(probs_copied, 1)
        pe.wait_ge(values_loaded, 16 * NV)
        for b in range(NSAMP):
            for n in range(4):
                for v in range(NV):
                    c = b * 512 + n * P
                    m = pe.matmul(ps[:, 6, b * AH + 2 * n:b * AH + 2 * n + 2], values[0:KEYS[v], v, c:c + P],
                                  probs[0:KEYS[v], v, b * AH + 2 * n:b * AH + 2 * n + 2], start=v == 0, stop=v == NV - 1)
        m.then_inc(pv_done, 1)

    def vector_start(dve):
        dve.wait_ge(loaded, 176)
        dve.wait_ge(consts_set, 2)
        dve.tensor_copy(q_by_sample[:, :, :], new[:, 0:4, :].rearrange("p n b -> p b n")).then_inc(q_sorted, 1)
        dve.wait_ge(q_sorted, 1)
        qcols = q_by_sample[:, :, :].rearrange("p b n -> p (b n)").rearrange("p (c o) -> p c o", o=1)
        dve.tensor_tensor(diag[:, :].rearrange("p (c j) -> p c j", j=P),
                          ident[:, :].rearrange("p (o j) -> p o j", o=1).broadcast_to([P, 4 * NSAMP, P]),
                          qcols.broadcast_to([P, 4 * NSAMP, P]), ALU.mult).then_inc(diag_done, 1)
        dve.tensor_tensor(prod[:, :, :], new[:, 0:4, :], new[:, 4:8, :], ALU.mult).then_inc(products, 1)
        dve.wait_ge(products, 1)
        for n in range(4):
            m = dve.tensor_tensor(masked[:, n, :, :],
                                  prod[:, n, :].rearrange("p (b o) -> p b o", o=1).broadcast_to([P, NSAMP, AH]),
                                  mask[:, n * AH:(n + 1) * AH].rearrange("p (o h) -> p o h", o=1).broadcast_to([P, NSAMP, AH]),
                                  ALU.mult)
        m.then_inc(masked_done, 1)

    def times_q(engine, v):
        kv = keys[0:KEYS[v], v, :]
        return engine.tensor_tensor(kv, kv, qrow[0:KEYS[v], :], ALU.mult)

    def gpsimd_program(pool):
        pool.wait_ge(spread_copied, NSAMP)
        pool.wait_ge(keys_loaded, 16 * NV)
        times_q(pool, 0).then_inc(first_times_q, 1)

    def vector_program(dve):
        dve.wait_ge(spread_copied, NSAMP)
        dve.wait_ge(keys_loaded, 16 * NV)
        for v in (1, 2, 0):
            kv = keys[0:KEYS[v], v, :]
            if v:
                times_q(dve, v).then_inc(keys_times_q, 1)
                dve.wait_ge(keys_times_q, v)
            else:
                dve.wait_ge(first_times_q, 1)
            dve.tensor_reduce(cols[0:KEYS[v], v, :], kv.rearrange("p (c e) -> p c e", e=HD), AX_X, ALU.add).then_inc(cols_done, 1)
        dve.wait_ge(self_dots, 1)
        dve.wait_ge(cols_turned, NV)
        for v in range(NV):
            dve.scalar_tensor_tensor(s[:, FIRST[v]:FIRST[v] + KEYS[v]], ps[0:NBH, 3, FIRST[v]:FIRST[v] + KEYS[v]],
                                     HD ** -0.5, bias[:, v, P - KEYS[v]:P], ALU.mult, ALU.add).then_inc(s_done, 1)
        dve.scalar_tensor_tensor(s[:, SELF:SELF + 1], ps[0:NBH, 2, 0:1], HD ** -0.5, bias[:, 0, P:P + 1],
                                 ALU.mult, ALU.add).then_inc(s_done, 1)
        dve.wait_ge(s_done, NV + 1)
        dve.tensor_reduce(negmax[:, :], s[:, :], AX_X, ALU.max, negate=True).then_inc(max_done, 1)
        dve.wait_ge(e_done, 1)
        dve.scalar_tensor_tensor(den[:, :], e[:, SELF:SELF + 1], NV - 1.0, den[:, :], ALU.mult, ALU.add).then_inc(den_done, 1)
        dve.wait_ge(den_done, 1)
        dve.reciprocal(den[:, :], den[:, :]).then_inc(recip_done, 1)
        dve.wait_ge(recip_done, 1)
        dve.tensor_scalar(e[:, :], e[:, :], den[:, 0:1], None, ALU.mult).then_inc(normalised, 1)
        dve.wait_ge(normalised, 1)
        dve.tensor_scalar(w0[:, :], e[:, SELF:SELF + 1], float(NV), None, ALU.mult).then_inc(w0_done, 1)
        dve.wait_ge(w0_done, 1)
        dve.tensor_scalar(diag0[:, :], ident[0:NBH, 0:NBH], w0[:, 0:1], None, ALU.mult).then_inc(diag0_done, 1)
        dve.wait_ge(w0_spread, 1)

        def of_head(bank, half):
            return ps[half * HD:(half + 1) * HD, bank, 0:NBH].rearrange("p (b n two) -> p n b two", b=NSAMP, two=2)[:, :, :, half]

        for half in range(2):
            rows_ = slice(half * HD, (half + 1) * HD)
            m = dve.tensor_tensor(own[rows_, :, :], new[rows_, 8:12, :], of_head(5, half), ALU.mult)
        m.then_inc(own_done, 1)
        dve.wait_ge(own_done, 1)
        dve.wait_ge(pv_done, 1)
        for half in range(2):
            rows_ = slice(half * HD, (half + 1) * HD)
            dve.tensor_tensor(out[rows_, :, 0:NSAMP], own[rows_, :, :], of_head(6, half), ALU.add).then_inc(out_done, 1)

    starts = (gpsimd_start, scalar_start, tensor_start, vector_start)
    return load_program, load_keys, load_values, store_program, starts, (gpsimd_program, scalar_program, tensor_program, vector_program)


def merge_and_attend_samples(nc, t):
    with ExitStack() as ctx:
        sbuf, psum, sem = allocators(nc, ctx)
        NV = len(DILS)
        NP = QB // 2
        u = sbuf("pm_u", [P, 2, 2, NV, UROW], F32)
        wt = sbuf("pm_wt", [P, 2, 2, NV, AH], F32)
        negmax = sbuf("pm_negmax", [P, 2, AH], F32)
        parts = sbuf("pm_parts", [P, 2, NV, AH], F32)
        total = sbuf("pm_total", [P, 2, AH], F32)
        out = sbuf("pm_out", [P, 2, 4, 2 * P], F32)
        ident = sbuf("pm_ident", [P, P], F32)
        ps = psum("pm_ps", [P, 8, 512], F32)
        loaded = [sem(f"pm_loaded{n}") for n in range(2)]
        stored = [sem(f"pm_stored{n}") for n in range(2)]
        (const_loaded, max_steps, w_ready, w_exp, parts_done, total_done, recip_done, weights_done, scaled01, scaled2,
         turned, copied) = named(sem, "pm_", """const_loaded max_steps w_ready w_exp parts_done total_done recip_done
            weights_done scaled01 scaled2 turned copied""")
        load_samples, load_keys, load_values, store_samples, starts, programs = attention_samples(t, sbuf, ps, sem)
        start_pool, start_act, start_pe, start_dve = starts
        pool_samples, act_samples, pe_samples, dve_samples = programs
        block = ctx.enter_context(nc.Block())

        def maxima(par, tile):
            return u[:, par, tile, :, AH * HD:AH * HD + AH]

        def denominators(par, tile):
            return u[:, par, tile, :, AH * HD + AH:UROW]

        def scale(engine, par, tile, v):
            rows = u[:, par, tile, v, 0:AH * HD].rearrange("p (h e) -> p h e", h=AH)
            w = wt[:, par, tile, v, :].rearrange("p (h o) -> p h o", o=1).broadcast_to([P, AH, HD])
            return engine.tensor_tensor(rows, rows, w, ALU.mult)

        @block.sync
        def _(sp):
            sp.dma_start(ident[:, :], t["consts"][:, 0:P]).then_inc(const_loaded, 16)

            def load(i, par):
                for tile in range(2):
                    for v, d in enumerate(DILS):
                        n = P // d
                        src = t["U"][v].rearrange("(r m) c -> m r c", r=d)[bass.ds(i * (2 * n) + tile * n, n)]
                        sp.dma_start(u[:, par, tile, v, :], src).then_inc(loaded[par], 16)

            def step(i, par, more=True):
                if more:
                    sp.wait_ge(turned, i + 1)
                    load(i + 2, par)
                sp.wait_ge(copied, i + 1)
                sp.dma_start(t["mix"].rearrange("n p s -> p n s")[:, HEADS:2 * HEADS, bass.ds(i * (2 * P), 2 * P)],
                             out[:, par, :, :]).then_inc(stored[par], 16)

            load_samples(sp)
            load(0, 0)
            load(1, 1)
            load_keys(sp)
            for_pairs(sp, NP - 2, step)
            load_values(sp)
            step(NP - 2, 0, False)
            step(NP - 1, 1, False)
            for par in range(2):
                sp.wait_ge(stored[par], 16 * NP // 2)
            store_samples(sp)

        @block.vector
        def _(dve):
            def step(i, par):
                dve.wait_ge(loaded[par], landed(i, par, 2 * NV))
                for tile in range(2):
                    nm = maxima(par, tile)
                    m = dve.tensor_tensor(negmax[:, tile, :], nm[:, 0, :], nm[:, 1, :], ALU.min)
                m.then_inc(max_steps, 1)
                dve.wait_ge(max_steps, i * 2 + 1)
                for tile in range(2):
                    m = dve.tensor_tensor(negmax[:, tile, :], negmax[:, tile, :], maxima(par, tile)[:, 2, :], ALU.min)
                m.then_inc(max_steps, 1)
                dve.wait_ge(max_steps, i * 2 + 2)
                for tile in range(2):
                    m = dve.tensor_tensor(wt[:, par, tile], negmax[:, tile:tile + 1, :].broadcast_to([P, NV, AH]),
                                          maxima(par, tile), ALU.subtract)
                m.then_inc(w_ready, 1)
                dve.wait_ge(w_exp, i + 1)
                for tile in range(2):
                    m = dve.tensor_tensor(parts[:, tile], wt[:, par, tile], denominators(par, tile), ALU.mult)
                m.then_inc(parts_done, 1)
                dve.wait_ge(parts_done, i + 1)
                for tile in range(2):
                    m = dve.tensor_reduce(total[:, tile, :], parts[:, tile].rearrange("p v h -> p h v"), AX_X, ALU.add)
                m.then_inc(total_done, 1)
                dve.wait_ge(total_done, i + 1)
                dve.reciprocal(total[:, :, :], total[:, :, :]).then_inc(recip_done, 1)
                dve.wait_ge(recip_done, i + 1)
                for tile in range(2):
                    m = dve.tensor_tensor(wt[:, par, tile], wt[:, par, tile],
                                          total[:, tile:tile + 1, :].broadcast_to([P, NV, AH]), ALU.mult)
                m.then_inc(weights_done, 1)
                dve.wait_ge(weights_done, i + 1)
                for tile in range(2):
                    for v in range(2):
                        m = scale(dve, par, tile, v)
                m.then_inc(scaled01, 1)

            start_dve(dve)
            for_pairs(dve, NP, step)
            dve_samples(dve)

        @block.gpsimd
        def _(pool):
            def step(i, par):
                pool.wait_ge(weights_done, i + 1)
                scale(pool, par, 0, 2)
                scale(pool, par, 1, 2).then_inc(scaled2, 1)

            start_pool(pool)
            for_pairs(pool, NP, step)
            pool_samples(pool)

        @block.tensor
        def _(pe):
            pe.wait_ge(const_loaded, 16)

            def step(i, par):
                pe.wait_ge(scaled01, i + 1)
                pe.wait_ge(scaled2, i + 1)
                for tile in range(2):
                    for n in range(4):
                        for v in range(NV):
                            m = pe.matmul(ps[:, 2 * par + tile, n * P:(n + 1) * P], u[:, par, tile, v, n * P:(n + 1) * P],
                                          ident[:, :], start=v == 0, stop=v == NV - 1)
                m.then_inc(turned, 1)

            start_pe(pe)
            for_pairs(pe, NP, step)
            pe.wait_ge(copied, NP)
            pe_samples(pe)

        @block.scalar
        def _(act):
            def take(i, par, first=False):
                act.wait_ge(turned, i + 1)
                if not first:
                    act.wait_ge(stored[par], i * 8 - par * 8)
                for tile in range(2):
                    m = act.activation(out[:, par, :, tile * P:(tile + 1) * P],
                                       ps[:, 2 * par + tile, :].rearrange("p (n s) -> p n s", n=4), ACT.Copy)
                m.then_inc(copied, 1)

            def exponents(i, par):
                act.wait_ge(w_ready, i + 1)
                act.activation(wt[:, par], wt[:, par], ACT.Exp).then_inc(w_exp, 1)

            start_act(act)
            exponents(0, 0)
            exponents(1, 1)
            take(0, 0, True)
            exponents(2, 0)
            take(1, 1, True)
            with act.Fori(1, NP // 2 - 1) as j:
                exponents(2 * j + 1, 1)
                take(2 * j, 0)
                exponents(2 * j + 2, 0)
                take(2 * j + 1, 1)
            exponents(NP - 1, 1)
            take(NP - 2, 0)
            take(NP - 1, 1)
            act_samples(act)


def blocks(engine, step):
    step(0, 0, True)
    with engine.Fori(1, (NB + 1) // 2) as j:
        step(2 * j - 1, 1, False)
        step(2 * j, 0, False)


def output_projection(nc, t):
    with ExitStack() as ctx:
        sbuf, psum, sem = allocators(nc, ctx)
        w_raw = sbuf("pc_w", [P, 2, KD * P], F32)
        w_hi = sbuf("pc_whi", [P, KD, KD * P], F32R)
        w_lo = sbuf("pc_wlo", [P, KD, KD * P], F32R)
        mix = sbuf("pc_mix", [P, KD, TB], F32)
        mix_hi = sbuf("pc_mixhi", [P, 2, KD, TB], F32R)
        mix_lo = sbuf("pc_mixlo", [P, 2, KD, TB], F32R)
        x = sbuf("pc_x", [P, 2, KD, TB], F32)
        out = sbuf("pc_out", [P, 2, KD, TB], F32)
        sq = sbuf("pc_sq", [P, KD, TB], F32)
        ssum = sbuf("pc_ssum", [P, TB], F32)
        rstd = sbuf("pc_rstd", [P, TB], F32)
        gains = sbuf("pc_gains", [P, 2, KD], F32)
        eps = sbuf("pc_eps", [P, 1], F32)
        ones_mean = sbuf("pc_ones", [P, P], F32)
        prod_ps = psum("pc_prod", [P, 7, 512], F32)
        mean_ps = psum("pc_mean", [P, 512], F32)
        gains_loaded = sem("pc_gains_loaded")
        consts_set = sem("pc_consts_set")
        w_loaded = (sem("pc_w_loaded0"), sem("pc_w_loaded1"))
        w_hi_done = sem("pc_w_hi_done")
        w_lo_done = sem("pc_w_lo_done")
        mix_loaded = sem("pc_mix_loaded")
        mix_hi_done = sem("pc_mix_hi_done")
        mix_lo_done = sem("pc_mix_lo_done")
        x_loaded = (sem("pc_x_loaded0"), sem("pc_x_loaded1"))
        prod_done = sem("pc_prod_done")
        bank_read = sem("pc_bank_read")
        squares_done = sem("pc_squares_done")
        sums_done = sem("pc_sums_done")
        means_done = sem("pc_means_done")
        roots_done = sem("pc_roots_done")
        recips_done = sem("pc_recips_done")
        scaled_done = sem("pc_scaled_done")
        x1_done = sem("pc_x1_done")
        h2_done = sem("pc_h2_done")
        stored = (sem("pc_stored0"), sem("pc_stored1"))
        block = ctx.enter_context(nc.Block())

        @block.sync
        def _(sp):
            sp.dma_start(gains[:, 0, :], t["g_post_mix"]).then_inc(gains_loaded, 16)
            sp.dma_start(gains[:, 1, :], t["g_pre_ffn"]).then_inc(gains_loaded, 16)

            def load_w(j, par):
                if not isinstance(j, int):
                    sp.wait_ge(w_lo_done, j - 1)
                sp.dma_start(w_raw[:, par, :], t["w_out"][j]).then_inc(w_loaded[par], 16)

            def load_mix(b):
                sp.wait_ge(mix_lo_done, b)
                sp.dma_start(mix[:, :, :], t["mix"].rearrange("k p t -> p k t")[:, :, bass.ds(b * TB, TB)]
                             ).then_inc(mix_loaded, 16)

            def load_x(b, par):
                sp.dma_start(x[:, par], t["xT"][b]).then_inc(x_loaded[par], 16)

            load_mix(0)
            load_w(0, 0)
            load_w(1, 1)
            with sp.Fori(1, KD // 2) as j:
                load_w(2 * j, 0)
                load_w(2 * j + 1, 1)
            load_x(0, 0)
            load_mix(1)
            load_x(1, 1)

            def finish(b, par):
                sp.wait_ge(x1_done, b + 1)
                sp.dma_start(t["x1"][b], x[:, par]).then_inc(stored[par], 16)
                sp.wait_ge(h2_done, b + 1)
                sp.dma_start(t["h2"][b], out[:, par]).then_inc(stored[par], 16)

            def block_io(b, par):
                load_mix(b + 2)
                finish(b, par)
                sp.wait_ge(stored[par], landed(b, par, 2))
                load_x(b + 2, par)

            for b in range(NB - 2):
                block_io(b, b % 2)
            for b in range(NB - 2, NB):
                finish(b, b % 2)
            for par in range(2):
                sp.wait_ge(stored[par], 32 * ((NB + 1 - par) // 2))

        @block.gpsimd
        def _(pool):
            pool.memset(ones_mean[:, :], 1.0 / D).then_inc(consts_set, 1)
            pool.memset(eps[:, :], EPS).then_inc(consts_set, 1)

            def split_mix(b, par, first):
                pool.wait_ge(mix_hi_done, b + 1)
                pool.tensor_tensor(mix_lo[:, par], mix[:, :, :], mix_hi[:, par].bitcast(F32),
                                   ALU.subtract).then_inc(mix_lo_done, 1)

            def split_w(j, par):
                pool.wait_ge(w_hi_done, j + 1)
                pool.tensor_tensor(w_lo[:, bass.ds(j, 1), :], w_raw[:, par:par + 1, :],
                                   w_hi[:, bass.ds(j, 1), :].bitcast(F32), ALU.subtract).then_inc(w_lo_done, 1)

            split_mix(0, 0, True)
            for_pairs(pool, KD, split_w)
            with pool.Fori(1, (NB + 1) // 2) as j:
                split_mix(2 * j - 1, 1, False)
                split_mix(2 * j, 0, False)

        @block.scalar
        def _(act):
            act.wait_ge(consts_set, 2)

            def split_mix(b, par):
                act.wait_ge(mix_loaded, 16 * b + 16)
                if not isinstance(b, int):
                    act.wait_ge(prod_done, b * KD - KD)
                act.activation(mix_hi[:, par], mix[:, :, :], ACT.Copy).then_inc(mix_hi_done, 1)

            def split_w(j, par):
                act.wait_ge(w_loaded[par], landed(j, par))
                act.activation(w_hi[:, bass.ds(j, 1), :], w_raw[:, par:par + 1, :], ACT.Copy).then_inc(w_hi_done, 1)

            split_mix(0, 0)
            for_pairs(act, KD, split_w)

            def block_work(b, par):
                if not isinstance(b, int):
                    act.wait_ge(stored[par], landed(b, par, 2) - 32)
                for j in range(KD):
                    act.wait_ge(prod_done, b * KD + (j + 1))
                    act.activation(out[:, par, j, :], prod_ps[:, j % 7, 0:TB], ACT.Copy).then_inc(bank_read, 1)
                act.wait_ge(bank_read, b * KD + KD)
                act.activation(sq[:, :, :], out[:, par], ACT.Square).then_inc(squares_done, 1)
                act.wait_ge(means_done, 2 * b + 1)
                act.activation(ssum[:, :], mean_ps[:, 0:TB], ACT.Sqrt, bias=eps[:, 0:1]).then_inc(roots_done, 1)
                act.wait_ge(x1_done, b + 1)
                act.activation(sq[:, :, :], x[:, par], ACT.Square).then_inc(squares_done, 1)
                act.wait_ge(means_done, 2 * b + 2)
                act.activation(ssum[:, :], mean_ps[:, 0:TB], ACT.Sqrt, bias=eps[:, 0:1]).then_inc(roots_done, 1)

            split_mix(1, 1)
            block_work(0, 0)
            with act.Fori(1, NB // 2) as j:
                split_mix(2 * j, 0)
                block_work(2 * j - 1, 1)
                split_mix(2 * j + 1, 1)
                block_work(2 * j, 0)
            split_mix(NB - 1, 0)
            act.wait_ge(stored[1], 32)
            block_work(NB - 2, 1)
            act.wait_ge(stored[0], 64)
            block_work(NB - 1, 0)

        @block.tensor
        def _(pe):
            pe.wait_ge(consts_set, 2)

            def mean(n):
                pe.wait_ge(sums_done, n + 1)
                pe.matmul(mean_ps[:, 0:TB], ones_mean[:, :], ssum[:, :], start=True, stop=True).then_inc(means_done, 1)

            def block_products(b, par, first):
                pe.wait_ge(mix_lo_done, b + 1)
                for j in range(KD):
                    if first:
                        pe.wait_ge(w_lo_done, j + 1)
                    if not first and j == 2:
                        mean(2 * b - 2)
                    if not first and j == 7:
                        mean(2 * b - 1)
                    if j == 7:
                        pe.wait_ge(bank_read, b * KD + 1)
                    elif not first:
                        pe.wait_ge(bank_read, b * KD + (j - 7 if j else 0))
                    for k in range(KD):
                        w = slice(k * P, (k + 1) * P)
                        mm = hi_lo_products(pe, prod_ps[:, j % 7, 0:TB], w_hi[:, j, w], w_lo[:, j, w],
                                            mix_hi[:, par, k, :], mix_lo[:, par, k, :], k == 0, k == KD - 1)
                    mm.then_inc(prod_done, 1)

            blocks(pe, block_products)
            mean(2 * NB - 2)
            mean(2 * NB - 1)

        @block.vector
        def _(dve):
            dve.wait_ge(gains_loaded, 32)

            def rms(n):
                dve.wait_ge(squares_done, n + 1)
                dve.tensor_reduce(ssum[:, :], sq[:, :, :].rearrange("p k t -> p t k"), AX_X, ALU.add).then_inc(sums_done, 1)
                dve.wait_ge(roots_done, n + 1)
                dve.reciprocal(rstd[:, :], ssum[:, :]).then_inc(recips_done, 1)
                dve.wait_ge(recips_done, n + 1)

            def norms(b, par, first):
                rms(2 * b)
                for k in range(KD):
                    m = dve.scalar_tensor_tensor(out[:, par, k, :], out[:, par, k, :], gains[:, 0, k:k + 1],
                                                 rstd[:, :], ALU.mult, ALU.mult)
                m.then_inc(scaled_done, 1)
                dve.wait_ge(x_loaded[par], landed(b, par))
                dve.wait_ge(scaled_done, b + 1)
                dve.tensor_tensor(x[:, par], x[:, par], out[:, par], ALU.add).then_inc(x1_done, 1)
                rms(2 * b + 1)
                for k in range(KD):
                    m = dve.scalar_tensor_tensor(out[:, par, k, :], x[:, par, k, :], gains[:, 1, k:k + 1],
                                                 rstd[:, :], ALU.mult, ALU.mult)
                m.then_inc(h2_done, 1)

            blocks(dve, norms)


def wait_at_least(engine, semaphore, value):
    if not isinstance(value, int) or value > 0:
        engine.wait_ge(semaphore, value)


def gate_and_up(nc, t, shifted):
    with ExitStack() as ctx:
        sbuf, psum, sem = allocators(nc, ctx)
        h_hi = sbuf("pd_h_hi", [P, KD, TOK], F32R)
        h_lo = sbuf("pd_h_lo", [P, KD, TOK], F32R)
        h_raw = sbuf("pd_h", [P, 2, KD, TB], F32)
        w_raw = sbuf("pd_w", [P, 2, KD * P], F32)
        w_hi = sbuf("pd_whi", [P, 2, KD * P], F32R)
        w_lo = sbuf("pd_wlo", [P, 2, KD * P], F32R)
        gate = sbuf("pd_gate", [P, TOK], F32)
        act_row = sbuf("pd_act", [P, TOK], F32)
        prod_ps = psum("pd_prod", [P, NB, 512], F32)
        h_loaded = (sem("pd_h_loaded0"), sem("pd_h_loaded1"))
        h_hi_done = sem("pd_h_hi_done")
        h_lo_done = sem("pd_h_lo_done")
        w_loaded = (sem("pd_w_loaded0"), sem("pd_w_loaded1"))
        w_hi_done = sem("pd_w_hi_done")
        w_lo_done = sem("pd_w_lo_done")
        prod_done = sem("pd_prod_done")
        gates_done = sem("pd_gates_done")
        acts_done = sem("pd_acts_done")
        stored = sem("pd_stored")
        block = ctx.enter_context(nc.Block())

        @block.sync
        def _(sp):
            def load_w(c, par):
                sp.dma_start(w_raw[:, par, :], t["w_gate_up"][c]).then_inc(w_loaded[par], 16)

            load_w(0, 0)
            for b in range(NB):
                if b >= 2:
                    sp.wait_ge(h_lo_done, b - 1)
                sp.dma_start(h_raw[:, b % 2], t["h2"][b]).then_inc(h_loaded[b % 2], 16)
            load_w(1, 1)

            def hidden_tile(j, more):
                if more:
                    sp.wait_ge(w_lo_done, 2 * j + 1)
                    load_w(2 * j + 2, 0)
                    sp.wait_ge(w_lo_done, 2 * j + 2)
                    load_w(2 * j + 3, 1)
                sp.wait_ge(acts_done, j * NB + NB)
                sp.dma_start(t["a"][j], act_row[:, :]).then_inc(stored, 16)

            with sp.Fori(0, NSAMP) as j:
                hidden_tile(j, True)
                for new, old in (("new_cache_k", "cache_k"), ("new_cache_v", "cache_v")):
                    sp.dma_start(t[new][bass.ds(j, 1), 0:PAST - 1], t[old][bass.ds(j, 1), 1:PAST]).then_inc(shifted, 16)
            with sp.Fori(NSAMP, KF - 1) as j:
                hidden_tile(j, True)
            hidden_tile(KF - 1, False)
            sp.wait_ge(stored, 16 * KF)

        @block.gpsimd
        def _(pool):
            def split_lo(c, par):
                pool.wait_ge(w_hi_done, c + 1)
                pool.tensor_tensor(w_lo[:, par, :], w_raw[:, par, :], w_hi[:, par, :].bitcast(F32),
                                   ALU.subtract).then_inc(w_lo_done, 1)

            split_lo(0, 0)
            split_lo(1, 1)
            with pool.Fori(1, KF) as j:
                split_lo(2 * j, 0)
                split_lo(2 * j + 1, 1)

        @block.scalar
        def _(act):
            def split_hi(c, par):
                act.wait_ge(w_loaded[par], landed(c, par))
                if not isinstance(c, int) or c >= 2:
                    act.wait_ge(prod_done, (c - 1) * NB)
                act.activation(w_hi[:, par, :], w_raw[:, par, :], ACT.Copy).then_inc(w_hi_done, 1)

            split_hi(0, 0)
            for b in range(NB):
                act.wait_ge(h_loaded[b % 2], 16 * (b // 2 + 1))
                act.activation(h_hi[:, :, b * TB:(b + 1) * TB], h_raw[:, b % 2], ACT.Copy).then_inc(h_hi_done, 1)
            split_hi(1, 1)

            def hidden_tile(j, more):
                wait_at_least(act, acts_done, j * NB)
                for b in range(NB):
                    act.wait_ge(prod_done, j * (2 * NB) + (b + 1))
                    act.activation(gate[:, b * TB:(b + 1) * TB], prod_ps[:, b, 0:TB], ACT.Silu).then_inc(gates_done, 1)
                if more:
                    split_hi(2 * j + 2, 0)
                    split_hi(2 * j + 3, 1)

            hidden_tile(0, True)
            with act.Fori(1, KF - 1) as j:
                hidden_tile(j, True)
            hidden_tile(KF - 1, False)

        @block.tensor
        def _(pe):
            def project(c, par, read, count, waited):
                pe.wait_ge(w_lo_done, c + 1)
                for b in range(NB):
                    if waited:
                        pe.wait_ge(read, count + (b + 1))
                    else:
                        pe.wait_ge(h_lo_done, b + 1)
                    cols = slice(b * TB, (b + 1) * TB)
                    for k in range(KD):
                        w = slice(k * P, (k + 1) * P)
                        mm = hi_lo_products(pe, prod_ps[:, b, 0:TB], w_hi[:, par, w], w_lo[:, par, w],
                                            h_hi[:, k, cols], h_lo[:, k, cols], k == 0, k == KD - 1)
                    mm.then_inc(prod_done, 1)

            project(0, 0, None, 0, False)
            project(1, 1, gates_done, 0, True)
            with pe.Fori(1, KF) as j:
                project(2 * j, 0, acts_done, j * NB - NB, True)
                project(2 * j + 1, 1, gates_done, j * NB, True)

        @block.vector
        def _(dve):
            for b in range(NB):
                cols = slice(b * TB, (b + 1) * TB)
                dve.wait_ge(h_hi_done, b + 1)
                dve.tensor_tensor(h_lo[:, :, cols], h_raw[:, b % 2], h_hi[:, :, cols].bitcast(F32),
                                  ALU.subtract).then_inc(h_lo_done, 1)

            def hidden_tile(j):
                wait_at_least(dve, stored, j * 16)
                for b in range(NB):
                    cols = slice(b * TB, (b + 1) * TB)
                    dve.wait_ge(prod_done, j * (2 * NB) + (NB + b + 1))
                    dve.wait_ge(gates_done, j * NB + (b + 1))
                    dve.tensor_tensor(act_row[:, cols], prod_ps[:, b, 0:TB], gate[:, cols],
                                      ALU.mult).then_inc(acts_done, 1)

            hidden_tile(0)
            with dve.Fori(1, KF) as j:
                hidden_tile(j)


KH = KF // 2


def down_projection(nc, t):
    with ExitStack() as ctx:
        sbuf, psum, sem = allocators(nc, ctx)
        a_raw = sbuf("pe_a", [P, KF, TB], F32)
        a_hi = sbuf("pe_ahi", [P, KF, TB], F32R)
        a_lo = sbuf("pe_alo", [P, KF, TB], F32R)
        w_raw = sbuf("pe_w", [P, 2, KH * P], F32)
        w_hi = sbuf("pe_whi", [P, 4, KH * P], F32R)
        w_lo = sbuf("pe_wlo", [P, 4, KH * P], F32R)
        x = sbuf("pe_x", [P, KD, TB], F32)
        out = sbuf("pe_out", [P, KD, TB], F32)
        sq = sbuf("pe_sq", [P, KD, TB], F32)
        ssum = sbuf("pe_ssum", [P, TB], F32)
        rstd = sbuf("pe_rstd", [P, TB], F32)
        gain = sbuf("pe_gain", [P, KD], F32)
        eps = sbuf("pe_eps", [P, 1], F32)
        ones_mean = sbuf("pe_ones", [P, P], F32)
        prod_ps = psum("pe_prod", [P, 4, 512], F32)
        mean_ps = psum("pe_mean", [P, 512], F32)
        gain_loaded = sem("pe_gain_loaded")
        consts_set = sem("pe_consts_set")
        a_loaded = sem("pe_a_loaded")
        a_hi_done = sem("pe_a_hi_done")
        a_lo_done = sem("pe_a_lo_done")
        a_read = sem("pe_a_read")
        w_loaded = (sem("pe_w_loaded0"), sem("pe_w_loaded1"))
        w_hi_done = sem("pe_w_hi_done")
        w_lo_done = sem("pe_w_lo_done")
        w_half_read = sem("pe_w_half_read")
        x_loaded = sem("pe_x_loaded")
        prod_done = sem("pe_prod_done")
        bank_read = sem("pe_bank_read")
        squares_done = sem("pe_squares_done")
        sums_done = sem("pe_sums_done")
        means_done = sem("pe_means_done")
        roots_done = sem("pe_roots_done")
        recips_done = sem("pe_recips_done")
        scaled_done = sem("pe_scaled_done")
        x2_done = sem("pe_x2_done")
        stored = sem("pe_stored")
        block = ctx.enter_context(nc.Block())

        @block.sync
        def _(sp):
            sp.dma_start(gain[:, :], t["g_post_ffn"]).then_inc(gain_loaded, 16)

            def load_w(n, half, j):
                wait_at_least(sp, w_lo_done, 2 * n + (half - 1))
                sp.dma_start(w_raw[:, half, :], t["w_down"][j][:, half * KH * P:(half + 1) * KH * P]
                             ).then_inc(w_loaded[half], 16)

            def load_a(b):
                wait_at_least(sp, a_lo_done, b * KH)
                sp.dma_start(a_raw[:, :, :], t["a"].rearrange("k p t -> p k t")[:, :, bass.ds(b * TB, TB)]
                             ).then_inc(a_loaded, 16)

            def store_x2(b):
                sp.wait_ge(x2_done, b + 1)
                sp.dma_start(t["x2"][b], x[:, :, :]).then_inc(stored, 16)

            def block_io(b, more):
                for j in range(KD if more else KD - 1):
                    load_w(b * KD + (j + 1), 0, (j + 1) % KD)
                    load_w(b * KD + (j + 1), 1, (j + 1) % KD)
                    if j == 1 and more:
                        load_a(b + 1)
                    if j == 4:
                        if not isinstance(b, int) or b:
                            store_x2(b - 1)
                            sp.wait_ge(stored, b * 16)
                        sp.dma_start(x[:, :, :], t["x1"][b]).then_inc(x_loaded, 16)

            load_w(0, 0, 0)
            load_w(0, 1, 0)
            load_a(0)
            block_io(0, True)
            with sp.Fori(1, NB - 1) as b:
                block_io(b, True)
            block_io(NB - 1, False)
            store_x2(NB - 1)
            sp.wait_ge(stored, 16 * NB)

        @block.gpsimd
        def _(pool):
            pool.memset(ones_mean[:, :], 1.0 / D).then_inc(consts_set, 1)
            pool.memset(eps[:, :], EPS).then_inc(consts_set, 1)
            with pool.Fori(0, KD * NB // 2) as m:
                for q in range(4):
                    pool.wait_ge(w_hi_done, 4 * m + (q + 1))
                    pool.tensor_tensor(w_lo[:, q, :], w_raw[:, q % 2, :], w_hi[:, q, :].bitcast(F32),
                                       ALU.subtract).then_inc(w_lo_done, 1)

        @block.scalar
        def _(act):
            act.wait_ge(consts_set, 2)

            def split_w(n, half, j):
                q = 2 * (j % 2) + half
                act.wait_ge(w_loaded[half], n * 16 + 16)
                wait_at_least(act, prod_done if half else w_half_read, n - 1)
                act.activation(w_hi[:, q, :], w_raw[:, half, :], ACT.Copy).then_inc(w_hi_done, 1)

            def split_a(b):
                act.wait_ge(a_loaded, b * 16 + 16)
                for g in range(KH):
                    if g < KH - 1:
                        wait_at_least(act, a_read, b * (KH - 1) + (g + 2 - KH))
                    else:
                        wait_at_least(act, prod_done, b * KD)
                    act.activation(a_hi[:, 2 * g:2 * g + 2, :], a_raw[:, 2 * g:2 * g + 2, :], ACT.Copy).then_inc(a_hi_done, 1)

            def block_work(b, more):
                for j in range(KD):
                    if more or j < KD - 1:
                        split_w(b * KD + (j + 1), 0, j + 1)
                        split_w(b * KD + (j + 1), 1, j + 1)
                    if more and j == KD - 1:
                        split_a(b + 1)
                    if j == 0:
                        wait_at_least(act, x2_done, b)
                    act.wait_ge(prod_done, b * KD + (j + 1))
                    act.activation(out[:, j, :], prod_ps[:, j % 4, 0:TB], ACT.Copy).then_inc(bank_read, 1)
                act.wait_ge(bank_read, b * KD + KD)
                act.activation(sq[:, :, :], out[:, :, :], ACT.Square).then_inc(squares_done, 1)
                act.wait_ge(means_done, b + 1)
                act.activation(ssum[:, :], mean_ps[:, 0:TB], ACT.Sqrt, bias=eps[:, 0:1]).then_inc(roots_done, 1)

            split_w(0, 0, 0)
            split_w(0, 1, 0)
            split_a(0)
            block_work(0, True)
            with act.Fori(1, NB - 1) as b:
                block_work(b, True)
            block_work(NB - 1, False)

        @block.tensor
        def _(pe):
            pe.wait_ge(consts_set, 2)

            def mean(b):
                pe.wait_ge(sums_done, b + 1)
                pe.matmul(mean_ps[:, 0:TB], ones_mean[:, :], ssum[:, :], start=True, stop=True).then_inc(means_done, 1)

            def block_products(b):
                for j in range(KD):
                    if j == 1 and not isinstance(b, int):
                        mean(b - 1)
                    wait_at_least(pe, bank_read, b * KD + (j - 3))
                    for k in range(KF):
                        if k % KH == 0:
                            pe.wait_ge(w_lo_done, b * (2 * KD) + (2 * j + k // KH + 1))
                        if j == 0 and k % 2 == 0:
                            pe.wait_ge(a_lo_done, b * KH + (k // 2 + 1))
                        q = 2 * (j % 2) + k // KH
                        w = slice(k % KH * P, (k % KH + 1) * P)
                        mm = hi_lo_products(pe, prod_ps[:, j % 4, 0:TB], w_hi[:, q, w], w_lo[:, q, w],
                                            a_hi[:, k, :], a_lo[:, k, :], k == 0, k == KF - 1)
                        if k == KH - 1:
                            mm.then_inc(w_half_read, 1)
                        if j == KD - 1 and k % 2 and k < KF - 1:
                            mm.then_inc(a_read, 1)
                    mm.then_inc(prod_done, 1)

            block_products(0)
            with pe.Fori(1, NB) as b:
                block_products(b)
            mean(NB - 1)

        @block.vector
        def _(dve):
            dve.wait_ge(gain_loaded, 16)

            def split_a(b):
                for g in range(KH):
                    pair = slice(2 * g, 2 * g + 2)
                    dve.wait_ge(a_hi_done, b * KH + (g + 1))
                    dve.tensor_tensor(a_lo[:, pair, :], a_raw[:, pair, :], a_hi[:, pair, :].bitcast(F32),
                                      ALU.subtract).then_inc(a_lo_done, 1)

            def norm(b):
                dve.wait_ge(squares_done, b + 1)
                dve.tensor_reduce(ssum[:, :], sq[:, :, :].rearrange("p k t -> p t k"), AX_X, ALU.add).then_inc(sums_done, 1)
                dve.wait_ge(roots_done, b + 1)
                dve.reciprocal(rstd[:, :], ssum[:, :]).then_inc(recips_done, 1)
                dve.wait_ge(recips_done, b + 1)
                for k in range(KD):
                    m = dve.scalar_tensor_tensor(out[:, k, :], out[:, k, :], gain[:, k:k + 1], rstd[:, :],
                                                 ALU.mult, ALU.mult)
                m.then_inc(scaled_done, 1)
                dve.wait_ge(x_loaded, b * 16 + 16)
                dve.wait_ge(scaled_done, b + 1)
                dve.tensor_tensor(x[:, :, :], x[:, :, :], out[:, :, :], ALU.add).then_inc(x2_done, 1)

            split_a(0)
            with dve.Fori(0, NB - 1) as b:
                split_a(b + 1)
                norm(b)
            norm(NB - 1)


def embedding_gate(nc, t):
    with ExitStack() as ctx:
        sbuf, psum, sem = allocators(nc, ctx)
        w_raw = (sbuf("pf_wp", [P, 2, KP * P], F32), sbuf("pf_wg", [P, 2, KD * P], F32))
        wg_hi = sbuf("pf_wghi", [P, KD, KD * P], F32R)
        wg_lo = sbuf("pf_wglo", [P, KD, KD * P], F32R)
        wp_hi = sbuf("pf_wphi", [P, KD, KP * P], F32R)
        wp_lo = sbuf("pf_wplo", [P, KD, KP * P], F32R)
        x = sbuf("pf_x", [P, 2, KD, TB], F32)
        x_hi = sbuf("pf_xhi", [P, KD, TB], F32R)
        x_lo = sbuf("pf_xlo", [P, KD, TB], F32R)
        p_raw = sbuf("pf_p", [P, KP, TB], F32)
        p_hi = sbuf("pf_phi", [P, KP, TB], F32R)
        p_lo = sbuf("pf_plo", [P, KP, TB], F32R)
        gated = sbuf("pf_gated", [P, 2, KD, TB], F32)
        sq = sbuf("pf_sq", [P, KD, TB], F32)
        ssum = sbuf("pf_ssum", [P, TB], F32)
        rstd = sbuf("pf_rstd", [P, TB], F32)
        gain = sbuf("pf_gain", [P, KD], F32)
        eps = sbuf("pf_eps", [P, 1], F32)
        ones_mean = sbuf("pf_ones", [P, P], F32)
        proj_ps = psum("pf_proj", [P, 4, 512], F32)
        gate_ps = psum("pf_gate", [P, 2, 512], F32)
        mean_ps = psum("pf_mean", [P, 512], F32)
        gain_loaded = sem("pf_gain_loaded")
        consts_set = sem("pf_consts_set")
        w_loaded = [[sem(f"pf_w_loaded{kind}{par}") for par in range(2)] for kind in range(2)]
        w_hi_done = sem("pf_w_hi_done")
        w_lo_done = sem("pf_w_lo_done")
        x_loaded = (sem("pf_x_loaded0"), sem("pf_x_loaded1"))
        x_hi_done = sem("pf_x_hi_done")
        x_lo_even_done = sem("pf_x_lo_even_done")
        x_lo_odd_done = sem("pf_x_lo_odd_done")
        x_read = sem("pf_x_read")
        p_loaded = sem("pf_p_loaded")
        p_hi_done = sem("pf_p_hi_done")
        p_lo_done = sem("pf_p_lo_done")
        proj_done = sem("pf_proj_done")
        gate_done = sem("pf_gate_done")
        sigmoids_done = sem("pf_sigmoids_done")
        gated_done = sem("pf_gated_done")
        squares_done = sem("pf_squares_done")
        sums_done = sem("pf_sums_done")
        means_done = sem("pf_means_done")
        roots_done = sem("pf_roots_done")
        recips_done = sem("pf_recips_done")
        scaled_done = sem("pf_scaled_done")
        y_done = sem("pf_y_done")
        stored = (sem("pf_stored0"), sem("pf_stored1"))
        block = ctx.enter_context(nc.Block())
        WEIGHTS = ((wp_hi, wp_lo), (wg_hi, wg_lo))

        AHEAD = 4

        @block.sync
        def _(sp):
            sp.dma_start(gain[:, :], t["g_ple"]).then_inc(gain_loaded, 16)

            def load_w(j, kind):
                wait_at_least(sp, w_lo_done, 2 * (j - 2) + kind + 1)
                src = t["w_ple_gate" if kind else "w_ple_proj"]
                sp.dma_start(w_raw[kind][:, j % 2, :], src[j]).then_inc(w_loaded[kind][j % 2], 16)

            def load_p(b):
                wait_at_least(sp, p_lo_done, b)
                sp.dma_start(p_raw[:, :, :], t["pT"][b]).then_inc(p_loaded, 16)

            def load_x(b, par):
                sp.dma_start(x[:, par], t["x2"][b]).then_inc(x_loaded[par], 16)

            load_p(0)
            load_x(0, 0)
            for j in range(KD):
                load_w(j, 0)
                load_w(j, 1)
            load_p(1)
            load_x(1, 1)
            for b in range(NB):
                par = b % 2
                if b < NB - 2:
                    load_p(b + 2)
                sp.wait_ge(y_done, b + 1)
                sp.dma_start(t["y"][b], x[:, par]).then_inc(stored[par], 16)
                if b < NB - 2:
                    sp.wait_ge(stored[par], landed(b, par))
                    load_x(b + 2, par)
            for par in range(2):
                sp.wait_ge(stored[par], 16 * ((NB + 1 - par) // 2))

        @block.gpsimd
        def _(pool):
            pool.memset(ones_mean[:, :], 1.0 / D).then_inc(consts_set, 1)
            pool.memset(eps[:, :], EPS).then_inc(consts_set, 1)

            def split_block(b, par):
                pool.wait_ge(p_hi_done, b + 1)
                pool.tensor_tensor(p_lo[:, :, :], p_raw[:, :, :], p_hi[:, :, :].bitcast(F32), ALU.subtract).then_inc(p_lo_done, 1)
                for k in range(0, KD, 2):
                    pool.wait_ge(x_hi_done, b * KD + (k + 1))
                    pool.tensor_tensor(x_lo[:, k, :], x[:, par, k, :], x_hi[:, k, :].bitcast(F32),
                                       ALU.subtract).then_inc(x_lo_even_done, 1)

            def add(b, par):
                pool.wait_ge(scaled_done, b + 1)
                pool.wait_ge(x_lo_odd_done, b * (KD // 2) + KD // 2)
                pool.tensor_tensor(x[:, par], x[:, par], gated[:, par], ALU.add).then_inc(y_done, 1)

            split_block(0, 0)
            with pool.Fori(0, NB // 2) as j:
                split_block(2 * j + 1, 1)
                add(2 * j, 0)
                split_block(2 * j + 2, 0)
                add(2 * j + 1, 1)
            add(NB - 1, 0)

        @block.scalar
        def _(act):
            act.wait_ge(consts_set, 2)

            def split_block(b, par):
                act.wait_ge(p_loaded, b * 16 + 16)
                wait_at_least(act, proj_done, b * KD)
                act.activation(p_hi[:, :, :], p_raw[:, :, :], ACT.Copy).then_inc(p_hi_done, 1)
                act.wait_ge(x_loaded[par], landed(b, par))
                for k in range(KD):
                    if k < KD - 1:
                        wait_at_least(act, x_read, b * (KD - 1) + (k + 2 - KD))
                    else:
                        wait_at_least(act, gate_done, b * KD)
                    act.activation(x_hi[:, k, :], x[:, par, k, :], ACT.Copy).then_inc(x_hi_done, 1)

            def block_work(b, par, more):
                if not isinstance(b, int) or b >= 2:
                    act.wait_ge(y_done, b - 1)
                for j in range(KD):
                    if isinstance(b, int) and b == 0 and j + AHEAD < KD:
                        split_w(j + AHEAD)
                    if j == KD - 1 and more:
                        split_block(b + 1, 1 - par)
                    act.wait_ge(gate_done, b * KD + (j + 1))
                    act.activation(gated[:, par, j, :], gate_ps[:, j % 2, 0:TB], ACT.Sigmoid).then_inc(sigmoids_done, 1)
                act.wait_ge(gated_done, b * KD + KD)
                act.activation(sq[:, :, :], gated[:, par], ACT.Square).then_inc(squares_done, 1)
                act.wait_ge(means_done, b + 1)
                act.activation(ssum[:, :], mean_ps[:, 0:TB], ACT.Sqrt, bias=eps[:, 0:1]).then_inc(roots_done, 1)

            def split_w(j):
                for kind, (hi, _) in enumerate(WEIGHTS):
                    act.wait_ge(w_loaded[kind][j % 2], 16 * (j // 2 + 1))
                    act.activation(hi[:, j, :], w_raw[kind][:, j % 2, :], ACT.Copy).then_inc(w_hi_done, 1)

            split_block(0, 0)
            for j in range(AHEAD):
                split_w(j)
            block_work(0, 0, True)
            with act.Fori(1, NB // 2) as j:
                block_work(2 * j - 1, 1, True)
                block_work(2 * j, 0, True)
            block_work(NB - 2, 1, True)
            block_work(NB - 1, 0, False)

        @block.tensor
        def _(pe):
            pe.wait_ge(consts_set, 2)
            LEAD = 2

            def mean(b):
                pe.wait_ge(sums_done, b + 1)
                pe.matmul(mean_ps[:, 0:TB], ones_mean[:, :], ssum[:, :], start=True, stop=True).then_inc(means_done, 1)

            def project(b, j, first):
                if first:
                    pe.wait_ge(w_lo_done, 2 * j + 1)
                wait_at_least(pe, gated_done, b * KD + (j - 3))
                for k in range(KP):
                    w = slice(k * P, (k + 1) * P)
                    mm = hi_lo_products(pe, proj_ps[:, j % 4, 0:TB], wp_hi[:, j, w], wp_lo[:, j, w],
                                        p_hi[:, k, :], p_lo[:, k, :], k == 0, k == KP - 1)
                mm.then_inc(proj_done, 1)

            def block_products(b, par, first):
                pe.wait_ge(p_lo_done, b + 1)
                for j in range(LEAD):
                    project(b, j, first)
                for j in range(KD):
                    if j == 1 and not first:
                        mean(b - 1)
                    if j + LEAD < KD:
                        project(b, j + LEAD, first)
                    if first:
                        pe.wait_ge(w_lo_done, 2 * j + 2)
                    wait_at_least(pe, sigmoids_done, b * KD + (j - 1))
                    for k in range(KD):
                        if j == 0:
                            pe.wait_ge(x_lo_odd_done if k % 2 else x_lo_even_done, b * (KD // 2) + (k // 2 + 1))
                        w = slice(k * P, (k + 1) * P)
                        mm = hi_lo_products(pe, gate_ps[:, j % 2, 0:TB], wg_hi[:, j, w], wg_lo[:, j, w],
                                            x_hi[:, k, :], x_lo[:, k, :], k == 0, k == KD - 1)
                        if j == KD - 1 and k < KD - 1:
                            mm.then_inc(x_read, 1)
                    mm.then_inc(gate_done, 1)

            blocks(pe, block_products)
            mean(NB - 1)

        @block.vector
        def _(dve):
            dve.wait_ge(gain_loaded, 16)

            def split_x(b, par):
                for k in range(1, KD, 2):
                    dve.wait_ge(x_hi_done, b * KD + (k + 1))
                    dve.tensor_tensor(x_lo[:, k, :], x[:, par, k, :], x_hi[:, k, :].bitcast(F32),
                                      ALU.subtract).then_inc(x_lo_odd_done, 1)

            def split_w(j):
                for kind, (hi, lo) in enumerate(WEIGHTS):
                    dve.wait_ge(w_hi_done, 2 * j + (kind + 1))
                    dve.tensor_tensor(lo[:, j, :], w_raw[kind][:, j % 2, :], hi[:, j, :].bitcast(F32),
                                      ALU.subtract).then_inc(w_lo_done, 1)

            def block_work(b, par, more):
                for j in range(KD):
                    if isinstance(b, int) and b == 0 and j + AHEAD < KD:
                        split_w(j + AHEAD)
                    if j == KD - 1 and more:
                        split_x(b + 1, 1 - par)
                    dve.wait_ge(proj_done, b * KD + (j + 1))
                    dve.wait_ge(sigmoids_done, b * KD + (j + 1))
                    dve.tensor_tensor(gated[:, par, j, :], proj_ps[:, j % 4, 0:TB], gated[:, par, j, :],
                                      ALU.mult).then_inc(gated_done, 1)
                dve.wait_ge(squares_done, b + 1)
                dve.tensor_reduce(ssum[:, :], sq[:, :, :].rearrange("p k t -> p t k"), AX_X, ALU.add).then_inc(sums_done, 1)
                dve.wait_ge(roots_done, b + 1)
                dve.reciprocal(rstd[:, :], ssum[:, :]).then_inc(recips_done, 1)
                dve.wait_ge(recips_done, b + 1)
                for k in range(KD):
                    m = dve.scalar_tensor_tensor(gated[:, par, k, :], gated[:, par, k, :], gain[:, k:k + 1],
                                                 rstd[:, :], ALU.mult, ALU.mult)
                m.then_inc(scaled_done, 1)

            split_x(0, 0)
            for j in range(AHEAD):
                split_w(j)
            block_work(0, 0, True)
            with dve.Fori(1, NB // 2) as j:
                block_work(2 * j - 1, 1, True)
                block_work(2 * j, 0, True)
            block_work(NB - 2, 1, True)
            block_work(NB - 1, 0, False)


def wait_for_caches(nc, shifted):
    with nc.Block() as block:

        @block.sync
        def _(sp):
            sp.wait_ge(shifted, 16 * 2 * NSAMP)


SCRATCH = {"dn": (12, P, S), "dn_samp": (12, P, NSAMP), "z": (4, P, TOK), "at4": (12, P, S), "at16": (12, P, S),
           "ba": (36, TOK), "bias_flat": (len(DILS), AH, FLAT), "U": (len(DILS), S, UROW), "mix": (KD, P, TOK),
           "x1": (NB, P, KD, TB), "h2": (NB, P, KD, TB), "a": (KF, P, TOK), "x2": (NB, P, KD, TB)}

RESULTS = {"y": (NB, P, KD, TB), "at": (12, P, TOK), "conv_tail": (12, P, 3), "conv_samp": (12, P, NSAMP, 3),
           "delta": (HEADS, P, P), "new_state": (NSAMP, HEADS, P, P),
           "new_cache_k": (NSAMP, PAST, AH * HD), "new_cache_v": (NSAMP, PAST, AH * HD)}


def build(nc, t):
    for name, shape in SCRATCH.items():
        t[name] = nc.dram_tensor("scratch_" + name, list(shape), F32, kind="Internal").ap()
    with nc.semaphore("caches_shifted") as shifted:
        norm_and_input_projection(nc, t)
        bias_and_delta_samples(nc, t)
        delta_and_attention(nc, t)
        merge_and_attend_samples(nc, t)
        output_projection(nc, t)
        gate_and_up(nc, t, shifted)
        down_projection(nc, t)
        embedding_gate(nc, t)
        wait_for_caches(nc, shifted)


def tiles_of(w, k, n):
    return np.ascontiguousarray(w.reshape(k, P, n, P).transpose(2, 1, 0, 3)).reshape(n, P, k * P)


def columns_of(g, k):
    return np.ascontiguousarray(g.reshape(k, P).T)


def blocks_of(prompt, sample, k):
    x = np.zeros((TOK, k * P), np.float32)
    x[:S] = prompt
    x[S:S + NSAMP] = sample
    return np.ascontiguousarray(x.reshape(NB, TB, k, P).transpose(0, 3, 2, 1)).reshape(NB, P, k, TB)


def layouts(i):
    dn_cols = (N_DN + N_Z) * P
    w_in = np.zeros((D, (NT + 1) * P), np.float32)
    w_in[:, :dn_cols] = i["w_in"][0][:, :dn_cols]
    w_in[:, dn_cols:NT * P] = i["w_in"][0][:, dn_cols + 2 * HEADS:]
    w_in[:, NT * P:NT * P + HEADS] = i["w_in"][0][:, dn_cols:dn_cols + HEADS]
    w_in[:, NT * P + 32:NT * P + 32 + HEADS] = i["w_in"][0][:, dn_cols + HEADS:dn_cols + 2 * HEADS]
    gate_up = i["w_gate_up"][0].reshape(D, 2, KF, P).transpose(0, 2, 1, 3).reshape(D, 2 * FF)
    return {
        "xT": blocks_of(i["x_prompt"][0], i["x_sample"][:, 0], KD),
        "pT": blocks_of(i["p_prompt"][0, 0], i["p_sample"][0, :, 0], KP),
        "w_in": tiles_of(w_in, KD, NT + 1),
        "conv_w": np.ascontiguousarray(i["conv_w"][0].reshape(4, N_DN, P).transpose(2, 1, 0)).reshape(P, 4 * N_DN),
        "cache_conv": np.ascontiguousarray(i["cache_conv"][0].reshape(NSAMP, 3, N_DN, P).transpose(2, 3, 0, 1)),
        "w_out": tiles_of(i["w_out"][0], KD, KD),
        "w_gate_up": tiles_of(gate_up, KD, 2 * KF),
        "w_down": tiles_of(i["w_down"][0], KF, KD),
        "w_ple_gate": tiles_of(i["w_ple_gate"][0], KD, KD),
        "w_ple_proj": tiles_of(i["w_ple_proj"][0], KP, KD),
        "g_pre_mix": columns_of(i["g_pre_mix"][0], KD),
        "g_post_mix": columns_of(i["g_post_mix"][0], KD),
        "g_pre_ffn": columns_of(i["g_pre_ffn"][0], KD),
        "g_post_ffn": columns_of(i["g_post_ffn"][0], KD),
        "g_ple": columns_of(i["g_ple"][0], KD),
        "g_dn_out": i["g_dn_out"][0].reshape(P, 1),
        "a_log": i["a_log"][0],
        "dt_bias": i["dt_bias"][0],
        "rel_bias": i["rel_bias"],
        "state": i["state_delta"][0],
        "cache_k": i["cache_win_k"][0].reshape(NSAMP, PAST, AH * HD),
        "cache_v": i["cache_win_v"][0].reshape(NSAMP, PAST, AH * HD),
        "consts": constant_tiles(),
        "buckets": bucket_tiles(),
        "head_mask": head_mask(),
    }


def kernel(**inputs):
    import concourse.bacc as bacc
    from concourse.bass_utils import run_bass_kernel_spmd

    nc = bacc.Bacc("TRN2", target_bir_lowering=False, num_devices=1)
    arrays, t = {}, {}
    for name, a in layouts({n: np.asarray(a) for n, a in inputs.items()}).items():
        arrays["in_" + name] = np.ascontiguousarray(a)
        t[name] = nc.dram_tensor("in_" + name, list(a.shape), F32, kind="ExternalInput").ap()
    for name, shape in RESULTS.items():
        t[name] = nc.dram_tensor("out_" + name, list(shape), F32, kind="ExternalOutput").ap()
    build(nc, t)
    result = run_bass_kernel_spmd(nc, [arrays], core_ids=[0]).results[0]
    r = {name: np.asarray(result["out_" + name]).reshape(shape) for name, shape in RESULTS.items()}

    y = r["y"].transpose(0, 3, 2, 1).reshape(TOK, D)
    k_prompt, v_prompt = (r["at"][4 * n:4 * n + 4, :, 0:S].reshape(AH * HD, S).T.reshape(1, 1, S, AH, HD) for n in (1, 2))
    channels = N_DN * P
    return (y[:S].reshape(1, S, D), y[S:S + NSAMP].reshape(NSAMP, 1, D),
            r["conv_tail"].reshape(channels, 3).T.reshape(1, 1, 3, channels),
            r["delta"].reshape(1, 1, HEADS, DK, DK), k_prompt, v_prompt,
            r["conv_samp"].transpose(2, 3, 0, 1).reshape(1, NSAMP, 3, channels),
            r["new_state"].reshape(1, NSAMP, HEADS, DK, DK),
            r["new_cache_k"].reshape(1, NSAMP, PAST, AH, HD), r["new_cache_v"].reshape(1, NSAMP, PAST, AH, HD))
```
